# Optimizing a Trainium2 kernel written in Bass

```python
import math, functools
import jax, jax.numpy as jnp
from jax import lax
import numpy as np

D_MODEL = 1024
BATCH = 1
SEQ = 1024
DEPTH = 1
DEC_BATCH = 8
DEC_SEQ = 8
PAST_LEN = 1024
PAGE_SIZE = 128

HEAD_DIM = 64
SSD_HEADS = 8
SSD_GROUPS = 2
SSD_STATE = 128
SSD_CONV = 4
SSD_CHUNK = 128
NSA_HEADS = 8
NSA_KV_HEADS = 2
CMP_BLOCK = 32
CMP_STRIDE = 16
CMP_HIDDEN = 256
SLC_BLOCK = 64
SLC_TOPN = 16
WINDOW = 512
REL_BUCKETS = 32
REL_MAX_DIST = 128
MEM_TOKENS = 256
MEM_HEADS = 4
D_FF = 2816
Q_BLOCK = 128
EPS = 1e-6
NEG = -1e30

SSD_INNER = SSD_HEADS * HEAD_DIM
NSA_INNER = NSA_HEADS * HEAD_DIM
MIX_WIDTH = SSD_INNER + NSA_INNER
SSD_CONV_DIM = SSD_INNER + 2 * SSD_GROUPS * SSD_STATE
KV_WIDTH = NSA_KV_HEADS * HEAD_DIM
NSA_GROUP = NSA_HEADS // NSA_KV_HEADS
MEM_INNER = MEM_HEADS * HEAD_DIM
IN_SPLITS = (SSD_INNER, SSD_CONV_DIM, SSD_HEADS, NSA_INNER, KV_WIDTH, KV_WIDTH, KV_WIDTH, KV_WIDTH, KV_WIDTH, KV_WIDTH, 3 * NSA_HEADS)
IN_COLS = sum(IN_SPLITS)

kernel_name = 'hymba_ssd_nsa_macaron_decode_step'

def rmsnorm(x, g):
    xf = x.astype(jnp.float32)
    xf = xf * lax.rsqrt(jnp.mean(xf * xf, axis=-1, keepdims=True) + EPS)
    return (xf * g.astype(jnp.float32)).astype(x.dtype)

def masked_softmax(logits, mask, axis):
    lf = jnp.where(mask, logits.astype(jnp.float32), NEG)
    m = jnp.max(lf, axis=axis, keepdims=True)
    e = jnp.where(mask, jnp.exp(lf - m), 0.0)
    return e / jnp.maximum(jnp.sum(e, axis=axis, keepdims=True), 1e-30)

def swiglu_ffn(x, g, w_in, w_out):
    h = rmsnorm(x, g) @ w_in
    gate, up = jnp.split(h, 2, axis=-1)
    return (jax.nn.silu(gate) * up) @ w_out

def t5_bucket(dist):
    n = jnp.maximum(dist, 0)
    exact = REL_BUCKETS // 2
    nf = jnp.maximum(n, exact).astype(jnp.float32)
    large = exact + (jnp.log(nf / exact) / math.log(REL_MAX_DIST / exact) * (REL_BUCKETS - exact)).astype(jnp.int32)
    return jnp.where(n < exact, n, jnp.minimum(large, REL_BUCKETS - 1))

def rel_bias_2d(rel_bias, dist):
    b = rel_bias[t5_bucket(dist)]
    return jnp.moveaxis(b, -1, 0).reshape(NSA_KV_HEADS, NSA_GROUP, dist.shape[0], dist.shape[1])

def project_mix(x, g, w_in):
    h = rmsnorm(x, g) @ w_in
    parts = []
    start = 0
    for size in IN_SPLITS:
        parts.append(h[..., start:start + size])
        start += size
    return parts

def causal_dwconv(xpad, w, b):
    out = lax.conv_general_dilated(xpad, w[:, None, :], (1,), 'VALID',
                                   dimension_numbers=('NWC', 'WIO', 'NWC'),
                                   feature_group_count=xpad.shape[-1])
    return out + b

def ssd_scan(x, dt, a, bm, cm, h0):
    bsz, L, H, P = x.shape
    G, N = bm.shape[2], bm.shape[3]
    R = H // G
    Q = SSD_CHUNK if L % SSD_CHUNK == 0 else L
    nc = L // Q
    x = x.reshape(bsz, nc, Q, G, R, P)
    dt = dt.reshape(bsz, nc, Q, G, R)
    bm = bm.reshape(bsz, nc, Q, G, N)
    cm = cm.reshape(bsz, nc, Q, G, N)
    acs = jnp.cumsum(dt.astype(jnp.float32) * a.reshape(G, R).astype(jnp.float32), axis=2)
    causal = jnp.tril(jnp.ones((Q, Q), bool))[:, :, None, None]
    seg = acs[:, :, :, None] - acs[:, :, None, :]
    decay = jnp.where(causal, jnp.exp(jnp.where(causal, seg, 0.0)), 0.0).astype(x.dtype)
    cb = jnp.einsum('bctgn,bcsgn->bctsg', cm, bm)
    w = cb[..., None] * decay * dt[:, :, None]
    y_intra = jnp.einsum('bctsgr,bcsgrp->bctgrp', w, x)
    to_end = jnp.exp(acs[:, :, -1:] - acs).astype(x.dtype) * dt
    states = jnp.einsum('bcsgn,bcsgr,bcsgrp->bcgrpn', bm, to_end, x)
    chunk_decay = jnp.exp(acs[:, :, -1]).astype(x.dtype)

    def step(h, inp):
        st, cd = inp
        return h * cd[..., None, None] + st, h

    h_final, h_prev = lax.scan(step, h0.reshape(bsz, G, R, P, N),
                               (jnp.moveaxis(states, 1, 0), jnp.moveaxis(chunk_decay, 1, 0)))
    h_prev = jnp.moveaxis(h_prev, 0, 1)
    y_inter = jnp.einsum('bctgn,bctgr,bcgrpn->bctgrp', cm, jnp.exp(acs).astype(x.dtype), h_prev)
    return (y_intra + y_inter).reshape(bsz, L, H, P), h_final.reshape(bsz, H, P, N)

def ssd_branch(z, xbc, dt_raw, conv_buf, h0, conv_w, conv_b, dt_bias, a_log, d_skip, norm_g):
    bsz, L, _ = xbc.shape
    xpad = jnp.concatenate([conv_buf, xbc], axis=1)
    new_conv = xpad[:, L:]
    xc = jax.nn.silu(causal_dwconv(xpad, conv_w, conv_b))
    xs = xc[..., :SSD_INNER].reshape(bsz, L, SSD_HEADS, HEAD_DIM)
    bm = xc[..., SSD_INNER:SSD_INNER + SSD_GROUPS * SSD_STATE].reshape(bsz, L, SSD_GROUPS, SSD_STATE)
    cm = xc[..., SSD_INNER + SSD_GROUPS * SSD_STATE:].reshape(bsz, L, SSD_GROUPS, SSD_STATE)
    dt = jax.nn.softplus(dt_raw + dt_bias)
    a = -jnp.exp(a_log)
    y, h = ssd_scan(xs, dt, a, bm, cm, h0)
    y = y + d_skip[:, None] * xs
    y = rmsnorm(y.reshape(bsz, L, SSD_INNER) * jax.nn.silu(z), norm_g)
    return y, h, new_conv

def compress(rows, pe, w1, w2):
    bsz, L = rows.shape[:2]
    r = CMP_BLOCK // CMP_STRIDE
    nch = L // CMP_STRIDE
    n_cmp = nch - r + 1
    chunks = rows[:, :nch * CMP_STRIDE].reshape(bsz, nch, CMP_STRIDE, NSA_KV_HEADS, HEAD_DIM)
    pe_r = pe.reshape(r, CMP_STRIDE, HEAD_DIM)
    w1_r = w1.reshape(r, CMP_STRIDE, HEAD_DIM, CMP_HIDDEN)
    hid = jnp.einsum('bnsgd,sdh->bngh', chunks[:, :n_cmp] + pe_r[0][:, None, :], w1_r[0])
    for j in range(1, r):
        hid = hid + jnp.einsum('bnsgd,sdh->bngh', chunks[:, j:j + n_cmp] + pe_r[j][:, None, :], w1_r[j])
    return jax.nn.silu(hid) @ w2

def nsa_core(q, q_pos, kc, vc, ks_blk, vs_blk, kw, vw, kw_pos, gates, rel_bias):
    bsz, tq = q.shape[:2]
    G = NSA_KV_HEADS
    scale = HEAD_DIM ** -0.5
    n_cmp = kc.shape[1]
    c_start = jnp.arange(n_cmp) * CMP_STRIDE
    c_end = c_start + CMP_BLOCK - 1
    dist_c = q_pos[:, None] - c_end[None, :]
    logit_c = jnp.einsum('bqgrd,bkgd->bgrqk', q, kc) * scale + rel_bias_2d(rel_bias, dist_c)
    p_c = masked_softmax(logit_c, dist_c >= 0, axis=-1)
    o_cmp = jnp.einsum('bgrqk,bkgd->bqgrd', p_c.astype(vc.dtype), vc)
    n_slc = ks_blk.shape[1]
    s_start = jnp.arange(n_slc) * SLC_BLOCK
    overlap = ((c_start[:, None] < s_start[None, :] + SLC_BLOCK) & (c_end[:, None] >= s_start[None, :])).astype(jnp.float32)
    imp = jnp.einsum('bgrqk,ks->bgqs', p_c, overlap)
    q_blk = q_pos // SLC_BLOCK
    blk = jnp.arange(n_slc)[None, :]
    forced = (blk == 0) | (blk == q_blk[:, None]) | (blk == q_blk[:, None] - 1)
    valid = s_start[None, :] <= q_pos[:, None]
    imp = jnp.where(forced, jnp.inf, imp)
    imp = jnp.where(valid, imp, -jnp.inf)
    _, idx = lax.top_k(imp, min(SLC_TOPN, n_slc))
    bi = jnp.arange(bsz)[:, None, None, None]
    gi = jnp.arange(G)[None, :, None, None]
    k_sel = jnp.moveaxis(ks_blk, 3, 1)[bi, gi, idx]
    v_sel = jnp.moveaxis(vs_blk, 3, 1)[bi, gi, idx]
    pos_sel = idx[..., None] * SLC_BLOCK + jnp.arange(SLC_BLOCK)
    dist_s = q_pos[:, None, None] - pos_sel
    tbl = rel_bias.reshape(REL_BUCKETS, G, NSA_GROUP)
    bias_s = tbl[t5_bucket(dist_s), gi[..., None]]
    logit_s = jnp.einsum('bqgrd,bgqkpd->bgqkpr', q, k_sel) * scale + bias_s
    kk = idx.shape[-1] * SLC_BLOCK
    p_s = masked_softmax(logit_s.reshape(bsz, G, tq, kk, NSA_GROUP), (dist_s >= 0).reshape(bsz, G, tq, kk, 1), axis=3)
    o_slc = jnp.einsum('bgqnr,bgqnd->bqgrd', p_s.astype(vs_blk.dtype), v_sel.reshape(bsz, G, tq, kk, HEAD_DIM))
    dist_w = q_pos[:, None] - kw_pos[None, :]
    mask_w = (dist_w >= 0) & (dist_w < WINDOW) & (kw_pos[None, :] >= 0)
    logit_w = jnp.einsum('bqgrd,bkgd->bgrqk', q, kw) * scale + rel_bias_2d(rel_bias, dist_w)
    p_w = masked_softmax(logit_w, mask_w, axis=-1)
    o_win = jnp.einsum('bgrqk,bkgd->bqgrd', p_w.astype(vw.dtype), vw)
    return gates[..., 0:1] * o_cmp + gates[..., 1:2] * o_slc + gates[..., 2:3] * o_win

def nsa_prompt(qh, kv_c, kv_s, kv_w, gates, cmp_params, rel_bias):
    bsz, L = qh.shape[:2]
    pe_k, w1_k, w2_k, pe_v, w1_v, w2_v = cmp_params
    kc = compress(kv_c[:, :, 0], pe_k, w1_k, w2_k)
    vc = compress(kv_c[:, :, 1], pe_v, w1_v, w2_v)
    n_slc = L // SLC_BLOCK
    ks_blk = kv_s[:, :n_slc * SLC_BLOCK, 0].reshape(bsz, n_slc, SLC_BLOCK, NSA_KV_HEADS, HEAD_DIM)
    vs_blk = kv_s[:, :n_slc * SLC_BLOCK, 1].reshape(bsz, n_slc, SLC_BLOCK, NSA_KV_HEADS, HEAD_DIM)
    kv_wp = jnp.pad(kv_w, ((0, 0), (WINDOW, 0), (0, 0), (0, 0), (0, 0)))

    def block(i):
        s = i * Q_BLOCK
        q_b = lax.dynamic_slice_in_dim(qh, s, Q_BLOCK, axis=1)
        g_b = lax.dynamic_slice_in_dim(gates, s, Q_BLOCK, axis=1)
        w_b = lax.dynamic_slice_in_dim(kv_wp, s, Q_BLOCK + WINDOW, axis=1)
        q_pos = s + jnp.arange(Q_BLOCK)
        kw_pos = s - WINDOW + jnp.arange(Q_BLOCK + WINDOW)
        return nsa_core(q_b, q_pos, kc, vc, ks_blk, vs_blk, w_b[:, :, 0], w_b[:, :, 1], kw_pos, g_b, rel_bias)

    o = lax.map(block, jnp.arange(L // Q_BLOCK))
    o = jnp.moveaxis(o, 0, 1).reshape(bsz, L, NSA_INNER)
    return o, (kv_c, kv_s, kv_w[:, L - min(WINDOW, L):])

def nsa_sample(qh, kv_c, kv_s, kv_w, gates, cmp_params, rel_bias, pool_c, pool_s, win_buf, page_table):
    bsz, L = qh.shape[:2]
    pe_k, w1_k, w2_k, pe_v, w1_v, w2_v = cmp_params
    total = PAST_LEN + L
    past_c = pool_c[page_table].reshape(bsz, PAST_LEN, 2, NSA_KV_HEADS, HEAD_DIM)
    full_c = jnp.concatenate([past_c, kv_c], axis=1)
    kc = compress(full_c[:, :, 0], pe_k, w1_k, w2_k)
    vc = compress(full_c[:, :, 1], pe_v, w1_v, w2_v)
    n_slc = -(-total // SLC_BLOCK)
    past_s = pool_s[page_table].reshape(bsz, PAST_LEN, 2, NSA_KV_HEADS, HEAD_DIM)
    full_s = jnp.pad(jnp.concatenate([past_s, kv_s], axis=1),
                     ((0, 0), (0, n_slc * SLC_BLOCK - total), (0, 0), (0, 0), (0, 0)))
    ks_blk = full_s[:, :, 0].reshape(bsz, n_slc, SLC_BLOCK, NSA_KV_HEADS, HEAD_DIM)
    vs_blk = full_s[:, :, 1].reshape(bsz, n_slc, SLC_BLOCK, NSA_KV_HEADS, HEAD_DIM)
    w_kept = win_buf.shape[1]
    win = jnp.concatenate([win_buf, kv_w], axis=1)
    q_pos = PAST_LEN + jnp.arange(L)
    kw_pos = PAST_LEN - w_kept + jnp.arange(w_kept + L)
    o = nsa_core(qh, q_pos, kc, vc, ks_blk, vs_blk, win[:, :, 0], win[:, :, 1], kw_pos, gates, rel_bias)
    return o.reshape(bsz, L, NSA_INNER), (kv_c, kv_s, win[:, L:])

def mem_kv_proj(mem, g, w_kv):
    bsz, m, _ = mem.shape
    return (rmsnorm(mem, g) @ w_kv).reshape(bsz, m, 2, MEM_HEADS, HEAD_DIM)

def mem_attend(x, kv, g, w_q, w_o):
    bsz, L, _ = x.shape
    q = (rmsnorm(x, g) @ w_q).reshape(bsz, L, MEM_HEADS, HEAD_DIM)
    logits = jnp.einsum('blhd,bmhd->bhlm', q, kv[:, :, 0]) * (HEAD_DIM ** -0.5)
    p = jax.nn.softmax(logits.astype(jnp.float32), axis=-1).astype(x.dtype)
    o = jnp.einsum('bhlm,bmhd->blhd', p, kv[:, :, 1]).reshape(bsz, L, MEM_INNER)
    return o @ w_o

def trunk_layer(x, lw, conv_buf, h0, nsa_fn, mem_kv):
    bsz, L, _ = x.shape
    x = x + 0.5 * swiglu_ffn(x, lw['norm_ffn1'], lw['w_ffn1_in'], lw['w_ffn1_out'])
    z, xbc, dt_raw, q, kc, vc, ks, vs, kw, vw, g_logit = project_mix(x, lw['norm_mix'], lw['w_in'])
    y_ssd, h_new, conv_new = ssd_branch(z, xbc, dt_raw, conv_buf, h0, lw['conv_w'], lw['conv_b'],
                                        lw['dt_bias'], lw['a_log'], lw['d_skip'], lw['norm_ssd_out'])

    def rows(kt, vt):
        return jnp.stack([kt.reshape(bsz, L, NSA_KV_HEADS, HEAD_DIM), vt.reshape(bsz, L, NSA_KV_HEADS, HEAD_DIM)], axis=2)

    qh = q.reshape(bsz, L, NSA_KV_HEADS, NSA_GROUP, HEAD_DIM)
    gates = jax.nn.sigmoid(g_logit).reshape(bsz, L, NSA_KV_HEADS, NSA_GROUP, 3)
    o_nsa, nsa_state = nsa_fn(qh, rows(kc, vc), rows(ks, vs), rows(kw, vw), gates)
    y_nsa = rmsnorm(o_nsa, lw['norm_nsa_out'])
    x = x + jnp.concatenate([y_ssd, y_nsa], axis=-1) @ lw['w_out']
    x = x + mem_attend(x, mem_kv, lw['norm_mem_q'], lw['w_mem_q'], lw['w_mem_out'])
    x = x + 0.5 * swiglu_ffn(x, lw['norm_ffn2'], lw['w_ffn2_in'], lw['w_ffn2_out'])
    return x, h_new, conv_new, nsa_state

def setup_inputs(seed: int = 0) -> dict:
    key = jax.random.key(seed)
    keys = iter(jax.random.split(key, 64))

    def nrm(shape, scale):
        return scale * jax.random.normal(next(keys), shape, jnp.float32)

    def gain(shape):
        return 1.0 + 0.1 * jax.random.normal(next(keys), shape, jnp.float32)

    n_pages = PAST_LEN // PAGE_SIZE
    n_used = DEC_BATCH * n_pages
    n_pool = n_used + max(1, n_used // 4)
    win_kept = min(WINDOW, PAST_LEN)
    page_table = jax.random.permutation(next(keys), n_pool)[:n_used].reshape(DEC_BATCH, n_pages).astype(jnp.int32)
    dt0 = jnp.exp(jax.random.uniform(next(keys), (DEPTH, SSD_HEADS), jnp.float32, math.log(1e-3), math.log(1e-1)))
    dt_bias = dt0 + jnp.log(-jnp.expm1(-dt0))
    a_log = jnp.log(jax.random.uniform(next(keys), (DEPTH, SSD_HEADS), jnp.float32, 1.0, 16.0))
    return {
        'x_prompt': nrm((BATCH, SEQ, D_MODEL), 1.0),
        'x_sample': nrm((DEC_BATCH, DEC_SEQ, D_MODEL), 1.0),
        'cache_kv_cmp': nrm((DEPTH, n_pool, PAGE_SIZE, 2, NSA_KV_HEADS, HEAD_DIM), 1.0),
        'cache_kv_slc': nrm((DEPTH, n_pool, PAGE_SIZE, 2, NSA_KV_HEADS, HEAD_DIM), 1.0),
        'state_win_kv': nrm((DEPTH, DEC_BATCH, win_kept, 2, NSA_KV_HEADS, HEAD_DIM), 1.0),
        'state_ssd': nrm((DEPTH, DEC_BATCH, SSD_HEADS, HEAD_DIM, SSD_STATE), 0.5),
        'state_conv': nrm((DEPTH, DEC_BATCH, SSD_CONV - 1, SSD_CONV_DIM), 1.0),
        'cache_mem_kv': nrm((DEPTH, DEC_BATCH, MEM_TOKENS, 2, MEM_HEADS, HEAD_DIM), 1.0),
        'page_table': page_table,
        'mem_prompt': nrm((BATCH, MEM_TOKENS, D_MODEL), 1.0),
        'norm_ffn1': gain((DEPTH, D_MODEL)),
        'w_ffn1_in': nrm((DEPTH, D_MODEL, 2 * D_FF), D_MODEL ** -0.5),
        'w_ffn1_out': nrm((DEPTH, D_FF, D_MODEL), D_FF ** -0.5),
        'norm_mix': gain((DEPTH, D_MODEL)),
        'w_in': nrm((DEPTH, D_MODEL, IN_COLS), D_MODEL ** -0.5),
        'conv_w': nrm((DEPTH, SSD_CONV, SSD_CONV_DIM), SSD_CONV ** -0.5),
        'conv_b': nrm((DEPTH, SSD_CONV_DIM), 0.02),
        'dt_bias': dt_bias,
        'a_log': a_log,
        'd_skip': gain((DEPTH, SSD_HEADS)),
        'norm_ssd_out': gain((DEPTH, SSD_INNER)),
        'cmp_pos_k': nrm((DEPTH, CMP_BLOCK, HEAD_DIM), 0.5),
        'cmp_w1_k': nrm((DEPTH, CMP_BLOCK * HEAD_DIM, CMP_HIDDEN), (CMP_BLOCK * HEAD_DIM) ** -0.5),
        'cmp_w2_k': nrm((DEPTH, CMP_HIDDEN, HEAD_DIM), CMP_HIDDEN ** -0.5),
        'cmp_pos_v': nrm((DEPTH, CMP_BLOCK, HEAD_DIM), 0.5),
        'cmp_w1_v': nrm((DEPTH, CMP_BLOCK * HEAD_DIM, CMP_HIDDEN), (CMP_BLOCK * HEAD_DIM) ** -0.5),
        'cmp_w2_v': nrm((DEPTH, CMP_HIDDEN, HEAD_DIM), CMP_HIDDEN ** -0.5),
        'norm_nsa_out': gain((DEPTH, NSA_INNER)),
        'w_out': nrm((DEPTH, MIX_WIDTH, D_MODEL), MIX_WIDTH ** -0.5),
        'norm_mem_q': gain((DEPTH, D_MODEL)),
        'norm_mem_kv': gain((DEPTH, D_MODEL)),
        'w_mem_q': nrm((DEPTH, D_MODEL, MEM_INNER), D_MODEL ** -0.5),
        'w_mem_kv': nrm((DEPTH, D_MODEL, 2 * MEM_INNER), D_MODEL ** -0.5),
        'w_mem_out': nrm((DEPTH, MEM_INNER, D_MODEL), MEM_INNER ** -0.5),
        'norm_ffn2': gain((DEPTH, D_MODEL)),
        'w_ffn2_in': nrm((DEPTH, D_MODEL, 2 * D_FF), D_MODEL ** -0.5),
        'w_ffn2_out': nrm((DEPTH, D_FF, D_MODEL), D_FF ** -0.5),
        'rel_bias': nrm((REL_BUCKETS, NSA_HEADS), 0.5),
        'norm_final': gain((D_MODEL,)),
    }

def reference(x_prompt, x_sample, cache_kv_cmp, cache_kv_slc, state_win_kv, state_ssd, state_conv, cache_mem_kv,
              page_table, mem_prompt, norm_ffn1, w_ffn1_in, w_ffn1_out, norm_mix, w_in, conv_w, conv_b, dt_bias,
              a_log, d_skip, norm_ssd_out, cmp_pos_k, cmp_w1_k, cmp_w2_k, cmp_pos_v, cmp_w1_v, cmp_w2_v,
              norm_nsa_out, w_out, norm_mem_q, norm_mem_kv, w_mem_q, w_mem_kv, w_mem_out, norm_ffn2, w_ffn2_in,
              w_ffn2_out, rel_bias, norm_final):
    xp, xs = x_prompt, x_sample
    outs_p = [[] for _ in range(6)]
    outs_s = [[] for _ in range(5)]
    for layer in range(DEPTH):
        lw = {
            'norm_ffn1': norm_ffn1[layer], 'w_ffn1_in': w_ffn1_in[layer], 'w_ffn1_out': w_ffn1_out[layer],
            'norm_mix': norm_mix[layer], 'w_in': w_in[layer], 'conv_w': conv_w[layer], 'conv_b': conv_b[layer],
            'dt_bias': dt_bias[layer], 'a_log': a_log[layer], 'd_skip': d_skip[layer],
            'norm_ssd_out': norm_ssd_out[layer], 'norm_nsa_out': norm_nsa_out[layer], 'w_out': w_out[layer],
            'norm_mem_q': norm_mem_q[layer], 'w_mem_q': w_mem_q[layer], 'w_mem_out': w_mem_out[layer],
            'norm_ffn2': norm_ffn2[layer], 'w_ffn2_in': w_ffn2_in[layer], 'w_ffn2_out': w_ffn2_out[layer],
        }
        cmp_params = (cmp_pos_k[layer], cmp_w1_k[layer], cmp_w2_k[layer], cmp_pos_v[layer], cmp_w1_v[layer], cmp_w2_v[layer])
        mem_kv_p = mem_kv_proj(mem_prompt, norm_mem_kv[layer], w_mem_kv[layer])
        conv0 = jnp.zeros((xp.shape[0], SSD_CONV - 1, SSD_CONV_DIM), xp.dtype)
        h0 = jnp.zeros((xp.shape[0], SSD_HEADS, HEAD_DIM, SSD_STATE), xp.dtype)
        nsa_p = functools.partial(nsa_prompt, cmp_params=cmp_params, rel_bias=rel_bias)
        xp, h_p, conv_p, (c_p, s_p, w_p) = trunk_layer(xp, lw, conv0, h0, nsa_p, mem_kv_p)
        nsa_s = functools.partial(nsa_sample, cmp_params=cmp_params, rel_bias=rel_bias, pool_c=cache_kv_cmp[layer],
                                  pool_s=cache_kv_slc[layer], win_buf=state_win_kv[layer], page_table=page_table)
        xs, h_s, conv_s, (c_s, s_s, w_s) = trunk_layer(xs, lw, state_conv[layer], state_ssd[layer], nsa_s, cache_mem_kv[layer])
        for lst, v in zip(outs_p, (c_p, s_p, w_p, h_p, conv_p, mem_kv_p)):
            lst.append(v)
        for lst, v in zip(outs_s, (c_s, s_s, w_s, h_s, conv_s)):
            lst.append(v)
    y_prompt = rmsnorm(xp, norm_final)
    y_sample = rmsnorm(xs, norm_final)
    return (y_prompt, y_sample,
            jnp.stack(outs_p[0]), jnp.stack(outs_p[1]), jnp.stack(outs_p[2]), jnp.stack(outs_p[3]),
            jnp.stack(outs_p[4]), jnp.stack(outs_p[5]),
            jnp.stack(outs_s[0]), jnp.stack(outs_s[1]), jnp.stack(outs_s[2]), jnp.stack(outs_s[3]),
            jnp.stack(outs_s[4]))


_drawn_inputs = setup_inputs


def setup_inputs(seed=0):
    import zlib

    import numpy as np

    out = dict(_drawn_inputs(seed))
    spreads = {}
    factors = {'norm_mem_q': 7.7}
    for name, (base, spread) in spreads.items():
        noise = np.random.default_rng([zlib.crc32(name.encode()), seed]).standard_normal(out[name].shape)
        drawn = base * np.exp(spread * noise) if base else spread * noise
        out[name] = __import__('jax').numpy.asarray(drawn.astype(out[name].dtype))
    for name, factor in factors.items():
        out[name] = (out[name] * factor).astype(out[name].dtype)
    return out
```

```python
from contextlib import ExitStack

import numpy as np

import concourse.bass as bass
from concourse import mybir

F32 = mybir.dt.float32
F32R = mybir.dt.float32r
I32 = mybir.dt.int32
ALU = mybir.AluOpType
ACT = mybir.ActivationFunctionType
AX_X = mybir.AxisListType.X

P = 128
D_MODEL = 1024
SEQ = 1024
DEC_BATCH = 8
DEC_SEQ = 8
SAMPLE = DEC_BATCH * DEC_SEQ
KT = D_MODEL // P
GROUPS = 3
TG = 364
TP = GROUPS * TG
D_FF = 2816
FT = D_FF // P
EPS = 1e-6
NEG = -1e30


def groups(g):
    return slice(g * TG, (g + 1) * TG)


class Core:

    def __init__(self, nc, ctx):
        self.nc, self.ctx, self.serial, self.in_use = nc, ctx, 0, []

    def sem(self, name):
        self.serial += 1
        handle = self.nc.alloc_semaphore(name=f"{name}_{self.serial}")
        self.in_use.append(handle)
        return handle

    def clear_sems(self):
        self.nc.clear_and_free_semaphores(self.in_use)
        self.in_use = []
        self.nc.all_engine_barrier()


def norm_stage(core, xT, gain, ones, h_hi, h_lo, tag, tiles=KT, width=TP, parts=GROUPS,
               store=None):
    nc = core.nc
    w = width // parts
    with ExitStack() as ctx:
        sb = lambda name, shape, dt=F32: ctx.enter_context(nc.sbuf_tensor(f"{tag}_{name}", shape, dt))
        sq = sb("squares", [P, 2, width])
        total = sb("square_total", [P, width])
        rms = sb("rms", [P, width])
        inv = sb("inv_rms", [P, width])
        h = sb("normed", [P, 2, width])
        ms = ctx.enter_context(nc.psum_tensor(f"{tag}_mean_square", [P, parts, 512], F32))
        sq_ready, added, ms_ready, rms_ready, inv_ready = map(
            core.sem, ("sq_ready", "sq_added", "ms_ready", "rms_ready", "inv_ready"))
        h_ready, hi_ready, lo_ready = map(core.sem, ("h_ready", "h_hi_ready", "h_lo_ready"))
        stored = [core.sem(f"h_stored_{s}") for s in range(2)]
        with nc.Block() as block:

            @block.sync
            def _(sp):
                if store is not None:
                    for k in range(tiles):
                        sp.wait_ge(h_ready, k + 1)
                        sp.dma_start(store[:, k, :], h[:, k % 2, :]).then_inc(stored[k % 2], 16)
                    for s in range(2):
                        sp.wait_ge(stored[s], 16 * (tiles // 2))

            @block.scalar
            def _(act):
                for k in range(tiles):
                    if k >= 2:
                        act.wait_ge(added, k - 1)
                    act.activation(sq[:, k % 2, :], xT[:, k, :width], ACT.Square).then_inc(sq_ready, 1)
                act.wait_ge(ms_ready, 1)
                act.activation(rms[:].rearrange("p (g w) -> p g w", w=w), ms[:, :, :w], ACT.Sqrt,
                               bias=core.eps[:, 0:1]).then_inc(rms_ready, 1)
                for k in range(tiles if store is None else 0):
                    act.wait_ge(h_ready, k + 1)
                    act.activation(h_hi[:, k, :width], h[:, k % 2, :], ACT.Copy).then_inc(hi_ready, 1)

            @block.tensor
            def _(pe):
                pe.wait_ge(added, tiles)
                for g in range(parts):
                    mm = pe.matmul(ms[:, g, :w], ones[:], total[:, g * w:(g + 1) * w],
                                   start=True, stop=True)
                mm.then_inc(ms_ready, 1)

            @block.vector
            def _(dve):
                for k in range(tiles):
                    dve.wait_ge(sq_ready, k + 1)
                    if k == 0:
                        dve.tensor_copy(total[:], sq[:, 0, :]).then_inc(added, 1)
                    else:
                        dve.wait_ge(added, k)
                        dve.tensor_tensor(total[:], total[:], sq[:, k % 2, :], ALU.add).then_inc(added, 1)
                dve.wait_ge(rms_ready, 1)
                dve.reciprocal(inv[:], rms[:]).then_inc(inv_ready, 1)
                dve.wait_ge(inv_ready, 1)

                def rest(k):
                    dve.wait_ge(hi_ready, k + 1)
                    dve.tensor_tensor(h_lo[:, k, :width], h[:, k % 2, :], h_hi[:, k, :width].bitcast(F32),
                                      ALU.subtract).then_inc(lo_ready, 1)

                for k in range(tiles):
                    if k >= 2 and store is None:
                        dve.wait_ge(lo_ready, k - 1)
                    if k >= 2 and store is not None:
                        dve.wait_ge(stored[k % 2], 16 * (k // 2))
                    dve.scalar_tensor_tensor(h[:, k % 2, :], xT[:, k, :width], gain[:, k:k + 1], inv[:],
                                             ALU.mult, ALU.mult).then_inc(h_ready, 1)
                    if k and store is None:
                        rest(k - 1)
                if store is None:
                    rest(tiles - 1)


def passes(pe, out, w_hi, w_lo, x_hi, x_lo, start, stop):
    pe.matmul(out, w_hi, x_hi, start=start, stop=False)
    pe.matmul(out, w_hi, x_lo, start=False, stop=False)
    return pe.matmul(out, w_lo, x_hi, start=False, stop=stop)


def ffn_stage(core, xT, h_hi, h_lo, w_in, w_out, tag):
    nc = core.nc
    chunks = FT // 2
    with ExitStack() as ctx:
        sb = lambda name, shape, dt=F32: ctx.enter_context(nc.sbuf_tensor(f"{tag}_{name}", shape, dt))
        up_raw = sb("up_raw", [P, 2 * KT * P])
        up_hi = sb("up_hi", [P, 2, 2, KT, P], F32R)
        up_lo = sb("up_lo", [P, 2, 2, KT, P], F32R)
        down_raw = sb("down_raw", [P, 2, D_MODEL])
        down_hi = sb("down_hi", [P, 2, D_MODEL], F32R)
        down_lo = sb("down_lo", [P, 2, D_MODEL], F32R)
        act_hi = sb("act_hi", [P, 3, TP], F32R)
        act_lo = sb("act_lo", [P, 3, TP], F32R)
        silu = sb("silu", [P, 2, TG])
        prod = sb("prod", [P, 2, TG])
        gu = ctx.enter_context(nc.psum_tensor(f"{tag}_gate_up", [P, 2, 2, 512], F32))
        dn = ctx.enter_context(nc.psum_tensor(f"{tag}_down", [P, 4, 512], F32))
        up_landed, up_hi_ready, up_lo_ready = map(
            core.sem, ("up_landed", "up_hi_ready", "up_lo_ready"))
        down_landed, down_hi_ready, down_lo_ready = map(
            core.sem, ("down_landed", "down_hi_ready", "down_lo_ready"))
        gu_ready, silu_ready, prod_ready, act_hi_ready, act_ready = map(
            core.sem, ("gu_ready", "silu_ready", "prod_ready", "act_hi_ready", "act_ready"))
        dn_ready, dn_added = map(core.sem, ("dn_ready", "dn_added"))

        def slot(par, f):
            return 2 if f else par

        def schedule(eng, chunk, last):
            chunk(0, 0, True, False)
            chunk(1, 1, True, True)
            chunk(2, 0, True, True)
            with eng.Fori(1, (chunks - 3) // 2) as it:
                chunk(it * 2 + 1, 1, True, True)
                chunk(it * 2 + 2, 0, True, True)
            chunk(chunks - 2, (chunks - 2) % 2, True, True)
            chunk(chunks - 1, (chunks - 1) % 2, False, True)
            last()

        with nc.Block() as block:

            @block.sync
            def _(sp):
                def load_up(n, guard):
                    if guard:
                        sp.wait_ge(up_lo_ready, n)
                    sp.dma_start(up_raw[:], w_in[bass.ds(n, 1)].rearrange("o p c -> (o p) c")
                                 ).then_inc(up_landed, 16)

                def load_down(c, guard):
                    if guard:
                        sp.wait_ge(down_lo_ready, c)
                    sp.dma_start(down_raw[:], w_out[bass.ds(c, 1)].rearrange("o p f c -> (o p) f c")
                                 ).then_inc(down_landed, 16)

                def chunk(c, par, more, full):
                    load_down(c, full)
                    if more:
                        load_up(c * 2 + 2, True)
                        load_up(c * 2 + 3, True)

                load_up(0, False)
                load_up(1, True)
                schedule(sp, chunk, lambda: None)

            @block.scalar
            def _(act):
                def split_up(n, s, reused):
                    act.wait_ge(up_landed, n * 16 + 16)
                    if reused:
                        act.wait_ge(gu_ready, (n - 1) * GROUPS)
                    act.activation(up_hi[:, s].rearrange("p u k c -> p (u k c)"), up_raw[:],
                                   ACT.Copy).then_inc(up_hi_ready, 1)

                def gate(c, f):
                    for g in range(GROUPS):
                        j = c * 6 + (3 * f + g)
                        act.wait_ge(gu_ready, j + 1)
                        if not (isinstance(c, int) and j < 2):
                            act.wait_ge(prod_ready, j - 1)
                        act.activation(silu[:, (f + g) % 2, :], gu[:, (f + g) % 2, 0, :TG],
                                       ACT.Silu).then_inc(silu_ready, 1)

                def chunk(c, par, more, full):
                    gate(c, 0)
                    if more:
                        split_up(c * 2 + 2, 0, True)
                    act.wait_ge(down_landed, c * 16 + 16)
                    if full:
                        act.wait_ge(dn_ready, c * (KT * GROUPS))
                    act.activation(down_hi[:].rearrange("p f c -> p (f c)"),
                                   down_raw[:].rearrange("p f c -> p (f c)"), ACT.Copy
                                   ).then_inc(down_hi_ready, 1)
                    gate(c, 1)
                    if more:
                        split_up(c * 2 + 3, 1, True)

                split_up(0, 0, False)
                split_up(1, 1, False)
                schedule(act, chunk, lambda: None)

            @block.tensor
            def _(pe):
                def up(c, f):
                    pe.wait_ge(up_lo_ready, c * 2 + (f + 1))
                    for g in range(GROUPS):
                        j = c * 6 + (3 * f + g)
                        if not (isinstance(c, int) and j < 2):
                            pe.wait_ge(prod_ready, j - 1)
                        for u in range(2):
                            for k in range(KT):
                                mm = passes(pe, gu[:, (f + g) % 2, u, :TG], up_hi[:, f, u, k, :],
                                            up_lo[:, f, u, k, :], h_hi[:, k, groups(g)],
                                            h_lo[:, k, groups(g)], k == 0, k == KT - 1)
                        mm.then_inc(gu_ready, 1)

                def down(c, par):
                    pe.wait_ge(down_lo_ready, c + 1)
                    pe.wait_ge(act_ready, c * 6 + 6)
                    for t in range(KT):
                        for g in range(GROUPS):
                            d = c * (KT * GROUPS) + (t * GROUPS + g)
                            if not (isinstance(c, int) and d < 4):
                                pe.wait_ge(dn_added, d - 3)
                            for f in range(2):
                                s = slot(par, f)
                                mm = passes(pe, dn[:, (t * GROUPS + g) % 4, :TG],
                                            down_hi[:, f, t * P:(t + 1) * P], down_lo[:, f, t * P:(t + 1) * P],
                                            act_hi[:, s, groups(g)], act_lo[:, s, groups(g)], f == 0, f == 1)
                            mm.then_inc(dn_ready, 1)

                def chunk(c, par, more, full):
                    up(c, 0)
                    if full:
                        down(c - 1, 1 - par)
                    up(c, 1)

                schedule(pe, chunk, lambda: down(chunks - 1, (chunks - 1) % 2))

            @block.vector
            def _(dve):
                def split_up(n, s):
                    dve.wait_ge(up_hi_ready, n + 1)
                    dve.tensor_tensor(up_lo[:, s].rearrange("p u k c -> p (u k c)"), up_raw[:],
                                      up_hi[:, s].rearrange("p u k c -> p (u k c)").bitcast(F32),
                                      ALU.subtract).then_inc(up_lo_ready, 1)

                def multiply(c, f, par):
                    if not (isinstance(c, int) and c < (1 if f else 2)):
                        dve.wait_ge(dn_ready, (c if f else c - 1) * (KT * GROUPS))
                    for g in range(GROUPS):
                        j = c * 6 + (3 * f + g)
                        b, s = (f + g) % 2, slot(par, f)
                        dve.wait_ge(silu_ready, j + 1)
                        dve.tensor_tensor(prod[:, b, :], silu[:, b, :], gu[:, b, 1, :TG],
                                          ALU.mult).then_inc(prod_ready, 1)
                        dve.wait_ge(prod_ready, j + 1)
                        dve.tensor_copy(act_hi[:, s, groups(g)], prod[:, b, :]).then_inc(act_hi_ready, 1)
                        dve.wait_ge(act_hi_ready, j + 1)
                        dve.tensor_tensor(act_lo[:, s, groups(g)], prod[:, b, :],
                                          act_hi[:, s, groups(g)].bitcast(F32), ALU.subtract
                                          ).then_inc(act_ready, 1)

                def add(c):
                    for t in range(KT):
                        for g in range(GROUPS):
                            d = c * (KT * GROUPS) + (t * GROUPS + g)
                            dve.wait_ge(dn_ready, d + 1)
                            dve.scalar_tensor_tensor(xT[:, t, groups(g)], dn[:, (t * GROUPS + g) % 4, :TG],
                                                     0.5, xT[:, t, groups(g)], ALU.mult, ALU.add
                                                     ).then_inc(dn_added, 1)

                def chunk(c, par, more, full):
                    multiply(c, 0, par)
                    if more:
                        split_up(c * 2 + 2, 0)
                    if full:
                        add(c - 1)
                    dve.wait_ge(down_hi_ready, c + 1)
                    dve.tensor_tensor(down_lo[:], down_raw[:], down_hi[:].bitcast(F32),
                                      ALU.subtract).then_inc(down_lo_ready, 1)
                    multiply(c, 1, par)
                    if more:
                        split_up(c * 2 + 3, 1)

                split_up(0, 0)
                split_up(1, 1)
                schedule(dve, chunk, lambda: add(chunks - 1))


def gemm_stage(core, x_hi, x_lo, w, k_tiles, n_tiles, tag, store=None, add_to=None):
    nc = core.nc
    with ExitStack() as ctx:
        sb = lambda name, shape, dt=F32: ctx.enter_context(nc.sbuf_tensor(f"{tag}_{name}", shape, dt))
        raw = sb("w_raw", [P, 2, k_tiles * P])
        w_hi = sb("w_hi", [P, 2, k_tiles, P], F32R)
        w_lo = sb("w_lo", [P, 2, k_tiles, P], F32R)
        out = sb("out", [P, 2, TP]) if store is not None else None
        ps = ctx.enter_context(nc.psum_tensor(f"{tag}_ps", [P, 6, 512], F32))
        landed = [core.sem(f"w_landed_{s}") for s in range(2)]
        hi_ready, lo_ready, ps_ready, taken = map(core.sem, ("w_hi_ready", "w_lo_ready", "ps_ready", "ps_taken"))
        stored = [core.sem(f"stored_{s}") for s in range(2)]
        pairs = n_tiles // 2

        def schedule(eng, pair):
            pair(0, True, pairs > 1)
            if pairs > 2:
                with eng.Fori(1, pairs - 1) as i:
                    pair(i, False, True)
            if pairs > 1:
                pair(pairs - 1, False, False)

        with nc.Block() as block:

            @block.sync
            def _(sp):
                def load(i, s, guard):
                    if guard:
                        sp.wait_ge(lo_ready, i * 2 + (s - 1))
                    sp.dma_start(raw[:, s, :], w[bass.ds(i * 2 + s, 1)].rearrange("o p c -> (o p) c")
                                 ).then_inc(landed[s], 16)

                def pair(i, first, more):
                    if more:
                        for s in range(2):
                            load(i + 1, s, True)

                for s in range(2):
                    load(0, s, False)
                schedule(sp, pair)

            @block.tensor
            def _(pe):
                def pair(i, first, more):
                    for s in range(2):
                        pe.wait_ge(lo_ready, i * 2 + (s + 1))
                        for g in range(GROUPS):
                            if not first:
                                pe.wait_ge(taken, i * 6 + (s * 3 + g - 5))
                            for k in range(k_tiles):
                                mm = passes(pe, ps[:, s * 3 + g, :TG], w_hi[:, s, k, :], w_lo[:, s, k, :],
                                            x_hi[k][:, groups(g)], x_lo[k][:, groups(g)],
                                            k == 0, k == k_tiles - 1)
                            mm.then_inc(ps_ready, 1)

                schedule(pe, pair)

            @block.scalar
            def _(act):
                def split(i, s, reused):
                    act.wait_ge(landed[s], i * 16 + 16)
                    if reused:
                        act.wait_ge(ps_ready, i * 6 + (s * 3 - 3))
                    act.activation(w_hi[:, s].rearrange("p k c -> p (k c)"), raw[:, s, :],
                                   ACT.Copy).then_inc(hi_ready, 1)

                def pair(i, first, more):
                    for s in range(2):
                        if store is not None:
                            if not first:
                                act.wait_ge(stored[s], i * 16)
                            for g in range(GROUPS):
                                act.wait_ge(ps_ready, i * 6 + (s * 3 + g + 1))
                                act.activation(out[:, s, groups(g)], ps[:, s * 3 + g, :TG], ACT.Copy
                                               ).then_inc(taken, 1)
                            act.wait_ge(taken, i * 6 + (s * 3 + 3))
                            act.dma_start(store[bass.ds(i * 2 + s, 1)].rearrange("o p c -> (o p) c"),
                                          out[:, s, :]).then_inc(stored[s], 16)
                        if more:
                            split(i + 1, s, True)

                split(0, 0, False)
                split(0, 1, False)
                schedule(act, pair)
                if store is not None:
                    for s in range(2):
                        act.wait_ge(stored[s], 16 * pairs)

            @block.vector
            def _(dve):
                def split(i, s):
                    dve.wait_ge(hi_ready, i * 2 + (s + 1))
                    dve.tensor_tensor(w_lo[:, s].rearrange("p k c -> p (k c)"), raw[:, s, :],
                                      w_hi[:, s].rearrange("p k c -> p (k c)").bitcast(F32),
                                      ALU.subtract).then_inc(lo_ready, 1)

                def pair(i, first, more):
                    for s in range(2):
                        if add_to is not None:
                            for g in range(GROUPS):
                                dve.wait_ge(ps_ready, i * 6 + (s * 3 + g + 1))
                                x = add_to[:, bass.ds(i * 2 + s, 1), groups(g)].rearrange("p o t -> p (o t)")
                                dve.tensor_tensor(x, ps[:, s * 3 + g, :TG], x, ALU.add).then_inc(taken, 1)
                        if more:
                            split(i + 1, s)

                split(0, 0)
                split(0, 1)
                schedule(dve, pair)


NAT = 288
TOK_TILES = 9


def tok_rows(t):
    return P if t < TOK_TILES - 1 else TP - P * (TOK_TILES - 1)


def natural_stage(core, h_hi, h_lo, w, nat, tag):
    nc = core.nc
    with ExitStack() as ctx:
        sb = lambda name, shape, dt=F32: ctx.enter_context(nc.sbuf_tensor(f"{tag}_{name}", shape, dt))
        raw = sb("w_raw", [P, KT, NAT])
        w_hi = sb("w_hi", [P, KT, NAT], F32R)
        w_lo = sb("w_lo", [P, KT, NAT], F32R)
        ps = ctx.enter_context(nc.psum_tensor(f"{tag}_ps", [P, 2, 512], F32))
        landed, hi_ready, lo_ready, cleared, ps_ready, taken = map(
            core.sem, ("nw_landed", "nw_hi_ready", "nw_lo_ready", "nat_cleared", "nat_ps_ready", "nat_taken"))
        with nc.Block() as block:

            @block.sync
            def _(sp):
                sp.dma_start(raw[:], w).then_inc(landed, 16)

            @block.scalar
            def _(act):
                act.wait_ge(landed, 16)
                act.activation(w_hi[:], raw[:], ACT.Copy).then_inc(hi_ready, 1)

            @block.vector
            def _(dve):
                dve.memset(nat[:, TOK_TILES - 1, :], 0.0).then_inc(cleared, 1)
                dve.wait_ge(hi_ready, 1)
                dve.tensor_tensor(w_lo[:], raw[:], w_hi[:].bitcast(F32), ALU.subtract).then_inc(lo_ready, 1)
                dve.wait_ge(cleared, 1)
                for t in range(TOK_TILES):
                    n = tok_rows(t)
                    dve.wait_ge(ps_ready, t + 1)
                    dve.tensor_copy(nat[:n, t, :], ps[:n, t % 2, :NAT]).then_inc(taken, 1)

            @block.tensor
            def _(pe):
                pe.wait_ge(lo_ready, 1)
                for t in range(TOK_TILES):
                    n = tok_rows(t)
                    if t >= 2:
                        pe.wait_ge(taken, t - 1)
                    for k in range(KT):
                        x = slice(t * P, t * P + n)
                        pe.matmul(ps[:n, t % 2, :NAT], h_hi[:, k, x], w_hi[:, k, :], start=k == 0, stop=False)
                        pe.matmul(ps[:n, t % 2, :NAT], h_lo[:, k, x], w_hi[:, k, :], start=False, stop=False)
                        mm = pe.matmul(ps[:n, t % 2, :NAT], h_hi[:, k, x], w_lo[:, k, :], start=False,
                                       stop=k == KT - 1)
                    mm.then_inc(ps_ready, 1)


SSD_HEADS = 8
HEAD_DIM = 64
INNER = SSD_HEADS * HEAD_DIM
XBC = 8
TAPS = 4
XBC_TILE0 = 4
TOKENS = SEQ + SAMPLE


def conv_stage(core, proj, conv_state, conv_w, conv_b, xc, y):
    nc = core.nc
    pad = TAPS - 1
    with ExitStack() as ctx:
        sb = lambda name, shape, dt=F32: ctx.enter_context(nc.sbuf_tensor(f"conv_{name}", shape, dt))
        prompt = sb("prompt", [P, 2, pad + SEQ])
        new = sb("new", [P, XBC, SAMPLE])
        old = sb("old", [P, XBC, DEC_BATCH * pad])
        sample = sb("sample", [P, XBC, DEC_BATCH, pad + DEC_SEQ])
        acc = sb("acc", [P, 2, TOKENS])
        w = sb("w", [P, XBC, TAPS])
        b = sb("b", [P, XBC])
        small_landed, zeroed, sample_ready, tap_done, xc_ready = map(
            core.sem, ("conv_small_landed", "conv_zeroed", "conv_sample_ready", "tap_done", "xc_ready"))
        landed = [core.sem(f"xbc_landed_{s}") for s in range(2)]
        z_landed, y_ready = core.sem("z_landed"), core.sem("z_silu_ready")
        with nc.Block() as block:

            @block.sync
            def _(sp):
                sp.dma_start(y[:], proj[0:4].rearrange("i p t -> p i t")).then_inc(z_landed, 16)
                sp.dma_start(w[:], conv_w).then_inc(small_landed, 16)
                sp.dma_start(b[:], conv_b).then_inc(small_landed, 16)
                sp.dma_start(old[:], conv_state).then_inc(small_landed, 16)
                sp.dma_start(new[:], proj[XBC_TILE0:XBC_TILE0 + XBC, :, SEQ:TOKENS].rearrange("i p t -> p i t")
                             ).then_inc(small_landed, 16)
                for i in range(XBC):
                    if i >= 2:
                        sp.wait_ge(tap_done, (i - 1) * 2 * TAPS)
                    sp.dma_start(prompt[:, i % 2, pad:], proj[XBC_TILE0 + i, :, 0:SEQ]).then_inc(landed[i % 2], 16)

            @block.gpsimd
            def _(pool):
                pool.memset(prompt[:, :, 0:pad], 0.0).then_inc(zeroed, 1)
                pool.wait_ge(small_landed, 64)
                rows = sample[:].rearrange("p i b t -> p (i b) t")
                pool.tensor_copy(rows[:, :, 0:pad], old[:].rearrange("p i (b t) -> p (i b) t", t=pad)
                                 ).then_inc(sample_ready, 1)
                pool.tensor_copy(rows[:, :, pad:], new[:].rearrange("p i (b t) -> p (i b) t", t=DEC_SEQ)
                                 ).then_inc(sample_ready, 1)

            @block.vector
            def _(dve):
                dve.wait_ge(zeroed, 1)
                dve.wait_ge(small_landed, 64)
                dve.wait_ge(sample_ready, 2)
                for i in range(XBC):
                    dve.wait_ge(landed[i % 2], 16 * (i // 2 + 1))
                    if i >= 2:
                        dve.wait_ge(xc_ready, 2 * (i - 1))
                    a = acc[:, i % 2, 0:SEQ]
                    s = acc[:, i % 2, SEQ:TOKENS].rearrange("p (b t) -> p b t", t=DEC_SEQ)
                    for j in range(TAPS):
                        at_p, at_s = prompt[:, i % 2, j:j + SEQ], sample[:, i, :, j:j + DEC_SEQ]
                        if j == 0:
                            dve.tensor_scalar(a, at_p, w[:, i, 0:1], b[:, i:i + 1], ALU.mult, ALU.add
                                              ).then_inc(tap_done, 1)
                            dve.tensor_scalar(s, at_s, w[:, i, 0:1], b[:, i:i + 1], ALU.mult, ALU.add
                                              ).then_inc(tap_done, 1)
                        else:
                            dve.wait_ge(tap_done, (i * TAPS + j) * 2)
                            dve.scalar_tensor_tensor(a, at_p, w[:, i, j:j + 1], a, ALU.mult, ALU.add
                                                     ).then_inc(tap_done, 1)
                            dve.scalar_tensor_tensor(s, at_s, w[:, i, j:j + 1], s, ALU.mult, ALU.add
                                                     ).then_inc(tap_done, 1)

            @block.scalar
            def _(act):
                act.wait_ge(z_landed, 16)
                act.activation(y[:], y[:], ACT.Silu).then_inc(y_ready, 1)
                for i in range(XBC):
                    act.wait_ge(tap_done, (i + 1) * 2 * TAPS)
                    act.activation(xc[:, i, 0:SEQ], acc[:, i % 2, 0:SEQ], ACT.Silu).then_inc(xc_ready, 1)
                    act.activation(xc[:, i, SEQ:], acc[:, i % 2, SEQ:], ACT.Silu).then_inc(xc_ready, 1)


def ssd_stage(core, nat, xc, dt_bias, a_log, d_skip, state_in, y, state_out_p, state_out_s):
    nc = core.nc
    H, HD = SSD_HEADS, HEAD_DIM
    chunks = TOK_TILES
    S = chunks - 1
    with ExitStack() as ctx:
        sb = lambda name, shape, dt=F32: ctx.enter_context(nc.sbuf_tensor(f"ssd_{name}", shape, dt))
        ps = lambda name, n: ctx.enter_context(nc.psum_tensor(f"ssd_{name}_ps", [P, n], F32))
        dtb, alog, dskip = sb("dt_bias", [P, H]), sb("a_log", [P, H]), sb("d_skip", [P, 4])
        xdt, nabs, u, w1p, ln, dt, dta = (sb(n, [P, chunks, H]) for n in
                                          ("xdt", "neg_abs", "exp_neg", "one_plus", "ln", "dt", "dt_a"))
        ea = sb("exp_a", [P, H])
        state = sb("state", [P, INNER])
        s_state = sb("sample_state", [P, DEC_BATCH, INNER])
        xn, bn = sb("x_nat", [P, INNER]), sb("b_nat", [P, 256])
        acs = sb("acs", [P, 2 * H])
        te, te_dt = sb("to_end", [P, H]), sb("to_end_dt", [P, H])
        seg = sb("seg", [P, H, P])
        grow = sb("exp_acs", [P, H, P])
        cs = sb("c_scaled", [P, H, P])
        cbm = sb("cb_masked", [P, 2, P])
        xs = sb("x_scaled", [P, INNER])
        xsb = [a[:SAMPLE, :, SAMPLE:] for a in (seg, cs)]
        yt = sb("y_skip", [P, 4, P])
        tp_x, tp_b, small, bc = ps("tp_x", 512), ps("tp_b", 512), ps("small", 512), ps("bc", 1024)
        yp = ps("y", 512)
        st = ctx.enter_context(nc.psum_tensor("ssd_st", [P, 2, 512], F32))
        in_landed, chain, sp_act, dt_ready = map(
            core.sem, ("ssd_in_landed", "softplus_dve", "softplus_act", "dt_ready"))
        prep_ready, acs_ready, te_arg_ready, te_ready, seg_ready, cbm_ready, decay_ready = map(
            core.sem, ("prep_ready", "acs_ready", "te_arg_ready", "te_ready", "seg_ready", "cbm_ready",
                       "decay_ready"))
        xn_ready, bn_ready, grow_ready, cs_ready, w_ready, te_dt_ready, xs_ready, xsb_ready = map(
            core.sem, ("xn_ready", "bn_ready", "grow_ready", "cs_ready", "w_ready", "te_dt_ready", "xs_ready",
                       "xsb_ready"))
        y_ready, st_ready, skip_done, y_done, decayed, state_ready, s_decayed, s_state_ready, stored = map(
            core.sem, ("y_ready", "st_ready", "skip_done", "y_done", "state_decayed", "state_ready",
                       "sample_decayed", "sample_state_ready", "states_stored"))

        def rows(c):
            return SAMPLE if c == S else P

        def cols(c):
            return slice(c * P, c * P + rows(c))

        with nc.Block() as block:

            @block.sync
            def _(sp):
                for dst, src in ((dtb, dt_bias), (alog, a_log), (dskip, d_skip), (s_state, state_in)):
                    sp.dma_start(dst[:], src).then_inc(in_landed, 16)
                sp.wait_ge(state_ready, S)
                sp.dma_start(state_out_p, state[:]).then_inc(stored, 16)
                sp.wait_ge(s_state_ready, DEC_BATCH)
                sp.dma_start(state_out_s, s_state[:]).then_inc(stored, 16)
                sp.wait_ge(stored, 32)

            @block.tensor
            def _(pe):
                pe.wait_ge(dt_ready, 1)
                for c in range(chunks):
                    T = rows(c)
                    tri = core.tri_seq if c == S else core.tri
                    whole = core.same_seq if c == S else core.ones
                    if c:
                        for sem in (xn_ready, bn_ready, cbm_ready, acs_ready, grow_ready):
                            pe.wait_ge(sem, c)
                        pe.wait_ge(seg_ready, c * H)
                    for i in range(4):
                        pe.transpose(tp_x[:T, i * P:(i + 1) * P], xc[:, i, cols(c)], core.ident[:])
                    for g in range(2):
                        pe.transpose(tp_b[:T, g * P:(g + 1) * P], xc[:, 4 + g, cols(c)], core.ident[:])
                    for g in range(2):
                        pe.matmul(small[:T, (1 + g) * P:(1 + g) * P + T], xc[:, 4 + g, cols(c)],
                                  xc[:, 6 + g, cols(c)], start=True, stop=True)
                    pe.matmul(small[:T, 0:H], tri[:T, :T], dta[:T, c, :], start=True, stop=True)
                    pe.matmul(small[:T, H:2 * H], whole[:T, :T], dta[:T, c, :], start=True, stop=True)
                    for h in range(H):
                        mm = pe.matmul(bc[:, h * P:h * P + T], dta[:T, c, h:h + 1].to_broadcast([T, P]),
                                       tri[:T, :T], start=True, stop=True)
                    mm.then_inc(prep_ready, 1)
                    pe.wait_ge(xn_ready, c + 1)
                    pe.wait_ge(w_ready, (c + 1) * H)
                    if c:
                        pe.wait_ge(skip_done, 4 * c)
                        pe.wait_ge(state_ready, min(c, S))
                        pe.wait_ge(cs_ready, 2 * (c + 1))
                    if c == S:
                        pe.wait_ge(in_landed, 64)
                    for h in range(H):
                        q = HD * (h % 2)
                        hs = slice(h * HD, (h + 1) * HD)
                        at = (h // 2) * P
                        mm = pe.matmul(yp[q:q + HD, at:at + T], xn[:T, hs], seg[:T, h, :T], start=True, stop=c in (0, S))
                        if c == S:
                            for b in range(DEC_BATCH):
                                t = slice(b * DEC_SEQ, (b + 1) * DEC_SEQ)
                                mm = pe.matmul(yp[q:q + HD, at + b * DEC_SEQ:at + (b + 1) * DEC_SEQ],
                                               s_state[:, b, hs], cs[:, h, t], start=False, stop=True,
                                               skip_group_check=True)
                        elif c:
                            mm = pe.matmul(yp[q:q + HD, at:at + T], state[:, hs], cs[:, h, :T],
                                           start=False, stop=True)
                    mm.then_inc(y_ready, 1)
                    pe.wait_ge(bn_ready, c + 1)
                    if c < S:
                        pe.wait_ge(xs_ready, c + 1)
                        for g in range(2):
                            mm = pe.matmul(st[:, 0, g * 256:(g + 1) * 256], bn[:T, g * P:(g + 1) * P],
                                           xs[:T, g * 256:(g + 1) * 256], start=True, stop=True)
                        mm.then_inc(st_ready, 1)
                    else:
                        for b in range(DEC_BATCH):
                            pe.wait_ge(xsb_ready, b + 1)
                            if b >= 2:
                                pe.wait_ge(s_state_ready, b - 1)
                            for g in range(2):
                                mm = pe.matmul(st[:, b % 2, g * 256:(g + 1) * 256], bn[:T, g * P:(g + 1) * P],
                                               xsb[b % 2][:, 4 * g:4 * g + 4, :], start=True, stop=True)
                            mm.then_inc(st_ready, 1)

            @block.scalar
            def _(act):
                act.wait_ge(in_landed, 64)
                act.activation(ea[:], alog[:], ACT.Exp).then_inc(sp_act, 1)
                act.wait_ge(chain, 3)
                act.activation(u[:], nabs[:], ACT.Exp).then_inc(sp_act, 1)
                act.wait_ge(chain, 4)
                act.activation(ln[:], w1p[:], ACT.Ln).then_inc(sp_act, 1)
                for c in range(chunks):
                    T = rows(c)
                    act.wait_ge(prep_ready, c + 1)
                    act.activation(xn[:T, :], tp_x[:T, :], ACT.Copy).then_inc(xn_ready, 1)
                    act.activation(bn[:T, :], tp_b[:T, 0:256], ACT.Copy).then_inc(bn_ready, 1)
                    if c:
                        act.wait_ge(cs_ready, 2 * c)
                        act.wait_ge(state_ready, c)
                    act.activation(grow[:, :, :T], bc[:].rearrange("p (h t) -> p h t", t=P)[:, :, :T],
                                   ACT.Exp).then_inc(grow_ready, 1)
                    act.wait_ge(te_arg_ready, c + 1)
                    act.activation(te[:T, :], te[:T, :], ACT.Exp).then_inc(te_ready, 1)
                    act.wait_ge(seg_ready, (c + 1) * H)
                    act.activation(seg[:T, :, :T], seg[:T, :, :T], ACT.Exp).then_inc(decay_ready, 1)

            @block.gpsimd
            def _(pool):
                for c in range(chunks):
                    T = rows(c)
                    pool.wait_ge(grow_ready, c + 1)
                    if c:
                        pool.wait_ge(y_ready, c)
                    for g in range(2):
                        pool.tensor_tensor(cs[:, 4 * g:4 * g + 4, :T], grow[:, 4 * g:4 * g + 4, :T],
                                           xc[:, 6 + g:7 + g, cols(c)].to_broadcast([P, 4, T]),
                                           ALU.mult).then_inc(cs_ready, 1)

            @block.vector
            def _(dve):
                done = 0

                def step(ins):
                    nonlocal done
                    done += 1
                    ins.then_inc(chain, 1)
                    dve.wait_ge(chain, done)

                dve.wait_ge(in_landed, 64)
                lanes = lambda a: a[:].rearrange("p (o h) -> p o h", o=1).to_broadcast([P, chunks, H])
                step(dve.tensor_tensor(xdt[:], nat[:, :, 256:256 + H], lanes(dtb), ALU.add))
                step(dve.tensor_scalar(nabs[:], xdt[:], -1.0, None, ALU.mult))
                step(dve.tensor_tensor(nabs[:], nabs[:], xdt[:], ALU.min))
                dve.wait_ge(sp_act, 2)
                step(dve.tensor_scalar(w1p[:], u[:], 1.0, None, ALU.add))
                step(dve.tensor_scalar(dt[:], w1p[:], -1.0, None, ALU.add))
                step(dve.tensor_tensor(dt[:], u[:], dt[:], ALU.subtract))
                dve.wait_ge(sp_act, 3)
                step(dve.reciprocal(w1p[:], w1p[:]))
                step(dve.tensor_tensor(dt[:], dt[:], w1p[:], ALU.mult))
                step(dve.tensor_tensor(dt[:], dt[:], ln[:], ALU.add))
                step(dve.scalar_tensor_tensor(dt[:], xdt[:], 0.0, dt[:], ALU.max, ALU.add))
                dve.scalar_tensor_tensor(dta[:], dt[:], -1.0, lanes(ea), ALU.mult, ALU.mult
                                         ).then_inc(dt_ready, 1)
                for c in range(chunks):
                    T = rows(c)
                    tri = core.tri_seq if c == S else core.tri
                    dve.wait_ge(prep_ready, c + 1)
                    dve.tensor_copy(acs[:T, :], small[:T, 0:2 * H]).then_inc(acs_ready, 1)
                    for g in range(2):
                        ins = dve.tensor_tensor(cbm[:T, g, :T], small[:T, (1 + g) * P:(1 + g) * P + T],
                                                tri[:T, :T], ALU.mult)
                    ins.then_inc(cbm_ready, 1)
                    dve.wait_ge(acs_ready, c + 1)
                    if c:
                        dve.wait_ge(te_dt_ready, c)
                    dve.tensor_tensor(te[:T, :], acs[:T, H:], acs[:T, :H], ALU.subtract).then_inc(te_arg_ready, 1)
                    dve.wait_ge(grow_ready, c + 1)
                    for h in range(H):
                        dve.tensor_scalar(seg[:T, h, :T], bc[:T, h * P:h * P + T], acs[:T, h:h + 1], 0.0,
                                          ALU.subtract, ALU.min).then_inc(seg_ready, 1)
                    dve.wait_ge(te_ready, c + 1)
                    dve.tensor_tensor(te_dt[:T, :], te[:T, :], dt[:T, c, :], ALU.mult).then_inc(te_dt_ready, 1)
                    dve.wait_ge(te_dt_ready, c + 1)
                    dve.wait_ge(xn_ready, c + 1)
                    dve.tensor_tensor(xs[:T, :].rearrange("p (h d) -> p h d", h=H),
                                      xn[:T, :].rearrange("p (h d) -> p h d", h=H),
                                      te_dt[:T, :].rearrange("p (h o) -> p h o", o=1).to_broadcast([T, H, HD]),
                                      ALU.mult).then_inc(xs_ready, 1)
                    dve.wait_ge(decay_ready, c + 1)
                    dve.wait_ge(cbm_ready, c + 1)
                    for h in range(H):
                        dve.scalar_tensor_tensor(seg[:T, h, :T], seg[:T, h, :T], dt[:T, c, h:h + 1],
                                                 cbm[:T, h // 4, :T], ALU.mult, ALU.mult).then_inc(w_ready, 1)
                    dve.wait_ge(y_ready, c + 1)
                    if c:
                        dve.wait_ge(y_done, c)
                    for i in range(4):
                        dve.scalar_tensor_tensor(yt[:, i, :T], xc[:, i, cols(c)], dskip[:, i:i + 1],
                                                 yp[:, i * P:i * P + T], ALU.mult, ALU.add).then_inc(skip_done, 1)
                    dve.wait_ge(skip_done, 4 * (c + 1))
                    dve.tensor_tensor(y[:, :, cols(c)], yt[:, :, :T], y[:, :, cols(c)], ALU.mult).then_inc(y_done, 1)
                    if c < S:
                        flat = state[:]
                        if c == 0:
                            dve.wait_ge(st_ready, 1)
                            dve.tensor_copy(flat, st[:, 0, :]).then_inc(state_ready, 1)
                        else:
                            dve.wait_ge(grow_ready, c + 1)
                            h3 = flat.rearrange("p (h d) -> p h d", h=H)
                            dve.tensor_tensor(h3, h3, grow[:, :, P - 1:P].to_broadcast([P, H, HD]), ALU.mult
                                              ).then_inc(decayed, 1)
                            dve.wait_ge(decayed, c)
                            dve.wait_ge(st_ready, c + 1)
                            dve.tensor_tensor(flat, flat, st[:, 0, :], ALU.add).then_inc(state_ready, 1)
                    else:
                        dve.wait_ge(xs_ready, S + 1)
                        for b in range(DEC_BATCH):
                            if b >= 2:
                                dve.wait_ge(st_ready, S + b - 1)
                            dve.tensor_scalar(xsb[b % 2], xs[:SAMPLE, :].rearrange("p (h d) -> p h d", h=H), core.seq_mask[:SAMPLE, b:b + 1],
                                              None, ALU.mult).then_inc(xsb_ready, 1)
                            h3 = s_state[:, b, :].rearrange("p (h d) -> p h d", h=H)
                            end = b * DEC_SEQ + DEC_SEQ - 1
                            dve.tensor_tensor(h3, h3, grow[:, :, end:end + 1].to_broadcast([P, H, HD]),
                                              ALU.mult).then_inc(s_decayed, 1)
                            dve.wait_ge(s_decayed, b + 1)
                            dve.wait_ge(st_ready, S + b + 1)
                            dve.tensor_tensor(s_state[:, b, :], s_state[:, b, :], st[:, b % 2, :], ALU.add
                                              ).then_inc(s_state_ready, 1)


CONSTS = 5 * P + DEC_BATCH + 1


def make_consts():
    c = np.zeros((P, CONSTS), np.float32)
    i = np.arange(P)
    same = (i[:, None] // DEC_SEQ == i[None, :] // DEC_SEQ) & (i[:, None] < SAMPLE) & (i[None, :] < SAMPLE)
    tri = i[:, None] <= i[None, :]
    c[:, 0:P] = np.eye(P)
    c[:, P:2 * P] = tri
    c[:, 2 * P:3 * P] = tri & same
    c[:, 3 * P:4 * P] = same
    c[:, 4 * P:5 * P] = 1.0
    c[:, 5 * P:-1] = (i[:, None] // DEC_SEQ == np.arange(DEC_BATCH)[None, :]) & (i[:, None] < SAMPLE)
    c[:, -1] = i >= CMP_BLOCK - 1
    return c


def consts_stage(core, consts):
    nc = core.nc
    sb = lambda name, shape, dt=F32: core.ctx.enter_context(nc.sbuf_tensor(f"const_{name}", shape, dt))
    all_consts = sb("all", [P, CONSTS])
    core.ident, core.tri, core.tri_seq, core.same_seq, core.ones = (
        all_consts[:, i * P:(i + 1) * P] for i in range(5))
    core.seq_mask = all_consts[:, 5 * P:5 * P + DEC_BATCH]
    core.sees_cmp = all_consts[:, CONSTS - 1:]
    core.mean_model, core.mean_inner = sb("mean_model", [P, P]), sb("mean_inner", [P, P])
    core.eps = sb("eps", [P, 1])
    landed = core.sem("consts_landed")
    filled = core.sem("consts_filled")
    with nc.Block() as block:

        @block.sync
        def _(sp):
            sp.dma_start(all_consts[:], consts).then_inc(landed, 16)
            sp.wait_ge(landed, 16)

        @block.vector
        def _(dve):
            dve.memset(core.mean_model[:], 1.0 / D_MODEL).then_inc(filled, 1)
            dve.memset(core.mean_inner[:], 1.0 / INNER).then_inc(filled, 1)
            dve.memset(core.eps[:], EPS).then_inc(filled, 1)


def lay_conv_state(a):
    return np.ascontiguousarray(a[0].transpose(2, 0, 1).reshape(XBC, P, -1).transpose(1, 0, 2))


def lay_conv_w(a):
    return np.ascontiguousarray(a[0].T.reshape(XBC, P, TAPS).transpose(1, 0, 2))


def lay_d_skip(a):
    return np.ascontiguousarray(np.repeat(a[0], HEAD_DIM).reshape(4, P).T)


def lay_state(a):
    return np.ascontiguousarray(a[0].transpose(3, 0, 1, 2).reshape(P, DEC_BATCH, INNER))


CMP_BLOCK, CMP_STRIDE, CMP_HIDDEN = 32, 16, 256
N_CHUNK = SEQ // CMP_STRIDE
N_CMP = N_CHUNK - 1
SEQS = DEC_BATCH + 1
PAIR_STEPS = CMP_STRIDE // 2
PAGES = 8
KV_TILE0 = 16


def compress_stage(core, kv, proj, pages_dram, page_table, w1, w2, pos, out, n_pool):
    nc = core.nc
    tag = f"cmp{kv}"
    halves = ((0, 5), (5, SEQS))
    with ExitStack() as ctx:
        sb = lambda name, shape, dt=F32: ctx.enter_context(nc.sbuf_tensor(f"{tag}_{name}", shape, dt))
        table = sb("page_table", [1, DEC_BATCH * PAGES], I32)
        raw = sb("raw_pages", [P, 2, PAGES, PAIR_STEPS, 2, PAGES])
        pairs = sb("pairs", [P, PAIR_STEPS, 2, SEQS, N_CHUNK])
        rows_t = sb("prompt_rows", [P, SEQ])
        w1s, w2s, ps_ = sb("w1", [P, 2 * PAIR_STEPS, CMP_HIDDEN]), sb("w2", [P, 2, HEAD_DIM]), sb("pos", [P, 2 * PAIR_STEPS])
        bias = sb("bias", [P, 2])
        hid = sb("hid", [P, 2, 2, SEQS * N_CMP])
        hp = ctx.enter_context(nc.psum_tensor(f"{tag}_hid_ps", [P, 4, 512], F32))
        bp = ctx.enter_context(nc.psum_tensor(f"{tag}_bias_ps", [P, 512], F32))
        op = ctx.enter_context(nc.psum_tensor(f"{tag}_out_ps", [P, 3, 512], F32))
        table_landed, w_landed, rows_landed, shuffled, prompt_ready = map(
            core.sem, ("table_landed", "cw_landed", "rows_landed", "shuffled", "prompt_pairs_ready"))
        pages_landed = [core.sem(f"pages_landed_{s}") for s in range(2)]
        pairs_ready, bias_ps, bias_ready, hid_ps, hid_ready, out_ps, out_ready = map(
            core.sem, ("pairs_ready", "bias_ps", "bias_ready", "hid_ps", "hid_ready", "out_ps", "out_ready"))
        with nc.Block() as block:

            @block.sync
            def _(sp):
                sp.dma_start(table[:], page_table).then_inc(table_landed, 16)
                sp.dma_start(rows_t[:], proj[KV_TILE0 + kv, :, 0:SEQ]).then_inc(rows_landed, 16)
                sp.wait_ge(table_landed, 16)

                def load(i, s, guard):
                    if guard:
                        sp.wait_ge(pairs_ready, i * 4 + (2 * s - 2))
                    for j in range(PAGES):
                        page = sp.value_load(table[0:1, bass.ds(i * (2 * PAGES) + (s * PAGES + j), 1)],
                                             min_val=0, max_val=n_pool - 1)
                        sp.dma_start(raw[:, s, j].rearrange("p a b c -> p (a b c)"),
                                     pages_dram[kv, bass.ds(page, 1)].rearrange("o p c -> (o p) c")
                                     ).then_inc(pages_landed[s], 16)

                for s in range(2):
                    load(0, s, False)
                with sp.Fori(1, DEC_BATCH // 2) as i:
                    for s in range(2):
                        load(i, s, True)

            @block.gpsimd
            def _(pool):
                with pool.Fori(0, DEC_BATCH // 2) as i:
                    for s in range(2):
                        pool.wait_ge(pages_landed[s], i * (16 * PAGES) + 16 * PAGES)
                        for g in range(2):
                            pool.tensor_copy(
                                pairs[:, :, g, bass.ds(i * 2 + s, 1), :].rearrange(
                                    "p r o (j n) -> p r (o j) n", j=PAGES),
                                raw[:, s, :, :, g, :].rearrange("p j r n -> p r j n")).then_inc(pairs_ready, 1)

            @block.scalar
            def _(act):
                for dst, src in ((w1s, w1), (w2s, w2), (ps_, pos)):
                    act.dma_start(dst[:], src).then_inc(w_landed, 16)
                for g in range(2):
                    act.wait_ge(shuffled, g + 1)
                    act.activation(pairs[:, :, g, SEQS - 1, :].rearrange("p r n -> p n r"),
                                   op[:, g, :].rearrange("p (n r) -> p n r", r=PAIR_STEPS), ACT.Copy
                                   ).then_inc(prompt_ready, 1)
                act.wait_ge(bias_ps, 1)
                act.activation(bias[:], bp[:, 0:2], ACT.Copy).then_inc(bias_ready, 1)
                act.wait_ge(bias_ready, 1)
                j = 0
                for g in range(2):
                    for b0, b1 in halves:
                        for hh in range(2):
                            act.wait_ge(hid_ps, j + 1)
                            act.activation(hid[:, hh, g, b0 * N_CMP:b1 * N_CMP],
                                           hp[:, j % 4, 0:(b1 - b0) * N_CMP], ACT.Silu,
                                           bias=bias[:, hh:hh + 1]).then_inc(hid_ready, 1)
                            j += 1

            @block.tensor
            def _(pe):
                pe.wait_ge(rows_landed, 16)
                for g in range(2):
                    gs = slice(g * HEAD_DIM, (g + 1) * HEAD_DIM)
                    for odd in range(2):
                        mm = pe.matmul(op[odd * HEAD_DIM:(odd + 1) * HEAD_DIM, g, :], core.ident[gs, gs],
                                       rows_t[gs, odd::2], start=True, stop=True)
                    mm.then_inc(shuffled, 1)
                pe.wait_ge(w_landed, 48)
                for hh in range(2):
                    for k in range(2 * PAIR_STEPS):
                        mm = pe.matmul(bp[:, hh:hh + 1], w1s[:, k, hh * P:(hh + 1) * P], ps_[:, k:k + 1],
                                       start=k == 0, stop=k == 2 * PAIR_STEPS - 1)
                mm.then_inc(bias_ps, 1)
                pe.wait_ge(prompt_ready, 2)
                pe.wait_ge(pairs_ready, 2 * DEC_BATCH)
                j = 0
                for g in range(2):
                    for b0, b1 in halves:
                        for hh in range(2):
                            if j >= 4:
                                pe.wait_ge(hid_ready, j - 3)
                            for k in range(2 * PAIR_STEPS):
                                later, r = divmod(k, PAIR_STEPS)
                                mm = pe.matmul(hp[:, j % 4, 0:(b1 - b0) * N_CMP].rearrange(
                                    "p (b n) -> p b n", n=N_CMP), w1s[:, k, hh * P:(hh + 1) * P],
                                    pairs[:, r, g, b0:b1, later:later + N_CMP],
                                    start=k == 0, stop=k == 2 * PAIR_STEPS - 1)
                            mm.then_inc(hid_ps, 1)
                            j += 1
                pe.wait_ge(hid_ready, 8)
                if kv == 0:
                    for n, (b0, b1) in enumerate(halves):
                        cols = slice(b0 * N_CMP, b1 * N_CMP)
                        for g in range(2):
                            for hh in range(2):
                                mm = pe.matmul(op[g * HEAD_DIM:(g + 1) * HEAD_DIM, n, 0:(b1 - b0) * N_CMP],
                                               w2s[:, hh, :], hid[:, hh, g, cols], start=hh == 0, stop=hh == 1)
                    mm.then_inc(out_ps, 1)
                else:
                    for b in range(SEQS):
                        for g in range(2):
                            at = ((b % 4) * 2 + g) * HEAD_DIM
                            for hh in range(2):
                                mm = pe.matmul(op[:N_CMP, b // 4, at:at + HEAD_DIM],
                                               hid[:, hh, g, b * N_CMP:(b + 1) * N_CMP], w2s[:, hh, :],
                                               start=hh == 0, stop=hh == 1)
                    mm.then_inc(out_ps, 1)

            @block.vector
            def _(dve):
                dve.wait_ge(out_ps, 1)
                if kv == 0:
                    for n, (b0, b1) in enumerate(halves):
                        dve.tensor_copy(out[:, b0 * N_CMP:b1 * N_CMP], op[:, n, 0:(b1 - b0) * N_CMP]
                                        ).then_inc(out_ready, 1)
                else:
                    for n in range(3):
                        m = min(4, SEQS - 4 * n) * 2 * HEAD_DIM
                        dve.tensor_copy(out[:N_CMP, n * 512:n * 512 + m], op[:N_CMP, n, 0:m]
                                        ).then_inc(out_ready, 1)


def lay_cmp_pages(a):
    n = a.shape[1]
    return np.ascontiguousarray(a[0].reshape(n, PAGES, PAIR_STEPS, 2, 2, 2, HEAD_DIM)
                                .transpose(4, 0, 3, 6, 2, 5, 1)).reshape(2, n, P, 2 * PAIR_STEPS * PAGES)


def lay_cmp_w1(a):
    return np.ascontiguousarray(a[0].reshape(2, PAIR_STEPS, 2, HEAD_DIM, CMP_HIDDEN).transpose(2, 3, 0, 1, 4)
                                ).reshape(P, 2 * PAIR_STEPS, CMP_HIDDEN)


def lay_cmp_w2(a):
    return np.ascontiguousarray(a[0].reshape(2, P, HEAD_DIM).transpose(1, 0, 2))


def lay_cmp_pos(a):
    return np.ascontiguousarray(a[0].reshape(2 * PAIR_STEPS, 2, HEAD_DIM).transpose(1, 2, 0)).reshape(P, -1)


NSA_HEADS, KV_GROUPS, GROUP_HEADS = 8, 2, 4
WINDOW = 512
BUCKETS, MAX_DIST = 32, 128
ROW_LEN = 400
ZERO_DIST = 255
SKEW, COPIES = ROW_LEN - 1, P * ROW_LEN
CMP_NEAR = 17
SCALE = HEAD_DIM ** -0.5


def make_bucket_rows():
    dist = ZERO_DIST - np.arange(ROW_LEN)
    n = np.maximum(dist, 0)
    exact = BUCKETS // 2
    large = exact + (np.log(np.maximum(n, exact).astype(np.float32) / exact) / np.log(MAX_DIST / exact)
                     * (BUCKETS - exact)).astype(np.int32)
    bucket = np.where(n < exact, n, np.minimum(large, BUCKETS - 1))
    rows = (bucket[None, :] == np.arange(BUCKETS)[:, None]).astype(np.float32)
    rows[BUCKETS - 1] -= 1.0
    return rows


def bias_rows_stage(core, rel_bias, bucket_rows, rows_dram):
    nc = core.nc
    with ExitStack() as ctx:
        sb = lambda name, shape: ctx.enter_context(nc.sbuf_tensor(f"rows_{name}", shape, F32))
        rel, hot = sb("rel", [BUCKETS, NSA_HEADS]), sb("hot", [BUCKETS, ROW_LEN])
        bias, win = sb("bias", [NSA_HEADS, ROW_LEN]), sb("win", [1, ROW_LEN])
        ps = ctx.enter_context(nc.psum_tensor("rows_ps", [P, 512], F32))
        landed, product, filled, stored = map(core.sem, ("rel_landed", "rows_product", "rows_filled", "rows_stored"))
        with nc.Block() as block:

            @block.sync
            def _(sp):
                sp.dma_start(rel[:], rel_bias).then_inc(landed, 16)
                sp.dma_start(hot[:], bucket_rows).then_inc(landed, 16)
                sp.wait_ge(filled, 4)
                for dst, src in ((rows_dram[0:NSA_HEADS], bias), (rows_dram[NSA_HEADS:NSA_HEADS + 1], win)):
                    n = src.shape[0]
                    sp.dma_start(dst, src[:].rearrange("h (o u) -> h o u", o=1).to_broadcast([n, P, ROW_LEN])
                                 ).then_inc(stored, 16)
                sp.wait_ge(stored, 32)

            @block.tensor
            def _(pe):
                pe.wait_ge(landed, 32)
                pe.matmul(ps[:NSA_HEADS, 0:ROW_LEN], rel[:], hot[:], start=True, stop=True).then_inc(product, 1)

            @block.vector
            def _(dve):
                dve.memset(win[:, 0:P], NEG).then_inc(filled, 1)
                dve.memset(win[:, P:], 0.0).then_inc(filled, 1)
                dve.memset(bias[:, ZERO_DIST + 1:], NEG).then_inc(filled, 1)
                dve.wait_ge(product, 1)
                dve.tensor_copy(bias[:, 0:ZERO_DIST + 1], ps[:NSA_HEADS, 0:ZERO_DIST + 1]).then_inc(filled, 1)


def from_rows(rows_dram, offset, dims):
    return bass.AP(rows_dram.tensor, offset, dims)


def prompt_nsa_stage(core, nat, kc, vc, proj, rows_dram, o_t):
    nc = core.nc
    H = NSA_HEADS
    tiles = SEQ // P
    with ExitStack() as ctx:
        sb = lambda name, shape, dt=F32: ctx.enter_context(nc.sbuf_tensor(f"pn_{name}", shape, dt))
        ps = lambda name, n: ctx.enter_context(nc.psum_tensor(f"pn_{name}_ps", [P, n, 512], F32))
        q, ks, kw = sb("q", [P, GROUP_HEADS, SEQ]), sb("ks", [P, SEQ]), sb("kw", [P, SEQ])
        near = sb("near_bias", [P, H, 2 * P])
        win = sb("window_mask", [P, P])
        cmp_width = N_CMP + 8 * (tiles - 1)
        cmpb = sb("cmp_bias", [P, H, cmp_width])
        near0 = 8 * (tiles - 1) - 9
        gates = sb("gates", [P, tiles, H, 3])
        prob = sb("prob", [P, 2, 1024])
        probt = sb("prob_t", [P, 2, 1024])
        neg_max = sb("neg_max", [P, 2, 2])
        sums, rec, mix = sb("sums", [P, 2, 3]), sb("rec", [P, 2, 3]), sb("mix", [P, 2, 3])
        o = sb("o", [P, 2, INNER])
        s_ps, t_ps, o_ps = ps("s", 4), ps("t", 2), ps("o", 2)
        landed, q_ready, gates_ready, cmpb_ready = map(core.sem, ("pn_landed", "q_ready", "gates_ready", "cmpb_ready"))
        s_ready, max_ready, p_ready, t_ready, pt_act, pt_dve = map(
            core.sem, ("s_ready", "max_ready", "p_ready", "t_ready", "pt_act", "pt_dve"))
        pv_ready, rec_ready, mix_ready, part_ready, o_ready, ot_ps, ot_ready = map(
            core.sem, ("pv_ready", "rec_ready", "mix_ready", "o_part_ready", "o_ready", "o_t_ps", "o_t_ready"))

        units = [(i, g, r, b) for i in range(tiles) for r in range(GROUP_HEADS) for g in range(KV_GROUPS)
                 for b in range(2)]
        U = len(units)

        def key_tiles(u):
            i, _, _, b = units[u]
            return range(max(0, i - WINDOW // P) if b else 0, i + 1)

        act_copies, dve_copies = [0], [0]
        for u in range(U):
            n, b = len(key_tiles(u)), units[u][3]
            act_copies.append(act_copies[-1] + (1 if not b else 1 + (n > 4)))
            dve_copies.append(dve_copies[-1] + (n > 4 if not b else 1))

        with nc.Block() as block:

            @block.sync
            def _(sp):
                sp.dma_start(q[:], proj[12:16, :, 0:SEQ].rearrange("i p t -> p i t")).then_inc(landed, 16)
                sp.dma_start(ks[:], proj[KV_TILE0 + 2, :, 0:SEQ]).then_inc(landed, 16)
                sp.dma_start(kw[:], proj[KV_TILE0 + 3, :, 0:SEQ]).then_inc(landed, 16)
                sp.dma_start(near[:], from_rows(rows_dram, P - 1, [[SKEW, P], [COPIES, H], [1, 2 * P]])
                             ).then_inc(landed, 16)
                sp.dma_start(win[:], from_rows(rows_dram, H * COPIES + P - 1, [[SKEW, P], [1, P]])
                             ).then_inc(landed, 16)
                for h in range(H):
                    sp.dma_start(cmpb[:, h, near0:near0 + CMP_NEAR],
                                 from_rows(rows_dram, h * COPIES + ZERO_DIST + CMP_BLOCK - 1 - 9 * CMP_STRIDE,
                                           [[SKEW, P], [CMP_STRIDE, CMP_NEAR]]),
                                 allow_slow_non_contiguous=True).then_inc(landed, 16)

            @block.gpsimd
            def _(pool):
                pool.memset(cmpb[:, :, 0:near0], 0.0).then_inc(cmpb_ready, 1)
                pool.memset(cmpb[:, :, near0 + CMP_NEAR:], NEG).then_inc(cmpb_ready, 1)

            @block.tensor
            def _(pe):
                def scores(u):
                    i, g, r, b = units[u]
                    h = g * GROUP_HEADS + r
                    gs = slice(g * HEAD_DIM, (g + 1) * HEAD_DIM)
                    qs = q[gs, r, i * P:(i + 1) * P]
                    keys = kw if b else ks
                    kt = key_tiles(u)
                    s = 2 * (u % 2)
                    if u >= 2:
                        pe.wait_ge(p_ready, u - 1)
                    for c in range(0, len(kt), 4):
                        part = kt[c:c + 4]
                        bank = s_ps[:, s + c // 4, :]
                        mm = pe.matmul(bank[:, 0:len(part) * P], qs, keys[gs, part[0] * P:(part[-1] + 1) * P],
                                       start=True, stop=True)
                        for n, j in enumerate(part):
                            at = bank[:, n * P:(n + 1) * P]
                            if i - j < 2:
                                mm = pe.matmul(at, core.ident[:], near[:, h, (1 - i + j) * P:(2 - i + j) * P],
                                               start=False, stop=True, skip_group_check=True)
                            if b and i - j == WINDOW // P:
                                mm = pe.matmul(at, core.ident[:], win[:], start=False, stop=True,
                                               skip_group_check=True)
                    if b:
                        at = s_ps[:, s + 1, P:P + N_CMP]
                        pe.matmul(at, qs, kc[gs, DEC_BATCH * N_CMP:], start=True, stop=False)
                        c0 = 8 * (tiles - 1 - i)
                        mm = pe.matmul(at, core.ident[:], cmpb[:, h, c0:c0 + N_CMP], start=False, stop=True)
                    mm.then_inc(s_ready, 1)

                def turn(u):
                    pe.wait_ge(p_ready, u + 1)
                    pe.wait_ge(pt_act, act_copies[u])
                    pe.wait_ge(pt_dve, dve_copies[u])
                    if units[u][1:] == (0, 0, 0) and units[u][0]:
                        pe.wait_ge(ot_ready, units[u][0])
                    for n in range(len(key_tiles(u))):
                        mm = pe.transpose(t_ps[:, n // 4, (n % 4) * P:(n % 4 + 1) * P],
                                          prob[:, u % 2, n * P:(n + 1) * P], core.ident[:])
                    if units[u][3]:
                        mm = pe.transpose(t_ps[:N_CMP, 1, P:2 * P], prob[:, u % 2, 5 * P:5 * P + N_CMP],
                                          core.ident[:])
                    mm.then_inc(t_ready, 1)

                def values(u):
                    i, g, r, b = units[u]
                    n = u // 2
                    pe.wait_ge(pt_act, act_copies[u + 1])
                    pe.wait_ge(pt_dve, dve_copies[u + 1])
                    if not b and n >= 2:
                        pe.wait_ge(o_ready, n - 1)
                    kt = key_tiles(u)
                    at = o_ps[:, n % 2, (1 + b) * HEAD_DIM:(2 + b) * HEAD_DIM]
                    vcol = b * P + g * HEAD_DIM
                    for m, j in enumerate(kt):
                        mm = pe.matmul(at, probt[:, u % 2, m * P:(m + 1) * P], nat[:, j, vcol:vcol + HEAD_DIM],
                                       start=m == 0, stop=m == len(kt) - 1)
                    if b:
                        vg = (DEC_BATCH * 2 + g) * HEAD_DIM
                        mm = pe.matmul(o_ps[:, n % 2, 0:HEAD_DIM], probt[:N_CMP, u % 2, 5 * P:6 * P],
                                       vc[:N_CMP, vg:vg + HEAD_DIM], start=True, stop=True)
                    mm.then_inc(pv_ready, 1)

                def turn_output(i):
                    pe.wait_ge(o_ready, (i + 1) * H)
                    for r in range(GROUP_HEADS):
                        mm = pe.transpose(t_ps[:, 0, r * P:(r + 1) * P], o[:, i % 2, r * P:(r + 1) * P],
                                          core.ident[:])
                    mm.then_inc(ot_ps, 1)

                pe.wait_ge(landed, 16 * (5 + H))
                pe.wait_ge(cmpb_ready, 2)
                pe.wait_ge(q_ready, 1)
                scores(0)
                scores(1)
                for u in range(U):
                    turn(u)
                    if u + 2 < U:
                        scores(u + 2)
                    values(u)
                    if u % (2 * H) == 2 * H - 1:
                        turn_output(units[u][0])

            @block.scalar
            def _(act):
                act.wait_ge(landed, 16 * (5 + H))
                act.activation(q[:], q[:], ACT.Copy, scale=SCALE).then_inc(q_ready, 1)
                act.activation(gates[:].rearrange("p t h c -> p t (h c)"), nat[:, 0:tiles, 264:288], ACT.Sigmoid
                               ).then_inc(gates_ready, 1)

                def exp(u):
                    i, g, r, b = units[u]
                    n = u // 2
                    w = len(key_tiles(u)) * P
                    s = s_ps[:, 2 * (u % 2):2 * (u % 2) + 2, :].rearrange("p a c -> p (a c)")
                    act.wait_ge(max_ready, u + 1)
                    if u >= 2:
                        act.wait_ge(t_ready, u - 1)
                    if n >= 2:
                        act.wait_ge(rec_ready, n - 1)
                    e = act.activation(prob[:, u % 2, 0:w], s[:, 0:w], ACT.Exp, bias=neg_max[:, u % 2, 0:1],
                                       accum_out=sums[:, n % 2, 1 + b:2 + b])
                    if b:
                        e = act.activation(prob[:, u % 2, 5 * P:5 * P + N_CMP], s[:, 5 * P:5 * P + N_CMP],
                                           ACT.Exp, bias=neg_max[:, u % 2, 1:2], accum_out=sums[:, n % 2, 0:1])
                    e.then_inc(p_ready, 1)

                def copy(u):
                    n, b = len(key_tiles(u)), units[u][3]
                    act.wait_ge(t_ready, u + 1)
                    if u >= 2:
                        act.wait_ge(pv_ready, u - 1)
                    if not b:
                        w = min(n, 4) * P
                        act.activation(probt[:, u % 2, 0:w], t_ps[:, 0, 0:w], ACT.Copy).then_inc(pt_act, 1)
                    else:
                        if n > 4:
                            act.activation(probt[:, u % 2, 4 * P:5 * P], t_ps[:, 1, 0:P], ACT.Copy
                                           ).then_inc(pt_act, 1)
                        act.activation(probt[:N_CMP, u % 2, 5 * P:6 * P], t_ps[:N_CMP, 1, P:2 * P], ACT.Copy
                                       ).then_inc(pt_act, 1)

                exp(0)
                for u in range(U):
                    if u + 1 < U:
                        exp(u + 1)
                    copy(u)
                    if u % (2 * H) == 2 * H - 1:
                        i = units[u][0]
                        act.wait_ge(ot_ps, i + 1)
                        act.activation(o_t[:, :, i * P:(i + 1) * P],
                                       t_ps[:, 0, :].rearrange("p (r t) -> p r t", t=P), ACT.Copy
                                       ).then_inc(ot_ready, 1)

            @block.vector
            def _(dve):
                def maxima(u):
                    b = units[u][3]
                    w = len(key_tiles(u)) * P
                    s = s_ps[:, 2 * (u % 2):2 * (u % 2) + 2, :].rearrange("p a c -> p (a c)")
                    dve.wait_ge(s_ready, u + 1)
                    m = dve.tensor_reduce(neg_max[:, u % 2, 0:1], s[:, 0:w], AX_X, ALU.max, negate=True)
                    if b:
                        m = dve.tensor_reduce(neg_max[:, u % 2, 1:2], s[:, 5 * P:5 * P + N_CMP], AX_X, ALU.max,
                                              negate=True)
                    m.then_inc(max_ready, 1)

                def copy(u):
                    n, b = len(key_tiles(u)), units[u][3]
                    dve.wait_ge(t_ready, u + 1)
                    if u >= 2:
                        dve.wait_ge(pv_ready, u - 1)
                    if b:
                        w = min(n, 4) * P
                        dve.tensor_copy(probt[:, u % 2, 0:w], t_ps[:, 0, 0:w]).then_inc(pt_dve, 1)
                    elif n > 4:
                        dve.tensor_copy(probt[:, u % 2, 4 * P:n * P], t_ps[:, 1, 0:(n - 4) * P]
                                        ).then_inc(pt_dve, 1)

                def weights(n):
                    i, g, r, _ = units[2 * n]
                    h = g * GROUP_HEADS + r
                    dve.wait_ge(p_ready, 2 * n + 2)
                    dve.reciprocal(rec[:, n % 2, :], sums[:, n % 2, :]).then_inc(rec_ready, 1)
                    dve.wait_ge(rec_ready, n + 1)
                    mixed = dve.tensor_tensor(mix[:, n % 2, :], rec[:, n % 2, :], gates[:, i, h, :], ALU.mult)
                    if i == 0:
                        mixed.then_inc(mix_ready, 1)
                        dve.wait_ge(mix_ready, 2 * n + 1)
                        mixed = dve.tensor_tensor(mix[:, n % 2, 0:1], mix[:, n % 2, 0:1], core.sees_cmp[:],
                                                  ALU.mult)
                    mixed.then_inc(mix_ready, 1)

                def mix_count(n):
                    return 2 * (n + 1) if n < H else n + 1 + H

                def combine(n):
                    i, g, r, _ = units[2 * n]
                    at = o[:, i % 2, (2 * r + g) * HEAD_DIM:(2 * r + g + 1) * HEAD_DIM]
                    dve.wait_ge(mix_ready, mix_count(n))
                    dve.wait_ge(pv_ready, 2 * n + 2)
                    if i >= 2:
                        dve.wait_ge(ot_ps, i - 1)
                    for k in range(3):
                        part = o_ps[:, n % 2, k * HEAD_DIM:(k + 1) * HEAD_DIM]
                        if k == 0:
                            dve.tensor_scalar(at, part, mix[:, n % 2, 0:1], None, ALU.mult
                                              ).then_inc(part_ready, 1)
                        else:
                            dve.wait_ge(part_ready, 2 * n + k)
                            dve.scalar_tensor_tensor(at, part, mix[:, n % 2, k:k + 1], at, ALU.mult, ALU.add
                                                     ).then_inc(part_ready if k == 1 else o_ready, 1)

                dve.wait_ge(gates_ready, 1)
                maxima(0)
                for u in range(U):
                    if u + 1 < U:
                        maxima(u + 1)
                    copy(u)
                    if units[u][3]:
                        weights(u // 2)
                    elif u % (2 * H):
                        combine(u // 2 - 1)
                    if u % (2 * H) == 2 * H - 1:
                        combine(u // 2)


SLC_BLOCK = 64
PAST = SEQ
N_SLC = -(-(PAST + DEC_SEQ) // SLC_BLOCK)
FREE_BLOCKS = N_SLC - 3
NEW = SAMPLE
PAIRS = DEC_BATCH // 2
RULES = P + N_SLC + FREE_BLOCKS


def make_rules():
    c = np.zeros((P, RULES), np.float32)
    i = np.arange(P)
    key = (i // 32) * DEC_SEQ + i % DEC_SEQ
    c[:, :P] = key[:, None] == key[None, :]
    start = np.arange(N_CMP) * CMP_STRIDE
    block = np.arange(N_SLC) * SLC_BLOCK
    c[:N_CMP, P:P + N_SLC] = (start[:, None] < block[None, :] + SLC_BLOCK) & \
        (start[:, None] + CMP_BLOCK - 1 >= block[None, :])
    c[:, P + N_SLC:] = 1.0 + np.arange(FREE_BLOCKS)
    return c


def sample_nsa_stage(core, nat, kc, vc, proj, rows_dram, rules, page_table, slc_pages, win_kv, gates_dram,
                     o_t, n_pool):
    nc = core.nc
    H = NSA_HEADS
    G = GROUP_HEADS * DEC_SEQ
    with ExitStack() as ctx:
        sb = lambda name, shape, dt=F32: ctx.enter_context(nc.sbuf_tensor(f"sn_{name}", shape, dt))
        ps = lambda name, n: ctx.enter_context(nc.psum_tensor(f"sn_{name}_ps", [P, n, 512], F32))
        q_in, q = sb("q_in", [P, GROUP_HEADS, NEW]), sb("q", [P, DEC_BATCH, G])
        ks, kw = sb("ks_new", [P, NEW]), sb("kw_new", [P, NEW])
        rule = sb("rules", [P, RULES])
        table = sb("page_table", [1, DEC_BATCH * PAGES], I32)
        past = sb("slc_pages", [P, 2, 2, PAGES, 2 * P])
        win = sb("win_kv", [P, 2, 2, 2 * WINDOW])
        near, edge, cmpb = sb("near", [P, P]), sb("window_edge", [P, DEC_SEQ]), sb("cmp_bias", [P, N_CMP])
        newb = sb("new_bias", [P, PAIRS, NEW])
        gate_nat, gates = sb("gate_nat", [NEW, 3 * H]), sb("gates", [P, PAIRS, 3])
        pc, pcn = sb("p_cmp", [P, PAIRS, N_CMP]), sb("p_cmp_normed", [P, PAIRS, N_CMP])
        pct = sb("p_cmp_t", [P, PAIRS, P])
        imp, least, ranked, last, drop = (sb("imp", [P, PAIRS, N_SLC]), sb("least", [P, PAIRS]),
                                          sb("ranked", [P, PAIRS, FREE_BLOCKS]), sb("last", [P, PAIRS]),
                                          sb("drop", [P, PAIRS, FREE_BLOCKS]))
        ncm, csum, crec = sb("cmp_neg_max", [P, PAIRS]), sb("cmp_sum", [P, PAIRS]), sb("cmp_rec", [P, PAIRS])
        parts, neg_max, sums, total = (sb("max_parts", [P, 2, 2]), sb("neg_max", [P, 2]),
                                       sb("sums", [P, 2, 2]), sb("sum_total", [P, 2]))
        mix = sb("mix", [P, 2])
        PW = PAST + NEW + WINDOW + NEW + N_CMP
        W0, C0 = PAST + NEW, PAST + NEW + WINDOW + NEW
        prob, probt = sb("prob", [P, PW]), sb("prob_t", [P, 16, P])
        s_ps, t_ps, o_ps, m_ps = ps("s", 4), ps("t", 2), ps("o", 1), ps("m", 1)

        landed, filled, gate_done, gate_stored, q_ready, table_landed = map(
            core.sem, ("sn_landed", "sn_filled", "gate_sigmoid", "gate_stored", "sn_q_ready", "sn_table"))
        new_landed = core.sem("new_bias_landed")
        past_landed = [core.sem(f"past_landed_{s}") for s in range(2)]
        c_ready, cmax, pc_ready, crec_ready, pcn_ready, pct_ps, pct_ready, imp_ps, imp_ready, impg_ps = map(
            core.sem, ("c_scores", "c_max", "pc_ready", "c_rec", "pcn_ready", "pct_ps", "pct_ready", "imp_ps",
                       "imp_ready", "imp_group_ps"))
        rank, drop_ready = map(core.sem, ("rank_steps", "drop_ready"))
        s_ready, dropped, parts_ready, max_ready, p_ready, total_ready, rec_ready, mix_ready, scaled = map(
            core.sem, ("sn_s_ready", "dropped", "max_parts_ready", "sn_max_ready", "sn_p_ready",
                       "sn_total", "sn_rec", "sn_mix", "sn_scaled"))
        t_ready, pt_act, pt_dve, pv_ready, o_ready = map(
            core.sem, ("sn_t_ready", "sn_pt_act", "sn_pt_dve", "sn_pv_ready", "sn_o_ready"))

        with nc.Block() as block:

            @block.sync
            def _(sp):
                sp.dma_start(table[:], page_table).then_inc(table_landed, 16)
                sp.dma_start(q_in[:], proj[12:16, :, SEQ:TOKENS].rearrange("i p t -> p i t")).then_inc(landed, 16)
                sp.dma_start(ks[:], proj[KV_TILE0 + 2, :, SEQ:TOKENS]).then_inc(landed, 16)
                sp.dma_start(kw[:], proj[KV_TILE0 + 3, :, SEQ:TOKENS]).then_inc(landed, 16)
                sp.dma_start(rule[:], rules).then_inc(landed, 16)
                sp.wait_ge(table_landed, 16)

                def load(bt):
                    s = bt % 2
                    if bt >= 2:
                        sp.wait_ge(pv_ready, bt - 1)
                    for b2 in range(2):
                        b = 2 * bt + b2
                        for j in range(PAGES):
                            page = sp.value_load(table[0:1, b * PAGES + j:b * PAGES + j + 1],
                                                 min_val=0, max_val=n_pool - 1)
                            sp.dma_start(past[:, s, b2, j, :],
                                         slc_pages[bass.ds(page, 1)].rearrange("o p c -> (o p) c")
                                         ).then_inc(past_landed[s], 16)
                        sp.dma_start(win[:, s, b2, :], win_kv[b]).then_inc(past_landed[s], 16)

                for bt in range(PAIRS):
                    load(bt)

            @block.gpsimd
            def _(pool):
                pool.memset(newb[:], NEG).then_inc(filled, 1)
                pool.memset(cmpb[:, 0:N_CMP - 8], 0.0).then_inc(filled, 1)
                pool.wait_ge(landed, 16 * 8)
                pool.tensor_copy(cmpb[:, N_CMP - 8:], near[:, CMP_STRIDE - 1::CMP_STRIDE]).then_inc(filled, 1)
                pool.wait_ge(q_ready, 1)
                for r in range(GROUP_HEADS):
                    pool.tensor_copy(q[:, :, r * DEC_SEQ:(r + 1) * DEC_SEQ],
                                     q_in[:, r, :].rearrange("p (b t) -> p b t", t=DEC_SEQ)).then_inc(q_ready, 1)

            @block.scalar
            def _(act):
                act.activation(gate_nat[:], nat[:NEW, TOK_TILES - 1, 264:288], ACT.Sigmoid).then_inc(gate_done, 1)
                act.wait_ge(gate_done, 1)
                act.dma_start(gates_dram, gate_nat[:]).then_inc(gate_stored, 16)
                half = H * DEC_SEQ
                for b2 in range(2):
                    rows = slice(b2 * half, (b2 + 1) * half)
                    act.dma_start(near[rows, :], from_rows(rows_dram, P - 1, [[COPIES, H], [SKEW, DEC_SEQ], [1, P]])
                                  ).then_inc(landed, 16)
                    act.dma_start(edge[rows, :], from_rows(rows_dram, H * COPIES + P - 1,
                                                           [[0, H], [SKEW, DEC_SEQ], [1, DEC_SEQ]])
                                  ).then_inc(landed, 16)
                act.wait_ge(filled, 2)
                for bt in range(PAIRS):
                    for b2 in range(2):
                        b = 2 * bt + b2
                        rows = slice(b2 * half, (b2 + 1) * half)
                        act.dma_start(newb[rows, bt, b * DEC_SEQ:(b + 1) * DEC_SEQ], from_rows(
                            rows_dram, 2 * P - 1, [[COPIES, H], [SKEW, DEC_SEQ], [1, DEC_SEQ]])
                                      ).then_inc(new_landed, 16)
                act.wait_ge(gate_stored, 16)
                for bt in range(PAIRS):
                    for b2 in range(2):
                        b = 2 * bt + b2
                        rows = slice(b2 * half, (b2 + 1) * half)
                        act.dma_start(gates[rows, bt, :], bass.AP(
                            gates_dram.tensor, b * DEC_SEQ * 3 * H, [[3, H], [3 * H, DEC_SEQ], [1, 3]])
                                      ).then_inc(new_landed, 16)
                act.wait_ge(landed, 16 * 8)
                act.activation(q_in[:], q_in[:], ACT.Copy, scale=SCALE).then_inc(q_ready, 1)
                act.wait_ge(cmax, 1)
                for bt in range(PAIRS):
                    act.activation(pc[:, bt, :], m_ps[:, 0, bt * N_CMP:(bt + 1) * N_CMP], ACT.Exp,
                                   bias=ncm[:, bt:bt + 1], accum_out=csum[:, bt:bt + 1]).then_inc(pc_ready, 1)
                act.wait_ge(pct_ps, 1)
                act.activation(pct[:N_CMP].rearrange("p b c -> p (b c)"), t_ps[:N_CMP, 0, :], ACT.Copy
                               ).then_inc(pct_ready, 1)
                for bt in range(PAIRS):
                    act.wait_ge(max_ready, bt + 1)
                    if bt:
                        act.wait_ge(t_ready, 4 * bt)
                        act.wait_ge(total_ready, bt)
                    for br, (c0, bank, n) in enumerate(((0, 0, PAST), (W0, 2, WINDOW))):
                        act.activation(prob[:, c0:c0 + n], s_ps[:, bank:bank + n // 512, :].rearrange(
                            "p a c -> p (a c)"), ACT.Exp, bias=neg_max[:, br:br + 1],
                            accum_out=sums[:, br, 0:1])
                        e = act.activation(prob[:, c0 + n:c0 + n + NEW], s_ps[:, 3, br * NEW:(br + 1) * NEW],
                                           ACT.Exp, bias=neg_max[:, br:br + 1], accum_out=sums[:, br, 1:2])
                    e.then_inc(p_ready, 1)
                    for n in range(0, 4, 2):
                        act.wait_ge(t_ready, 4 * bt + n + 1)
                        if bt:
                            act.wait_ge(pv_ready, bt)
                        act.activation(probt[:, 4 * n:4 * n + 4, :].rearrange("p a c -> p (a c)"), t_ps[:, 0, :],
                                       ACT.Copy).then_inc(pt_act, 1)

            @block.tensor
            def _(pe):
                def row(b2, g):
                    return slice((2 * b2 + g) * G, (2 * b2 + g + 1) * G)

                def group(g):
                    return slice(g * HEAD_DIM, (g + 1) * HEAD_DIM)

                every = [(b2, g) for b2 in range(2) for g in range(KV_GROUPS)]
                pe.wait_ge(q_ready, 1 + GROUP_HEADS)
                pe.wait_ge(landed, 16 * 8)
                pe.wait_ge(filled, 3)
                for bt in range(PAIRS):
                    at = m_ps[:, 0, bt * N_CMP:(bt + 1) * N_CMP]
                    for b2, g in every:
                        b = 2 * bt + b2
                        pe.matmul(at[row(b2, g)], q[group(g), b, :], kc[group(g), b * N_CMP:(b + 1) * N_CMP],
                                  start=True, stop=True)
                    mm = pe.matmul(at, core.ident[:], cmpb[:], start=False, stop=True, skip_group_check=True)
                mm.then_inc(c_ready, 1)
                pe.wait_ge(pcn_ready, PAIRS)
                for bt in range(PAIRS):
                    mm = pe.transpose(t_ps[:N_CMP, 0, bt * P:(bt + 1) * P], pcn[:, bt, :], core.ident[:])
                mm.then_inc(pct_ps, 1)
                pe.wait_ge(pct_ready, 1)
                for bt in range(PAIRS):
                    mm = pe.matmul(m_ps[:, 0, bt * N_SLC:(bt + 1) * N_SLC], pct[:N_CMP, bt, :],
                                   rule[:N_CMP, P:P + N_SLC], start=True, stop=True)
                mm.then_inc(imp_ps, 1)
                pe.wait_ge(imp_ready, 1)
                pe.matmul(m_ps[:, 0, 256:256 + PAIRS * N_SLC], rule[:, 0:P],
                          imp[:].rearrange("p b s -> p (b s)"), start=True, stop=True).then_inc(impg_ps, 1)
                pe.wait_ge(new_landed, 16 * 16)
                for bt in range(PAIRS):
                    s = bt % 2
                    pe.wait_ge(past_landed[s], 16 * 2 * (PAGES + 1) * (bt // 2 + 1))
                    if bt:
                        pe.wait_ge(p_ready, bt)
                    for half in range(2):
                        for b2, g in every:
                            pe.matmul(s_ps[row(b2, g), half, :].rearrange("p (j t) -> p j t", t=P),
                                      q[group(g), 2 * bt + b2, :], past[group(g), s, b2, 4 * half:4 * half + 4, 0:P],
                                      start=True, stop=True)
                    pe.matmul(s_ps[:, 1, 3 * P:], core.ident[:], near[:], start=False, stop=True,
                              skip_group_check=True)
                    for b2, g in every:
                        pe.matmul(s_ps[row(b2, g), 2, :], q[group(g), 2 * bt + b2, :], win[group(g), s, b2, 0:WINDOW],
                                  start=True, stop=True)
                    pe.matmul(s_ps[:, 2, 3 * P:], core.ident[:], near[:], start=False, stop=True,
                              skip_group_check=True)
                    pe.matmul(s_ps[:, 2, 0:DEC_SEQ], core.ident[:], edge[:], start=False, stop=True,
                              skip_group_check=True)
                    for br, keys in enumerate((ks, kw)):
                        at = s_ps[:, 3, br * NEW:(br + 1) * NEW]
                        for b2, g in every:
                            pe.matmul(at[row(b2, g)], q[group(g), 2 * bt + b2, :], keys[group(g), :],
                                      start=True, stop=True)
                        mm = pe.matmul(at, core.ident[:], newb[:, bt, :], start=False, stop=True,
                                       skip_group_check=True)
                    mm.then_inc(s_ready, 1)
                    pe.wait_ge(scaled, 3 * (bt + 1))
                    for n in range(4):
                        if n >= 2 or bt:
                            if n % 2 == 0:
                                pe.wait_ge(pt_act, 2 * bt + n // 2)
                            else:
                                pe.wait_ge(pt_dve, 2 * bt + n // 2)
                        if n < 3:
                            c0 = (0, 4 * P, W0)[n]
                            for m in range(4):
                                mm = pe.transpose(t_ps[:, n % 2, m * P:(m + 1) * P],
                                                  prob[:, c0 + m * P:c0 + (m + 1) * P], core.ident[:])
                        else:
                            for m, (c0, w) in enumerate(((PAST, NEW), (W0 + WINDOW, NEW), (C0, N_CMP))):
                                mm = pe.transpose(t_ps[:w, 1, m * P:(m + 1) * P], prob[:, c0:c0 + w], core.ident[:])
                        mm.then_inc(t_ready, 1)
                    pe.wait_ge(pt_act, 2 * bt + 2)
                    pe.wait_ge(pt_dve, 2 * bt + 2)
                    for b2, g in every:
                        b = 2 * bt + b2
                        at = o_ps[group(g), 0, 0:GROUP_HEADS * NEW].rearrange("p (r t) -> p r t", t=NEW)[
                            :, :, b * DEC_SEQ:(b + 1) * DEC_SEQ]
                        tiles = [(past[:, s, b2, j, P + g * HEAD_DIM:P + (g + 1) * HEAD_DIM], P, j)
                                 for j in range(PAGES)]
                        tiles += [(win[:, s, b2, WINDOW + j * P + g * HEAD_DIM:WINDOW + j * P + (g + 1) * HEAD_DIM],
                                   P, 8 + j) for j in range(WINDOW // P)]
                        tiles += [(nat[:NEW, TOK_TILES - 1, br * P + g * HEAD_DIM:br * P + (g + 1) * HEAD_DIM],
                                   NEW, 12 + br) for br in range(2)]
                        tiles += [(vc[:N_CMP, (2 * b + g) * HEAD_DIM:(2 * b + g + 1) * HEAD_DIM], N_CMP, 14)]
                        for n, (v, k, slot) in enumerate(tiles):
                            mm = pe.matmul(at, v, probt[:k, slot, row(b2, g)].rearrange(
                                "p (r t) -> p r t", t=DEC_SEQ), start=n == 0, stop=n == len(tiles) - 1)
                    mm.then_inc(pv_ready, 1)

            @block.vector
            def _(dve):
                dve.wait_ge(c_ready, 1)
                dve.tensor_reduce(ncm[:], m_ps[:, 0, 0:PAIRS * N_CMP].rearrange("p (b n) -> p b n", n=N_CMP), AX_X,
                                  ALU.max, negate=True).then_inc(cmax, 1)
                dve.wait_ge(pc_ready, PAIRS)
                dve.reciprocal(crec[:], csum[:]).then_inc(crec_ready, 1)
                dve.wait_ge(crec_ready, 1)
                for bt in range(PAIRS):
                    dve.tensor_scalar(pcn[:, bt, :], pc[:, bt, :], crec[:, bt:bt + 1], None, ALU.mult
                                      ).then_inc(pcn_ready, 1)
                dve.wait_ge(imp_ps, 1)
                dve.tensor_copy(imp[:].rearrange("p b s -> p (b s)"), m_ps[:, 0, 0:PAIRS * N_SLC]
                                ).then_inc(imp_ready, 1)
                dve.wait_ge(impg_ps, 1)
                ranks = m_ps[:, 0, 256:256 + PAIRS * N_SLC].rearrange("p (b s) -> p b s", s=N_SLC)[
                    :, :, 1:1 + FREE_BLOCKS]
                number = rule[:, P + N_SLC:]
                dve.tensor_reduce(least[:], ranks, AX_X, ALU.min).then_inc(rank, 1)
                dve.wait_ge(rank, 1)
                for bt in range(PAIRS):
                    dve.scalar_tensor_tensor(ranked[:, bt, :], ranks[:, bt, :], least[:, bt:bt + 1], number,
                                             ALU.is_le, ALU.mult).then_inc(rank, 1)
                dve.wait_ge(rank, 1 + PAIRS)
                dve.tensor_reduce(last[:], ranked[:], AX_X, ALU.max).then_inc(rank, 1)
                dve.wait_ge(rank, 2 + PAIRS)
                for bt in range(PAIRS):
                    dve.tensor_scalar(drop[:, bt, :], number, last[:, bt:bt + 1], NEG, ALU.is_equal, ALU.mult
                                      ).then_inc(drop_ready, 1)
                dve.wait_ge(drop_ready, PAIRS)
                dve.wait_ge(new_landed, 16 * 16)
                for bt in range(PAIRS):
                    dve.wait_ge(s_ready, bt + 1)
                    flat = s_ps[:, 0:2, :].rearrange("p a c -> p (a c)")
                    ranked_keys = flat[:, SLC_BLOCK:SLC_BLOCK * (1 + FREE_BLOCKS)].rearrange(
                        "p (s t) -> p s t", t=SLC_BLOCK)
                    dve.tensor_tensor(ranked_keys, ranked_keys,
                                      drop[:, bt, :].rearrange("p (s o) -> p s o", o=1).to_broadcast(
                                          [P, FREE_BLOCKS, SLC_BLOCK]), ALU.add).then_inc(dropped, 1)
                    dve.wait_ge(dropped, bt + 1)
                    dve.tensor_reduce(parts[:, 0, 0:1], flat, AX_X, ALU.max, negate=True)
                    dve.tensor_reduce(parts[:, 0, 1:2], s_ps[:, 2, :], AX_X, ALU.max, negate=True)
                    dve.tensor_reduce(parts[:, 1, :], s_ps[:, 3, 0:2 * NEW].rearrange("p (b t) -> p b t", t=NEW),
                                      AX_X, ALU.max, negate=True).then_inc(parts_ready, 1)
                    dve.wait_ge(parts_ready, bt + 1)
                    dve.tensor_tensor(neg_max[:], parts[:, 0, :], parts[:, 1, :], ALU.min).then_inc(max_ready, 1)
                    dve.wait_ge(p_ready, bt + 1)
                    dve.tensor_tensor(total[:], sums[:, :, 0], sums[:, :, 1], ALU.add).then_inc(total_ready, 1)
                    dve.wait_ge(total_ready, bt + 1)
                    dve.reciprocal(total[:], total[:]).then_inc(rec_ready, 1)
                    dve.wait_ge(rec_ready, bt + 1)
                    dve.tensor_tensor(mix[:], total[:], gates[:, bt, 1:3], ALU.mult).then_inc(mix_ready, 1)
                    dve.wait_ge(mix_ready, bt + 1)
                    dve.tensor_scalar(prob[:, 0:W0], prob[:, 0:W0], mix[:, 0:1], None, ALU.mult).then_inc(scaled, 1)
                    dve.tensor_scalar(prob[:, W0:C0], prob[:, W0:C0], mix[:, 1:2], None, ALU.mult
                                      ).then_inc(scaled, 1)
                    dve.tensor_scalar(prob[:, C0:], pcn[:, bt, :], gates[:, bt, 0:1], None, ALU.mult
                                      ).then_inc(scaled, 1)
                    for n in range(1, 4, 2):
                        dve.wait_ge(t_ready, 4 * bt + n + 1)
                        if bt:
                            dve.wait_ge(pv_ready, bt)
                        if n == 1:
                            dve.tensor_copy(probt[:, 4:8, :].rearrange("p a c -> p (a c)"), t_ps[:, 1, :]
                                            ).then_inc(pt_dve, 1)
                        else:
                            dve.tensor_copy(probt[:NEW, 12:14, :].rearrange("p a c -> p (a c)"),
                                            t_ps[:NEW, 1, 0:2 * P])
                            dve.tensor_copy(probt[:N_CMP, 14, :], t_ps[:N_CMP, 1, 2 * P:3 * P]).then_inc(pt_dve, 1)
                dve.wait_ge(pv_ready, PAIRS)
                dve.tensor_copy(o_t[:, :, SEQ:TOKENS],
                                o_ps[:, 0, 0:GROUP_HEADS * NEW].rearrange("p (r t) -> p r t", t=NEW)
                                ).then_inc(o_ready, 1)
                dve.memset(o_t[:, :, TOKENS:], 0.0).then_inc(o_ready, 1)


def lay_slc_pages(a):
    k = a[0, :, :, 0].reshape(-1, P, P).transpose(0, 2, 1)
    return np.ascontiguousarray(np.concatenate([k, a[0, :, :, 1].reshape(-1, P, P)], axis=2))


def lay_win(a):
    k = a[0, :, :, 0].reshape(DEC_BATCH, WINDOW, P).transpose(0, 2, 1)
    v = a[0, :, :, 1].reshape(DEC_BATCH, WINDOW // P, P, P).transpose(0, 2, 1, 3).reshape(DEC_BATCH, P, WINDOW)
    return np.ascontiguousarray(np.concatenate([k, v], axis=2))


MEM_TOKENS, MEM_HEADS = 256, 4
MT = MEM_TOKENS // P
MI = MEM_HEADS * HEAD_DIM


def mem_kv_stage(core, m_hi, m_lo, w, kt_out, v_out):
    nc = core.nc
    with ExitStack() as ctx:
        sb = lambda name, shape, dt=F32: ctx.enter_context(nc.sbuf_tensor(f"mkv_{name}", shape, dt))
        raw = sb("w_raw", [P, KT, 2 * MI])
        w_hi, w_lo = sb("w_hi", [P, KT, 2 * MI], F32R), sb("w_lo", [P, KT, 2 * MI], F32R)
        out = sb("out", [P, 2 * MT, MI])
        ps = ctx.enter_context(nc.psum_tensor("mkv_ps", [P, 2 * MT, 512], F32))
        landed, hi_ready, lo_ready, ps_ready, out_ready, stored = map(
            core.sem, ("mkv_landed", "mkv_hi", "mkv_lo", "mkv_ps_ready", "mkv_out", "mkv_stored"))
        with nc.Block() as block:

            @block.sync
            def _(sp):
                sp.dma_start(raw[:], w).then_inc(landed, 16)
                for n in range(2 * MT):
                    sp.wait_ge(out_ready, n + 1)
                    sp.dma_start((kt_out if n < MT else v_out)[:, n % MT, :], out[:, n, :]).then_inc(stored, 16)
                sp.wait_ge(stored, 16 * 2 * MT)

            @block.scalar
            def _(act):
                act.wait_ge(landed, 16)
                act.activation(w_hi[:], raw[:], ACT.Copy).then_inc(hi_ready, 1)

            @block.vector
            def _(dve):
                dve.wait_ge(hi_ready, 1)
                dve.tensor_tensor(w_lo[:], raw[:], w_hi[:].bitcast(F32), ALU.subtract).then_inc(lo_ready, 1)
                for n in range(2 * MT):
                    dve.wait_ge(ps_ready, n + 1)
                    dve.tensor_copy(out[:, n, :], ps[:, n, 0:MI]).then_inc(out_ready, 1)

            @block.tensor
            def _(pe):
                pe.wait_ge(lo_ready, 1)
                for n in range(MT):
                    c = slice(n * P, (n + 1) * P)
                    for k in range(KT):
                        mm = passes(pe, ps[:, n, 0:MEM_TOKENS], w_hi[:, k, c], w_lo[:, k, c],
                                    m_hi[:, k, 0:MEM_TOKENS], m_lo[:, k, 0:MEM_TOKENS], k == 0, k == KT - 1)
                    mm.then_inc(ps_ready, 1)
                for n in range(MT):
                    c = slice(n * P, (n + 1) * P)
                    for k in range(KT):
                        mm = passes(pe, ps[:, MT + n, 0:MI], m_hi[:, k, c], m_lo[:, k, c],
                                    w_hi[:, k, MI:], w_lo[:, k, MI:], k == 0, k == KT - 1)
                    mm.then_inc(ps_ready, 1)


def mem_attend_stage(core, q_dram, kt_p, v_p, kv_s, o_hi, o_lo):
    nc = core.nc
    units = SEQ // P + 2
    prompt_units = SEQ // P
    PADQ = 32
    with ExitStack() as ctx:
        sb = lambda name, shape, dt=F32: ctx.enter_context(nc.sbuf_tensor(f"ma_{name}", shape, dt))
        ps = lambda name, n: ctx.enter_context(nc.psum_tensor(f"ma_{name}_ps", [P, n, 512], F32))
        q = sb("q", [P, MT, TOKENS])
        qp = sb("q_padded", [P, MT, DEC_BATCH, PADQ])
        kt, v = sb("kt", [P, MT, MEM_TOKENS]), sb("v", [P, MT, MI])
        kvs = sb("kv_sample", [P, DEC_BATCH, 4, MEM_TOKENS])
        prob, probt = sb("prob", [P, 2, 4, MEM_TOKENS]), sb("prob_t", [P, 2, 8, P])
        neg_max, sums, rec = sb("neg_max", [P, 2, 4]), sb("sums", [P, 2, 4]), sb("rec", [P, 2, 4])
        s_ps, t_ps, o_ps = ps("s", 4), ps("t", 2), ps("o", 2)
        landed, q_ready, pad_ready = map(core.sem, ("ma_landed", "ma_q_ready", "ma_pad_ready"))
        s_ready, max_ready, p_ready, rec_ready, scaled, t_ready, pt_act, pt_dve, pv_ready, hi_ready, lo_ready = map(
            core.sem, ("ma_s", "ma_max", "ma_p", "ma_rec", "ma_scaled", "ma_t", "ma_pt_act", "ma_pt_dve", "ma_pv",
                       "ma_hi", "ma_lo"))

        def out_cols(u):
            if u < prompt_units:
                return slice(u * P, (u + 1) * P)
            half = SAMPLE // 2
            return slice(SEQ + (u - prompt_units) * half, SEQ + (u - prompt_units + 1) * half)

        def out_tile(u):
            n = out_cols(u)
            return o_ps[:, u % 2, 0:MT * P].rearrange("p (m t) -> p m t", t=P)[:, :, 0:n.stop - n.start]

        with nc.Block() as block:

            @block.sync
            def _(sp):
                sp.dma_start(q[:], q_dram[:, :, 0:TOKENS].rearrange("i p t -> p i t")).then_inc(landed, 16)
                sp.dma_start(kt[:], kt_p).then_inc(landed, 16)
                sp.dma_start(v[:], v_p).then_inc(landed, 16)
                sp.dma_start(kvs[:], kv_s).then_inc(landed, 16)

            @block.gpsimd
            def _(pool):
                pool.memset(qp[:], 0.0).then_inc(pad_ready, 1)
                pool.wait_ge(pad_ready, 1)
                pool.wait_ge(q_ready, 1)
                for m in range(MT):
                    pool.tensor_copy(qp[:, m, :, 0:DEC_SEQ],
                                     q[:, m, SEQ:].rearrange("p (b t) -> p b t", t=DEC_SEQ)).then_inc(pad_ready, 1)

            @block.scalar
            def _(act):
                act.wait_ge(landed, 64)
                act.activation(q[:], q[:], ACT.Copy, scale=SCALE).then_inc(q_ready, 1)

                def exp(u):
                    act.wait_ge(max_ready, u + 1)
                    if u >= 2:
                        act.wait_ge(t_ready, 2 * (u - 1))
                    for n in range(4):
                        at = s_ps[:, 2 * (u % 2) + n // 2, (n % 2) * MEM_TOKENS:(n % 2 + 1) * MEM_TOKENS]
                        e = act.activation(prob[:, u % 2, n, :], at, ACT.Exp, bias=neg_max[:, u % 2, n:n + 1],
                                           accum_out=sums[:, u % 2, n:n + 1])
                    e.then_inc(p_ready, 1)

                exp(0)
                for u in range(units):
                    if u + 1 < units:
                        exp(u + 1)
                    act.wait_ge(t_ready, 2 * u + 1)
                    if u >= 2:
                        act.wait_ge(pv_ready, u - 1)
                    act.activation(probt[:, u % 2, 0:4, :].rearrange("p a c -> p (a c)"), t_ps[:, 0, :], ACT.Copy
                                   ).then_inc(pt_act, 1)
                    act.wait_ge(pv_ready, u + 1)
                    act.activation(o_hi[:, 0:MT, out_cols(u)], out_tile(u), ACT.Copy).then_inc(hi_ready, 1)

            @block.vector
            def _(dve):
                def maxima(u):
                    dve.wait_ge(s_ready, u + 1)
                    s = s_ps[:, 2 * (u % 2):2 * (u % 2) + 2, :].rearrange("p a (h m) -> p (a h) m", m=MEM_TOKENS)
                    dve.tensor_reduce(neg_max[:, u % 2, :], s, AX_X, ALU.max, negate=True).then_inc(max_ready, 1)

                maxima(0)
                for u in range(units):
                    if u + 1 < units:
                        maxima(u + 1)
                    dve.wait_ge(p_ready, u + 1)
                    dve.reciprocal(rec[:, u % 2, :], sums[:, u % 2, :]).then_inc(rec_ready, 1)
                    dve.wait_ge(rec_ready, u + 1)
                    dve.tensor_tensor(prob[:, u % 2], prob[:, u % 2],
                                      rec[:, u % 2, :].rearrange("p (n o) -> p n o", o=1).to_broadcast(
                                          [P, 4, MEM_TOKENS]), ALU.mult).then_inc(scaled, 1)
                    dve.wait_ge(t_ready, 2 * u + 2)
                    if u >= 2:
                        dve.wait_ge(pv_ready, u - 1)
                    dve.tensor_copy(probt[:, u % 2, 4:8, :].rearrange("p a c -> p (a c)"), t_ps[:, 1, :]
                                    ).then_inc(pt_dve, 1)
                    dve.wait_ge(hi_ready, u + 1)
                    dve.tensor_tensor(o_lo[:, 0:MT, out_cols(u)], out_tile(u),
                                      o_hi[:, 0:MT, out_cols(u)].bitcast(F32), ALU.subtract).then_inc(lo_ready, 1)

            @block.tensor
            def _(pe):
                def head_rows(h):
                    return slice((h % 2) * HEAD_DIM, (h % 2 + 1) * HEAD_DIM)

                def head_of(n):
                    return (n % 2) * 2 + n // 2

                def scores(u):
                    if u >= 2:
                        pe.wait_ge(p_ready, u - 1)
                    for n in range(4):
                        at = s_ps[:, 2 * (u % 2) + n // 2, (n % 2) * MEM_TOKENS:(n % 2 + 1) * MEM_TOKENS]
                        if u < prompt_units:
                            h = head_of(n)
                            mm = pe.matmul(at, q[head_rows(h), h // 2, u * P:(u + 1) * P],
                                           kt[head_rows(h), h // 2, :], start=True, stop=True)
                            continue
                        b = (u - prompt_units) * 4 + n
                        for h in range(MEM_HEADS):
                            mm = pe.matmul(at[h * PADQ:(h + 1) * PADQ], qp[head_rows(h), h // 2, b, :],
                                           kvs[head_rows(h), b, h // 2, :], start=True, stop=True)
                    mm.then_inc(s_ready, 1)

                def values(u):
                    pe.wait_ge(pt_act, u + 1)
                    pe.wait_ge(pt_dve, u + 1)
                    if u >= 2:
                        pe.wait_ge(lo_ready, u - 1)
                    for n in range(4):
                        for h in ([head_of(n)] if u < prompt_units else range(MEM_HEADS)):
                            hc = slice(h * HEAD_DIM, (h + 1) * HEAD_DIM)
                            for m in range(MT):
                                turned = probt[:, u % 2, 2 * n + m, :]
                                if u < prompt_units:
                                    at = o_ps[head_rows(h), u % 2, (h // 2) * P:(h // 2 + 1) * P]
                                    mm = pe.matmul(at, v[:, m, hc], turned, start=m == 0, stop=m == MT - 1)
                                else:
                                    b = (u - prompt_units) * 4 + n
                                    c = (h // 2) * P + n * DEC_SEQ
                                    mm = pe.matmul(o_ps[head_rows(h), u % 2, c:c + DEC_SEQ], kvs[:, b, 2 + m, hc],
                                                   turned[:, h * PADQ:h * PADQ + DEC_SEQ],
                                                   start=m == 0, stop=m == MT - 1)
                    mm.then_inc(pv_ready, 1)

                pe.wait_ge(landed, 64)
                pe.wait_ge(q_ready, 1)
                pe.wait_ge(pad_ready, 1 + MT)
                scores(0)
                scores(1)
                for u in range(units):
                    pe.wait_ge(scaled, u + 1)
                    if u:
                        pe.wait_ge(pt_act, u)
                        pe.wait_ge(pt_dve, u)
                    for n in range(4):
                        for m in range(MT):
                            mm = pe.transpose(t_ps[:, n // 2, ((n % 2) * MT + m) * P:((n % 2) * MT + m + 1) * P],
                                              prob[:, u % 2, n, m * P:(m + 1) * P], core.ident[:])
                        if n % 2:
                            mm.then_inc(t_ready, 1)
                    if u + 2 < units:
                        scores(u + 2)
                    values(u)


GAINS = ("norm_ffn1", "norm_mix", "norm_mem_q", "norm_mem_kv", "norm_ffn2", "norm_final")


def load_stage(core, pairs, dram_pairs=()):
    landed, copied = core.sem("inputs_landed"), core.sem("dram_copied")
    with core.nc.Block() as block:

        @block.sync
        def _(sp):
            for dst, src in pairs:
                sp.dma_start(dst, src).then_inc(landed, 16)
            for dst, src in dram_pairs:
                sp.dma_start(dst, src).then_inc(copied, 16)
            sp.wait_ge(landed, 16 * len(pairs))
            if dram_pairs:
                sp.wait_ge(copied, 16 * len(dram_pairs))


def trunk(nc, i, o):
    with ExitStack() as ctx:
        core = Core(nc, ctx)
        sb = lambda stack, name, shape, dt=F32: stack.enter_context(nc.sbuf_tensor(name, shape, dt))
        n_pool = i["slc_pages"].shape[0]
        rows = nc.dram_tensor("scratch_bias_rows", (NSA_HEADS + 1, P, ROW_LEN), F32, kind="Internal").ap()
        gates_dram = nc.dram_tensor("scratch_gates", (NEW, 3 * NSA_HEADS), F32, kind="Internal").ap()
        q_mem = nc.dram_tensor("scratch_mem_q", (MT, P, TP), F32, kind="Internal").ap()
        consts_stage(core, i["consts"])
        gains = sb(ctx, "gains", [P, len(GAINS), KT])
        inner_gains = sb(ctx, "inner_gains", [P, 2, 4])
        gain = {name: gains[:, n, :] for n, name in enumerate(GAINS)}
        x = sb(ctx, "x", [P, KT, TP])
        def split(stack, name, tiles=KT):
            return [sb(stack, f"{name}_{part}", [P, tiles, TP], F32R) for part in ("hi", "lo")]

        def by_tile(*buffers):
            return [b[:, k, :] for b in buffers for k in range(b.shape[1])]

        load_stage(core, [(x[:], i["x"]), (gains[:], i["gains"]), (inner_gains[:], i["inner_gains"])],
                   [(o["win_old"], i["win_rows"])])
        bias_rows_stage(core, i["rel_bias"], i["bucket_rows"], rows)
        with ExitStack() as c:
            h_hi, h_lo = split(c, "h_ffn1")
            with ExitStack() as c2:
                mem = sb(c2, "mem", [P, KT, MEM_TOKENS])
                load_stage(core, [(mem[:], i["mem"])])
                norm_stage(core, mem, gain["norm_mem_kv"], core.mean_model, h_hi, h_lo, "norm_mem_kv",
                           width=MEM_TOKENS, parts=1)
                mem_kv_stage(core, h_hi, h_lo, i["w_mem_kv"], o["mem_kt"], o["mem_v"])
            core.clear_sems()
            norm_stage(core, x, gain["norm_ffn1"], core.mean_model, h_hi, h_lo, "norm_ffn1")
            ffn_stage(core, x, h_hi, h_lo, i["w_ffn1_in"], i["w_ffn1_out"], "ffn1")
        core.clear_sems()
        with ExitStack() as c:
            nat = sb(c, "nat", [P, TOK_TILES, NAT])
            with ExitStack() as c2:
                h_hi, h_lo = split(c2, "h_mix")
                norm_stage(core, x, gain["norm_mix"], core.mean_model, h_hi, h_lo, "norm_mix")
                gemm_stage(core, by_tile(h_hi), by_tile(h_lo), i["w_mix"], KT, 20, "mix", store=o["proj"])
                natural_stage(core, h_hi, h_lo, i["w_nat"], nat, "nat")
            ssd_hi, ssd_lo = split(c, "ssd_out", 4)
            with ExitStack() as c2:
                y = sb(c2, "y_ssd", [P, 4, TP])
                with ExitStack() as c3:
                    xc = sb(c3, "xc", [P, XBC, TOKENS])
                    conv_stage(core, o["proj"], i["conv_state"], i["conv_w"], i["conv_b"], xc, y)
                    ssd_stage(core, nat, xc, i["dt_bias"], i["a_log"], i["d_skip"], i["ssd_state"], y,
                              o["ssd_p"], o["ssd_s"])
                norm_stage(core, y, inner_gains[:, 0, :], core.mean_inner, ssd_hi, ssd_lo, "norm_ssd", tiles=4)
            core.clear_sems()
            with ExitStack() as c2:
                o_t = sb(c2, "o_nsa", [P, 4, TP])
                with ExitStack() as c3:
                    kc, vc = sb(c3, "kc", [P, SEQS * N_CMP]), sb(c3, "vc", [P, SEQS * 2 * HEAD_DIM])
                    for kv, out in ((0, kc), (1, vc)):
                        compress_stage(core, kv, o["proj"], i["cmp_pages"], i["page_table"], i[f"cmp_w1_{kv}"],
                                       i[f"cmp_w2_{kv}"], i[f"cmp_pos_{kv}"], out, n_pool)
                    core.clear_sems()
                    prompt_nsa_stage(core, nat, kc, vc, o["proj"], rows, o_t)
                    sample_nsa_stage(core, nat, kc, vc, o["proj"], rows, i["rules"], i["page_table"],
                                     i["slc_pages"], i["win_kv"], gates_dram, o_t, n_pool)
                core.clear_sems()
                load_stage(core, [], [(o["v_rows"], nat[:, :, 0:2 * P])])
                nsa_hi, nsa_lo = split(c2, "nsa_out", 4)
                norm_stage(core, o_t, inner_gains[:, 1, :], core.mean_inner, nsa_hi, nsa_lo, "norm_nsa", tiles=4)
                gemm_stage(core, by_tile(ssd_hi, nsa_hi), by_tile(ssd_lo, nsa_lo), i["w_out"], KT, KT, "wout",
                           add_to=x)
        h_hi, h_lo = split(ctx, "h")
        norm_stage(core, x, gain["norm_mem_q"], core.mean_model, h_hi, h_lo, "norm_mem_q")
        gemm_stage(core, by_tile(h_hi), by_tile(h_lo), i["w_mem_q"], KT, MT, "memq", store=q_mem)
        mem_attend_stage(core, q_mem, o["mem_kt"], o["mem_v"], i["mem_kv_sample"], h_hi, h_lo)
        gemm_stage(core, by_tile(h_hi), by_tile(h_lo), i["w_mem_out"], MT, KT, "memout", add_to=x)
        core.clear_sems()
        norm_stage(core, x, gain["norm_ffn2"], core.mean_model, h_hi, h_lo, "norm_ffn2")
        ffn_stage(core, x, h_hi, h_lo, i["w_ffn2_in"], i["w_ffn2_out"], "ffn2")
        norm_stage(core, x, gain["norm_final"], core.mean_model, None, None, "norm_final", store=o["y"])



def lay_tokens(*parts):
    t = np.concatenate([a.reshape(-1, a.shape[-1]) for a in parts])
    return np.ascontiguousarray(t.T.reshape(-1, P, t.shape[0]).transpose(1, 0, 2))


def lay_tiles(w):
    k = w.shape[0] // P
    return np.ascontiguousarray(w.reshape(k, P, -1, P).transpose(2, 1, 0, 3)).reshape(-1, P, k * P)


def lay_ffn_in(w):
    return np.ascontiguousarray(w.reshape(KT, P, 2, FT, P).transpose(3, 1, 2, 0, 4)).reshape(FT, P, 2 * KT * P)


def lay_ffn_out(w):
    return np.ascontiguousarray(w.reshape(FT // 2, 2, P, D_MODEL).transpose(0, 2, 1, 3))


def group_major():
    f = np.arange(INNER).reshape(KV_GROUPS, GROUP_HEADS, HEAD_DIM)
    return f.transpose(1, 0, 2).reshape(-1)


Z0, XBC0, DT0 = 0, INNER, INNER + XBC * P
Q0 = DT0 + SSD_HEADS
KV0 = Q0 + INNER
GL0 = KV0 + 6 * P


def kernel(x_prompt, x_sample, cache_kv_cmp, cache_kv_slc, state_win_kv, state_ssd, state_conv, cache_mem_kv,
           page_table, mem_prompt, norm_ffn1, w_ffn1_in, w_ffn1_out, norm_mix, w_in, conv_w, conv_b, dt_bias,
           a_log, d_skip, norm_ssd_out, cmp_pos_k, cmp_w1_k, cmp_w2_k, cmp_pos_v, cmp_w1_v, cmp_w2_v,
           norm_nsa_out, w_out, norm_mem_q, norm_mem_kv, w_mem_q, w_mem_kv, w_mem_out, norm_ffn2, w_ffn2_in,
           w_ffn2_out, rel_bias, norm_final):
    import concourse.bacc as bacc
    from concourse.bass_utils import run_bass_kernel_spmd

    a = np.asarray
    per_tile = lambda g: np.ascontiguousarray(a(g).reshape(-1, P).T)
    spread = lambda v: np.ascontiguousarray(np.broadcast_to(a(v), (P, SSD_HEADS)))
    order = group_major()
    w = a(w_in)[0]
    kv_cols = [np.arange(KV0 + n * P, KV0 + (n + 1) * P) for n in range(6)]
    mix = np.concatenate([np.arange(Z0, DT0), Q0 + order, kv_cols[0], kv_cols[1], kv_cols[2], kv_cols[4]])
    natural = np.concatenate([kv_cols[3], kv_cols[5], np.arange(DT0, Q0), np.arange(GL0, w.shape[1])])
    pad = np.zeros((TP - TOKENS, D_MODEL), np.float32)
    mem_kv = a(cache_mem_kv)[0]
    mem_k = mem_kv[:, :, 0].reshape(DEC_BATCH, MEM_TOKENS, MT, P).transpose(3, 0, 2, 1)
    mem_v = mem_kv[:, :, 1].reshape(DEC_BATCH, MT, P, MI).transpose(2, 0, 1, 3)
    ins = {
        "x": lay_tokens(a(x_prompt), a(x_sample), pad),
        "mem": lay_tokens(a(mem_prompt)),
        "gains": np.ascontiguousarray(np.stack([per_tile(g) for g in (
            norm_ffn1, norm_mix, norm_mem_q, norm_mem_kv, norm_ffn2, norm_final)], axis=1)),
        "inner_gains": np.ascontiguousarray(np.stack([per_tile(norm_ssd_out),
                                                      per_tile(a(norm_nsa_out)[0][order])], axis=1)),
        "consts": make_consts(), "rules": make_rules(), "bucket_rows": make_bucket_rows(),
        "rel_bias": np.ascontiguousarray(a(rel_bias)),
        "w_ffn1_in": lay_ffn_in(a(w_ffn1_in)[0]), "w_ffn1_out": lay_ffn_out(a(w_ffn1_out)[0]),
        "w_ffn2_in": lay_ffn_in(a(w_ffn2_in)[0]), "w_ffn2_out": lay_ffn_out(a(w_ffn2_out)[0]),
        "w_mix": lay_tiles(w[:, mix]),
        "w_nat": np.ascontiguousarray(w[:, natural].reshape(KT, P, NAT).transpose(1, 0, 2)),
        "w_out": lay_tiles(a(w_out)[0][np.concatenate([np.arange(INNER), INNER + order])]),
        "w_mem_q": lay_tiles(a(w_mem_q)[0]), "w_mem_out": lay_tiles(a(w_mem_out)[0]),
        "w_mem_kv": np.ascontiguousarray(a(w_mem_kv)[0].reshape(KT, P, 2 * MI).transpose(1, 0, 2)),
        "conv_state": lay_conv_state(a(state_conv)), "conv_w": lay_conv_w(a(conv_w)), "conv_b": per_tile(conv_b),
        "dt_bias": spread(dt_bias), "a_log": spread(a_log), "d_skip": lay_d_skip(a(d_skip)),
        "ssd_state": lay_state(a(state_ssd)),
        "page_table": np.ascontiguousarray(a(page_table).reshape(1, -1)),
        "cmp_pages": lay_cmp_pages(a(cache_kv_cmp)), "slc_pages": lay_slc_pages(a(cache_kv_slc)),
        "win_kv": lay_win(a(state_win_kv)),
        "win_rows": np.ascontiguousarray(a(state_win_kv)[0, :, DEC_SEQ:].reshape(DEC_BATCH, -1)),
        "mem_kv_sample": np.ascontiguousarray(np.concatenate([mem_k, mem_v], axis=2)),
    }
    for kv, (pos, w1, w2) in enumerate(((cmp_pos_k, cmp_w1_k, cmp_w2_k), (cmp_pos_v, cmp_w1_v, cmp_w2_v))):
        ins[f"cmp_pos_{kv}"], ins[f"cmp_w1_{kv}"] = lay_cmp_pos(a(pos)), lay_cmp_w1(a(w1))
        ins[f"cmp_w2_{kv}"] = lay_cmp_w2(a(w2))
    outs = {
        "y": (P, KT, TP), "proj": (20, P, TP), "v_rows": (P, TOK_TILES, 2 * P),
        "ssd_p": (P, INNER), "ssd_s": (P, DEC_BATCH, INNER),
        "mem_kt": (P, MT, MEM_TOKENS), "mem_v": (P, MT, MI),
        "win_old": (DEC_BATCH, (WINDOW - DEC_SEQ) * 4 * HEAD_DIM),
    }
    nc = bacc.Bacc("TRN2", target_bir_lowering=False, num_devices=1)
    i = {k: nc.dram_tensor(f"in_{k}", v.shape, mybir.dt.from_np(v.dtype), kind="ExternalInput").ap()
         for k, v in ins.items()}
    o = {k: nc.dram_tensor(f"out_{k}", s, F32, kind="ExternalOutput").ap() for k, s in outs.items()}
    trunk(nc, i, o)
    r = run_bass_kernel_spmd(nc, [{f"in_{k}": v for k, v in ins.items()}], core_ids=[0]).results[0]
    r = {k: a(r[f"out_{k}"]) for k in outs}

    y = r["y"].transpose(1, 0, 2).reshape(D_MODEL, TP).T
    proj = r["proj"].transpose(0, 2, 1)
    v = r["v_rows"].transpose(1, 0, 2).reshape(-1, 2 * P)
    kc, vc, ks, kw = (proj[KV_TILE0 + n] for n in range(4))
    vs, vw = v[:TP, :P], v[:TP, P:]
    heads = (KV_GROUPS, HEAD_DIM)

    def rows_p(k, v_, first=0):
        return np.stack([k[first:SEQ].reshape(1, -1, *heads), v_[first:SEQ].reshape(1, -1, *heads)], axis=2)[None]

    def rows_s(k, v_):
        return np.stack([k[SEQ:TOKENS].reshape(DEC_BATCH, DEC_SEQ, *heads),
                         v_[SEQ:TOKENS].reshape(DEC_BATCH, DEC_SEQ, *heads)], axis=2)[None]

    xbc = proj[XBC_TILE0:XBC_TILE0 + XBC].transpose(1, 0, 2).reshape(TP, -1)
    pad = TAPS - 1
    mem_k = r["mem_kt"].transpose(1, 0, 2).reshape(MI, MEM_TOKENS).T.reshape(MEM_TOKENS, MEM_HEADS, HEAD_DIM)
    mem_v = r["mem_v"].transpose(1, 0, 2).reshape(MEM_TOKENS, MEM_HEADS, HEAD_DIM)
    win_old = r["win_old"].reshape(1, DEC_BATCH, WINDOW - DEC_SEQ, 2, *heads)
    c = np.ascontiguousarray
    return (
        c(y[:SEQ]).reshape(1, SEQ, D_MODEL), c(y[SEQ:TOKENS]).reshape(DEC_BATCH, DEC_SEQ, D_MODEL),
        c(rows_p(kc, vc)), c(rows_p(ks, vs)), c(rows_p(kw, vw, SEQ - WINDOW)),
        c(r["ssd_p"].reshape(P, SSD_HEADS, HEAD_DIM).transpose(1, 2, 0))[None, None],
        c(xbc[SEQ - pad:SEQ])[None, None],
        c(np.stack([mem_k, mem_v], axis=1))[None, None],
        c(rows_s(kc, vc)), c(rows_s(ks, vs)),
        c(np.concatenate([win_old, rows_s(kw, vw)], axis=2)),
        c(r["ssd_s"].reshape(P, DEC_BATCH, SSD_HEADS, HEAD_DIM).transpose(1, 2, 3, 0))[None],
        c(xbc[SEQ:TOKENS].reshape(DEC_BATCH, DEC_SEQ, -1)[:, DEC_SEQ - pad:])[None],
    )
```

```python
from contextlib import ExitStack

import numpy as np

import concourse.bass as bass
from concourse import mybir

F32 = mybir.dt.float32
BF16 = mybir.dt.bfloat16
F32R = mybir.dt.float32r
I32 = mybir.dt.int32
ALU = mybir.AluOpType
ACT = mybir.ActivationFunctionType
AX_X = mybir.AxisListType.X

P = 128
D_MODEL = 1024
SEQ = 1024
DEC_BATCH = 8
DEC_SEQ = 8
SAMPLE = DEC_BATCH * DEC_SEQ
KT = D_MODEL // P
GROUPS = 3
TG = 364
TP = GROUPS * TG
D_FF = 2816
FT = D_FF // P
EPS = 1e-6
NEG = -1e30


def groups(g):
    return slice(g * TG, (g + 1) * TG)


class Core:

    def __init__(self, nc, ctx):
        self.nc, self.ctx, self.serial, self.in_use = nc, ctx, 0, []

    def sem(self, name):
        self.serial += 1
        handle = self.nc.alloc_semaphore(name=f"{name}_{self.serial}")
        self.in_use.append(handle)
        return handle

    def clear_sems(self):
        self.nc.clear_and_free_semaphores(self.in_use)
        self.in_use = []
        self.nc.all_engine_barrier()


def norm_stage(core, xT, gain, ones, h_hi, h_lo, tag, tiles=KT, width=TP, parts=GROUPS,
               store=None):
    nc = core.nc
    w = width // parts
    with ExitStack() as ctx:
        sb = lambda name, shape, dt=F32: ctx.enter_context(nc.sbuf_tensor(f"{tag}_{name}", shape, dt))
        sq = sb("squares", [P, 2, width])
        total = sb("square_total", [P, width])
        rms = sb("rms", [P, width])
        inv = sb("inv_rms", [P, width])
        h = sb("normed", [P, 2, width])
        ms = ctx.enter_context(nc.psum_tensor(f"{tag}_mean_square", [P, parts, 512], F32))
        sq_ready, added, ms_ready, rms_ready, inv_ready = map(
            core.sem, ("sq_ready", "sq_added", "ms_ready", "rms_ready", "inv_ready"))
        h_ready, hi_ready, lo_ready = map(core.sem, ("h_ready", "h_hi_ready", "h_lo_ready"))
        stored = [core.sem(f"h_stored_{s}") for s in range(2)]
        with nc.Block() as block:

            @block.sync
            def _(sp):
                if store is not None:
                    for k in range(tiles):
                        sp.wait_ge(h_ready, k + 1)
                        sp.dma_start(store[:, k, :], h[:, k % 2, :]).then_inc(stored[k % 2], 16)
                    for s in range(2):
                        sp.wait_ge(stored[s], 16 * (tiles // 2))

            @block.scalar
            def _(act):
                for k in range(tiles):
                    if k >= 2:
                        act.wait_ge(added, k - 1)
                    act.activation(sq[:, k % 2, :], xT[:, k, :width], ACT.Square).then_inc(sq_ready, 1)
                act.wait_ge(ms_ready, 1)
                act.activation(rms[:].rearrange("p (g w) -> p g w", w=w), ms[:, :, :w], ACT.Sqrt,
                               bias=core.eps[:, 0:1]).then_inc(rms_ready, 1)
                for k in range(tiles if store is None else 0):
                    act.wait_ge(h_ready, k + 1)
                    act.activation(h_hi[:, k, :width], h[:, k % 2, :], ACT.Copy).then_inc(hi_ready, 1)

            @block.tensor
            def _(pe):
                pe.wait_ge(added, tiles)
                for g in range(parts):
                    mm = pe.matmul(ms[:, g, :w], ones[:], total[:, g * w:(g + 1) * w],
                                   start=True, stop=True)
                mm.then_inc(ms_ready, 1)

            @block.vector
            def _(dve):
                for k in range(tiles):
                    dve.wait_ge(sq_ready, k + 1)
                    if k == 0:
                        dve.tensor_copy(total[:], sq[:, 0, :]).then_inc(added, 1)
                    else:
                        dve.wait_ge(added, k)
                        dve.tensor_tensor(total[:], total[:], sq[:, k % 2, :], ALU.add).then_inc(added, 1)
                dve.wait_ge(rms_ready, 1)
                dve.reciprocal(inv[:], rms[:]).then_inc(inv_ready, 1)
                dve.wait_ge(inv_ready, 1)

                def rest(k):
                    dve.wait_ge(hi_ready, k + 1)
                    dve.tensor_tensor(h_lo[:, k, :width], h[:, k % 2, :], h_hi[:, k, :width].bitcast(F32),
                                      ALU.subtract).then_inc(lo_ready, 1)

                for k in range(tiles):
                    if k >= 2 and store is None:
                        dve.wait_ge(lo_ready, k - 1)
                    if k >= 2 and store is not None:
                        dve.wait_ge(stored[k % 2], 16 * (k // 2))
                    dve.scalar_tensor_tensor(h[:, k % 2, :], xT[:, k, :width], gain[:, k:k + 1], inv[:],
                                             ALU.mult, ALU.mult).then_inc(h_ready, 1)
                    if k and store is None:
                        rest(k - 1)
                if store is None:
                    rest(tiles - 1)


class FusedNorm:

    def __init__(self, core, ctx, xT, gain, sets, h_hi, h_lo, tag, bank, pairs=None):
        self.core, self.xT, self.gain, self.h_hi, self.h_lo, self.bank = core, xT, gain, h_hi, h_lo, bank
        self.units = [(g, s) for g in range(GROUPS) for s in sets]
        self.per_group = sum(s[1] for s in sets)
        sb = lambda name, n: ctx.enter_context(core.nc.sbuf_tensor(f"{tag}_{name}", [P, n, TG], F32))
        self.sq, self.h = pairs or (sb("squares", 2), sb("normed", 2))
        self.rms, self.inv = sb("rms", 1), sb("inv_rms", 1)
        self.sq_ready, self.summed, self.rms_ready, self.inv_ready = map(
            core.sem, ("sq_ready", "sq_summed", "rms_ready", "inv_ready"))
        self.h_ready, self.hi_ready, self.lo_ready = map(core.sem, ("h_ready", "h_hi_ready", "h_lo_ready"))

    def before(self, u):
        return sum(self.units[v][1][1] for v in range(u))

    def scalar(self, act, meanwhile):
        def squares(u):
            g, (first, tiles, _) = self.units[u]
            for k in range(tiles):
                j = self.before(u) + k
                if j >= 2:
                    act.wait_ge(self.summed, j - 1)
                act.activation(self.sq[:, j % 2, :], self.xT[:, first + k, groups(g)], ACT.Square
                               ).then_inc(self.sq_ready, 1)

        def roots(u):
            act.wait_ge(self.summed, self.before(u + 1))
            if u:
                act.wait_ge(self.inv_ready, u)
            act.activation(self.rms[:, 0, :], self.bank(u)[:, :TG], ACT.Sqrt, bias=self.core.eps[:, 0:1]
                           ).then_inc(self.rms_ready, 1)

        def round_hi(u):
            g, (first, tiles, _) = self.units[u]
            for k in range(tiles):
                j = self.before(u) + k
                act.wait_ge(self.h_ready, j + 1)
                act.activation(self.h_hi[:, first + k, groups(g)], self.h[:, j % 2, :], ACT.Copy
                               ).then_inc(self.hi_ready, 1)

        squares(0)
        meanwhile()
        roots(0)
        for u in range(len(self.units)):
            if u + 1 < len(self.units):
                squares(u + 1)
            round_hi(u)
            if u + 1 < len(self.units):
                roots(u + 1)

    def tensor(self, pe):
        for u, (g, (first, tiles, ones)) in enumerate(self.units):
            for k in range(tiles):
                j = self.before(u) + k
                pe.wait_ge(self.sq_ready, j + 1)
                pe.matmul(self.bank(u)[:, :TG], ones[:], self.sq[:, j % 2, :], start=k == 0,
                          stop=k == tiles - 1).then_inc(self.summed, 1)

    def vector(self, dve):
        def rest(j, first, k, g):
            dve.wait_ge(self.hi_ready, j + 1)
            dve.tensor_tensor(self.h_lo[:, first + k, groups(g)], self.h[:, j % 2, :],
                              self.h_hi[:, first + k, groups(g)].bitcast(F32), ALU.subtract
                              ).then_inc(self.lo_ready, 1)

        for u, (g, (first, tiles, _)) in enumerate(self.units):
            dve.wait_ge(self.rms_ready, u + 1)
            if u:
                dve.wait_ge(self.h_ready, self.before(u))
            dve.reciprocal(self.inv[:, 0, :], self.rms[:, 0, :]).then_inc(self.inv_ready, 1)
            dve.wait_ge(self.inv_ready, u + 1)
            for k in range(tiles):
                j = self.before(u) + k
                if j >= 2:
                    dve.wait_ge(self.lo_ready, j - 1)
                dve.scalar_tensor_tensor(self.h[:, j % 2, :], self.xT[:, first + k, groups(g)],
                                         self.gain[:, first + k:first + k + 1], self.inv[:, 0, :],
                                         ALU.mult, ALU.mult).then_inc(self.h_ready, 1)
                if k:
                    rest(j - 1, first, k - 1, g)
            rest(j, first, tiles - 1, g)
        dve.wait_ge(self.lo_ready, GROUPS * self.per_group)

    def wait_group(self, pe, g):
        pe.wait_ge(self.lo_ready, (g + 1) * self.per_group)


def passes(pe, out, w_hi, w_lo, x_hi, x_lo, start, stop):
    pe.matmul(out, w_hi, x_hi, start=start, stop=False)
    pe.matmul(out, w_hi, x_lo, start=False, stop=False)
    return pe.matmul(out, w_lo, x_hi, start=False, stop=stop)


def ffn_stage(core, xT, gain, h_hi, h_lo, w_in, w_out, tag):
    nc = core.nc
    chunks = FT // 2
    with ExitStack() as ctx:
        sb = lambda name, shape, dt=F32: ctx.enter_context(nc.sbuf_tensor(f"{tag}_{name}", shape, dt))
        up_raw = sb("up_raw", [P, 2 * KT * P])
        up_hi = sb("up_hi", [P, 2, 2, KT, P], F32R)
        up_lo = sb("up_lo", [P, 2, 2, KT, P], F32R)
        down_raw = sb("down_raw", [P, 2, D_MODEL])
        down_hi = sb("down_hi", [P, 2, D_MODEL], F32R)
        down_lo = sb("down_lo", [P, 2, D_MODEL], F32R)
        act_hi = sb("act_hi", [P, 3, TP], F32R)
        act_lo = sb("act_lo", [P, 3, TP], F32R)
        silu = sb("silu", [P, 2, TG])
        prod = sb("prod", [P, 2, TG])
        gu = ctx.enter_context(nc.psum_tensor(f"{tag}_gate_up", [P, 2, 2, 512], F32))
        dn = ctx.enter_context(nc.psum_tensor(f"{tag}_down", [P, 4, 512], F32))
        up_landed, up_hi_ready, up_lo_ready = map(
            core.sem, ("up_landed", "up_hi_ready", "up_lo_ready"))
        down_landed, down_hi_ready, down_lo_ready = map(
            core.sem, ("down_landed", "down_hi_ready", "down_lo_ready"))
        gu_ready, silu_ready, prod_ready, act_hi_ready, act_ready = map(
            core.sem, ("gu_ready", "silu_ready", "prod_ready", "act_hi_ready", "act_ready"))
        dn_ready, dn_added = map(core.sem, ("dn_ready", "dn_added"))
        norm = FusedNorm(core, ctx, xT, gain, ((0, KT, core.mean_model),), h_hi, h_lo, f"{tag}_norm",
                         lambda u: dn[:, u, :], (silu, prod))

        def slot(par, f):
            return 2 if f else par

        def schedule(eng, chunk, last):
            chunk(0, 0, True, False)
            chunk(1, 1, True, True)
            chunk(2, 0, True, True)
            with eng.Fori(1, (chunks - 3) // 2) as it:
                chunk(it * 2 + 1, 1, True, True)
                chunk(it * 2 + 2, 0, True, True)
            chunk(chunks - 2, (chunks - 2) % 2, True, True)
            chunk(chunks - 1, (chunks - 1) % 2, False, True)
            last()

        with nc.Block() as block:

            @block.sync
            def _(sp):
                def load_up(n, guard):
                    if guard:
                        sp.wait_ge(up_lo_ready, n)
                    sp.dma_start(up_raw[:], w_in[bass.ds(n, 1)].rearrange("o p c -> (o p) c")
                                 ).then_inc(up_landed, 16)

                def load_down(c, guard):
                    if guard:
                        sp.wait_ge(down_lo_ready, c)
                    sp.dma_start(down_raw[:], w_out[bass.ds(c, 1)].rearrange("o p f c -> (o p) f c")
                                 ).then_inc(down_landed, 16)

                def chunk(c, par, more, full):
                    load_down(c, full)
                    if more:
                        load_up(c * 2 + 2, True)
                        load_up(c * 2 + 3, True)

                load_up(0, False)
                load_up(1, True)
                schedule(sp, chunk, lambda: None)

            @block.scalar
            def _(act):
                def split_up(n, s, reused):
                    act.wait_ge(up_landed, n * 16 + 16)
                    if reused:
                        act.wait_ge(gu_ready, (n - 1) * GROUPS)
                    act.activation(up_hi[:, s].rearrange("p u k c -> p (u k c)"), up_raw[:],
                                   ACT.Copy).then_inc(up_hi_ready, 1)

                def gate(c, f):
                    for g in range(GROUPS):
                        j = c * 6 + (3 * f + g)
                        act.wait_ge(gu_ready, j + 1)
                        if not (isinstance(c, int) and j < 2):
                            act.wait_ge(prod_ready, j - 1)
                        act.activation(silu[:, (f + g) % 2, :], gu[:, (f + g) % 2, 0, :TG],
                                       ACT.Silu).then_inc(silu_ready, 1)

                def chunk(c, par, more, full):
                    gate(c, 0)
                    if more:
                        split_up(c * 2 + 2, 0, True)
                    act.wait_ge(down_landed, c * 16 + 16)
                    if full:
                        act.wait_ge(dn_ready, c * (KT * GROUPS))
                    act.activation(down_hi[:].rearrange("p f c -> p (f c)"),
                                   down_raw[:].rearrange("p f c -> p (f c)"), ACT.Copy
                                   ).then_inc(down_hi_ready, 1)
                    gate(c, 1)
                    if more:
                        split_up(c * 2 + 3, 1, True)

                def first_weights():
                    split_up(0, 0, False)
                    split_up(1, 1, False)

                norm.scalar(act, first_weights)
                schedule(act, chunk, lambda: None)

            @block.tensor
            def _(pe):
                def up(c, f):
                    pe.wait_ge(up_lo_ready, c * 2 + (f + 1))
                    for g in range(GROUPS):
                        j = c * 6 + (3 * f + g)
                        if isinstance(c, int) and j < GROUPS:
                            norm.wait_group(pe, g)
                        if not (isinstance(c, int) and j < 2):
                            pe.wait_ge(prod_ready, j - 1)
                        for u in range(2):
                            for k in range(KT):
                                mm = passes(pe, gu[:, (f + g) % 2, u, :TG], up_hi[:, f, u, k, :],
                                            up_lo[:, f, u, k, :], h_hi[:, k, groups(g)],
                                            h_lo[:, k, groups(g)], k == 0, k == KT - 1)
                        mm.then_inc(gu_ready, 1)

                def down(c, par):
                    pe.wait_ge(down_lo_ready, c + 1)
                    pe.wait_ge(act_ready, c * 6 + 6)
                    for t in range(KT):
                        for g in range(GROUPS):
                            d = c * (KT * GROUPS) + (t * GROUPS + g)
                            if not (isinstance(c, int) and d < 4):
                                pe.wait_ge(dn_added, d - 3)
                            for f in range(2):
                                s = slot(par, f)
                                mm = passes(pe, dn[:, (t * GROUPS + g) % 4, :TG],
                                            down_hi[:, f, t * P:(t + 1) * P], down_lo[:, f, t * P:(t + 1) * P],
                                            act_hi[:, s, groups(g)], act_lo[:, s, groups(g)], f == 0, f == 1)
                            mm.then_inc(dn_ready, 1)

                def chunk(c, par, more, full):
                    up(c, 0)
                    if full:
                        down(c - 1, 1 - par)
                    up(c, 1)

                norm.tensor(pe)
                schedule(pe, chunk, lambda: down(chunks - 1, (chunks - 1) % 2))

            @block.vector
            def _(dve):
                def split_up(n, s):
                    dve.wait_ge(up_hi_ready, n + 1)
                    dve.tensor_tensor(up_lo[:, s].rearrange("p u k c -> p (u k c)"), up_raw[:],
                                      up_hi[:, s].rearrange("p u k c -> p (u k c)").bitcast(F32),
                                      ALU.subtract).then_inc(up_lo_ready, 1)

                def multiply(c, f, par):
                    if not (isinstance(c, int) and c < (1 if f else 2)):
                        dve.wait_ge(dn_ready, (c if f else c - 1) * (KT * GROUPS))
                    for g in range(GROUPS):
                        j = c * 6 + (3 * f + g)
                        b, s = (f + g) % 2, slot(par, f)
                        dve.wait_ge(silu_ready, j + 1)
                        dve.tensor_tensor(prod[:, b, :], silu[:, b, :], gu[:, b, 1, :TG],
                                          ALU.mult).then_inc(prod_ready, 1)
                        dve.wait_ge(prod_ready, j + 1)
                        dve.tensor_copy(act_hi[:, s, groups(g)], prod[:, b, :]).then_inc(act_hi_ready, 1)
                        dve.wait_ge(act_hi_ready, j + 1)
                        dve.tensor_tensor(act_lo[:, s, groups(g)], prod[:, b, :],
                                          act_hi[:, s, groups(g)].bitcast(F32), ALU.subtract
                                          ).then_inc(act_ready, 1)

                def add(c):
                    for t in range(KT):
                        for g in range(GROUPS):
                            d = c * (KT * GROUPS) + (t * GROUPS + g)
                            dve.wait_ge(dn_ready, d + 1)
                            dve.scalar_tensor_tensor(xT[:, t, groups(g)], dn[:, (t * GROUPS + g) % 4, :TG],
                                                     0.5, xT[:, t, groups(g)], ALU.mult, ALU.add
                                                     ).then_inc(dn_added, 1)

                def chunk(c, par, more, full):
                    multiply(c, 0, par)
                    if more:
                        split_up(c * 2 + 2, 0)
                    if full:
                        add(c - 1)
                    dve.wait_ge(down_hi_ready, c + 1)
                    dve.tensor_tensor(down_lo[:], down_raw[:], down_hi[:].bitcast(F32),
                                      ALU.subtract).then_inc(down_lo_ready, 1)
                    multiply(c, 1, par)
                    if more:
                        split_up(c * 2 + 3, 1)

                split_up(0, 0)
                split_up(1, 1)
                norm.vector(dve)
                schedule(dve, chunk, lambda: add(chunks - 1))


def gemm_stage(core, x_hi, x_lo, w, k_tiles, n_tiles, tag, store=None, add_to=None, norm_of=None):
    nc = core.nc
    with ExitStack() as ctx:
        sb = lambda name, shape, dt=F32: ctx.enter_context(nc.sbuf_tensor(f"{tag}_{name}", shape, dt))
        raw = sb("w_raw", [P, 2, k_tiles * P])
        w_hi = sb("w_hi", [P, 2, k_tiles, P], F32R)
        w_lo = sb("w_lo", [P, 2, k_tiles, P], F32R)
        out = sb("out", [P, 2, TP]) if store is not None else None
        ps = ctx.enter_context(nc.psum_tensor(f"{tag}_ps", [P, 6, 512], F32))
        landed = [core.sem(f"w_landed_{s}") for s in range(2)]
        hi_ready, lo_ready, ps_ready, taken = map(core.sem, ("w_hi_ready", "w_lo_ready", "ps_ready", "ps_taken"))
        stored = [core.sem(f"stored_{s}") for s in range(2)]
        pairs = n_tiles // 2
        norm = None
        if norm_of is not None:
            norm = FusedNorm(core, ctx, *norm_of, x_hi, x_lo, f"{tag}_norm", lambda u: ps[:, u, :])

        def schedule(eng, pair):
            pair(0, True, pairs > 1)
            if pairs > 2:
                with eng.Fori(1, pairs - 1) as i:
                    pair(i, False, True)
            if pairs > 1:
                pair(pairs - 1, False, False)

        with nc.Block() as block:

            @block.sync
            def _(sp):
                def load(i, s, guard):
                    if guard:
                        sp.wait_ge(lo_ready, i * 2 + (s - 1))
                    sp.dma_start(raw[:, s, :], w[bass.ds(i * 2 + s, 1)].rearrange("o p c -> (o p) c")
                                 ).then_inc(landed[s], 16)

                def pair(i, first, more):
                    if more:
                        for s in range(2):
                            load(i + 1, s, True)

                for s in range(2):
                    load(0, s, False)
                schedule(sp, pair)

            @block.tensor
            def _(pe):
                def pair(i, first, more):
                    for s in range(2):
                        pe.wait_ge(lo_ready, i * 2 + (s + 1))
                        for g in range(GROUPS):
                            if norm is not None and first and s == 0:
                                norm.wait_group(pe, g)
                            if not first:
                                pe.wait_ge(taken, i * 6 + (s * 3 + g - 5))
                            for k in range(k_tiles):
                                mm = passes(pe, ps[:, s * 3 + g, :TG], w_hi[:, s, k, :], w_lo[:, s, k, :],
                                            x_hi[:, k, groups(g)], x_lo[:, k, groups(g)],
                                            k == 0, k == k_tiles - 1)
                            mm.then_inc(ps_ready, 1)

                if norm is not None:
                    norm.tensor(pe)
                schedule(pe, pair)

            @block.scalar
            def _(act):
                def split(i, s, reused):
                    act.wait_ge(landed[s], i * 16 + 16)
                    if reused:
                        act.wait_ge(ps_ready, i * 6 + (s * 3 - 3))
                    act.activation(w_hi[:, s].rearrange("p k c -> p (k c)"), raw[:, s, :],
                                   ACT.Copy).then_inc(hi_ready, 1)

                def pair(i, first, more):
                    for s in range(2):
                        if store is not None:
                            if not first:
                                act.wait_ge(stored[s], i * 16)
                            for g in range(GROUPS):
                                act.wait_ge(ps_ready, i * 6 + (s * 3 + g + 1))
                                act.activation(out[:, s, groups(g)], ps[:, s * 3 + g, :TG], ACT.Copy
                                               ).then_inc(taken, 1)
                            act.wait_ge(taken, i * 6 + (s * 3 + 3))
                            act.dma_start(store[bass.ds(i * 2 + s, 1)].rearrange("o p c -> (o p) c"),
                                          out[:, s, :]).then_inc(stored[s], 16)
                        if more:
                            split(i + 1, s, True)

                def first_weights():
                    split(0, 0, False)
                    split(0, 1, False)

                if norm is not None:
                    norm.scalar(act, first_weights)
                else:
                    first_weights()
                schedule(act, pair)
                if store is not None:
                    for s in range(2):
                        act.wait_ge(stored[s], 16 * pairs)

            @block.vector
            def _(dve):
                def split(i, s):
                    dve.wait_ge(hi_ready, i * 2 + (s + 1))
                    dve.tensor_tensor(w_lo[:, s].rearrange("p k c -> p (k c)"), raw[:, s, :],
                                      w_hi[:, s].rearrange("p k c -> p (k c)").bitcast(F32),
                                      ALU.subtract).then_inc(lo_ready, 1)

                def pair(i, first, more):
                    for s in range(2):
                        if add_to is not None:
                            for g in range(GROUPS):
                                dve.wait_ge(ps_ready, i * 6 + (s * 3 + g + 1))
                                x = add_to[:, bass.ds(i * 2 + s, 1), groups(g)].rearrange("p o t -> p (o t)")
                                dve.tensor_tensor(x, ps[:, s * 3 + g, :TG], x, ALU.add).then_inc(taken, 1)
                        if more:
                            split(i + 1, s)

                split(0, 0)
                split(0, 1)
                if norm is not None:
                    norm.vector(dve)
                schedule(dve, pair)


NAT = 288
TOK_TILES = 9


def tok_rows(t):
    return P if t < TOK_TILES - 1 else TP - P * (TOK_TILES - 1)


def natural_stage(core, h_hi, h_lo, w, nat, tag):
    nc = core.nc
    with ExitStack() as ctx:
        sb = lambda name, shape, dt=F32: ctx.enter_context(nc.sbuf_tensor(f"{tag}_{name}", shape, dt))
        raw = sb("w_raw", [P, KT, NAT])
        w_hi = sb("w_hi", [P, KT, NAT], F32R)
        w_lo = sb("w_lo", [P, KT, NAT], F32R)
        ps = ctx.enter_context(nc.psum_tensor(f"{tag}_ps", [P, 2, 512], F32))
        landed, hi_ready, lo_ready, cleared, ps_ready, taken = map(
            core.sem, ("nw_landed", "nw_hi_ready", "nw_lo_ready", "nat_cleared", "nat_ps_ready", "nat_taken"))
        with nc.Block() as block:

            @block.sync
            def _(sp):
                sp.dma_start(raw[:], w).then_inc(landed, 16)

            @block.scalar
            def _(act):
                act.wait_ge(landed, 16)
                act.activation(w_hi[:], raw[:], ACT.Copy).then_inc(hi_ready, 1)

            @block.vector
            def _(dve):
                dve.memset(nat[:, TOK_TILES - 1, :], 0.0).then_inc(cleared, 1)
                dve.wait_ge(hi_ready, 1)
                dve.tensor_tensor(w_lo[:], raw[:], w_hi[:].bitcast(F32), ALU.subtract).then_inc(lo_ready, 1)
                dve.wait_ge(cleared, 1)
                for t in range(TOK_TILES):
                    n = tok_rows(t)
                    dve.wait_ge(ps_ready, t + 1)
                    dve.tensor_copy(nat[:n, t, :], ps[:n, t % 2, :NAT]).then_inc(taken, 1)

            @block.tensor
            def _(pe):
                pe.wait_ge(lo_ready, 1)
                for t in range(TOK_TILES):
                    n = tok_rows(t)
                    if t >= 2:
                        pe.wait_ge(taken, t - 1)
                    for k in range(KT):
                        x = slice(t * P, t * P + n)
                        pe.matmul(ps[:n, t % 2, :NAT], h_hi[:, k, x], w_hi[:, k, :], start=k == 0, stop=False)
                        pe.matmul(ps[:n, t % 2, :NAT], h_lo[:, k, x], w_hi[:, k, :], start=False, stop=False)
                        mm = pe.matmul(ps[:n, t % 2, :NAT], h_hi[:, k, x], w_lo[:, k, :], start=False,
                                       stop=k == KT - 1)
                    mm.then_inc(ps_ready, 1)


SSD_HEADS = 8
HEAD_DIM = 64
INNER = SSD_HEADS * HEAD_DIM
XBC = 8
TAPS = 4
XBC_TILE0 = 4
TOKENS = SEQ + SAMPLE


def conv_stage(core, proj, conv_state, conv_w, conv_b, xc, y):
    nc = core.nc
    pad = TAPS - 1
    with ExitStack() as ctx:
        sb = lambda name, shape, dt=F32: ctx.enter_context(nc.sbuf_tensor(f"conv_{name}", shape, dt))
        prompt = sb("prompt", [P, 2, pad + SEQ])
        new = sb("new", [P, XBC, SAMPLE])
        old = sb("old", [P, XBC, DEC_BATCH * pad])
        sample = sb("sample", [P, XBC, DEC_BATCH, pad + DEC_SEQ])
        acc = sb("acc", [P, 2, TOKENS])
        w = sb("w", [P, XBC, TAPS])
        b = sb("b", [P, XBC])
        small_landed, zeroed, sample_ready, tap_done, xc_ready = map(
            core.sem, ("conv_small_landed", "conv_zeroed", "conv_sample_ready", "tap_done", "xc_ready"))
        landed = [core.sem(f"xbc_landed_{s}") for s in range(2)]
        z_landed, y_ready = core.sem("z_landed"), core.sem("z_silu_ready")
        with nc.Block() as block:

            @block.sync
            def _(sp):
                sp.dma_start(y, proj[0:4].rearrange("i p t -> p i t")).then_inc(z_landed, 16)
                sp.dma_start(w[:], conv_w).then_inc(small_landed, 16)
                sp.dma_start(b[:], conv_b).then_inc(small_landed, 16)
                sp.dma_start(old[:], conv_state).then_inc(small_landed, 16)
                sp.dma_start(new[:], proj[XBC_TILE0:XBC_TILE0 + XBC, :, SEQ:TOKENS].rearrange("i p t -> p i t")
                             ).then_inc(small_landed, 16)
                for i in range(XBC):
                    if i >= 2:
                        sp.wait_ge(tap_done, (i - 1) * 2 * TAPS)
                    sp.dma_start(prompt[:, i % 2, pad:], proj[XBC_TILE0 + i, :, 0:SEQ]).then_inc(landed[i % 2], 16)

            @block.gpsimd
            def _(pool):
                pool.memset(prompt[:, :, 0:pad], 0.0).then_inc(zeroed, 1)
                pool.wait_ge(small_landed, 64)
                rows = sample[:].rearrange("p i b t -> p (i b) t")
                pool.tensor_copy(rows[:, :, 0:pad], old[:].rearrange("p i (b t) -> p (i b) t", t=pad)
                                 ).then_inc(sample_ready, 1)
                pool.tensor_copy(rows[:, :, pad:], new[:].rearrange("p i (b t) -> p (i b) t", t=DEC_SEQ)
                                 ).then_inc(sample_ready, 1)

            @block.vector
            def _(dve):
                dve.wait_ge(zeroed, 1)
                dve.wait_ge(small_landed, 64)
                dve.wait_ge(sample_ready, 2)
                for i in range(XBC):
                    dve.wait_ge(landed[i % 2], 16 * (i // 2 + 1))
                    if i >= 2:
                        dve.wait_ge(xc_ready, 2 * (i - 1))
                    a = acc[:, i % 2, 0:SEQ]
                    s = acc[:, i % 2, SEQ:TOKENS].rearrange("p (b t) -> p b t", t=DEC_SEQ)
                    for j in range(TAPS):
                        at_p, at_s = prompt[:, i % 2, j:j + SEQ], sample[:, i, :, j:j + DEC_SEQ]
                        if j == 0:
                            dve.tensor_scalar(a, at_p, w[:, i, 0:1], b[:, i:i + 1], ALU.mult, ALU.add
                                              ).then_inc(tap_done, 1)
                            dve.tensor_scalar(s, at_s, w[:, i, 0:1], b[:, i:i + 1], ALU.mult, ALU.add
                                              ).then_inc(tap_done, 1)
                        else:
                            dve.wait_ge(tap_done, (i * TAPS + j) * 2)
                            dve.scalar_tensor_tensor(a, at_p, w[:, i, j:j + 1], a, ALU.mult, ALU.add
                                                     ).then_inc(tap_done, 1)
                            dve.scalar_tensor_tensor(s, at_s, w[:, i, j:j + 1], s, ALU.mult, ALU.add
                                                     ).then_inc(tap_done, 1)

            @block.scalar
            def _(act):
                act.wait_ge(z_landed, 16)
                act.activation(y, y, ACT.Silu).then_inc(y_ready, 1)
                for i in range(XBC):
                    act.wait_ge(tap_done, (i + 1) * 2 * TAPS)
                    act.activation(xc[:, i, 0:SEQ], acc[:, i % 2, 0:SEQ], ACT.Silu).then_inc(xc_ready, 1)
                    act.activation(xc[:, i, SEQ:], acc[:, i % 2, SEQ:], ACT.Silu).then_inc(xc_ready, 1)


def ssd_stage(core, nat, xc, dt_bias, a_log, d_skip, state_in, y, state_out_p, state_out_s):
    nc = core.nc
    H, HD = SSD_HEADS, HEAD_DIM
    chunks = TOK_TILES
    S = chunks - 1
    with ExitStack() as ctx:
        sb = lambda name, shape, dt=F32: ctx.enter_context(nc.sbuf_tensor(f"ssd_{name}", shape, dt))
        ps = lambda name, n: ctx.enter_context(nc.psum_tensor(f"ssd_{name}_ps", [P, n], F32))
        dtb, alog, dskip = sb("dt_bias", [P, H]), sb("a_log", [P, H]), sb("d_skip", [P, 4])
        xdt, nabs, u, w1p, ln, dt, dta = (sb(n, [P, chunks, H]) for n in
                                          ("xdt", "neg_abs", "exp_neg", "one_plus", "ln", "dt", "dt_a"))
        ea = sb("exp_a", [P, H])
        state = sb("state", [P, INNER])
        s_state = sb("sample_state", [P, DEC_BATCH, INNER])
        xn, bn = sb("x_nat", [P, INNER]), sb("b_nat", [P, 256])
        acs = sb("acs", [P, 2 * H])
        te, te_dt = sb("to_end", [P, H]), sb("to_end_dt", [P, H])
        seg = sb("seg", [P, H, P])
        grow = sb("exp_acs", [P, H, P])
        cs = sb("c_scaled", [P, H, P])
        cbm = sb("cb_masked", [P, 2, P])
        xs = sb("x_scaled", [P, INNER])
        xsb = [a[:SAMPLE, :, SAMPLE:] for a in (seg, cs)]
        yt = sb("y_skip", [P, 4, P])
        tp_x, tp_b, small, bc = ps("tp_x", 512), ps("tp_b", 512), ps("small", 512), ps("bc", 1024)
        yp = ps("y", 512)
        st = ctx.enter_context(nc.psum_tensor("ssd_st", [P, 2, 512], F32))
        in_landed, chain, sp_act, dt_ready = map(
            core.sem, ("ssd_in_landed", "softplus_dve", "softplus_act", "dt_ready"))
        prep_ready, acs_ready, te_arg_ready, te_ready, seg_ready, cbm_ready, decay_ready = map(
            core.sem, ("prep_ready", "acs_ready", "te_arg_ready", "te_ready", "seg_ready", "cbm_ready",
                       "decay_ready"))
        xn_ready, bn_ready, grow_ready, cs_ready, w_ready, te_dt_ready, xs_ready, xsb_ready = map(
            core.sem, ("xn_ready", "bn_ready", "grow_ready", "cs_ready", "w_ready", "te_dt_ready", "xs_ready",
                       "xsb_ready"))
        y_ready, st_ready, skip_done, y_done, decayed, state_ready, s_decayed, s_state_ready, stored = map(
            core.sem, ("y_ready", "st_ready", "skip_done", "y_done", "state_decayed", "state_ready",
                       "sample_decayed", "sample_state_ready", "states_stored"))

        def rows(c):
            return SAMPLE if c == S else P

        def cols(c):
            return slice(c * P, c * P + rows(c))

        with nc.Block() as block:

            @block.sync
            def _(sp):
                for dst, src in ((dtb, dt_bias), (alog, a_log), (dskip, d_skip), (s_state, state_in)):
                    sp.dma_start(dst[:], src).then_inc(in_landed, 16)
                sp.wait_ge(state_ready, S)
                sp.dma_start(state_out_p, state[:]).then_inc(stored, 16)
                sp.wait_ge(s_state_ready, DEC_BATCH)
                sp.dma_start(state_out_s, s_state[:]).then_inc(stored, 16)
                sp.wait_ge(stored, 32)

            @block.tensor
            def _(pe):
                pe.wait_ge(dt_ready, 1)
                for c in range(chunks):
                    T = rows(c)
                    tri = core.tri_seq if c == S else core.tri
                    whole = core.same_seq if c == S else core.ones
                    if c:
                        for sem in (xn_ready, bn_ready, cbm_ready, acs_ready, grow_ready):
                            pe.wait_ge(sem, c)
                        pe.wait_ge(seg_ready, c * H)
                    for i in range(4):
                        pe.transpose(tp_x[:T, i * P:(i + 1) * P], xc[:, i, cols(c)], core.ident[:])
                    for g in range(2):
                        pe.transpose(tp_b[:T, g * P:(g + 1) * P], xc[:, 4 + g, cols(c)], core.ident[:])
                    for g in range(2):
                        pe.matmul(small[:T, (1 + g) * P:(1 + g) * P + T], xc[:, 4 + g, cols(c)],
                                  xc[:, 6 + g, cols(c)], start=True, stop=True)
                    pe.matmul(small[:T, 0:H], tri[:T, :T], dta[:T, c, :], start=True, stop=True)
                    pe.matmul(small[:T, H:2 * H], whole[:T, :T], dta[:T, c, :], start=True, stop=True)
                    for h in range(H):
                        mm = pe.matmul(bc[:, h * P:h * P + T], dta[:T, c, h:h + 1].to_broadcast([T, P]),
                                       tri[:T, :T], start=True, stop=True)
                    mm.then_inc(prep_ready, 1)
                    pe.wait_ge(xn_ready, c + 1)
                    pe.wait_ge(w_ready, (c + 1) * H)
                    if c:
                        pe.wait_ge(skip_done, 4 * c)
                        pe.wait_ge(state_ready, min(c, S))
                        pe.wait_ge(cs_ready, 2 * (c + 1))
                    if c == S:
                        pe.wait_ge(in_landed, 64)
                    for h in range(H):
                        q = HD * (h % 2)
                        hs = slice(h * HD, (h + 1) * HD)
                        at = (h // 2) * P
                        mm = pe.matmul(yp[q:q + HD, at:at + T], xn[:T, hs], seg[:T, h, :T], start=True, stop=c in (0, S))
                        if c == S:
                            for b in range(DEC_BATCH):
                                t = slice(b * DEC_SEQ, (b + 1) * DEC_SEQ)
                                mm = pe.matmul(yp[q:q + HD, at + b * DEC_SEQ:at + (b + 1) * DEC_SEQ],
                                               s_state[:, b, hs], cs[:, h, t], start=False, stop=True,
                                               skip_group_check=True)
                        elif c:
                            mm = pe.matmul(yp[q:q + HD, at:at + T], state[:, hs], cs[:, h, :T],
                                           start=False, stop=True)
                    mm.then_inc(y_ready, 1)
                    pe.wait_ge(bn_ready, c + 1)
                    if c < S:
                        pe.wait_ge(xs_ready, c + 1)
                        for g in range(2):
                            mm = pe.matmul(st[:, 0, g * 256:(g + 1) * 256], bn[:T, g * P:(g + 1) * P],
                                           xs[:T, g * 256:(g + 1) * 256], start=True, stop=True)
                        mm.then_inc(st_ready, 1)
                    else:
                        for b in range(DEC_BATCH):
                            pe.wait_ge(xsb_ready, b + 1)
                            if b >= 2:
                                pe.wait_ge(s_state_ready, b - 1)
                            for g in range(2):
                                mm = pe.matmul(st[:, b % 2, g * 256:(g + 1) * 256], bn[:T, g * P:(g + 1) * P],
                                               xsb[b % 2][:, 4 * g:4 * g + 4, :], start=True, stop=True)
                            mm.then_inc(st_ready, 1)

            @block.scalar
            def _(act):
                act.wait_ge(in_landed, 64)
                act.activation(ea[:], alog[:], ACT.Exp).then_inc(sp_act, 1)
                act.wait_ge(chain, 3)
                act.activation(u[:], nabs[:], ACT.Exp).then_inc(sp_act, 1)
                act.wait_ge(chain, 4)
                act.activation(ln[:], w1p[:], ACT.Ln).then_inc(sp_act, 1)
                for c in range(chunks):
                    T = rows(c)
                    act.wait_ge(prep_ready, c + 1)
                    act.activation(xn[:T, :], tp_x[:T, :], ACT.Copy).then_inc(xn_ready, 1)
                    act.activation(bn[:T, :], tp_b[:T, 0:256], ACT.Copy).then_inc(bn_ready, 1)
                    if c:
                        act.wait_ge(cs_ready, 2 * c)
                        act.wait_ge(state_ready, c)
                    act.activation(grow[:, :, :T], bc[:].rearrange("p (h t) -> p h t", t=P)[:, :, :T],
                                   ACT.Exp).then_inc(grow_ready, 1)
                    act.wait_ge(te_arg_ready, c + 1)
                    act.activation(te[:T, :], te[:T, :], ACT.Exp).then_inc(te_ready, 1)
                    act.wait_ge(seg_ready, (c + 1) * H)
                    act.activation(seg[:T, :, :T], seg[:T, :, :T], ACT.Exp).then_inc(decay_ready, 1)

            @block.gpsimd
            def _(pool):
                for c in range(chunks):
                    T = rows(c)
                    pool.wait_ge(grow_ready, c + 1)
                    if c:
                        pool.wait_ge(y_ready, c)
                    for g in range(2):
                        pool.tensor_tensor(cs[:, 4 * g:4 * g + 4, :T], grow[:, 4 * g:4 * g + 4, :T],
                                           xc[:, 6 + g:7 + g, cols(c)].to_broadcast([P, 4, T]),
                                           ALU.mult).then_inc(cs_ready, 1)

            @block.vector
            def _(dve):
                done = 0

                def step(ins):
                    nonlocal done
                    done += 1
                    ins.then_inc(chain, 1)
                    dve.wait_ge(chain, done)

                dve.wait_ge(in_landed, 64)
                lanes = lambda a: a[:].rearrange("p (o h) -> p o h", o=1).to_broadcast([P, chunks, H])
                step(dve.tensor_tensor(xdt[:], nat[:, :, 256:256 + H], lanes(dtb), ALU.add))
                step(dve.tensor_scalar(nabs[:], xdt[:], -1.0, None, ALU.mult))
                step(dve.tensor_tensor(nabs[:], nabs[:], xdt[:], ALU.min))
                dve.wait_ge(sp_act, 2)
                step(dve.tensor_scalar(w1p[:], u[:], 1.0, None, ALU.add))
                step(dve.tensor_scalar(dt[:], w1p[:], -1.0, None, ALU.add))
                step(dve.tensor_tensor(dt[:], u[:], dt[:], ALU.subtract))
                dve.wait_ge(sp_act, 3)
                step(dve.reciprocal(w1p[:], w1p[:]))
                step(dve.tensor_tensor(dt[:], dt[:], w1p[:], ALU.mult))
                step(dve.tensor_tensor(dt[:], dt[:], ln[:], ALU.add))
                step(dve.scalar_tensor_tensor(dt[:], xdt[:], 0.0, dt[:], ALU.max, ALU.add))
                dve.scalar_tensor_tensor(dta[:], dt[:], -1.0, lanes(ea), ALU.mult, ALU.mult
                                         ).then_inc(dt_ready, 1)
                for c in range(chunks):
                    T = rows(c)
                    tri = core.tri_seq if c == S else core.tri
                    dve.wait_ge(prep_ready, c + 1)
                    dve.tensor_copy(acs[:T, :], small[:T, 0:2 * H]).then_inc(acs_ready, 1)
                    for g in range(2):
                        ins = dve.tensor_tensor(cbm[:T, g, :T], small[:T, (1 + g) * P:(1 + g) * P + T],
                                                tri[:T, :T], ALU.mult)
                    ins.then_inc(cbm_ready, 1)
                    dve.wait_ge(acs_ready, c + 1)
                    if c:
                        dve.wait_ge(te_dt_ready, c)
                    dve.tensor_tensor(te[:T, :], acs[:T, H:], acs[:T, :H], ALU.subtract).then_inc(te_arg_ready, 1)
                    dve.wait_ge(grow_ready, c + 1)
                    for h in range(H):
                        dve.tensor_scalar(seg[:T, h, :T], bc[:T, h * P:h * P + T], acs[:T, h:h + 1], 0.0,
                                          ALU.subtract, ALU.min).then_inc(seg_ready, 1)
                    dve.wait_ge(te_ready, c + 1)
                    dve.tensor_tensor(te_dt[:T, :], te[:T, :], dt[:T, c, :], ALU.mult).then_inc(te_dt_ready, 1)
                    dve.wait_ge(te_dt_ready, c + 1)
                    dve.wait_ge(xn_ready, c + 1)
                    dve.tensor_tensor(xs[:T, :].rearrange("p (h d) -> p h d", h=H),
                                      xn[:T, :].rearrange("p (h d) -> p h d", h=H),
                                      te_dt[:T, :].rearrange("p (h o) -> p h o", o=1).to_broadcast([T, H, HD]),
                                      ALU.mult).then_inc(xs_ready, 1)
                    dve.wait_ge(decay_ready, c + 1)
                    dve.wait_ge(cbm_ready, c + 1)
                    for h in range(H):
                        dve.scalar_tensor_tensor(seg[:T, h, :T], seg[:T, h, :T], dt[:T, c, h:h + 1],
                                                 cbm[:T, h // 4, :T], ALU.mult, ALU.mult).then_inc(w_ready, 1)
                    dve.wait_ge(y_ready, c + 1)
                    if c:
                        dve.wait_ge(y_done, c)
                    for i in range(4):
                        dve.scalar_tensor_tensor(yt[:, i, :T], xc[:, i, cols(c)], dskip[:, i:i + 1],
                                                 yp[:, i * P:i * P + T], ALU.mult, ALU.add).then_inc(skip_done, 1)
                    dve.wait_ge(skip_done, 4 * (c + 1))
                    dve.tensor_tensor(y[:, :, cols(c)], yt[:, :, :T], y[:, :, cols(c)], ALU.mult).then_inc(y_done, 1)
                    if c < S:
                        flat = state[:]
                        if c == 0:
                            dve.wait_ge(st_ready, 1)
                            dve.tensor_copy(flat, st[:, 0, :]).then_inc(state_ready, 1)
                        else:
                            dve.wait_ge(grow_ready, c + 1)
                            h3 = flat.rearrange("p (h d) -> p h d", h=H)
                            dve.tensor_tensor(h3, h3, grow[:, :, P - 1:P].to_broadcast([P, H, HD]), ALU.mult
                                              ).then_inc(decayed, 1)
                            dve.wait_ge(decayed, c)
                            dve.wait_ge(st_ready, c + 1)
                            dve.tensor_tensor(flat, flat, st[:, 0, :], ALU.add).then_inc(state_ready, 1)
                    else:
                        dve.wait_ge(xs_ready, S + 1)
                        for b in range(DEC_BATCH):
                            if b >= 2:
                                dve.wait_ge(st_ready, S + b - 1)
                            dve.tensor_scalar(xsb[b % 2], xs[:SAMPLE, :].rearrange("p (h d) -> p h d", h=H), core.seq_mask[:SAMPLE, b:b + 1],
                                              None, ALU.mult).then_inc(xsb_ready, 1)
                            h3 = s_state[:, b, :].rearrange("p (h d) -> p h d", h=H)
                            end = b * DEC_SEQ + DEC_SEQ - 1
                            dve.tensor_tensor(h3, h3, grow[:, :, end:end + 1].to_broadcast([P, H, HD]),
                                              ALU.mult).then_inc(s_decayed, 1)
                            dve.wait_ge(s_decayed, b + 1)
                            dve.wait_ge(st_ready, S + b + 1)
                            dve.tensor_tensor(s_state[:, b, :], s_state[:, b, :], st[:, b % 2, :], ALU.add
                                              ).then_inc(s_state_ready, 1)


CONSTS = 5 * P + DEC_BATCH + 1


def make_consts():
    c = np.zeros((P, CONSTS), np.float32)
    i = np.arange(P)
    same = (i[:, None] // DEC_SEQ == i[None, :] // DEC_SEQ) & (i[:, None] < SAMPLE) & (i[None, :] < SAMPLE)
    tri = i[:, None] <= i[None, :]
    c[:, 0:P] = np.eye(P)
    c[:, P:2 * P] = tri
    c[:, 2 * P:3 * P] = tri & same
    c[:, 3 * P:4 * P] = same
    c[:, 4 * P:5 * P] = 1.0
    c[:, 5 * P:-1] = (i[:, None] // DEC_SEQ == np.arange(DEC_BATCH)[None, :]) & (i[:, None] < SAMPLE)
    c[:, -1] = i >= CMP_BLOCK - 1
    return c


def consts_stage(core, consts):
    nc = core.nc
    sb = lambda name, shape, dt=F32: core.ctx.enter_context(nc.sbuf_tensor(f"const_{name}", shape, dt))
    all_consts = sb("all", [P, CONSTS])
    core.ident, core.tri, core.tri_seq, core.same_seq, core.ones = (
        all_consts[:, i * P:(i + 1) * P] for i in range(5))
    core.seq_mask = all_consts[:, 5 * P:5 * P + DEC_BATCH]
    core.sees_cmp = all_consts[:, CONSTS - 1:]
    core.mean_model, core.mean_inner = sb("mean_model", [P, P]), sb("mean_inner", [P, P])
    core.eps = sb("eps", [P, 1])
    landed = core.sem("consts_landed")
    filled = core.sem("consts_filled")
    with nc.Block() as block:

        @block.sync
        def _(sp):
            sp.dma_start(all_consts[:], consts).then_inc(landed, 16)
            sp.wait_ge(landed, 16)

        @block.vector
        def _(dve):
            dve.memset(core.mean_model[:], 1.0 / D_MODEL).then_inc(filled, 1)
            dve.memset(core.mean_inner[:], 1.0 / INNER).then_inc(filled, 1)
            dve.memset(core.eps[:], EPS).then_inc(filled, 1)


def lay_conv_state(a):
    return np.ascontiguousarray(a[0].transpose(2, 0, 1).reshape(XBC, P, -1).transpose(1, 0, 2))


def lay_conv_w(a):
    return np.ascontiguousarray(a[0].T.reshape(XBC, P, TAPS).transpose(1, 0, 2))


def lay_d_skip(a):
    return np.ascontiguousarray(np.repeat(a[0], HEAD_DIM).reshape(4, P).T)


def lay_state(a):
    return np.ascontiguousarray(a[0].transpose(3, 0, 1, 2).reshape(P, DEC_BATCH, INNER))


CMP_BLOCK, CMP_STRIDE, CMP_HIDDEN = 32, 16, 256
N_CHUNK = SEQ // CMP_STRIDE
N_CMP = N_CHUNK - 1
SEQS = DEC_BATCH + 1
PAIR_STEPS = CMP_STRIDE // 2
PAGES = 8
KV_TILE0 = 16


def compress_stage(core, proj, pages_dram, page_table, w1, w2, pos, kc, vc, scratch, n_pool):
    nc = core.nc
    quad = DEC_BATCH // 2
    parts = ((DEC_BATCH, SEQS), (0, quad), (quad, DEC_BATCH))
    units = [(part, kv, g, hh) for part in range(3) for kv in range(2) for g in range(2) for hh in range(2)]
    with ExitStack() as ctx:
        sb = lambda name, shape, dt=F32: ctx.enter_context(nc.sbuf_tensor(f"cmp_{name}", shape, dt))
        ps = lambda name, n: ctx.enter_context(nc.psum_tensor(f"cmp_{name}_ps", [P, n, 512], F32))
        table = sb("page_table", [1, DEC_BATCH * PAGES], I32)
        pages = sb("pages", [P, DEC_BATCH * PAGES, 2, PAIR_STEPS, 2, PAGES])
        own = sb("prompt_pairs", [P, 2, PAIR_STEPS, 2, N_CHUNK])
        w1s = sb("w1", [P, 2, 2 * PAIR_STEPS, CMP_HIDDEN])
        w2s, ps_ = sb("w2", [P, 2, 2, HEAD_DIM]), sb("pos", [P, 2, 2 * PAIR_STEPS])
        bias = sb("bias", [P, 4])
        zeros = sb("zeros", [1, 1 + quad * N_CHUNK], BF16)
        hid_cols = 2 * 2 * SEQS * N_CHUNK
        rows_t = scratch[:, 0:2 * SEQ].rearrange("p (v t) -> p v t", v=2)
        hid = [a.rearrange("p (h g c) -> p h g c", h=2, g=2) for a in (
            scratch[:, 2 * SEQ:2 * SEQ + hid_cols], sb("hid", [P, hid_cols])[:])]
        hp, bp, op = ps("hid", 4), ps("bias", 1), ps("out", 3)
        table_landed, rows_landed, shuffled, own_ready = map(
            core.sem, ("table_landed", "rows_landed", "shuffled", "prompt_pairs_ready"))
        w_landed = [core.sem(f"cw_landed_{kv}") for kv in range(2)]
        pages_landed = [core.sem(f"pages_landed_{half}") for half in range(2)]
        bias_ps, bias_ready, hid_ps, hid_ready, out_ps, out_ready = map(
            core.sem, ("bias_ps", "bias_ready", "hid_ps", "hid_ready", "out_ps", "out_ready"))
        zeroed = core.sem("cmp_zeros_ready")
        turn_bank = lambda kv, g: hp[:, 2 + g, :] if kv else op[:, g, :]
        done_of = [max(j for j, u in enumerate(units) if u[1] == kv) + 1 for kv in range(2)]
        vc_banks = -(-SEQS // 4)

        with nc.Block() as block:

            @block.sync
            def _(sp):
                sp.dma_start(table[:], page_table).then_inc(table_landed, 16)
                for kv in range(2):
                    sp.dma_start(rows_t[:, kv, :], proj[KV_TILE0 + kv, :, 0:SEQ]).then_inc(rows_landed, 16)
                sp.wait_ge(table_landed, 16)
                for half in range(2):
                    with sp.Fori(half * quad, (half + 1) * quad) as b:
                        for j in range(PAGES):
                            at = b * PAGES + j
                            page = sp.value_load(table[0:1, bass.ds(at, 1)], min_val=0, max_val=n_pool - 1)
                            sp.dma_start(pages[:, bass.ds(at, 1)].rearrange("p o v r g n -> p (o v r g n)"),
                                         pages_dram[bass.ds(page, 1)].rearrange("o p c -> (o p) c")
                                         ).then_inc(pages_landed[half], 16)

            @block.scalar
            def _(act):
                for kv in range(2):
                    for dst, src in ((w1s, w1), (w2s, w2), (ps_, pos)):
                        act.dma_start(dst[:, kv], src[kv]).then_inc(w_landed[kv], 16)
                for kv in range(2):
                    for g in range(2):
                        act.wait_ge(shuffled, 2 * kv + g + 1)
                        act.activation(own[:, kv, :, g, :].rearrange("p r n -> p n r"),
                                       turn_bank(kv, g).rearrange("p (n r) -> p n r", r=PAIR_STEPS), ACT.Copy
                                       ).then_inc(own_ready, 1)
                act.wait_ge(bias_ps, 1)
                act.activation(bias[:], bp[:, 0, 0:4], ACT.Copy).then_inc(bias_ready, 1)
                act.wait_ge(bias_ready, 1)
                for j, (part, kv, g, hh) in enumerate(units):
                    b0, b1 = parts[part]
                    act.wait_ge(hid_ps, j + 1)
                    if j == 0:
                        act.wait_ge(own_ready, 4)
                    act.activation(hid[kv][:, hh, g, b0 * N_CHUNK:b1 * N_CHUNK],
                                   hp[:, j % 4, 1:1 + (b1 - b0) * N_CHUNK], ACT.Silu,
                                   bias=bias[:, 2 * kv + hh:2 * kv + hh + 1]).then_inc(hid_ready, 1)

            @block.tensor
            def _(pe):
                pe.wait_ge(rows_landed, 32)
                for kv in range(2):
                    for g in range(2):
                        gs = slice(g * HEAD_DIM, (g + 1) * HEAD_DIM)
                        for odd in range(2):
                            mm = pe.matmul(turn_bank(kv, g)[odd * HEAD_DIM:(odd + 1) * HEAD_DIM, :],
                                           core.ident[gs, gs], rows_t[gs, kv, odd::2], start=True, stop=True)
                        mm.then_inc(shuffled, 1)
                for kv in range(2):
                    pe.wait_ge(w_landed[kv], 48)
                    for hh in range(2):
                        for k in range(2 * PAIR_STEPS):
                            mm = pe.matmul(bp[:, 0, 2 * kv + hh:2 * kv + hh + 1],
                                           w1s[:, kv, k, hh * P:(hh + 1) * P], ps_[:, kv, k:k + 1],
                                           start=k == 0, stop=k == 2 * PAIR_STEPS - 1)
                mm.then_inc(bias_ps, 1)
                pe.wait_ge(own_ready, 4)
                pe.wait_ge(zeroed, 1)
                for j, (part, kv, g, hh) in enumerate(units):
                    b0, b1 = parts[part]
                    if part and (kv, g, hh) == (0, 0, 0):
                        pe.wait_ge(pages_landed[part - 1], quad * PAGES * 16)
                    if j >= 4:
                        pe.wait_ge(hid_ready, j - 3)
                    pe.matmul(hp[:, j % 4, 0:1 + (b1 - b0) * N_CHUNK], zeros[:, 0:P],
                              zeros[:, 0:1 + (b1 - b0) * N_CHUNK], start=True, stop=False)
                    for k in range(2 * PAIR_STEPS):
                        later, r = divmod(k, PAIR_STEPS)
                        at = hp[:, j % 4, 1 - later:1 - later + (b1 - b0) * N_CHUNK]
                        if part:
                            mm = pe.matmul(at.rearrange("p (b n) -> p b n", n=PAGES),
                                           w1s[:, kv, k, hh * P:(hh + 1) * P],
                                           pages[:, b0 * PAGES:b1 * PAGES, kv, r, g, :],
                                           start=False, stop=k == 2 * PAIR_STEPS - 1)
                        else:
                            mm = pe.matmul(at, w1s[:, kv, k, hh * P:(hh + 1) * P], own[:, kv, r, g, :],
                                           start=False, stop=k == 2 * PAIR_STEPS - 1)
                    mm.then_inc(hid_ps, 1)
                pe.wait_ge(hid_ready, done_of[0])
                for n, c in ((0, slice(0, DEC_BATCH * N_CHUNK)), (1, slice(DEC_BATCH * N_CHUNK, SEQS * N_CHUNK))):
                    for g in range(2):
                        for hh in range(2):
                            mm = pe.matmul(op[g * HEAD_DIM:(g + 1) * HEAD_DIM, n, 0:c.stop - c.start],
                                           w2s[:, 0, hh, :], hid[0][:, hh, g, c], start=hh == 0, stop=hh == 1)
                mm.then_inc(out_ps, 1)
                pe.wait_ge(hid_ready, done_of[1])
                pe.wait_ge(out_ready, 2)
                for b in range(SEQS):
                    for g in range(2):
                        at = ((b % 4) * 2 + g) * HEAD_DIM
                        for hh in range(2):
                            mm = pe.matmul(op[:N_CMP, b // 4, at:at + HEAD_DIM],
                                           hid[1][:, hh, g, b * N_CHUNK:b * N_CHUNK + N_CMP], w2s[:, 1, hh, :],
                                           start=hh == 0, stop=hh == 1)
                    if b % 4 == 3 or b == SEQS - 1:
                        mm.then_inc(out_ps, 1)

            @block.vector
            def _(dve):
                dve.memset(zeros[:], 0.0).then_inc(zeroed, 1)
                dve.wait_ge(out_ps, 1)
                for n, (b0, b1) in enumerate(((0, DEC_BATCH), (DEC_BATCH, SEQS))):
                    dve.tensor_copy(kc[:, b0 * N_CMP:b1 * N_CMP].rearrange("p (b n) -> p b n", n=N_CMP),
                                    op[:, n, 0:(b1 - b0) * N_CHUNK].rearrange("p (b n) -> p b n", n=N_CHUNK)
                                    [:, :, 0:N_CMP]).then_inc(out_ready, 1)
                for n in range(vc_banks):
                    cols = min(4, SEQS - 4 * n) * 2 * HEAD_DIM
                    dve.wait_ge(out_ps, n + 2)
                    dve.tensor_copy(vc[:N_CMP, n * 512:n * 512 + cols], op[:N_CMP, n, 0:cols]
                                    ).then_inc(out_ready, 1)


def lay_cmp_pages(a):
    n = a.shape[1]
    return np.ascontiguousarray(a[0].reshape(n, PAGES, PAIR_STEPS, 2, 2, 2, HEAD_DIM)
                                .transpose(0, 3, 6, 4, 2, 5, 1)).reshape(n, P, 4 * PAIR_STEPS * PAGES)


def lay_cmp_w1(a):
    return np.ascontiguousarray(a[0].reshape(2, PAIR_STEPS, 2, HEAD_DIM, CMP_HIDDEN).transpose(2, 3, 0, 1, 4)
                                ).reshape(P, 2 * PAIR_STEPS, CMP_HIDDEN)


def lay_cmp_w2(a):
    return np.ascontiguousarray(a[0].reshape(2, P, HEAD_DIM).transpose(1, 0, 2))


def lay_cmp_pos(a):
    return np.ascontiguousarray(a[0].reshape(2 * PAIR_STEPS, 2, HEAD_DIM).transpose(1, 2, 0)).reshape(P, -1)


NSA_HEADS, KV_GROUPS, GROUP_HEADS = 8, 2, 4
WINDOW = 512
BUCKETS, MAX_DIST = 32, 128
ROW_LEN = 400
ZERO_DIST = 255
SKEW, COPIES = ROW_LEN - 1, P * ROW_LEN
CMP_NEAR = 17
SCALE = HEAD_DIM ** -0.5


def make_bucket_rows():
    dist = ZERO_DIST - np.arange(ROW_LEN)
    n = np.maximum(dist, 0)
    exact = BUCKETS // 2
    large = exact + (np.log(np.maximum(n, exact).astype(np.float32) / exact) / np.log(MAX_DIST / exact)
                     * (BUCKETS - exact)).astype(np.int32)
    bucket = np.where(n < exact, n, np.minimum(large, BUCKETS - 1))
    rows = (bucket[None, :] == np.arange(BUCKETS)[:, None]).astype(np.float32)
    rows[BUCKETS - 1] -= 1.0
    return rows


def bias_rows_stage(core, rel_bias, bucket_rows, rows_dram):
    nc = core.nc
    with ExitStack() as ctx:
        sb = lambda name, shape: ctx.enter_context(nc.sbuf_tensor(f"rows_{name}", shape, F32))
        rel, hot = sb("rel", [BUCKETS, NSA_HEADS]), sb("hot", [BUCKETS, ROW_LEN])
        bias, win = sb("bias", [NSA_HEADS, ROW_LEN]), sb("win", [1, ROW_LEN])
        ps = ctx.enter_context(nc.psum_tensor("rows_ps", [P, 512], F32))
        landed, product, filled, stored = map(core.sem, ("rel_landed", "rows_product", "rows_filled", "rows_stored"))
        with nc.Block() as block:

            @block.sync
            def _(sp):
                sp.dma_start(rel[:], rel_bias).then_inc(landed, 16)
                sp.dma_start(hot[:], bucket_rows).then_inc(landed, 16)
                sp.wait_ge(filled, 4)
                for dst, src in ((rows_dram[0:NSA_HEADS], bias), (rows_dram[NSA_HEADS:NSA_HEADS + 1], win)):
                    n = src.shape[0]
                    sp.dma_start(dst, src[:].rearrange("h (o u) -> h o u", o=1).to_broadcast([n, P, ROW_LEN])
                                 ).then_inc(stored, 16)
                sp.wait_ge(stored, 32)

            @block.tensor
            def _(pe):
                pe.wait_ge(landed, 32)
                pe.matmul(ps[:NSA_HEADS, 0:ROW_LEN], rel[:], hot[:], start=True, stop=True).then_inc(product, 1)

            @block.vector
            def _(dve):
                dve.memset(win[:, 0:P], NEG).then_inc(filled, 1)
                dve.memset(win[:, P:], 0.0).then_inc(filled, 1)
                dve.memset(bias[:, ZERO_DIST + 1:], NEG).then_inc(filled, 1)
                dve.wait_ge(product, 1)
                dve.tensor_copy(bias[:, 0:ZERO_DIST + 1], ps[:NSA_HEADS, 0:ZERO_DIST + 1]).then_inc(filled, 1)


def from_rows(rows_dram, offset, dims):
    return bass.AP(rows_dram.tensor, offset, dims)


def prompt_nsa_stage(core, nat, kc, vc, proj, rows_dram, o_t):
    nc = core.nc
    H = NSA_HEADS
    tiles = SEQ // P
    with ExitStack() as ctx:
        sb = lambda name, shape, dt=F32: ctx.enter_context(nc.sbuf_tensor(f"pn_{name}", shape, dt))
        ps = lambda name, n: ctx.enter_context(nc.psum_tensor(f"pn_{name}_ps", [P, n, 512], F32))
        q_raw, q = sb("q_raw", [P, 2, H, P]), sb("q", [P, 2, H, P], F32R)
        raw = sb("raw", [P, 2, KV_GROUPS * SEQ])
        k_hi, k_lo = (sb(f"k_{part}", [P, 2, KV_GROUPS * SEQ], F32R) for part in ("hi", "lo"))
        near_hi, near_lo = (sb(f"near_bias_{part}", [P, H, 2 * P], F32R) for part in ("hi", "lo"))
        win_raw, win, eye = sb("window_raw", [P, P]), sb("window_mask", [P, P], F32R), sb("eye", [P, P], F32R)
        cmp_width = N_CHUNK + 8 * (tiles - 1)
        cmpb = sb("cmp_bias", [P, H, cmp_width])
        cmpb_hi, cmpb_lo = (sb(f"cmp_bias_{part}", [P, H, cmp_width], F32R) for part in ("hi", "lo"))
        kc_raw = sb("kc_raw", [P, KV_GROUPS, N_CHUNK])
        kc_hi, kc_lo = (sb(f"kc_{part}", [P, KV_GROUPS, N_CHUNK], F32R) for part in ("hi", "lo"))
        near0 = 8 * (tiles - 1) - 9
        gates = sb("gates", [P, tiles, H, 3])
        prob = sb("prob", [P, 2, 1024])
        probt = sb("prob_t", [P, 2, 1024])
        neg_max = sb("neg_max", [P, 2, 2])
        sums, rec, mix = sb("sums", [P, 2, 3]), sb("rec", [P, 2, 3]), sb("mix", [P, 2, 3])
        o = sb("o", [P, 2, INNER])
        s_ps, t_ps, o_ps = ps("s", 4), ps("t", 2), ps("o", 2)
        gates_ready, filled, near_landed, win_landed, cmpb_landed, kc_landed = map(
            core.sem, ("gates_ready", "pn_filled", "near_landed", "window_landed", "cmp_bias_landed",
                       "kc_landed"))
        k_landed = [core.sem(f"k_landed_{n}") for n in range(2)]
        q_landed = [core.sem(f"q_landed_{n}") for n in range(2)]
        hi_done, split_done, q_hi, q_ready = map(core.sem, ("pn_hi_done", "pn_split_done", "q_hi", "q_ready"))
        s_ready, max_ready, p_ready, t_ready, pt_act, pt_dve = map(
            core.sem, ("s_ready", "max_ready", "p_ready", "t_ready", "pt_act", "pt_dve"))
        pv_ready, rec_ready, mix_ready, part_ready, o_ready, ot_ps, ot_ready = map(
            core.sem, ("pv_ready", "rec_ready", "mix_ready", "o_part_ready", "o_ready", "o_t_ps", "o_t_ready"))

        units = [(i, g, r, b) for i in range(tiles) for r in range(GROUP_HEADS) for g in range(KV_GROUPS)
                 for b in range(2)]
        U = len(units)

        def key_tiles(u):
            i, _, _, b = units[u]
            return range(max(0, i - WINDOW // P) if b else 0, i + 1)

        to_split = [
            (raw[:, 0, :], k_hi[:, 0, :], k_lo[:, 0, :], k_landed[0], 64),
            (raw[:, 1, :], k_hi[:, 1, :], k_lo[:, 1, :], k_landed[1], 64),
            (kc_raw[:], kc_hi[:], kc_lo[:], kc_landed, 64),
            (cmpb[:], cmpb_hi[:], cmpb_lo[:], cmpb_landed, 16 * H),
            (raw[:, 0, :], near_hi[:].rearrange("p h c -> p (h c)"), near_lo[:].rearrange("p h c -> p (h c)"),
             near_landed, 16),
            (win_raw[:], win[:], None, win_landed, 16),
            (core.ident, eye[:], None, None, 0)]
        splits = sum(lo is not None for _, _, lo, _, _ in to_split)
        per_tile = 2 * H
        turn_at = 3
        pack_at = 6

        def load_q(sp, i):
            if i >= 2:
                sp.wait_ge(q_ready, i - 1)
            for part in (0, 1):
                for g in range(KV_GROUPS):
                    sp.dma_start(q_raw[part * HEAD_DIM:(part + 1) * HEAD_DIM, i % 2,
                                       g * GROUP_HEADS:(g + 1) * GROUP_HEADS, :],
                                 proj[12:16, g * HEAD_DIM:(g + 1) * HEAD_DIM, i * P:(i + 1) * P]
                                 .rearrange("r d t -> d r t")).then_inc(q_landed[i % 2], 16)

        act_copies, dve_copies = [0], [0]
        for u in range(U):
            n, b = len(key_tiles(u)), units[u][3]
            act_copies.append(act_copies[-1] + (1 if not b else 1 + (n > 4)))
            dve_copies.append(dve_copies[-1] + (n > 4 if not b else 1))

        with nc.Block() as block:

            @block.sync
            def _(sp):
                for n in range(2):
                    for part in (0, 1):
                        for g in range(KV_GROUPS):
                            sp.dma_start(raw[part * HEAD_DIM:(part + 1) * HEAD_DIM, n, g * SEQ:(g + 1) * SEQ],
                                         proj[KV_TILE0 + 2 + n, g * HEAD_DIM:(g + 1) * HEAD_DIM, 0:SEQ]
                                         ).then_inc(k_landed[n], 16)
                load_q(sp, 0)
                for h in range(H):
                    if h == 0:
                        sp.wait_ge(filled, 3)
                    sp.dma_start(cmpb[:, h, near0:near0 + CMP_NEAR],
                                 from_rows(rows_dram, h * COPIES + ZERO_DIST + CMP_BLOCK - 1 - 9 * CMP_STRIDE,
                                           [[SKEW, P], [CMP_STRIDE, CMP_NEAR]]),
                                 allow_slow_non_contiguous=True).then_inc(cmpb_landed, 16)
                sp.dma_start(win_raw[:], from_rows(rows_dram, H * COPIES + P - 1, [[SKEW, P], [1, P]])
                             ).then_inc(win_landed, 16)
                for part in (0, 1):
                    for g in range(KV_GROUPS):
                        sp.dma_start(kc_raw[part * HEAD_DIM:(part + 1) * HEAD_DIM, g, 0:N_CMP],
                                     kc[g * HEAD_DIM:(g + 1) * HEAD_DIM, DEC_BATCH * N_CMP:]
                                     ).then_inc(kc_landed, 16)
                sp.wait_ge(split_done, 1)
                sp.dma_start(raw[:, 0, :].rearrange("p (h c) -> p h c", h=H),
                             from_rows(rows_dram, P - 1, [[SKEW, P], [COPIES, H], [1, 2 * P]])
                             ).then_inc(near_landed, 16)
                for i in range(1, tiles):
                    load_q(sp, i)

            @block.gpsimd
            def _(pool):
                pool.memset(cmpb[:, :, 0:near0], 0.0).then_inc(filled, 1)
                pool.memset(cmpb[:, :, near0 + CMP_NEAR:], NEG).then_inc(filled, 1)
                pool.memset(kc_raw[:], 0.0).then_inc(filled, 1)

            @block.tensor
            def _(pe):
                def scores(u):
                    i, g, r, b = units[u]
                    h = g * GROUP_HEADS + r
                    qs = q[:, i % 2, h, :]
                    kt = key_tiles(u)
                    s = 2 * (u % 2)
                    if u % per_tile == 0:
                        pe.wait_ge(q_ready, i + 1)
                    if u >= 2:
                        pe.wait_ge(p_ready, u - 1)
                    for c in range(0, len(kt), 4):
                        part = kt[c:c + 4]
                        bank = s_ps[:, s + c // 4, :]
                        keys = slice(g * SEQ + part[0] * P, g * SEQ + (part[-1] + 1) * P)
                        pe.matmul(bank[:, 0:len(part) * P], qs, k_hi[:, b, keys], start=True, stop=False)
                        mm = pe.matmul(bank[:, 0:len(part) * P], qs, k_lo[:, b, keys], start=False, stop=True)
                        close = [j for j in part if i - j < 2]
                        if close:
                            at = bank[:, (close[0] - part[0]) * P:(close[-1] - part[0] + 1) * P]
                            cols = slice((1 - i + close[0]) * P, (2 - i + close[-1]) * P)
                            for table in (near_hi, near_lo):
                                mm = pe.matmul(at, eye[:], table[:, h, cols], start=False, stop=True,
                                               skip_group_check=True)
                        if b and i - part[0] == WINDOW // P:
                            mm = pe.matmul(bank[:, 0:P], eye[:], win[:], start=False, stop=True,
                                           skip_group_check=True)
                    if b:
                        at = s_ps[:, s + 1, P:P + N_CHUNK]
                        pe.matmul(at, qs, kc_hi[:, g, :], start=True, stop=False)
                        pe.matmul(at, qs, kc_lo[:, g, :], start=False, stop=False)
                        c0 = 8 * (tiles - 1 - i)
                        pe.matmul(at, eye[:], cmpb_hi[:, h, c0:c0 + N_CHUNK], start=False, stop=False)
                        mm = pe.matmul(at, eye[:], cmpb_lo[:, h, c0:c0 + N_CHUNK], start=False, stop=True)
                    mm.then_inc(s_ready, 1)

                def turn(u):
                    pe.wait_ge(p_ready, u + 1)
                    pe.wait_ge(pt_act, act_copies[u])
                    pe.wait_ge(pt_dve, dve_copies[u])
                    if u % per_tile == turn_at + 1 and units[u][0]:
                        pe.wait_ge(ot_ready, units[u][0])
                    for n in range(len(key_tiles(u))):
                        mm = pe.transpose(t_ps[:, n // 4, (n % 4) * P:(n % 4 + 1) * P],
                                          prob[:, u % 2, n * P:(n + 1) * P], core.ident[:])
                    if units[u][3]:
                        mm = pe.transpose(t_ps[:N_CMP, 1, P:2 * P], prob[:, u % 2, 5 * P:5 * P + N_CMP],
                                          core.ident[:])
                    mm.then_inc(t_ready, 1)

                def values(u):
                    i, g, r, b = units[u]
                    n = u // 2
                    pe.wait_ge(pt_act, act_copies[u + 1])
                    pe.wait_ge(pt_dve, dve_copies[u + 1])
                    if not b and n >= 2:
                        pe.wait_ge(o_ready, n - 1)
                    kt = key_tiles(u)
                    at = o_ps[:, n % 2, (1 + b) * HEAD_DIM:(2 + b) * HEAD_DIM]
                    vcol = b * P + g * HEAD_DIM
                    for m, j in enumerate(kt):
                        mm = pe.matmul(at, probt[:, u % 2, m * P:(m + 1) * P], nat[:, j, vcol:vcol + HEAD_DIM],
                                       start=m == 0, stop=m == len(kt) - 1)
                    if b:
                        vg = (DEC_BATCH * 2 + g) * HEAD_DIM
                        mm = pe.matmul(o_ps[:, n % 2, 0:HEAD_DIM], probt[:N_CMP, u % 2, 5 * P:6 * P],
                                       vc[:N_CMP, vg:vg + HEAD_DIM], start=True, stop=True)
                    mm.then_inc(pv_ready, 1)

                def turn_output(i, u):
                    pe.wait_ge(o_ready, (i + 1) * H)
                    pe.wait_ge(pt_act, act_copies[u + 1])
                    pe.wait_ge(pt_dve, dve_copies[u + 1])
                    for r in range(GROUP_HEADS):
                        mm = pe.transpose(t_ps[:, 0, r * P:(r + 1) * P], o[:, i % 2, r * P:(r + 1) * P],
                                          core.ident[:])
                    mm.then_inc(ot_ps, 1)

                pe.wait_ge(hi_done, len(to_split))
                pe.wait_ge(split_done, splits)
                scores(0)
                scores(1)
                for u in range(U):
                    turn(u)
                    if u + 2 < U:
                        scores(u + 2)
                    if u:
                        values(u - 1)
                    if u % per_tile == turn_at and units[u][0]:
                        turn_output(units[u][0] - 1, u)
                values(U - 1)
                turn_output(tiles - 1, U - 1)

            @block.scalar
            def _(act):
                def pack(i):
                    act.wait_ge(q_landed[i % 2], 64 * (i // 2 + 1))
                    if i >= 2:
                        act.wait_ge(s_ready, per_tile * (i - 1))
                    act.activation(q[:, i % 2], q_raw[:, i % 2], ACT.Copy, scale=SCALE).then_inc(q_hi, 1)

                for n, (source, hi, _, arrival, count) in enumerate(to_split):
                    if n == 2:
                        pack(0)
                    if arrival is not None:
                        act.wait_ge(arrival, count)
                    act.activation(hi, source, ACT.Copy).then_inc(hi_done, 1)
                act.activation(gates[:].rearrange("p t h c -> p t (h c)"), nat[:, 0:tiles, 264:288], ACT.Sigmoid
                               ).then_inc(gates_ready, 1)

                def exp(u):
                    i, g, r, b = units[u]
                    n = u // 2
                    w = len(key_tiles(u)) * P
                    s = s_ps[:, 2 * (u % 2):2 * (u % 2) + 2, :].rearrange("p a c -> p (a c)")
                    act.wait_ge(max_ready, u + 1)
                    if u >= 2:
                        act.wait_ge(t_ready, u - 1)
                    if n >= 2:
                        act.wait_ge(rec_ready, n - 1)
                    e = act.activation(prob[:, u % 2, 0:w], s[:, 0:w], ACT.Exp, bias=neg_max[:, u % 2, 0:1],
                                       accum_out=sums[:, n % 2, 1 + b:2 + b])
                    if b:
                        e = act.activation(prob[:, u % 2, 5 * P:5 * P + N_CMP], s[:, 5 * P:5 * P + N_CMP],
                                           ACT.Exp, bias=neg_max[:, u % 2, 1:2], accum_out=sums[:, n % 2, 0:1])
                    e.then_inc(p_ready, 1)

                def copy(u):
                    n, b = len(key_tiles(u)), units[u][3]
                    act.wait_ge(t_ready, u + 1)
                    if u >= 2:
                        act.wait_ge(pv_ready, u - 1)
                    if not b:
                        w = min(n, 4) * P
                        act.activation(probt[:, u % 2, 0:w], t_ps[:, 0, 0:w], ACT.Copy).then_inc(pt_act, 1)
                    else:
                        if n > 4:
                            act.activation(probt[:, u % 2, 4 * P:5 * P], t_ps[:, 1, 0:P], ACT.Copy
                                           ).then_inc(pt_act, 1)
                        act.activation(probt[:N_CMP, u % 2, 5 * P:6 * P], t_ps[:N_CMP, 1, P:2 * P], ACT.Copy
                                       ).then_inc(pt_act, 1)

                def take_output(i):
                    act.wait_ge(ot_ps, i + 1)
                    act.activation(o_t[:, :, i * P:(i + 1) * P],
                                   t_ps[:, 0, :].rearrange("p (r t) -> p r t", t=P), ACT.Copy
                                   ).then_inc(ot_ready, 1)

                exp(0)
                for u in range(U):
                    if u % per_tile == pack_at and u + per_tile < U:
                        pack(units[u][0] + 1)
                    if u + 1 < U:
                        exp(u + 1)
                    copy(u)
                    if u % per_tile == turn_at and units[u][0]:
                        take_output(units[u][0] - 1)
                take_output(tiles - 1)

            @block.vector
            def _(dve):
                def maxima(u):
                    b = units[u][3]
                    w = len(key_tiles(u)) * P
                    s = s_ps[:, 2 * (u % 2):2 * (u % 2) + 2, :].rearrange("p a c -> p (a c)")
                    dve.wait_ge(s_ready, u + 1)
                    m = dve.tensor_reduce(neg_max[:, u % 2, 0:1], s[:, 0:w], AX_X, ALU.max, negate=True)
                    if b:
                        m = dve.tensor_reduce(neg_max[:, u % 2, 1:2], s[:, 5 * P:5 * P + N_CMP], AX_X, ALU.max,
                                              negate=True)
                    m.then_inc(max_ready, 1)

                def copy(u):
                    n, b = len(key_tiles(u)), units[u][3]
                    dve.wait_ge(t_ready, u + 1)
                    if u >= 2:
                        dve.wait_ge(pv_ready, u - 1)
                    if b:
                        w = min(n, 4) * P
                        dve.tensor_copy(probt[:, u % 2, 0:w], t_ps[:, 0, 0:w]).then_inc(pt_dve, 1)
                    elif n > 4:
                        dve.tensor_copy(probt[:, u % 2, 4 * P:n * P], t_ps[:, 1, 0:(n - 4) * P]
                                        ).then_inc(pt_dve, 1)

                def weights(n):
                    i, g, r, _ = units[2 * n]
                    h = g * GROUP_HEADS + r
                    dve.wait_ge(p_ready, 2 * n + 2)
                    dve.reciprocal(rec[:, n % 2, :], sums[:, n % 2, :]).then_inc(rec_ready, 1)
                    dve.wait_ge(rec_ready, n + 1)
                    mixed = dve.tensor_tensor(mix[:, n % 2, :], rec[:, n % 2, :], gates[:, i, h, :], ALU.mult)
                    if i == 0:
                        mixed.then_inc(mix_ready, 1)
                        dve.wait_ge(mix_ready, 2 * n + 1)
                        mixed = dve.tensor_tensor(mix[:, n % 2, 0:1], mix[:, n % 2, 0:1], core.sees_cmp[:],
                                                  ALU.mult)
                    mixed.then_inc(mix_ready, 1)

                def mix_count(n):
                    return 2 * (n + 1) if n < H else n + 1 + H

                def combine(n):
                    i, g, r, _ = units[2 * n]
                    at = o[:, i % 2, (2 * r + g) * HEAD_DIM:(2 * r + g + 1) * HEAD_DIM]
                    dve.wait_ge(mix_ready, mix_count(n))
                    dve.wait_ge(pv_ready, 2 * n + 2)
                    if i >= 2:
                        dve.wait_ge(ot_ps, i - 1)
                    for k in range(3):
                        part = o_ps[:, n % 2, k * HEAD_DIM:(k + 1) * HEAD_DIM]
                        if k == 0:
                            dve.tensor_scalar(at, part, mix[:, n % 2, 0:1], None, ALU.mult
                                              ).then_inc(part_ready, 1)
                        else:
                            dve.wait_ge(part_ready, 2 * n + k)
                            dve.scalar_tensor_tensor(at, part, mix[:, n % 2, k:k + 1], at, ALU.mult, ALU.add
                                                     ).then_inc(part_ready if k == 1 else o_ready, 1)

                def pack(i):
                    up = slice(HEAD_DIM, P)
                    dve.wait_ge(q_hi, i + 1)
                    dve.scalar_tensor_tensor(q[up, i % 2], q_raw[up, i % 2], SCALE, q[up, i % 2].bitcast(F32),
                                             ALU.mult, ALU.subtract).then_inc(q_ready, 1)

                for n, (source, hi, lo, _, _) in enumerate(to_split):
                    if n == 2:
                        pack(0)
                    if lo is not None:
                        dve.wait_ge(hi_done, n + 1)
                        dve.tensor_tensor(lo, source, hi.bitcast(F32), ALU.subtract).then_inc(split_done, 1)
                dve.wait_ge(gates_ready, 1)
                maxima(0)
                for u in range(U):
                    if u % per_tile == pack_at and u + per_tile < U:
                        pack(units[u][0] + 1)
                    if u + 1 < U:
                        maxima(u + 1)
                    copy(u)
                    if units[u][3]:
                        weights(u // 2)
                        if u > 1:
                            combine(u // 2 - 1)
                combine(U // 2 - 1)


SLC_BLOCK = 64
PAST = SEQ
N_SLC = -(-(PAST + DEC_SEQ) // SLC_BLOCK)
FREE_BLOCKS = N_SLC - 3
NEW = SAMPLE
PAIRS = DEC_BATCH // 2
RULES = P + N_SLC + FREE_BLOCKS


def make_rules():
    c = np.zeros((P, RULES), np.float32)
    i = np.arange(P)
    key = (i // 32) * DEC_SEQ + i % DEC_SEQ
    c[:, :P] = key[:, None] == key[None, :]
    start = np.arange(N_CMP) * CMP_STRIDE
    block = np.arange(N_SLC) * SLC_BLOCK
    c[:N_CMP, P:P + N_SLC] = (start[:, None] < block[None, :] + SLC_BLOCK) & \
        (start[:, None] + CMP_BLOCK - 1 >= block[None, :])
    c[:, P + N_SLC:] = 1.0 + np.arange(FREE_BLOCKS)
    return c


def sample_nsa_stage(core, nat, kc, vc, proj, rows_dram, rules, page_table, slc_pages, win_kv, gates_dram,
                     o_t, n_pool):
    nc = core.nc
    H = NSA_HEADS
    G = GROUP_HEADS * DEC_SEQ
    with ExitStack() as ctx:
        sb = lambda name, shape, dt=F32: ctx.enter_context(nc.sbuf_tensor(f"sn_{name}", shape, dt))
        ps = lambda name, n: ctx.enter_context(nc.psum_tensor(f"sn_{name}_ps", [P, n, 512], F32))
        q_in, q = sb("q_in", [P, GROUP_HEADS, NEW]), sb("q", [P, DEC_BATCH, G])
        ks, kw = sb("ks_new", [P, NEW]), sb("kw_new", [P, NEW])
        rule = sb("rules", [P, RULES])
        table = sb("page_table", [1, DEC_BATCH * PAGES], I32)
        past = sb("slc_pages", [P, 2, 2, PAGES, 2 * P])
        win = sb("win_kv", [P, 2, 2, 2 * WINDOW])
        near, edge, cmpb = sb("near", [P, P]), sb("window_edge", [P, DEC_SEQ]), sb("cmp_bias", [P, N_CMP])
        newb = sb("new_bias", [P, PAIRS, NEW])
        gate_nat, gates = sb("gate_nat", [NEW, 3 * H]), sb("gates", [P, PAIRS, 3])
        pc, pcn = sb("p_cmp", [P, PAIRS, N_CMP]), sb("p_cmp_normed", [P, PAIRS, N_CMP])
        pct = sb("p_cmp_t", [P, PAIRS, P])
        imp, least, ranked, last, drop = (sb("imp", [P, PAIRS, N_SLC]), sb("least", [P, PAIRS]),
                                          sb("ranked", [P, PAIRS, FREE_BLOCKS]), sb("last", [P, PAIRS]),
                                          sb("drop", [P, PAIRS, FREE_BLOCKS]))
        ncm, csum, crec = sb("cmp_neg_max", [P, PAIRS]), sb("cmp_sum", [P, PAIRS]), sb("cmp_rec", [P, PAIRS])
        parts, neg_max, sums, total = (sb("max_parts", [P, 2, 2]), sb("neg_max", [P, 2]),
                                       sb("sums", [P, 2, 2]), sb("sum_total", [P, 2]))
        mix = sb("mix", [P, 2])
        PW = PAST + NEW + WINDOW + NEW + N_CMP
        W0, C0 = PAST + NEW, PAST + NEW + WINDOW + NEW
        prob, probt = sb("prob", [P, PW]), sb("prob_t", [P, 16, P])
        s_ps, t_ps, o_ps, m_ps = ps("s", 4), ps("t", 2), ps("o", 1), ps("m", 1)

        landed, filled, gate_done, gate_stored, q_ready, table_landed = map(
            core.sem, ("sn_landed", "sn_filled", "gate_sigmoid", "gate_stored", "sn_q_ready", "sn_table"))
        new_landed = core.sem("new_bias_landed")
        past_landed = [core.sem(f"past_landed_{s}") for s in range(2)]
        c_ready, cmax, pc_ready, crec_ready, pcn_ready, pct_ps, pct_ready, imp_ps, imp_ready, impg_ps = map(
            core.sem, ("c_scores", "c_max", "pc_ready", "c_rec", "pcn_ready", "pct_ps", "pct_ready", "imp_ps",
                       "imp_ready", "imp_group_ps"))
        rank, drop_ready = map(core.sem, ("rank_steps", "drop_ready"))
        s_ready, dropped, parts_ready, max_ready, p_ready, total_ready, rec_ready, mix_ready, scaled = map(
            core.sem, ("sn_s_ready", "dropped", "max_parts_ready", "sn_max_ready", "sn_p_ready",
                       "sn_total", "sn_rec", "sn_mix", "sn_scaled"))
        t_ready, pt_act, pt_dve, pv_ready, o_ready = map(
            core.sem, ("sn_t_ready", "sn_pt_act", "sn_pt_dve", "sn_pv_ready", "sn_o_ready"))

        with nc.Block() as block:

            @block.sync
            def _(sp):
                sp.dma_start(table[:], page_table).then_inc(table_landed, 16)
                sp.dma_start(q_in[:], proj[12:16, :, SEQ:TOKENS].rearrange("i p t -> p i t")).then_inc(landed, 16)
                sp.dma_start(ks[:], proj[KV_TILE0 + 2, :, SEQ:TOKENS]).then_inc(landed, 16)
                sp.dma_start(kw[:], proj[KV_TILE0 + 3, :, SEQ:TOKENS]).then_inc(landed, 16)
                sp.dma_start(rule[:], rules).then_inc(landed, 16)
                sp.wait_ge(table_landed, 16)

                def load(bt):
                    s = bt % 2
                    if bt >= 2:
                        sp.wait_ge(pv_ready, bt - 1)
                    for b2 in range(2):
                        b = 2 * bt + b2
                        for j in range(PAGES):
                            page = sp.value_load(table[0:1, b * PAGES + j:b * PAGES + j + 1],
                                                 min_val=0, max_val=n_pool - 1)
                            sp.dma_start(past[:, s, b2, j, :],
                                         slc_pages[bass.ds(page, 1)].rearrange("o p c -> (o p) c")
                                         ).then_inc(past_landed[s], 16)
                        sp.dma_start(win[:, s, b2, :], win_kv[b]).then_inc(past_landed[s], 16)

                for bt in range(PAIRS):
                    load(bt)

            @block.gpsimd
            def _(pool):
                pool.memset(newb[:], NEG).then_inc(filled, 1)
                pool.memset(cmpb[:, 0:N_CMP - 8], 0.0).then_inc(filled, 1)
                pool.wait_ge(landed, 16 * 8)
                pool.tensor_copy(cmpb[:, N_CMP - 8:], near[:, CMP_STRIDE - 1::CMP_STRIDE]).then_inc(filled, 1)
                pool.wait_ge(q_ready, 1)
                for r in range(GROUP_HEADS):
                    pool.tensor_copy(q[:, :, r * DEC_SEQ:(r + 1) * DEC_SEQ],
                                     q_in[:, r, :].rearrange("p (b t) -> p b t", t=DEC_SEQ)).then_inc(q_ready, 1)

            @block.scalar
            def _(act):
                act.activation(gate_nat[:], nat[:NEW, TOK_TILES - 1, 264:288], ACT.Sigmoid).then_inc(gate_done, 1)
                act.wait_ge(gate_done, 1)
                act.dma_start(gates_dram, gate_nat[:]).then_inc(gate_stored, 16)
                half = H * DEC_SEQ
                for b2 in range(2):
                    rows = slice(b2 * half, (b2 + 1) * half)
                    act.dma_start(near[rows, :], from_rows(rows_dram, P - 1, [[COPIES, H], [SKEW, DEC_SEQ], [1, P]])
                                  ).then_inc(landed, 16)
                    act.dma_start(edge[rows, :], from_rows(rows_dram, H * COPIES + P - 1,
                                                           [[0, H], [SKEW, DEC_SEQ], [1, DEC_SEQ]])
                                  ).then_inc(landed, 16)
                act.wait_ge(filled, 2)
                for bt in range(PAIRS):
                    for b2 in range(2):
                        b = 2 * bt + b2
                        rows = slice(b2 * half, (b2 + 1) * half)
                        act.dma_start(newb[rows, bt, b * DEC_SEQ:(b + 1) * DEC_SEQ], from_rows(
                            rows_dram, 2 * P - 1, [[COPIES, H], [SKEW, DEC_SEQ], [1, DEC_SEQ]])
                                      ).then_inc(new_landed, 16)
                act.wait_ge(gate_stored, 16)
                for bt in range(PAIRS):
                    for b2 in range(2):
                        b = 2 * bt + b2
                        rows = slice(b2 * half, (b2 + 1) * half)
                        act.dma_start(gates[rows, bt, :], bass.AP(
                            gates_dram.tensor, b * DEC_SEQ * 3 * H, [[3, H], [3 * H, DEC_SEQ], [1, 3]])
                                      ).then_inc(new_landed, 16)
                act.wait_ge(landed, 16 * 8)
                act.activation(q_in[:], q_in[:], ACT.Copy, scale=SCALE).then_inc(q_ready, 1)
                act.wait_ge(cmax, 1)
                for bt in range(PAIRS):
                    act.activation(pc[:, bt, :], m_ps[:, 0, bt * N_CMP:(bt + 1) * N_CMP], ACT.Exp,
                                   bias=ncm[:, bt:bt + 1], accum_out=csum[:, bt:bt + 1]).then_inc(pc_ready, 1)
                act.wait_ge(pct_ps, 1)
                act.activation(pct[:N_CMP].rearrange("p b c -> p (b c)"), t_ps[:N_CMP, 0, :], ACT.Copy
                               ).then_inc(pct_ready, 1)
                for bt in range(PAIRS):
                    act.wait_ge(max_ready, bt + 1)
                    if bt:
                        act.wait_ge(t_ready, 4 * bt)
                        act.wait_ge(total_ready, bt)
                    for br, (c0, bank, n) in enumerate(((0, 0, PAST), (W0, 2, WINDOW))):
                        act.activation(prob[:, c0:c0 + n], s_ps[:, bank:bank + n // 512, :].rearrange(
                            "p a c -> p (a c)"), ACT.Exp, bias=neg_max[:, br:br + 1],
                            accum_out=sums[:, br, 0:1])
                        e = act.activation(prob[:, c0 + n:c0 + n + NEW], s_ps[:, 3, br * NEW:(br + 1) * NEW],
                                           ACT.Exp, bias=neg_max[:, br:br + 1], accum_out=sums[:, br, 1:2])
                    e.then_inc(p_ready, 1)
                    for n in range(0, 4, 2):
                        act.wait_ge(t_ready, 4 * bt + n + 1)
                        if bt:
                            act.wait_ge(pv_ready, bt)
                        act.activation(probt[:, 4 * n:4 * n + 4, :].rearrange("p a c -> p (a c)"), t_ps[:, 0, :],
                                       ACT.Copy).then_inc(pt_act, 1)

            @block.tensor
            def _(pe):
                def row(b2, g):
                    return slice((2 * b2 + g) * G, (2 * b2 + g + 1) * G)

                def group(g):
                    return slice(g * HEAD_DIM, (g + 1) * HEAD_DIM)

                every = [(b2, g) for b2 in range(2) for g in range(KV_GROUPS)]
                pe.wait_ge(q_ready, 1 + GROUP_HEADS)
                pe.wait_ge(landed, 16 * 8)
                pe.wait_ge(filled, 3)
                for bt in range(PAIRS):
                    at = m_ps[:, 0, bt * N_CMP:(bt + 1) * N_CMP]
                    for b2, g in every:
                        b = 2 * bt + b2
                        pe.matmul(at[row(b2, g)], q[group(g), b, :], kc[group(g), b * N_CMP:(b + 1) * N_CMP],
                                  start=True, stop=True)
                    mm = pe.matmul(at, core.ident[:], cmpb[:], start=False, stop=True, skip_group_check=True)
                mm.then_inc(c_ready, 1)
                pe.wait_ge(pcn_ready, PAIRS)
                for bt in range(PAIRS):
                    mm = pe.transpose(t_ps[:N_CMP, 0, bt * P:(bt + 1) * P], pcn[:, bt, :], core.ident[:])
                mm.then_inc(pct_ps, 1)
                pe.wait_ge(pct_ready, 1)
                for bt in range(PAIRS):
                    mm = pe.matmul(m_ps[:, 0, bt * N_SLC:(bt + 1) * N_SLC], pct[:N_CMP, bt, :],
                                   rule[:N_CMP, P:P + N_SLC], start=True, stop=True)
                mm.then_inc(imp_ps, 1)
                pe.wait_ge(imp_ready, 1)
                pe.matmul(m_ps[:, 0, 256:256 + PAIRS * N_SLC], rule[:, 0:P],
                          imp[:].rearrange("p b s -> p (b s)"), start=True, stop=True).then_inc(impg_ps, 1)
                pe.wait_ge(new_landed, 16 * 16)
                for bt in range(PAIRS):
                    s = bt % 2
                    pe.wait_ge(past_landed[s], 16 * 2 * (PAGES + 1) * (bt // 2 + 1))
                    if bt:
                        pe.wait_ge(p_ready, bt)
                    for half in range(2):
                        for b2, g in every:
                            pe.matmul(s_ps[row(b2, g), half, :].rearrange("p (j t) -> p j t", t=P),
                                      q[group(g), 2 * bt + b2, :], past[group(g), s, b2, 4 * half:4 * half + 4, 0:P],
                                      start=True, stop=True)
                    pe.matmul(s_ps[:, 1, 3 * P:], core.ident[:], near[:], start=False, stop=True,
                              skip_group_check=True)
                    for b2, g in every:
                        pe.matmul(s_ps[row(b2, g), 2, :], q[group(g), 2 * bt + b2, :], win[group(g), s, b2, 0:WINDOW],
                                  start=True, stop=True)
                    pe.matmul(s_ps[:, 2, 3 * P:], core.ident[:], near[:], start=False, stop=True,
                              skip_group_check=True)
                    pe.matmul(s_ps[:, 2, 0:DEC_SEQ], core.ident[:], edge[:], start=False, stop=True,
                              skip_group_check=True)
                    for br, keys in enumerate((ks, kw)):
                        at = s_ps[:, 3, br * NEW:(br + 1) * NEW]
                        for b2, g in every:
                            pe.matmul(at[row(b2, g)], q[group(g), 2 * bt + b2, :], keys[group(g), :],
                                      start=True, stop=True)
                        mm = pe.matmul(at, core.ident[:], newb[:, bt, :], start=False, stop=True,
                                       skip_group_check=True)
                    mm.then_inc(s_ready, 1)
                    pe.wait_ge(scaled, 3 * (bt + 1))
                    for n in range(4):
                        if n >= 2 or bt:
                            if n % 2 == 0:
                                pe.wait_ge(pt_act, 2 * bt + n // 2)
                            else:
                                pe.wait_ge(pt_dve, 2 * bt + n // 2)
                        if n < 3:
                            c0 = (0, 4 * P, W0)[n]
                            for m in range(4):
                                mm = pe.transpose(t_ps[:, n % 2, m * P:(m + 1) * P],
                                                  prob[:, c0 + m * P:c0 + (m + 1) * P], core.ident[:])
                        else:
                            for m, (c0, w) in enumerate(((PAST, NEW), (W0 + WINDOW, NEW), (C0, N_CMP))):
                                mm = pe.transpose(t_ps[:w, 1, m * P:(m + 1) * P], prob[:, c0:c0 + w], core.ident[:])
                        mm.then_inc(t_ready, 1)
                    pe.wait_ge(pt_act, 2 * bt + 2)
                    pe.wait_ge(pt_dve, 2 * bt + 2)
                    for b2, g in every:
                        b = 2 * bt + b2
                        at = o_ps[group(g), 0, 0:GROUP_HEADS * NEW].rearrange("p (r t) -> p r t", t=NEW)[
                            :, :, b * DEC_SEQ:(b + 1) * DEC_SEQ]
                        tiles = [(past[:, s, b2, j, P + g * HEAD_DIM:P + (g + 1) * HEAD_DIM], P, j)
                                 for j in range(PAGES)]
                        tiles += [(win[:, s, b2, WINDOW + j * P + g * HEAD_DIM:WINDOW + j * P + (g + 1) * HEAD_DIM],
                                   P, 8 + j) for j in range(WINDOW // P)]
                        tiles += [(nat[:NEW, TOK_TILES - 1, br * P + g * HEAD_DIM:br * P + (g + 1) * HEAD_DIM],
                                   NEW, 12 + br) for br in range(2)]
                        tiles += [(vc[:N_CMP, (2 * b + g) * HEAD_DIM:(2 * b + g + 1) * HEAD_DIM], N_CMP, 14)]
                        for n, (v, k, slot) in enumerate(tiles):
                            mm = pe.matmul(at, v, probt[:k, slot, row(b2, g)].rearrange(
                                "p (r t) -> p r t", t=DEC_SEQ), start=n == 0, stop=n == len(tiles) - 1)
                    mm.then_inc(pv_ready, 1)

            @block.vector
            def _(dve):
                dve.wait_ge(c_ready, 1)
                dve.tensor_reduce(ncm[:], m_ps[:, 0, 0:PAIRS * N_CMP].rearrange("p (b n) -> p b n", n=N_CMP), AX_X,
                                  ALU.max, negate=True).then_inc(cmax, 1)
                dve.wait_ge(pc_ready, PAIRS)
                dve.reciprocal(crec[:], csum[:]).then_inc(crec_ready, 1)
                dve.wait_ge(crec_ready, 1)
                for bt in range(PAIRS):
                    dve.tensor_scalar(pcn[:, bt, :], pc[:, bt, :], crec[:, bt:bt + 1], None, ALU.mult
                                      ).then_inc(pcn_ready, 1)
                dve.wait_ge(imp_ps, 1)
                dve.tensor_copy(imp[:].rearrange("p b s -> p (b s)"), m_ps[:, 0, 0:PAIRS * N_SLC]
                                ).then_inc(imp_ready, 1)
                dve.wait_ge(impg_ps, 1)
                ranks = m_ps[:, 0, 256:256 + PAIRS * N_SLC].rearrange("p (b s) -> p b s", s=N_SLC)[
                    :, :, 1:1 + FREE_BLOCKS]
                number = rule[:, P + N_SLC:]
                dve.tensor_reduce(least[:], ranks, AX_X, ALU.min).then_inc(rank, 1)
                dve.wait_ge(rank, 1)
                for bt in range(PAIRS):
                    dve.scalar_tensor_tensor(ranked[:, bt, :], ranks[:, bt, :], least[:, bt:bt + 1], number,
                                             ALU.is_le, ALU.mult).then_inc(rank, 1)
                dve.wait_ge(rank, 1 + PAIRS)
                dve.tensor_reduce(last[:], ranked[:], AX_X, ALU.max).then_inc(rank, 1)
                dve.wait_ge(rank, 2 + PAIRS)
                for bt in range(PAIRS):
                    dve.tensor_scalar(drop[:, bt, :], number, last[:, bt:bt + 1], NEG, ALU.is_equal, ALU.mult
                                      ).then_inc(drop_ready, 1)
                dve.wait_ge(drop_ready, PAIRS)
                dve.wait_ge(new_landed, 16 * 16)
                for bt in range(PAIRS):
                    dve.wait_ge(s_ready, bt + 1)
                    flat = s_ps[:, 0:2, :].rearrange("p a c -> p (a c)")
                    ranked_keys = flat[:, SLC_BLOCK:SLC_BLOCK * (1 + FREE_BLOCKS)].rearrange(
                        "p (s t) -> p s t", t=SLC_BLOCK)
                    dve.tensor_tensor(ranked_keys, ranked_keys,
                                      drop[:, bt, :].rearrange("p (s o) -> p s o", o=1).to_broadcast(
                                          [P, FREE_BLOCKS, SLC_BLOCK]), ALU.add).then_inc(dropped, 1)
                    dve.wait_ge(dropped, bt + 1)
                    dve.tensor_reduce(parts[:, 0, 0:1], flat, AX_X, ALU.max, negate=True)
                    dve.tensor_reduce(parts[:, 0, 1:2], s_ps[:, 2, :], AX_X, ALU.max, negate=True)
                    dve.tensor_reduce(parts[:, 1, :], s_ps[:, 3, 0:2 * NEW].rearrange("p (b t) -> p b t", t=NEW),
                                      AX_X, ALU.max, negate=True).then_inc(parts_ready, 1)
                    dve.wait_ge(parts_ready, bt + 1)
                    dve.tensor_tensor(neg_max[:], parts[:, 0, :], parts[:, 1, :], ALU.min).then_inc(max_ready, 1)
                    dve.wait_ge(p_ready, bt + 1)
                    dve.tensor_tensor(total[:], sums[:, :, 0], sums[:, :, 1], ALU.add).then_inc(total_ready, 1)
                    dve.wait_ge(total_ready, bt + 1)
                    dve.reciprocal(total[:], total[:]).then_inc(rec_ready, 1)
                    dve.wait_ge(rec_ready, bt + 1)
                    dve.tensor_tensor(mix[:], total[:], gates[:, bt, 1:3], ALU.mult).then_inc(mix_ready, 1)
                    dve.wait_ge(mix_ready, bt + 1)
                    dve.tensor_scalar(prob[:, 0:W0], prob[:, 0:W0], mix[:, 0:1], None, ALU.mult).then_inc(scaled, 1)
                    dve.tensor_scalar(prob[:, W0:C0], prob[:, W0:C0], mix[:, 1:2], None, ALU.mult
                                      ).then_inc(scaled, 1)
                    dve.tensor_scalar(prob[:, C0:], pcn[:, bt, :], gates[:, bt, 0:1], None, ALU.mult
                                      ).then_inc(scaled, 1)
                    for n in range(1, 4, 2):
                        dve.wait_ge(t_ready, 4 * bt + n + 1)
                        if bt:
                            dve.wait_ge(pv_ready, bt)
                        if n == 1:
                            dve.tensor_copy(probt[:, 4:8, :].rearrange("p a c -> p (a c)"), t_ps[:, 1, :]
                                            ).then_inc(pt_dve, 1)
                        else:
                            dve.tensor_copy(probt[:NEW, 12:14, :].rearrange("p a c -> p (a c)"),
                                            t_ps[:NEW, 1, 0:2 * P])
                            dve.tensor_copy(probt[:N_CMP, 14, :], t_ps[:N_CMP, 1, 2 * P:3 * P]).then_inc(pt_dve, 1)
                dve.wait_ge(pv_ready, PAIRS)
                dve.tensor_copy(o_t[:, :, SEQ:TOKENS],
                                o_ps[:, 0, 0:GROUP_HEADS * NEW].rearrange("p (r t) -> p r t", t=NEW)
                                ).then_inc(o_ready, 1)
                dve.memset(o_t[:, :, TOKENS:], 0.0).then_inc(o_ready, 1)


def lay_slc_pages(a):
    k = a[0, :, :, 0].reshape(-1, P, P).transpose(0, 2, 1)
    return np.ascontiguousarray(np.concatenate([k, a[0, :, :, 1].reshape(-1, P, P)], axis=2))


def lay_win(a):
    k = a[0, :, :, 0].reshape(DEC_BATCH, WINDOW, P).transpose(0, 2, 1)
    v = a[0, :, :, 1].reshape(DEC_BATCH, WINDOW // P, P, P).transpose(0, 2, 1, 3).reshape(DEC_BATCH, P, WINDOW)
    return np.ascontiguousarray(np.concatenate([k, v], axis=2))


MEM_TOKENS, MEM_HEADS = 256, 4
MT = MEM_TOKENS // P
MI = MEM_HEADS * HEAD_DIM


def mem_kv_stage(core, m_hi, m_lo, w, kt_out, v_out):
    nc = core.nc
    with ExitStack() as ctx:
        sb = lambda name, shape, dt=F32: ctx.enter_context(nc.sbuf_tensor(f"mkv_{name}", shape, dt))
        raw = sb("w_raw", [P, KT, 2 * MI])
        w_hi, w_lo = sb("w_hi", [P, KT, 2 * MI], F32R), sb("w_lo", [P, KT, 2 * MI], F32R)
        out = sb("out", [P, 2 * MT, MI])
        ps = ctx.enter_context(nc.psum_tensor("mkv_ps", [P, 2 * MT, 512], F32))
        landed, hi_ready, lo_ready, ps_ready, out_ready, stored = map(
            core.sem, ("mkv_landed", "mkv_hi", "mkv_lo", "mkv_ps_ready", "mkv_out", "mkv_stored"))
        with nc.Block() as block:

            @block.sync
            def _(sp):
                sp.dma_start(raw[:], w).then_inc(landed, 16)
                for n in range(2 * MT):
                    sp.wait_ge(out_ready, n + 1)
                    sp.dma_start((kt_out if n < MT else v_out)[:, n % MT, :], out[:, n, :]).then_inc(stored, 16)
                sp.wait_ge(stored, 16 * 2 * MT)

            @block.scalar
            def _(act):
                act.wait_ge(landed, 16)
                act.activation(w_hi[:], raw[:], ACT.Copy).then_inc(hi_ready, 1)

            @block.vector
            def _(dve):
                dve.wait_ge(hi_ready, 1)
                dve.tensor_tensor(w_lo[:], raw[:], w_hi[:].bitcast(F32), ALU.subtract).then_inc(lo_ready, 1)
                for n in range(2 * MT):
                    dve.wait_ge(ps_ready, n + 1)
                    dve.tensor_copy(out[:, n, :], ps[:, n, 0:MI]).then_inc(out_ready, 1)

            @block.tensor
            def _(pe):
                pe.wait_ge(lo_ready, 1)
                for n in range(MT):
                    c = slice(n * P, (n + 1) * P)
                    for k in range(KT):
                        mm = passes(pe, ps[:, n, 0:MEM_TOKENS], w_hi[:, k, c], w_lo[:, k, c],
                                    m_hi[:, k, 0:MEM_TOKENS], m_lo[:, k, 0:MEM_TOKENS], k == 0, k == KT - 1)
                    mm.then_inc(ps_ready, 1)
                for n in range(MT):
                    c = slice(n * P, (n + 1) * P)
                    for k in range(KT):
                        mm = passes(pe, ps[:, MT + n, 0:MI], m_hi[:, k, c], m_lo[:, k, c],
                                    w_hi[:, k, MI:], w_lo[:, k, MI:], k == 0, k == KT - 1)
                    mm.then_inc(ps_ready, 1)


def mem_attend_stage(core, q_dram, kt_p, v_p, kv_s, o_hi, o_lo):
    nc = core.nc
    units = SEQ // P + 2
    prompt_units = SEQ // P
    PADQ = 32
    with ExitStack() as ctx:
        sb = lambda name, shape, dt=F32: ctx.enter_context(nc.sbuf_tensor(f"ma_{name}", shape, dt))
        ps = lambda name, n: ctx.enter_context(nc.psum_tensor(f"ma_{name}_ps", [P, n, 512], F32))
        q = sb("q", [P, MT, TOKENS])
        qp = sb("q_padded", [P, MT, DEC_BATCH, PADQ])
        kt, v = sb("kt", [P, MT, MEM_TOKENS]), sb("v", [P, MT, MI])
        kvs = sb("kv_sample", [P, DEC_BATCH, 4, MEM_TOKENS])
        prob, probt = sb("prob", [P, 2, 4, MEM_TOKENS]), sb("prob_t", [P, 2, 8, P])
        neg_max, sums, rec = sb("neg_max", [P, 2, 4]), sb("sums", [P, 2, 4]), sb("rec", [P, 2, 4])
        s_ps, t_ps, o_ps = ps("s", 4), ps("t", 2), ps("o", 2)
        landed, q_ready, pad_ready = map(core.sem, ("ma_landed", "ma_q_ready", "ma_pad_ready"))
        s_ready, max_ready, p_ready, rec_ready, scaled, t_ready, pt_act, pt_dve, pv_ready, hi_ready, lo_ready = map(
            core.sem, ("ma_s", "ma_max", "ma_p", "ma_rec", "ma_scaled", "ma_t", "ma_pt_act", "ma_pt_dve", "ma_pv",
                       "ma_hi", "ma_lo"))

        def out_cols(u):
            if u < prompt_units:
                return slice(u * P, (u + 1) * P)
            half = SAMPLE // 2
            return slice(SEQ + (u - prompt_units) * half, SEQ + (u - prompt_units + 1) * half)

        def out_tile(u):
            n = out_cols(u)
            return o_ps[:, u % 2, 0:MT * P].rearrange("p (m t) -> p m t", t=P)[:, :, 0:n.stop - n.start]

        with nc.Block() as block:

            @block.sync
            def _(sp):
                sp.dma_start(q[:], q_dram[:, :, 0:TOKENS].rearrange("i p t -> p i t")).then_inc(landed, 16)
                sp.dma_start(kt[:], kt_p).then_inc(landed, 16)
                sp.dma_start(v[:], v_p).then_inc(landed, 16)
                sp.dma_start(kvs[:], kv_s).then_inc(landed, 16)

            @block.gpsimd
            def _(pool):
                pool.memset(qp[:], 0.0).then_inc(pad_ready, 1)
                pool.wait_ge(pad_ready, 1)
                pool.wait_ge(q_ready, 1)
                for m in range(MT):
                    pool.tensor_copy(qp[:, m, :, 0:DEC_SEQ],
                                     q[:, m, SEQ:].rearrange("p (b t) -> p b t", t=DEC_SEQ)).then_inc(pad_ready, 1)

            @block.scalar
            def _(act):
                act.wait_ge(landed, 64)
                act.activation(q[:], q[:], ACT.Copy, scale=SCALE).then_inc(q_ready, 1)

                def exp(u):
                    act.wait_ge(max_ready, u + 1)
                    if u >= 2:
                        act.wait_ge(t_ready, 2 * (u - 1))
                    for n in range(4):
                        at = s_ps[:, 2 * (u % 2) + n // 2, (n % 2) * MEM_TOKENS:(n % 2 + 1) * MEM_TOKENS]
                        e = act.activation(prob[:, u % 2, n, :], at, ACT.Exp, bias=neg_max[:, u % 2, n:n + 1],
                                           accum_out=sums[:, u % 2, n:n + 1])
                    e.then_inc(p_ready, 1)

                exp(0)
                for u in range(units):
                    if u + 1 < units:
                        exp(u + 1)
                    act.wait_ge(t_ready, 2 * u + 1)
                    if u >= 2:
                        act.wait_ge(pv_ready, u - 1)
                    act.activation(probt[:, u % 2, 0:4, :].rearrange("p a c -> p (a c)"), t_ps[:, 0, :], ACT.Copy
                                   ).then_inc(pt_act, 1)
                    act.wait_ge(pv_ready, u + 1)
                    act.activation(o_hi[:, 0:MT, out_cols(u)], out_tile(u), ACT.Copy).then_inc(hi_ready, 1)

            @block.vector
            def _(dve):
                def maxima(u):
                    dve.wait_ge(s_ready, u + 1)
                    s = s_ps[:, 2 * (u % 2):2 * (u % 2) + 2, :].rearrange("p a (h m) -> p (a h) m", m=MEM_TOKENS)
                    dve.tensor_reduce(neg_max[:, u % 2, :], s, AX_X, ALU.max, negate=True).then_inc(max_ready, 1)

                maxima(0)
                for u in range(units):
                    if u + 1 < units:
                        maxima(u + 1)
                    dve.wait_ge(p_ready, u + 1)
                    dve.reciprocal(rec[:, u % 2, :], sums[:, u % 2, :]).then_inc(rec_ready, 1)
                    dve.wait_ge(rec_ready, u + 1)
                    dve.tensor_tensor(prob[:, u % 2], prob[:, u % 2],
                                      rec[:, u % 2, :].rearrange("p (n o) -> p n o", o=1).to_broadcast(
                                          [P, 4, MEM_TOKENS]), ALU.mult).then_inc(scaled, 1)
                    dve.wait_ge(t_ready, 2 * u + 2)
                    if u >= 2:
                        dve.wait_ge(pv_ready, u - 1)
                    dve.tensor_copy(probt[:, u % 2, 4:8, :].rearrange("p a c -> p (a c)"), t_ps[:, 1, :]
                                    ).then_inc(pt_dve, 1)
                    dve.wait_ge(hi_ready, u + 1)
                    dve.tensor_tensor(o_lo[:, 0:MT, out_cols(u)], out_tile(u),
                                      o_hi[:, 0:MT, out_cols(u)].bitcast(F32), ALU.subtract).then_inc(lo_ready, 1)

            @block.tensor
            def _(pe):
                def head_rows(h):
                    return slice((h % 2) * HEAD_DIM, (h % 2 + 1) * HEAD_DIM)

                def head_of(n):
                    return (n % 2) * 2 + n // 2

                def scores(u):
                    if u >= 2:
                        pe.wait_ge(p_ready, u - 1)
                    for n in range(4):
                        at = s_ps[:, 2 * (u % 2) + n // 2, (n % 2) * MEM_TOKENS:(n % 2 + 1) * MEM_TOKENS]
                        if u < prompt_units:
                            h = head_of(n)
                            mm = pe.matmul(at, q[head_rows(h), h // 2, u * P:(u + 1) * P],
                                           kt[head_rows(h), h // 2, :], start=True, stop=True)
                            continue
                        b = (u - prompt_units) * 4 + n
                        for h in range(MEM_HEADS):
                            mm = pe.matmul(at[h * PADQ:(h + 1) * PADQ], qp[head_rows(h), h // 2, b, :],
                                           kvs[head_rows(h), b, h // 2, :], start=True, stop=True)
                    mm.then_inc(s_ready, 1)

                def values(u):
                    pe.wait_ge(pt_act, u + 1)
                    pe.wait_ge(pt_dve, u + 1)
                    if u >= 2:
                        pe.wait_ge(lo_ready, u - 1)
                    for n in range(4):
                        for h in ([head_of(n)] if u < prompt_units else range(MEM_HEADS)):
                            hc = slice(h * HEAD_DIM, (h + 1) * HEAD_DIM)
                            for m in range(MT):
                                turned = probt[:, u % 2, 2 * n + m, :]
                                if u < prompt_units:
                                    at = o_ps[head_rows(h), u % 2, (h // 2) * P:(h // 2 + 1) * P]
                                    mm = pe.matmul(at, v[:, m, hc], turned, start=m == 0, stop=m == MT - 1)
                                else:
                                    b = (u - prompt_units) * 4 + n
                                    c = (h // 2) * P + n * DEC_SEQ
                                    mm = pe.matmul(o_ps[head_rows(h), u % 2, c:c + DEC_SEQ], kvs[:, b, 2 + m, hc],
                                                   turned[:, h * PADQ:h * PADQ + DEC_SEQ],
                                                   start=m == 0, stop=m == MT - 1)
                    mm.then_inc(pv_ready, 1)

                pe.wait_ge(landed, 64)
                pe.wait_ge(q_ready, 1)
                pe.wait_ge(pad_ready, 1 + MT)
                scores(0)
                scores(1)
                for u in range(units):
                    pe.wait_ge(scaled, u + 1)
                    if u:
                        pe.wait_ge(pt_act, u)
                        pe.wait_ge(pt_dve, u)
                    for n in range(4):
                        for m in range(MT):
                            mm = pe.transpose(t_ps[:, n // 2, ((n % 2) * MT + m) * P:((n % 2) * MT + m + 1) * P],
                                              prob[:, u % 2, n, m * P:(m + 1) * P], core.ident[:])
                        if n % 2:
                            mm.then_inc(t_ready, 1)
                    if u + 2 < units:
                        scores(u + 2)
                    values(u)


GAINS = ("norm_ffn1", "norm_mix", "norm_mem_q", "norm_mem_kv", "norm_ffn2", "norm_final")


def load_stage(core, pairs, dram_pairs=()):
    landed, copied = core.sem("inputs_landed"), core.sem("dram_copied")
    with core.nc.Block() as block:

        @block.sync
        def _(sp):
            for dst, src in pairs:
                sp.dma_start(dst, src).then_inc(landed, 16)
            for dst, src in dram_pairs:
                sp.dma_start(dst, src).then_inc(copied, 16)
            sp.wait_ge(landed, 16 * len(pairs))
            if dram_pairs:
                sp.wait_ge(copied, 16 * len(dram_pairs))


def trunk(nc, i, o):
    with ExitStack() as ctx:
        core = Core(nc, ctx)
        sb = lambda stack, name, shape, dt=F32: stack.enter_context(nc.sbuf_tensor(name, shape, dt))
        n_pool = i["slc_pages"].shape[0]
        rows = nc.dram_tensor("scratch_bias_rows", (NSA_HEADS + 1, P, ROW_LEN), F32, kind="Internal").ap()
        gates_dram = nc.dram_tensor("scratch_gates", (NEW, 3 * NSA_HEADS), F32, kind="Internal").ap()
        q_mem = nc.dram_tensor("scratch_mem_q", (MT, P, TP), F32, kind="Internal").ap()
        consts_stage(core, i["consts"])
        gains = sb(ctx, "gains", [P, len(GAINS), KT])
        inner_gains = sb(ctx, "inner_gains", [P, 2 * 4])
        gain = {name: gains[:, n, :] for n, name in enumerate(GAINS)}
        x = sb(ctx, "x", [P, KT, TP])
        def split(stack, name, tiles=KT):
            return [sb(stack, f"{name}_{part}", [P, tiles, TP], F32R) for part in ("hi", "lo")]

        model = ((0, KT, core.mean_model),)

        load_stage(core, [(x[:], i["x"]), (gains[:], i["gains"]), (inner_gains[:], i["inner_gains"])],
                   [(o["win_old"], i["win_rows"])])
        bias_rows_stage(core, i["rel_bias"], i["bucket_rows"], rows)
        with ExitStack() as c:
            h_hi, h_lo = split(c, "h_ffn1")
            with ExitStack() as c2:
                mem = sb(c2, "mem", [P, KT, MEM_TOKENS])
                load_stage(core, [(mem[:], i["mem"])])
                norm_stage(core, mem, gain["norm_mem_kv"], core.mean_model, h_hi, h_lo, "norm_mem_kv",
                           width=MEM_TOKENS, parts=1)
                mem_kv_stage(core, h_hi, h_lo, i["w_mem_kv"], o["mem_kt"], o["mem_v"])
            core.clear_sems()
            ffn_stage(core, x, gain["norm_ffn1"], h_hi, h_lo, i["w_ffn1_in"], i["w_ffn1_out"], "ffn1")
        core.clear_sems()
        with ExitStack() as c:
            mixed = sb(c, "mixed", [P, 2 * 4, TP])
            with ExitStack() as c1:
                nat = sb(c1, "nat", [P, TOK_TILES, NAT])
                with ExitStack() as c2:
                    h_hi, h_lo = split(c2, "h_mix")
                    gemm_stage(core, h_hi, h_lo, i["w_mix"], KT, 20, "mix", store=o["proj"],
                               norm_of=(x, gain["norm_mix"], model))
                    natural_stage(core, h_hi, h_lo, i["w_nat"], nat, "nat")
                with ExitStack() as c2:
                    xc = sb(c2, "xc", [P, XBC, TOKENS])
                    y = mixed[:, 0:4, :]
                    conv_stage(core, o["proj"], i["conv_state"], i["conv_w"], i["conv_b"], xc, y)
                    ssd_stage(core, nat, xc, i["dt_bias"], i["a_log"], i["d_skip"], i["ssd_state"], y,
                              o["ssd_p"], o["ssd_s"])
                core.clear_sems()
                kc, vc = sb(c1, "kc", [P, SEQS * N_CMP]), sb(c1, "vc", [P, SEQS * 2 * HEAD_DIM])
                compress_stage(core, o["proj"], i["cmp_pages"], i["page_table"],
                               *([i[f"{name}_{kv}"] for kv in range(2)] for name in ("cmp_w1", "cmp_w2", "cmp_pos")),
                               kc, vc, mixed[:, 4:8, :].rearrange("p i t -> p (i t)"), n_pool)
                core.clear_sems()
                o_t = mixed[:, 4:8, :]
                prompt_nsa_stage(core, nat, kc, vc, o["proj"], rows, o_t)
                sample_nsa_stage(core, nat, kc, vc, o["proj"], rows, i["rules"], i["page_table"],
                                 i["slc_pages"], i["win_kv"], gates_dram, o_t, n_pool)
                core.clear_sems()
                load_stage(core, [], [(o["v_rows"], nat[:, :, 0:2 * P])])
            h_hi, h_lo = split(c, "h_out")
            gemm_stage(core, h_hi, h_lo, i["w_out"], KT, KT, "wout", add_to=x,
                       norm_of=(mixed, inner_gains, ((0, 4, core.mean_inner), (4, 4, core.mean_inner))))
        h_hi, h_lo = split(ctx, "h")
        gemm_stage(core, h_hi, h_lo, i["w_mem_q"], KT, MT, "memq", store=q_mem,
                   norm_of=(x, gain["norm_mem_q"], model))
        mem_attend_stage(core, q_mem, o["mem_kt"], o["mem_v"], i["mem_kv_sample"], h_hi, h_lo)
        gemm_stage(core, h_hi, h_lo, i["w_mem_out"], MT, KT, "memout", add_to=x)
        core.clear_sems()
        ffn_stage(core, x, gain["norm_ffn2"], h_hi, h_lo, i["w_ffn2_in"], i["w_ffn2_out"], "ffn2")
        norm_stage(core, x, gain["norm_final"], core.mean_model, None, None, "norm_final", store=o["y"])



def lay_tokens(*parts):
    t = np.concatenate([a.reshape(-1, a.shape[-1]) for a in parts])
    return np.ascontiguousarray(t.T.reshape(-1, P, t.shape[0]).transpose(1, 0, 2))


def lay_tiles(w):
    k = w.shape[0] // P
    return np.ascontiguousarray(w.reshape(k, P, -1, P).transpose(2, 1, 0, 3)).reshape(-1, P, k * P)


def lay_ffn_in(w):
    return np.ascontiguousarray(w.reshape(KT, P, 2, FT, P).transpose(3, 1, 2, 0, 4)).reshape(FT, P, 2 * KT * P)


def lay_ffn_out(w):
    return np.ascontiguousarray(w.reshape(FT // 2, 2, P, D_MODEL).transpose(0, 2, 1, 3))


def group_major():
    f = np.arange(INNER).reshape(KV_GROUPS, GROUP_HEADS, HEAD_DIM)
    return f.transpose(1, 0, 2).reshape(-1)


Z0, XBC0, DT0 = 0, INNER, INNER + XBC * P
Q0 = DT0 + SSD_HEADS
KV0 = Q0 + INNER
GL0 = KV0 + 6 * P


def kernel(x_prompt, x_sample, cache_kv_cmp, cache_kv_slc, state_win_kv, state_ssd, state_conv, cache_mem_kv,
           page_table, mem_prompt, norm_ffn1, w_ffn1_in, w_ffn1_out, norm_mix, w_in, conv_w, conv_b, dt_bias,
           a_log, d_skip, norm_ssd_out, cmp_pos_k, cmp_w1_k, cmp_w2_k, cmp_pos_v, cmp_w1_v, cmp_w2_v,
           norm_nsa_out, w_out, norm_mem_q, norm_mem_kv, w_mem_q, w_mem_kv, w_mem_out, norm_ffn2, w_ffn2_in,
           w_ffn2_out, rel_bias, norm_final):
    import concourse.bacc as bacc
    from concourse.bass_utils import run_bass_kernel_spmd

    a = np.asarray
    per_tile = lambda g: np.ascontiguousarray(a(g).reshape(-1, P).T)
    spread = lambda v: np.ascontiguousarray(np.broadcast_to(a(v), (P, SSD_HEADS)))
    order = group_major()
    w = a(w_in)[0]
    kv_cols = [np.arange(KV0 + n * P, KV0 + (n + 1) * P) for n in range(6)]
    mix = np.concatenate([np.arange(Z0, DT0), Q0 + order, kv_cols[0], kv_cols[1], kv_cols[2], kv_cols[4]])
    natural = np.concatenate([kv_cols[3], kv_cols[5], np.arange(DT0, Q0), np.arange(GL0, w.shape[1])])
    pad = np.zeros((TP - TOKENS, D_MODEL), np.float32)
    mem_kv = a(cache_mem_kv)[0]
    mem_k = mem_kv[:, :, 0].reshape(DEC_BATCH, MEM_TOKENS, MT, P).transpose(3, 0, 2, 1)
    mem_v = mem_kv[:, :, 1].reshape(DEC_BATCH, MT, P, MI).transpose(2, 0, 1, 3)
    ins = {
        "x": lay_tokens(a(x_prompt), a(x_sample), pad),
        "mem": lay_tokens(a(mem_prompt)),
        "gains": np.ascontiguousarray(np.stack([per_tile(g) for g in (
            norm_ffn1, norm_mix, norm_mem_q, norm_mem_kv, norm_ffn2, norm_final)], axis=1)),
        "inner_gains": np.ascontiguousarray(np.concatenate([per_tile(norm_ssd_out),
                                                      per_tile(a(norm_nsa_out)[0][order])], axis=1)),
        "consts": make_consts(), "rules": make_rules(), "bucket_rows": make_bucket_rows(),
        "rel_bias": np.ascontiguousarray(a(rel_bias)),
        "w_ffn1_in": lay_ffn_in(a(w_ffn1_in)[0]), "w_ffn1_out": lay_ffn_out(a(w_ffn1_out)[0]),
        "w_ffn2_in": lay_ffn_in(a(w_ffn2_in)[0]), "w_ffn2_out": lay_ffn_out(a(w_ffn2_out)[0]),
        "w_mix": lay_tiles(w[:, mix]),
        "w_nat": np.ascontiguousarray(w[:, natural].reshape(KT, P, NAT).transpose(1, 0, 2)),
        "w_out": lay_tiles(a(w_out)[0][np.concatenate([np.arange(INNER), INNER + order])]),
        "w_mem_q": lay_tiles(a(w_mem_q)[0]), "w_mem_out": lay_tiles(a(w_mem_out)[0]),
        "w_mem_kv": np.ascontiguousarray(a(w_mem_kv)[0].reshape(KT, P, 2 * MI).transpose(1, 0, 2)),
        "conv_state": lay_conv_state(a(state_conv)), "conv_w": lay_conv_w(a(conv_w)), "conv_b": per_tile(conv_b),
        "dt_bias": spread(dt_bias), "a_log": spread(a_log), "d_skip": lay_d_skip(a(d_skip)),
        "ssd_state": lay_state(a(state_ssd)),
        "page_table": np.ascontiguousarray(a(page_table).reshape(1, -1)),
        "cmp_pages": lay_cmp_pages(a(cache_kv_cmp)), "slc_pages": lay_slc_pages(a(cache_kv_slc)),
        "win_kv": lay_win(a(state_win_kv)),
        "win_rows": np.ascontiguousarray(a(state_win_kv)[0, :, DEC_SEQ:].reshape(DEC_BATCH, -1)),
        "mem_kv_sample": np.ascontiguousarray(np.concatenate([mem_k, mem_v], axis=2)),
    }
    for kv, (pos, w1, w2) in enumerate(((cmp_pos_k, cmp_w1_k, cmp_w2_k), (cmp_pos_v, cmp_w1_v, cmp_w2_v))):
        ins[f"cmp_pos_{kv}"], ins[f"cmp_w1_{kv}"] = lay_cmp_pos(a(pos)), lay_cmp_w1(a(w1))
        ins[f"cmp_w2_{kv}"] = lay_cmp_w2(a(w2))
    outs = {
        "y": (P, KT, TP), "proj": (20, P, TP), "v_rows": (P, TOK_TILES, 2 * P),
        "ssd_p": (P, INNER), "ssd_s": (P, DEC_BATCH, INNER),
        "mem_kt": (P, MT, MEM_TOKENS), "mem_v": (P, MT, MI),
        "win_old": (DEC_BATCH, (WINDOW - DEC_SEQ) * 4 * HEAD_DIM),
    }
    nc = bacc.Bacc("TRN2", target_bir_lowering=False, num_devices=1)
    i = {k: nc.dram_tensor(f"in_{k}", v.shape, mybir.dt.from_np(v.dtype), kind="ExternalInput").ap()
         for k, v in ins.items()}
    o = {k: nc.dram_tensor(f"out_{k}", s, F32, kind="ExternalOutput").ap() for k, s in outs.items()}
    trunk(nc, i, o)
    r = run_bass_kernel_spmd(nc, [{f"in_{k}": v for k, v in ins.items()}], core_ids=[0]).results[0]
    r = {k: a(r[f"out_{k}"]) for k in outs}

    y = r["y"].transpose(1, 0, 2).reshape(D_MODEL, TP).T
    proj = r["proj"].transpose(0, 2, 1)
    v = r["v_rows"].transpose(1, 0, 2).reshape(-1, 2 * P)
    kc, vc, ks, kw = (proj[KV_TILE0 + n] for n in range(4))
    vs, vw = v[:TP, :P], v[:TP, P:]
    heads = (KV_GROUPS, HEAD_DIM)

    def rows_p(k, v_, first=0):
        return np.stack([k[first:SEQ].reshape(1, -1, *heads), v_[first:SEQ].reshape(1, -1, *heads)], axis=2)[None]

    def rows_s(k, v_):
        return np.stack([k[SEQ:TOKENS].reshape(DEC_BATCH, DEC_SEQ, *heads),
                         v_[SEQ:TOKENS].reshape(DEC_BATCH, DEC_SEQ, *heads)], axis=2)[None]

    xbc = proj[XBC_TILE0:XBC_TILE0 + XBC].transpose(1, 0, 2).reshape(TP, -1)
    pad = TAPS - 1
    mem_k = r["mem_kt"].transpose(1, 0, 2).reshape(MI, MEM_TOKENS).T.reshape(MEM_TOKENS, MEM_HEADS, HEAD_DIM)
    mem_v = r["mem_v"].transpose(1, 0, 2).reshape(MEM_TOKENS, MEM_HEADS, HEAD_DIM)
    win_old = r["win_old"].reshape(1, DEC_BATCH, WINDOW - DEC_SEQ, 2, *heads)
    c = np.ascontiguousarray
    return (
        c(y[:SEQ]).reshape(1, SEQ, D_MODEL), c(y[SEQ:TOKENS]).reshape(DEC_BATCH, DEC_SEQ, D_MODEL),
        c(rows_p(kc, vc)), c(rows_p(ks, vs)), c(rows_p(kw, vw, SEQ - WINDOW)),
        c(r["ssd_p"].reshape(P, SSD_HEADS, HEAD_DIM).transpose(1, 2, 0))[None, None],
        c(xbc[SEQ - pad:SEQ])[None, None],
        c(np.stack([mem_k, mem_v], axis=1))[None, None],
        c(rows_s(kc, vc)), c(rows_s(ks, vs)),
        c(np.concatenate([win_old, rows_s(kw, vw)], axis=2)),
        c(r["ssd_s"].reshape(P, DEC_BATCH, SSD_HEADS, HEAD_DIM).transpose(1, 2, 3, 0))[None],
        c(xbc[SEQ:TOKENS].reshape(DEC_BATCH, DEC_SEQ, -1)[:, DEC_SEQ - pad:])[None],
    )
```

```python
from contextlib import ExitStack

import numpy as np

import concourse.bass as bass
from concourse import mybir

F32 = mybir.dt.float32
BF16 = mybir.dt.bfloat16
F32R = mybir.dt.float32r
I32 = mybir.dt.int32
ALU = mybir.AluOpType
ACT = mybir.ActivationFunctionType
AX_X = mybir.AxisListType.X

P = 128
D_MODEL = 1024
SEQ = 1024
DEC_BATCH = 8
DEC_SEQ = 8
SAMPLE = DEC_BATCH * DEC_SEQ
KT = D_MODEL // P
GROUPS = 3
TG = 364
TP = GROUPS * TG
D_FF = 2816
FT = D_FF // P
EPS = 1e-6
NEG = -1e30


def groups(g):
    return slice(g * TG, (g + 1) * TG)


class Core:

    def __init__(self, nc, ctx):
        self.nc, self.ctx, self.serial, self.in_use = nc, ctx, 0, []

    def sem(self, name):
        self.serial += 1
        handle = self.nc.alloc_semaphore(name=f"{name}_{self.serial}")
        self.in_use.append(handle)
        return handle

    def clear_sems(self):
        self.nc.clear_and_free_semaphores(self.in_use)
        self.in_use = []
        self.nc.all_engine_barrier()


def norm_stage(core, xT, gain, ones, h_hi, h_lo, tag, tiles=KT, width=TP, parts=GROUPS):
    nc = core.nc
    w = width // parts
    with ExitStack() as ctx:
        sb = lambda name, shape, dt=F32: ctx.enter_context(nc.sbuf_tensor(f"{tag}_{name}", shape, dt))
        sq = sb("squares", [P, 2, width])
        total = sb("square_total", [P, width])
        rms = sb("rms", [P, width])
        inv = sb("inv_rms", [P, width])
        h = sb("normed", [P, 2, width])
        ms = ctx.enter_context(nc.psum_tensor(f"{tag}_mean_square", [P, parts, 512], F32))
        sq_ready, added, ms_ready, rms_ready, inv_ready = map(
            core.sem, ("sq_ready", "sq_added", "ms_ready", "rms_ready", "inv_ready"))
        h_ready, hi_ready, lo_ready = map(core.sem, ("h_ready", "h_hi_ready", "h_lo_ready"))
        with nc.Block() as block:

            @block.scalar
            def _(act):
                for k in range(tiles):
                    if k >= 2:
                        act.wait_ge(added, k - 1)
                    act.activation(sq[:, k % 2, :], xT[:, k, :width], ACT.Square).then_inc(sq_ready, 1)
                act.wait_ge(ms_ready, 1)
                act.activation(rms[:].rearrange("p (g w) -> p g w", w=w), ms[:, :, :w], ACT.Sqrt,
                               bias=core.eps[:, 0:1]).then_inc(rms_ready, 1)
                for k in range(tiles):
                    act.wait_ge(h_ready, k + 1)
                    act.activation(h_hi[:, k, :width], h[:, k % 2, :], ACT.Copy).then_inc(hi_ready, 1)

            @block.tensor
            def _(pe):
                pe.wait_ge(added, tiles)
                for g in range(parts):
                    mm = pe.matmul(ms[:, g, :w], ones[:], total[:, g * w:(g + 1) * w],
                                   start=True, stop=True)
                mm.then_inc(ms_ready, 1)

            @block.vector
            def _(dve):
                for k in range(tiles):
                    dve.wait_ge(sq_ready, k + 1)
                    if k == 0:
                        dve.tensor_copy(total[:], sq[:, 0, :]).then_inc(added, 1)
                    else:
                        dve.wait_ge(added, k)
                        dve.tensor_tensor(total[:], total[:], sq[:, k % 2, :], ALU.add).then_inc(added, 1)
                dve.wait_ge(rms_ready, 1)
                dve.reciprocal(inv[:], rms[:]).then_inc(inv_ready, 1)
                dve.wait_ge(inv_ready, 1)

                def rest(k):
                    dve.wait_ge(hi_ready, k + 1)
                    dve.tensor_tensor(h_lo[:, k, :width], h[:, k % 2, :], h_hi[:, k, :width].bitcast(F32),
                                      ALU.subtract).then_inc(lo_ready, 1)

                for k in range(tiles):
                    if k >= 2:
                        dve.wait_ge(lo_ready, k - 1)
                    dve.scalar_tensor_tensor(h[:, k % 2, :], xT[:, k, :width], gain[:, k:k + 1], inv[:],
                                             ALU.mult, ALU.mult).then_inc(h_ready, 1)
                    if k:
                        rest(k - 1)
                rest(tiles - 1)


class FusedNorm:

    def __init__(self, core, ctx, xT, gain, sets, h_hi, h_lo, tag, bank, pairs=None):
        self.core, self.xT, self.gain, self.h_hi, self.h_lo, self.bank = core, xT, gain, h_hi, h_lo, bank
        self.units = [(g, s) for g in range(GROUPS) for s in sets]
        self.per_group = sum(s[1] for s in sets)
        sb = lambda name, n: ctx.enter_context(core.nc.sbuf_tensor(f"{tag}_{name}", [P, n, TG], F32))
        self.sq, self.h = pairs or (sb("squares", 2), sb("normed", 2))
        self.rms, self.inv = sb("rms", 1), sb("inv_rms", 1)
        self.sq_ready, self.summed, self.rms_ready, self.inv_ready = map(
            core.sem, ("sq_ready", "sq_summed", "rms_ready", "inv_ready"))
        self.h_ready, self.hi_ready, self.lo_ready = map(core.sem, ("h_ready", "h_hi_ready", "h_lo_ready"))

    def before(self, u):
        return sum(self.units[v][1][1] for v in range(u))

    def scalar(self, act, stage_work=()):
        def squares(u):
            g, (first, tiles, _) = self.units[u]
            for k in range(tiles):
                j = self.before(u) + k
                if j >= 2:
                    act.wait_ge(self.summed, j - 1)
                act.activation(self.sq[:, j % 2, :], self.xT[:, first + k, groups(g)], ACT.Square
                               ).then_inc(self.sq_ready, 1)

        def roots(u):
            act.wait_ge(self.summed, self.before(u + 1))
            if u:
                act.wait_ge(self.inv_ready, u)
            act.activation(self.rms[:, 0, :], self.bank(u)[:, :TG], ACT.Sqrt, bias=self.core.eps[:, 0:1]
                           ).then_inc(self.rms_ready, 1)

        def round_hi(u):
            g, (first, tiles, _) = self.units[u]
            for k in range(tiles):
                j = self.before(u) + k
                act.wait_ge(self.h_ready, j + 1)
                act.activation(self.h_hi[:, first + k, groups(g)], self.h[:, j % 2, :], ACT.Copy
                               ).then_inc(self.hi_ready, 1)

        squares(0)
        roots(0)
        for u in range(len(self.units)):
            if u < len(stage_work):
                stage_work[u]()
            if u + 1 < len(self.units):
                squares(u + 1)
            if self.h_lo is not None:
                round_hi(u)
            if u + 1 < len(self.units):
                roots(u + 1)

    def tensor(self, pe):
        for u, (g, (first, tiles, ones)) in enumerate(self.units):
            for k in range(tiles):
                j = self.before(u) + k
                pe.wait_ge(self.sq_ready, j + 1)
                pe.matmul(self.bank(u)[:, :TG], ones[:], self.sq[:, j % 2, :], start=k == 0,
                          stop=k == tiles - 1).then_inc(self.summed, 1)

    def vector(self, dve, stage_work=()):
        def rest(j, first, k, g):
            dve.wait_ge(self.hi_ready, j + 1)
            dve.tensor_tensor(self.h_lo[:, first + k, groups(g)], self.h[:, j % 2, :],
                              self.h_hi[:, first + k, groups(g)].bitcast(F32), ALU.subtract
                              ).then_inc(self.lo_ready, 1)

        for u, (g, (first, tiles, _)) in enumerate(self.units):
            dve.wait_ge(self.rms_ready, u + 1)
            if u:
                dve.wait_ge(self.h_ready, self.before(u))
            dve.reciprocal(self.inv[:, 0, :], self.rms[:, 0, :]).then_inc(self.inv_ready, 1)
            if u < len(stage_work):
                stage_work[u]()
            dve.wait_ge(self.inv_ready, u + 1)
            for k in range(tiles):
                j = self.before(u) + k
                if self.h_lo is None:
                    dve.scalar_tensor_tensor(self.h_hi[:, first + k, groups(g)].bitcast(F32),
                                             self.xT[:, first + k, groups(g)],
                                             self.gain[:, first + k:first + k + 1], self.inv[:, 0, :],
                                             ALU.mult, ALU.mult).then_inc(self.h_ready, 1)
                    continue
                if j >= 2:
                    dve.wait_ge(self.lo_ready, j - 1)
                dve.scalar_tensor_tensor(self.h[:, j % 2, :], self.xT[:, first + k, groups(g)],
                                         self.gain[:, first + k:first + k + 1], self.inv[:, 0, :],
                                         ALU.mult, ALU.mult).then_inc(self.h_ready, 1)
                if k:
                    rest(j - 1, first, k - 1, g)
            if self.h_lo is not None:
                rest(j, first, tiles - 1, g)
        if self.h_lo is not None:
            dve.wait_ge(self.lo_ready, GROUPS * self.per_group)

    def wait_group(self, pe, g):
        pe.wait_ge(self.lo_ready, (g + 1) * self.per_group)


def final_norm_stage(core, xT, gain, h, store):
    nc = core.nc
    with ExitStack() as ctx:
        ms = ctx.enter_context(nc.psum_tensor("final_mean_square", [P, GROUPS, 512], F32))
        norm = FusedNorm(core, ctx, xT, gain, ((0, KT, core.mean_model),), h, None, "final_norm",
                         lambda u: ms[:, u, :])
        stored = core.sem("y_stored")
        with nc.Block() as block:

            @block.sync
            def _(sp):
                for g in range(GROUPS):
                    sp.wait_ge(norm.h_ready, (g + 1) * KT)
                    sp.dma_start(store[:, :, groups(g)], h[:, :, groups(g)].bitcast(F32)).then_inc(stored, 16)
                sp.wait_ge(stored, 16 * GROUPS)

            @block.scalar
            def _(act):
                norm.scalar(act)

            @block.tensor
            def _(pe):
                norm.tensor(pe)

            @block.vector
            def _(dve):
                norm.vector(dve)


def passes(pe, out, w_hi, w_lo, x_hi, x_lo, start, stop):
    pe.matmul(out, w_hi, x_hi, start=start, stop=False)
    pe.matmul(out, w_hi, x_lo, start=False, stop=False)
    return pe.matmul(out, w_lo, x_hi, start=False, stop=stop)


def ffn_stage(core, xT, gain, h_hi, h_lo, w_in, w_out, tag):
    nc = core.nc
    chunks = FT // 2
    with ExitStack() as ctx:
        sb = lambda name, shape, dt=F32: ctx.enter_context(nc.sbuf_tensor(f"{tag}_{name}", shape, dt))
        up_raw = sb("up_raw", [P, 2 * KT * P])
        up_hi = sb("up_hi", [P, 2, 2, KT, P], F32R)
        up_lo = sb("up_lo", [P, 2, 2, KT, P], F32R)
        down_raw = sb("down_raw", [P, 2, D_MODEL])
        down_hi = sb("down_hi", [P, 2, D_MODEL], F32R)
        down_lo = sb("down_lo", [P, 2, D_MODEL], F32R)
        act_hi = sb("act_hi", [P, 3, TP], F32R)
        act_lo = sb("act_lo", [P, 3, TP], F32R)
        silu = sb("silu", [P, 2, TG])
        prod = sb("prod", [P, 2, TG])
        gu = ctx.enter_context(nc.psum_tensor(f"{tag}_gate_up", [P, 2, 2, 512], F32))
        dn = ctx.enter_context(nc.psum_tensor(f"{tag}_down", [P, 4, 512], F32))
        up_landed, up_hi_ready, up_lo_ready = map(
            core.sem, ("up_landed", "up_hi_ready", "up_lo_ready"))
        down_landed, down_hi_ready, down_lo_ready = map(
            core.sem, ("down_landed", "down_hi_ready", "down_lo_ready"))
        gu_ready, silu_ready, prod_ready, act_hi_ready, act_ready = map(
            core.sem, ("gu_ready", "silu_ready", "prod_ready", "act_hi_ready", "act_ready"))
        dn_ready, dn_added = map(core.sem, ("dn_ready", "dn_added"))
        norm = FusedNorm(core, ctx, xT, gain, ((0, KT, core.mean_model),), h_hi, h_lo, f"{tag}_norm",
                         lambda u: dn[:, u, :], (silu, prod))

        def slot(par, f):
            return 2 if f else par

        def schedule(eng, chunk, last):
            chunk(0, 0, True, False)
            chunk(1, 1, True, True)
            chunk(2, 0, True, True)
            with eng.Fori(1, (chunks - 3) // 2) as it:
                chunk(it * 2 + 1, 1, True, True)
                chunk(it * 2 + 2, 0, True, True)
            chunk(chunks - 2, (chunks - 2) % 2, True, True)
            chunk(chunks - 1, (chunks - 1) % 2, False, True)
            last()

        with nc.Block() as block:

            @block.sync
            def _(sp):
                def load_up(n, guard):
                    if guard:
                        sp.wait_ge(up_lo_ready, n)
                    sp.dma_start(up_raw[:], w_in[bass.ds(n, 1)].rearrange("o p c -> (o p) c")
                                 ).then_inc(up_landed, 16)

                def load_down(c, guard):
                    if guard:
                        sp.wait_ge(down_lo_ready, c)
                    sp.dma_start(down_raw[:], w_out[bass.ds(c, 1)].rearrange("o p f c -> (o p) f c")
                                 ).then_inc(down_landed, 16)

                def chunk(c, par, more, full):
                    load_down(c, full)
                    if more:
                        load_up(c * 2 + 2, True)
                        load_up(c * 2 + 3, True)

                load_up(0, False)
                load_up(1, True)
                schedule(sp, chunk, lambda: None)

            @block.scalar
            def _(act):
                def split_up(n, s, reused):
                    act.wait_ge(up_landed, n * 16 + 16)
                    if reused:
                        act.wait_ge(gu_ready, (n - 1) * GROUPS)
                    act.activation(up_hi[:, s].rearrange("p u k c -> p (u k c)"), up_raw[:],
                                   ACT.Copy).then_inc(up_hi_ready, 1)

                def gate(c, f):
                    for g in range(GROUPS):
                        j = c * 6 + (3 * f + g)
                        act.wait_ge(gu_ready, j + 1)
                        if not (isinstance(c, int) and j < 2):
                            act.wait_ge(prod_ready, j - 1)
                        act.activation(silu[:, (f + g) % 2, :], gu[:, (f + g) % 2, 0, :TG],
                                       ACT.Silu).then_inc(silu_ready, 1)

                def chunk(c, par, more, full):
                    gate(c, 0)
                    if more:
                        split_up(c * 2 + 2, 0, True)
                    act.wait_ge(down_landed, c * 16 + 16)
                    if full:
                        act.wait_ge(dn_ready, c * (KT * GROUPS))
                    act.activation(down_hi[:].rearrange("p f c -> p (f c)"),
                                   down_raw[:].rearrange("p f c -> p (f c)"), ACT.Copy
                                   ).then_inc(down_hi_ready, 1)
                    gate(c, 1)
                    if more:
                        split_up(c * 2 + 3, 1, True)

                norm.scalar(act, [lambda: split_up(0, 0, False), lambda: split_up(1, 1, False)])
                schedule(act, chunk, lambda: None)

            @block.tensor
            def _(pe):
                def up(c, f):
                    pe.wait_ge(up_lo_ready, c * 2 + (f + 1))
                    for g in range(GROUPS):
                        j = c * 6 + (3 * f + g)
                        if isinstance(c, int) and j < GROUPS:
                            norm.wait_group(pe, g)
                        if not (isinstance(c, int) and j < 2):
                            pe.wait_ge(prod_ready, j - 1)
                        for u in range(2):
                            for k in range(KT):
                                mm = passes(pe, gu[:, (f + g) % 2, u, :TG], up_hi[:, f, u, k, :],
                                            up_lo[:, f, u, k, :], h_hi[:, k, groups(g)],
                                            h_lo[:, k, groups(g)], k == 0, k == KT - 1)
                        mm.then_inc(gu_ready, 1)

                def down(c, par):
                    pe.wait_ge(down_lo_ready, c + 1)
                    pe.wait_ge(act_ready, c * 6 + 6)
                    for t in range(KT):
                        for g in range(GROUPS):
                            d = c * (KT * GROUPS) + (t * GROUPS + g)
                            if not (isinstance(c, int) and d < 4):
                                pe.wait_ge(dn_added, d - 3)
                            for f in range(2):
                                s = slot(par, f)
                                mm = passes(pe, dn[:, (t * GROUPS + g) % 4, :TG],
                                            down_hi[:, f, t * P:(t + 1) * P], down_lo[:, f, t * P:(t + 1) * P],
                                            act_hi[:, s, groups(g)], act_lo[:, s, groups(g)], f == 0, f == 1)
                            mm.then_inc(dn_ready, 1)

                def chunk(c, par, more, full):
                    up(c, 0)
                    if full:
                        down(c - 1, 1 - par)
                    up(c, 1)

                norm.tensor(pe)
                schedule(pe, chunk, lambda: down(chunks - 1, (chunks - 1) % 2))

            @block.vector
            def _(dve):
                def split_up(n, s):
                    dve.wait_ge(up_hi_ready, n + 1)
                    dve.tensor_tensor(up_lo[:, s].rearrange("p u k c -> p (u k c)"), up_raw[:],
                                      up_hi[:, s].rearrange("p u k c -> p (u k c)").bitcast(F32),
                                      ALU.subtract).then_inc(up_lo_ready, 1)

                def multiply(c, f, par):
                    if not (isinstance(c, int) and c < (1 if f else 2)):
                        dve.wait_ge(dn_ready, (c if f else c - 1) * (KT * GROUPS))
                    for g in range(GROUPS):
                        j = c * 6 + (3 * f + g)
                        b, s = (f + g) % 2, slot(par, f)
                        dve.wait_ge(silu_ready, j + 1)
                        dve.tensor_tensor(prod[:, b, :], silu[:, b, :], gu[:, b, 1, :TG],
                                          ALU.mult).then_inc(prod_ready, 1)
                        dve.wait_ge(prod_ready, j + 1)
                        dve.tensor_copy(act_hi[:, s, groups(g)], prod[:, b, :]).then_inc(act_hi_ready, 1)
                        dve.wait_ge(act_hi_ready, j + 1)
                        dve.tensor_tensor(act_lo[:, s, groups(g)], prod[:, b, :],
                                          act_hi[:, s, groups(g)].bitcast(F32), ALU.subtract
                                          ).then_inc(act_ready, 1)

                def add(c):
                    for t in range(KT):
                        for g in range(GROUPS):
                            d = c * (KT * GROUPS) + (t * GROUPS + g)
                            dve.wait_ge(dn_ready, d + 1)
                            dve.scalar_tensor_tensor(xT[:, t, groups(g)], dn[:, (t * GROUPS + g) % 4, :TG],
                                                     0.5, xT[:, t, groups(g)], ALU.mult, ALU.add
                                                     ).then_inc(dn_added, 1)

                def chunk(c, par, more, full):
                    multiply(c, 0, par)
                    if more:
                        split_up(c * 2 + 2, 0)
                    if full:
                        add(c - 1)
                    dve.wait_ge(down_hi_ready, c + 1)
                    dve.tensor_tensor(down_lo[:], down_raw[:], down_hi[:].bitcast(F32),
                                      ALU.subtract).then_inc(down_lo_ready, 1)
                    multiply(c, 1, par)
                    if more:
                        split_up(c * 2 + 3, 1)

                norm.vector(dve, [lambda: split_up(0, 0), lambda: split_up(1, 1)])
                schedule(dve, chunk, lambda: add(chunks - 1))


def gemm_stage(core, x_hi, x_lo, w, k_tiles, n_tiles, tag, store=None, add_to=None, norm_of=None):
    nc = core.nc
    with ExitStack() as ctx:
        sb = lambda name, shape, dt=F32: ctx.enter_context(nc.sbuf_tensor(f"{tag}_{name}", shape, dt))
        raw = sb("w_raw", [P, 2, k_tiles * P])
        w_hi = sb("w_hi", [P, 2, k_tiles, P], F32R)
        w_lo = sb("w_lo", [P, 2, k_tiles, P], F32R)
        out = sb("out", [P, 2, TP]) if store is not None else None
        ps = ctx.enter_context(nc.psum_tensor(f"{tag}_ps", [P, 6, 512], F32))
        landed = [core.sem(f"w_landed_{s}") for s in range(2)]
        hi_ready, lo_ready, ps_ready, taken = map(core.sem, ("w_hi_ready", "w_lo_ready", "ps_ready", "ps_taken"))
        stored = [core.sem(f"stored_{s}") for s in range(2)]
        pairs = n_tiles // 2
        norm = None
        if norm_of is not None:
            norm = FusedNorm(core, ctx, *norm_of, x_hi, x_lo, f"{tag}_norm", lambda u: ps[:, u, :])

        def schedule(eng, pair):
            pair(0, True, pairs > 1)
            if pairs > 2:
                with eng.Fori(1, pairs - 1) as i:
                    pair(i, False, True)
            if pairs > 1:
                pair(pairs - 1, False, False)

        with nc.Block() as block:

            @block.sync
            def _(sp):
                def load(i, s, guard):
                    if guard:
                        sp.wait_ge(lo_ready, i * 2 + (s - 1))
                    sp.dma_start(raw[:, s, :], w[bass.ds(i * 2 + s, 1)].rearrange("o p c -> (o p) c")
                                 ).then_inc(landed[s], 16)

                def pair(i, first, more):
                    if more:
                        for s in range(2):
                            load(i + 1, s, True)

                for s in range(2):
                    load(0, s, False)
                schedule(sp, pair)

            @block.tensor
            def _(pe):
                def pair(i, first, more):
                    for s in range(2):
                        pe.wait_ge(lo_ready, i * 2 + (s + 1))
                        for g in range(GROUPS):
                            if norm is not None and first and s == 0:
                                norm.wait_group(pe, g)
                            if not first:
                                pe.wait_ge(taken, i * 6 + (s * 3 + g - 5))
                            for k in range(k_tiles):
                                mm = passes(pe, ps[:, s * 3 + g, :TG], w_hi[:, s, k, :], w_lo[:, s, k, :],
                                            x_hi[:, k, groups(g)], x_lo[:, k, groups(g)],
                                            k == 0, k == k_tiles - 1)
                            mm.then_inc(ps_ready, 1)

                if norm is not None:
                    norm.tensor(pe)
                schedule(pe, pair)

            @block.scalar
            def _(act):
                def split(i, s, reused):
                    act.wait_ge(landed[s], i * 16 + 16)
                    if reused:
                        act.wait_ge(ps_ready, i * 6 + (s * 3 - 3))
                    act.activation(w_hi[:, s].rearrange("p k c -> p (k c)"), raw[:, s, :],
                                   ACT.Copy).then_inc(hi_ready, 1)

                def pair(i, first, more):
                    for s in range(2):
                        if store is not None:
                            if not first:
                                act.wait_ge(stored[s], i * 16)
                            for g in range(GROUPS):
                                act.wait_ge(ps_ready, i * 6 + (s * 3 + g + 1))
                                act.activation(out[:, s, groups(g)], ps[:, s * 3 + g, :TG], ACT.Copy
                                               ).then_inc(taken, 1)
                            act.wait_ge(taken, i * 6 + (s * 3 + 3))
                            act.dma_start(store[bass.ds(i * 2 + s, 1)].rearrange("o p c -> (o p) c"),
                                          out[:, s, :]).then_inc(stored[s], 16)
                        if more:
                            split(i + 1, s, True)

                first_weights = [lambda: split(0, 0, False), lambda: split(0, 1, False)]
                if norm is not None:
                    norm.scalar(act, first_weights)
                else:
                    for work in first_weights:
                        work()
                schedule(act, pair)
                if store is not None:
                    for s in range(2):
                        act.wait_ge(stored[s], 16 * pairs)

            @block.vector
            def _(dve):
                def split(i, s):
                    dve.wait_ge(hi_ready, i * 2 + (s + 1))
                    dve.tensor_tensor(w_lo[:, s].rearrange("p k c -> p (k c)"), raw[:, s, :],
                                      w_hi[:, s].rearrange("p k c -> p (k c)").bitcast(F32),
                                      ALU.subtract).then_inc(lo_ready, 1)

                def pair(i, first, more):
                    for s in range(2):
                        if add_to is not None:
                            for g in range(GROUPS):
                                dve.wait_ge(ps_ready, i * 6 + (s * 3 + g + 1))
                                x = add_to[:, bass.ds(i * 2 + s, 1), groups(g)].rearrange("p o t -> p (o t)")
                                dve.tensor_tensor(x, ps[:, s * 3 + g, :TG], x, ALU.add).then_inc(taken, 1)
                        if more:
                            split(i + 1, s)

                first_weights = [lambda: split(0, 0), lambda: split(0, 1)]
                if norm is not None:
                    norm.vector(dve, first_weights)
                else:
                    for work in first_weights:
                        work()
                schedule(dve, pair)


NAT = 288
TOK_TILES = 9


def tok_rows(t):
    return P if t < TOK_TILES - 1 else TP - P * (TOK_TILES - 1)


def natural_stage(core, h_hi, h_lo, w, nat, tag):
    nc = core.nc
    with ExitStack() as ctx:
        sb = lambda name, shape, dt=F32: ctx.enter_context(nc.sbuf_tensor(f"{tag}_{name}", shape, dt))
        raw = sb("w_raw", [P, KT, NAT])
        w_hi = sb("w_hi", [P, KT, NAT], F32R)
        w_lo = sb("w_lo", [P, KT, NAT], F32R)
        ps = ctx.enter_context(nc.psum_tensor(f"{tag}_ps", [P, 2, 512], F32))
        landed, hi_ready, lo_ready, cleared, ps_ready, taken = map(
            core.sem, ("nw_landed", "nw_hi_ready", "nw_lo_ready", "nat_cleared", "nat_ps_ready", "nat_taken"))
        with nc.Block() as block:

            @block.sync
            def _(sp):
                sp.dma_start(raw[:], w).then_inc(landed, 16)

            @block.scalar
            def _(act):
                act.wait_ge(landed, 16)
                act.activation(w_hi[:], raw[:], ACT.Copy).then_inc(hi_ready, 1)

            @block.vector
            def _(dve):
                dve.memset(nat[:, TOK_TILES - 1, :], 0.0).then_inc(cleared, 1)
                dve.wait_ge(hi_ready, 1)
                dve.tensor_tensor(w_lo[:], raw[:], w_hi[:].bitcast(F32), ALU.subtract).then_inc(lo_ready, 1)
                dve.wait_ge(cleared, 1)
                for t in range(TOK_TILES):
                    n = tok_rows(t)
                    dve.wait_ge(ps_ready, t + 1)
                    dve.tensor_copy(nat[:n, t, :], ps[:n, t % 2, :NAT]).then_inc(taken, 1)

            @block.tensor
            def _(pe):
                pe.wait_ge(lo_ready, 1)
                for t in range(TOK_TILES):
                    n = tok_rows(t)
                    if t >= 2:
                        pe.wait_ge(taken, t - 1)
                    for k in range(KT):
                        x = slice(t * P, t * P + n)
                        pe.matmul(ps[:n, t % 2, :NAT], h_hi[:, k, x], w_hi[:, k, :], start=k == 0, stop=False)
                        pe.matmul(ps[:n, t % 2, :NAT], h_lo[:, k, x], w_hi[:, k, :], start=False, stop=False)
                        mm = pe.matmul(ps[:n, t % 2, :NAT], h_hi[:, k, x], w_lo[:, k, :], start=False,
                                       stop=k == KT - 1)
                    mm.then_inc(ps_ready, 1)


SSD_HEADS = 8
HEAD_DIM = 64
INNER = SSD_HEADS * HEAD_DIM
XBC = 8
TAPS = 4
XBC_TILE0 = 4
TOKENS = SEQ + SAMPLE


def conv_stage(core, proj, conv_state, conv_w, conv_b, xc, y):
    nc = core.nc
    pad = TAPS - 1
    with ExitStack() as ctx:
        sb = lambda name, shape, dt=F32: ctx.enter_context(nc.sbuf_tensor(f"conv_{name}", shape, dt))
        prompt = sb("prompt", [P, 2, pad + SEQ])
        new = sb("new", [P, XBC, SAMPLE])
        old = sb("old", [P, XBC, DEC_BATCH * pad])
        sample = sb("sample", [P, XBC, DEC_BATCH, pad + DEC_SEQ])
        acc = sb("acc", [P, 2, TOKENS])
        w = sb("w", [P, XBC, TAPS])
        b = sb("b", [P, XBC])
        small_landed, zeroed, sample_ready, tap_done, xc_ready = map(
            core.sem, ("conv_small_landed", "conv_zeroed", "conv_sample_ready", "tap_done", "xc_ready"))
        landed = [core.sem(f"xbc_landed_{s}") for s in range(2)]
        z_landed, y_ready = core.sem("z_landed"), core.sem("z_silu_ready")
        first_done = core.sem("first_tap_done")

        def sums(i):
            return acc[:, i % 2, 0:SEQ], acc[:, i % 2, SEQ:TOKENS].rearrange("p (b t) -> p b t", t=DEC_SEQ)

        with nc.Block() as block:

            @block.sync
            def _(sp):
                sp.dma_start(w[:], conv_w).then_inc(small_landed, 16)
                sp.dma_start(b[:], conv_b).then_inc(small_landed, 16)
                sp.dma_start(old[:], conv_state).then_inc(small_landed, 16)
                sp.dma_start(new[:], proj[XBC_TILE0:XBC_TILE0 + XBC, :, SEQ:TOKENS].rearrange("i p t -> p i t")
                             ).then_inc(small_landed, 16)
                for i in range(XBC):
                    if i >= 2:
                        sp.wait_ge(tap_done, (i - 1) * 2 * (TAPS - 1))
                    sp.dma_start(prompt[:, i % 2, pad:], proj[XBC_TILE0 + i, :, 0:SEQ]).then_inc(landed[i % 2], 16)
                    if i == 1:
                        sp.dma_start(y, proj[0:4].rearrange("i p t -> p i t")).then_inc(z_landed, 16)

            @block.gpsimd
            def _(pool):
                pool.memset(prompt[:, :, 0:pad], 0.0).then_inc(zeroed, 1)
                pool.wait_ge(small_landed, 64)
                rows = sample[:].rearrange("p i b t -> p (i b) t")
                pool.tensor_copy(rows[:, :, 0:pad], old[:].rearrange("p i (b t) -> p (i b) t", t=pad)
                                 ).then_inc(sample_ready, 1)
                pool.tensor_copy(rows[:, :, pad:], new[:].rearrange("p i (b t) -> p (i b) t", t=DEC_SEQ)
                                 ).then_inc(sample_ready, 1)

            @block.vector
            def _(dve):
                for i in range(XBC):
                    dve.wait_ge(first_done, 2 * (i + 1))
                    a, s = sums(i)
                    for j in range(1, TAPS):
                        at_p, at_s = prompt[:, i % 2, j:j + SEQ], sample[:, i, :, j:j + DEC_SEQ]
                        if j > 1:
                            dve.wait_ge(tap_done, (i * (TAPS - 1) + j - 1) * 2)
                        dve.scalar_tensor_tensor(a, at_p, w[:, i, j:j + 1], a, ALU.mult, ALU.add
                                                 ).then_inc(tap_done, 1)
                        dve.scalar_tensor_tensor(s, at_s, w[:, i, j:j + 1], s, ALU.mult, ALU.add
                                                 ).then_inc(tap_done, 1)

            @block.scalar
            def _(act):
                def first_tap(i):
                    act.wait_ge(landed[i % 2], 16 * (i // 2 + 1))
                    if i >= 2:
                        act.wait_ge(xc_ready, 2 * (i - 1))
                    for out, at in zip(sums(i), (prompt[:, i % 2, 0:SEQ], sample[:, i, :, 0:DEC_SEQ])):
                        act.activation(out, at, ACT.Identity, scale=w[:, i, 0:1], bias=b[:, i:i + 1]
                                       ).then_inc(first_done, 1)

                act.wait_ge(zeroed, 1)
                act.wait_ge(small_landed, 64)
                act.wait_ge(sample_ready, 2)
                first_tap(0)
                for i in range(XBC):
                    if i + 1 < XBC:
                        first_tap(i + 1)
                    act.wait_ge(tap_done, (i + 1) * 2 * (TAPS - 1))
                    act.activation(xc[:, i, 0:SEQ], acc[:, i % 2, 0:SEQ], ACT.Silu).then_inc(xc_ready, 1)
                    act.activation(xc[:, i, SEQ:], acc[:, i % 2, SEQ:], ACT.Silu).then_inc(xc_ready, 1)
                act.wait_ge(z_landed, 16)
                act.activation(y, y, ACT.Silu).then_inc(y_ready, 1)


def ssd_stage(core, nat, xc, dt_bias, a_log, d_skip, state_in, y, state_out_p, state_out_s):
    nc = core.nc
    H, HD = SSD_HEADS, HEAD_DIM
    chunks = TOK_TILES
    S = chunks - 1
    with ExitStack() as ctx:
        sb = lambda name, shape, dt=F32: ctx.enter_context(nc.sbuf_tensor(f"ssd_{name}", shape, dt))
        ps = lambda name, n: ctx.enter_context(nc.psum_tensor(f"ssd_{name}_ps", [P, n], F32))
        dtb, alog, dskip = sb("dt_bias", [P, H]), sb("a_log", [P, H]), sb("d_skip", [P, 4])
        xdt, nabs, u, w1p, ln, dt, dta = (sb(n, [P, chunks, H]) for n in
                                          ("xdt", "neg_abs", "exp_neg", "one_plus", "ln", "dt", "dt_a"))
        ea = sb("exp_a", [P, H])
        state = sb("state", [P, INNER])
        s_state = sb("sample_state", [P, DEC_BATCH, INNER])
        xns, bns = sb("x_nat", [P, 2, INNER]), sb("b_nat", [P, 2, 256])
        acss = sb("acs", [P, 2, 2 * H])
        tes, te_dts = sb("to_end", [P, 2, H]), sb("to_end_dt", [P, 2, H])
        segs = sb("seg", [P, 2, H, P])
        grows = sb("exp_acs", [P, 2, H, P])
        css = sb("c_scaled", [P, 2, H, P])
        cbms = sb("cb_masked", [P, 2, 2, P])
        xss = sb("x_scaled", [P, 2, INNER])
        xsb = [a[:SAMPLE, S % 2, :, SAMPLE:] for a in (segs, css)]
        yt = sb("y_skip", [P, 4, P])
        tp_x, tp_b, small, bc = ps("tp_x", 512), ps("tp_b", 512), ps("small", 512), ps("bc", 1024)
        yp = ps("y", 512)
        st = ctx.enter_context(nc.psum_tensor("ssd_st", [P, 2, 512], F32))
        in_landed, chain, sp_act, dt_ready = map(
            core.sem, ("ssd_in_landed", "softplus_dve", "softplus_act", "dt_ready"))
        prep_ready, acs_ready, te_arg_ready, te_ready, seg_ready, cbm_ready, decay_ready = map(
            core.sem, ("prep_ready", "acs_ready", "te_arg_ready", "te_ready", "seg_ready", "cbm_ready",
                       "decay_ready"))
        xn_ready, bn_ready, grow_ready, cs_ready, w_ready, te_dt_ready, xs_ready, xsb_ready = map(
            core.sem, ("xn_ready", "bn_ready", "grow_ready", "cs_ready", "w_ready", "te_dt_ready", "xs_ready",
                       "xsb_ready"))
        y_ready, st_ready, skip_done, y_done, decayed, state_ready, s_decayed, s_state_ready, stored = map(
            core.sem, ("y_ready", "st_ready", "skip_done", "y_done", "state_decayed", "state_ready",
                       "sample_decayed", "sample_state_ready", "states_stored"))

        def rows(c):
            return SAMPLE if c == S else P

        def cols(c):
            return slice(c * P, c * P + rows(c))

        with nc.Block() as block:

            @block.sync
            def _(sp):
                for dst, src in ((dtb, dt_bias), (alog, a_log), (dskip, d_skip), (s_state, state_in)):
                    sp.dma_start(dst[:], src).then_inc(in_landed, 16)
                sp.wait_ge(state_ready, S)
                sp.dma_start(state_out_p, state[:]).then_inc(stored, 16)
                sp.wait_ge(s_state_ready, DEC_BATCH)
                sp.dma_start(state_out_s, s_state[:]).then_inc(stored, 16)
                sp.wait_ge(stored, 32)

            @block.tensor
            def _(pe):
                def prepare(c):
                    T = rows(c)
                    tri = core.tri_seq if c == S else core.tri
                    whole = core.same_seq if c == S else core.ones
                    if c:
                        for sem in (xn_ready, bn_ready, cbm_ready, acs_ready, grow_ready):
                            pe.wait_ge(sem, c)
                        pe.wait_ge(seg_ready, c * H)
                    for i in range(4):
                        pe.transpose(tp_x[:T, i * P:(i + 1) * P], xc[:, i, cols(c)], core.ident[:])
                    for g in range(2):
                        pe.transpose(tp_b[:T, g * P:(g + 1) * P], xc[:, 4 + g, cols(c)], core.ident[:])
                    for g in range(2):
                        pe.matmul(small[:T, (1 + g) * P:(1 + g) * P + T], xc[:, 4 + g, cols(c)],
                                  xc[:, 6 + g, cols(c)], start=True, stop=True)
                    pe.matmul(small[:T, 0:H], tri[:T, :T], dta[:T, c, :], start=True, stop=True)
                    pe.matmul(small[:T, H:2 * H], whole[:T, :T], dta[:T, c, :], start=True, stop=True)
                    for h in range(H):
                        mm = pe.matmul(bc[:, h * P:h * P + T], dta[:T, c, h:h + 1].to_broadcast([T, P]),
                                       tri[:T, :T], start=True, stop=True)
                    mm.then_inc(prep_ready, 1)

                pe.wait_ge(dt_ready, 1)
                prepare(0)
                for c in range(chunks):
                    T = rows(c)
                    xn, bn, seg, cs, xs = (a[:, c % 2] for a in (xns, bns, segs, css, xss))
                    if c < S:
                        prepare(c + 1)
                    pe.wait_ge(xn_ready, c + 1)
                    pe.wait_ge(w_ready, (c + 1) * H)
                    if c:
                        pe.wait_ge(skip_done, 4 * c)
                        pe.wait_ge(state_ready, min(c, S))
                        pe.wait_ge(cs_ready, 2 * (c + 1))
                    if c == S:
                        pe.wait_ge(in_landed, 64)
                    for h in range(H):
                        q = HD * (h % 2)
                        hs = slice(h * HD, (h + 1) * HD)
                        at = (h // 2) * P
                        mm = pe.matmul(yp[q:q + HD, at:at + T], xn[:T, hs], seg[:T, h, :T], start=True, stop=c in (0, S))
                        if c == S:
                            for b in range(DEC_BATCH):
                                t = slice(b * DEC_SEQ, (b + 1) * DEC_SEQ)
                                mm = pe.matmul(yp[q:q + HD, at + b * DEC_SEQ:at + (b + 1) * DEC_SEQ],
                                               s_state[:, b, hs], cs[:, h, t], start=False, stop=True,
                                               skip_group_check=True)
                        elif c:
                            mm = pe.matmul(yp[q:q + HD, at:at + T], state[:, hs], cs[:, h, :T],
                                           start=False, stop=True)
                    mm.then_inc(y_ready, 1)
                    pe.wait_ge(bn_ready, c + 1)
                    if c < S:
                        pe.wait_ge(xs_ready, c + 1)
                        for g in range(2):
                            mm = pe.matmul(st[:, 0, g * 256:(g + 1) * 256], bn[:T, g * P:(g + 1) * P],
                                           xs[:T, g * 256:(g + 1) * 256], start=True, stop=True)
                        mm.then_inc(st_ready, 1)
                    else:
                        for b in range(DEC_BATCH):
                            pe.wait_ge(xsb_ready, b + 1)
                            if b >= 2:
                                pe.wait_ge(s_state_ready, b - 1)
                            for g in range(2):
                                mm = pe.matmul(st[:, b % 2, g * 256:(g + 1) * 256], bn[:T, g * P:(g + 1) * P],
                                               xsb[b % 2][:, 4 * g:4 * g + 4, :], start=True, stop=True)
                            mm.then_inc(st_ready, 1)

            @block.scalar
            def _(act):
                act.wait_ge(in_landed, 64)
                act.activation(ea[:], alog[:], ACT.Exp).then_inc(sp_act, 1)
                act.wait_ge(chain, 3)
                act.activation(u[:], nabs[:], ACT.Exp).then_inc(sp_act, 1)
                act.wait_ge(chain, 4)
                act.activation(ln[:], w1p[:], ACT.Ln).then_inc(sp_act, 1)
                for c in range(chunks):
                    T = rows(c)
                    xn, bn, grow, te, seg = (a[:, c % 2] for a in (xns, bns, grows, tes, segs))
                    act.wait_ge(prep_ready, c + 1)
                    if c >= 2:
                        act.wait_ge(st_ready, c - 1)
                    act.activation(xn[:T, :], tp_x[:T, :], ACT.Copy).then_inc(xn_ready, 1)
                    act.activation(bn[:T, :], tp_b[:T, 0:256], ACT.Copy).then_inc(bn_ready, 1)
                    if c >= 2:
                        act.wait_ge(cs_ready, 2 * (c - 1))
                        act.wait_ge(state_ready, c - 1)
                    act.activation(grow[:, :, :T], bc[:].rearrange("p (h t) -> p h t", t=P)[:, :, :T],
                                   ACT.Exp).then_inc(grow_ready, 1)
                    act.wait_ge(te_arg_ready, c + 1)
                    act.activation(te[:T, :], te[:T, :], ACT.Exp).then_inc(te_ready, 1)
                    act.wait_ge(seg_ready, (c + 1) * H)
                    act.activation(seg[:T, :, :T], seg[:T, :, :T], ACT.Exp).then_inc(decay_ready, 1)

            @block.gpsimd
            def _(pool):
                for c in range(chunks):
                    T = rows(c)
                    grow, cs = grows[:, c % 2], css[:, c % 2]
                    pool.wait_ge(grow_ready, c + 1)
                    if c >= 2:
                        pool.wait_ge(y_ready, c - 1)
                    for g in range(2):
                        pool.tensor_tensor(cs[:, 4 * g:4 * g + 4, :T], grow[:, 4 * g:4 * g + 4, :T],
                                           xc[:, 6 + g:7 + g, cols(c)].to_broadcast([P, 4, T]),
                                           ALU.mult).then_inc(cs_ready, 1)

            @block.vector
            def _(dve):
                done = 0

                def step(ins):
                    nonlocal done
                    done += 1
                    ins.then_inc(chain, 1)
                    dve.wait_ge(chain, done)

                dve.wait_ge(in_landed, 64)
                lanes = lambda a: a[:].rearrange("p (o h) -> p o h", o=1).to_broadcast([P, chunks, H])
                step(dve.tensor_tensor(xdt[:], nat[:, :, 256:256 + H], lanes(dtb), ALU.add))
                step(dve.tensor_scalar(nabs[:], xdt[:], -1.0, None, ALU.mult))
                step(dve.tensor_tensor(nabs[:], nabs[:], xdt[:], ALU.min))
                dve.wait_ge(sp_act, 2)
                step(dve.tensor_scalar(w1p[:], u[:], 1.0, None, ALU.add))
                step(dve.tensor_scalar(dt[:], w1p[:], -1.0, None, ALU.add))
                step(dve.tensor_tensor(dt[:], u[:], dt[:], ALU.subtract))
                dve.wait_ge(sp_act, 3)
                step(dve.reciprocal(w1p[:], w1p[:]))
                step(dve.tensor_tensor(dt[:], dt[:], w1p[:], ALU.mult))
                step(dve.tensor_tensor(dt[:], dt[:], ln[:], ALU.add))
                step(dve.scalar_tensor_tensor(dt[:], xdt[:], 0.0, dt[:], ALU.max, ALU.add))
                dve.scalar_tensor_tensor(dta[:], dt[:], -1.0, lanes(ea), ALU.mult, ALU.mult
                                         ).then_inc(dt_ready, 1)
                def front(c):
                    T = rows(c)
                    acs, te, te_dt, seg, cbm, xs, xn = (a[:, c % 2] for a in (acss, tes, te_dts, segs, cbms, xss, xns))
                    tri = core.tri_seq if c == S else core.tri
                    dve.wait_ge(prep_ready, c + 1)
                    dve.tensor_copy(acs[:T, :], small[:T, 0:2 * H]).then_inc(acs_ready, 1)
                    for g in range(2):
                        ins = dve.tensor_tensor(cbm[:T, g, :T], small[:T, (1 + g) * P:(1 + g) * P + T],
                                                tri[:T, :T], ALU.mult)
                    ins.then_inc(cbm_ready, 1)
                    dve.wait_ge(acs_ready, c + 1)
                    if c:
                        dve.wait_ge(te_dt_ready, c)
                    dve.tensor_tensor(te[:T, :], acs[:T, H:], acs[:T, :H], ALU.subtract).then_inc(te_arg_ready, 1)
                    dve.wait_ge(grow_ready, c + 1)
                    for h in range(H):
                        dve.tensor_scalar(seg[:T, h, :T], bc[:T, h * P:h * P + T], acs[:T, h:h + 1], 0.0,
                                          ALU.subtract, ALU.min).then_inc(seg_ready, 1)
                    dve.wait_ge(te_ready, c + 1)
                    dve.tensor_tensor(te_dt[:T, :], te[:T, :], dt[:T, c, :], ALU.mult).then_inc(te_dt_ready, 1)
                    dve.wait_ge(te_dt_ready, c + 1)
                    dve.wait_ge(xn_ready, c + 1)
                    dve.tensor_tensor(xs[:T, :].rearrange("p (h d) -> p h d", h=H),
                                      xn[:T, :].rearrange("p (h d) -> p h d", h=H),
                                      te_dt[:T, :].rearrange("p (h o) -> p h o", o=1).to_broadcast([T, H, HD]),
                                      ALU.mult).then_inc(xs_ready, 1)

                def weights(c):
                    T = rows(c)
                    seg, cbm = segs[:, c % 2], cbms[:, c % 2]
                    dve.wait_ge(decay_ready, c + 1)
                    dve.wait_ge(cbm_ready, c + 1)
                    for h in range(H):
                        dve.scalar_tensor_tensor(seg[:T, h, :T], seg[:T, h, :T], dt[:T, c, h:h + 1],
                                                 cbm[:T, h // 4, :T], ALU.mult, ALU.mult).then_inc(w_ready, 1)

                front(0)
                for c in range(chunks):
                    T = rows(c)
                    grow, xs = grows[:, c % 2], xss[:, c % 2]
                    weights(c)
                    if c < S:
                        front(c + 1)
                    dve.wait_ge(y_ready, c + 1)
                    if c:
                        dve.wait_ge(y_done, c)
                    for i in range(4):
                        dve.scalar_tensor_tensor(yt[:, i, :T], xc[:, i, cols(c)], dskip[:, i:i + 1],
                                                 yp[:, i * P:i * P + T], ALU.mult, ALU.add).then_inc(skip_done, 1)
                    dve.wait_ge(skip_done, 4 * (c + 1))
                    dve.tensor_tensor(y[:, :, cols(c)], yt[:, :, :T], y[:, :, cols(c)], ALU.mult).then_inc(y_done, 1)
                    if c < S:
                        flat = state[:]
                        if c == 0:
                            dve.wait_ge(st_ready, 1)
                            dve.tensor_copy(flat, st[:, 0, :]).then_inc(state_ready, 1)
                        else:
                            dve.wait_ge(grow_ready, c + 1)
                            h3 = flat.rearrange("p (h d) -> p h d", h=H)
                            dve.tensor_tensor(h3, h3, grow[:, :, P - 1:P].to_broadcast([P, H, HD]), ALU.mult
                                              ).then_inc(decayed, 1)
                            dve.wait_ge(decayed, c)
                            dve.wait_ge(st_ready, c + 1)
                            dve.tensor_tensor(flat, flat, st[:, 0, :], ALU.add).then_inc(state_ready, 1)
                    else:
                        dve.wait_ge(xs_ready, S + 1)
                        for b in range(DEC_BATCH):
                            if b >= 2:
                                dve.wait_ge(st_ready, S + b - 1)
                            dve.tensor_scalar(xsb[b % 2], xs[:SAMPLE, :].rearrange("p (h d) -> p h d", h=H), core.seq_mask[:SAMPLE, b:b + 1],
                                              None, ALU.mult).then_inc(xsb_ready, 1)
                            h3 = s_state[:, b, :].rearrange("p (h d) -> p h d", h=H)
                            end = b * DEC_SEQ + DEC_SEQ - 1
                            dve.tensor_tensor(h3, h3, grow[:, :, end:end + 1].to_broadcast([P, H, HD]),
                                              ALU.mult).then_inc(s_decayed, 1)
                            dve.wait_ge(s_decayed, b + 1)
                            dve.wait_ge(st_ready, S + b + 1)
                            dve.tensor_tensor(s_state[:, b, :], s_state[:, b, :], st[:, b % 2, :], ALU.add
                                              ).then_inc(s_state_ready, 1)


CONSTS = 5 * P + DEC_BATCH + 1


def make_consts():
    c = np.zeros((P, CONSTS), np.float32)
    i = np.arange(P)
    same = (i[:, None] // DEC_SEQ == i[None, :] // DEC_SEQ) & (i[:, None] < SAMPLE) & (i[None, :] < SAMPLE)
    tri = i[:, None] <= i[None, :]
    c[:, 0:P] = np.eye(P)
    c[:, P:2 * P] = tri
    c[:, 2 * P:3 * P] = tri & same
    c[:, 3 * P:4 * P] = same
    c[:, 4 * P:5 * P] = 1.0
    c[:, 5 * P:-1] = (i[:, None] // DEC_SEQ == np.arange(DEC_BATCH)[None, :]) & (i[:, None] < SAMPLE)
    c[:, -1] = i >= CMP_BLOCK - 1
    return c


def consts_stage(core, consts):
    nc = core.nc
    sb = lambda name, shape, dt=F32: core.ctx.enter_context(nc.sbuf_tensor(f"const_{name}", shape, dt))
    all_consts = sb("all", [P, CONSTS])
    core.ident, core.tri, core.tri_seq, core.same_seq, core.ones = (
        all_consts[:, i * P:(i + 1) * P] for i in range(5))
    core.seq_mask = all_consts[:, 5 * P:5 * P + DEC_BATCH]
    core.sees_cmp = all_consts[:, CONSTS - 1:]
    core.mean_model, core.mean_inner = sb("mean_model", [P, P]), sb("mean_inner", [P, P])
    core.eps = sb("eps", [P, 1])
    landed = core.sem("consts_landed")
    filled = core.sem("consts_filled")
    with nc.Block() as block:

        @block.sync
        def _(sp):
            sp.dma_start(all_consts[:], consts).then_inc(landed, 16)
            sp.wait_ge(landed, 16)

        @block.vector
        def _(dve):
            dve.memset(core.mean_model[:], 1.0 / D_MODEL).then_inc(filled, 1)
            dve.memset(core.mean_inner[:], 1.0 / INNER).then_inc(filled, 1)
            dve.memset(core.eps[:], EPS).then_inc(filled, 1)


def lay_conv_state(a):
    return np.ascontiguousarray(a[0].transpose(2, 0, 1).reshape(XBC, P, -1).transpose(1, 0, 2))


def lay_conv_w(a):
    return np.ascontiguousarray(a[0].T.reshape(XBC, P, TAPS).transpose(1, 0, 2))


def lay_d_skip(a):
    return np.ascontiguousarray(np.repeat(a[0], HEAD_DIM).reshape(4, P).T)


def lay_state(a):
    return np.ascontiguousarray(a[0].transpose(3, 0, 1, 2).reshape(P, DEC_BATCH, INNER))


CMP_BLOCK, CMP_STRIDE, CMP_HIDDEN = 32, 16, 256
N_CHUNK = SEQ // CMP_STRIDE
N_CMP = N_CHUNK - 1
SEQS = DEC_BATCH + 1
PAIR_STEPS = CMP_STRIDE // 2
PAGES = 8
KV_TILE0 = 16


def compress_stage(core, proj, pages_dram, page_table, w1, w2, pos, kc, vc, scratch, n_pool):
    nc = core.nc
    parts = ((0, 2), (2, 4), (4, SEQS))
    units = [(part, kv, g, hh) for part in range(len(parts)) for kv in range(2) for g in range(2) for hh in range(2)]
    with ExitStack() as ctx:
        sb = lambda name, shape, dt=F32: ctx.enter_context(nc.sbuf_tensor(f"cmp_{name}", shape, dt))
        ps = lambda name, n: ctx.enter_context(nc.psum_tensor(f"cmp_{name}_ps", [P, n, 512], F32))
        table = sb("page_table", [1, DEC_BATCH * PAGES], I32)
        pages = sb("pages", [P, SEQS * PAGES, 2, PAIR_STEPS, 2, PAGES])
        w1s = sb("w1", [P, 2, 2 * PAIR_STEPS, CMP_HIDDEN])
        w2s, ps_ = sb("w2", [P, 2, 2, HEAD_DIM]), sb("pos", [P, 2, 2 * PAIR_STEPS])
        bias = sb("bias", [P, 4])
        zeros = sb("zeros", [1, 1 + (SEQS - 4) * N_CHUNK], BF16)
        hid_cols = 2 * 2 * SEQS * N_CHUNK
        rows_t = scratch[:, 0:2 * SEQ].rearrange("p (v t) -> p v t", v=2)
        hid = [a.rearrange("p (h g c) -> p h g c", h=2, g=2) for a in (
            scratch[:, 2 * SEQ:2 * SEQ + hid_cols], sb("hid", [P, hid_cols])[:])]
        hp, bp, op = ps("hid", 4), ps("bias", 1), ps("out", 3)
        table_landed, rows_landed, shuffled, own_ready = map(
            core.sem, ("table_landed", "rows_landed", "shuffled", "prompt_pairs_ready"))
        w_landed = [core.sem(f"cw_landed_{kv}") for kv in range(2)]
        pages_landed = [core.sem(f"pages_landed_{part}") for part in range(len(parts))]
        bias_ps, bias_ready, hid_ps, hid_ready, out_ps, out_ready = map(
            core.sem, ("bias_ps", "bias_ready", "hid_ps", "hid_ready", "out_ps", "out_ready"))
        zeroed = core.sem("cmp_zeros_ready")
        turn_bank = lambda kv, g: hp[:, 2 + g, :] if kv else op[:, g, :]
        done_of = [max(j for j, u in enumerate(units) if u[1] == kv) + 1 for kv in range(2)]
        first_of = [min(j for j, u in enumerate(units) if u[1] == kv) for kv in range(2)]
        vc_banks = -(-SEQS // 4)

        with nc.Block() as block:

            @block.sync
            def _(sp):
                sp.dma_start(table[:], page_table).then_inc(table_landed, 16)
                for kv in range(2):
                    sp.dma_start(rows_t[:, kv, :], proj[KV_TILE0 + kv, :, 0:SEQ]).then_inc(rows_landed, 16)
                sp.wait_ge(table_landed, 16)
                for part, (b0, b1) in enumerate(parts):
                    with sp.Fori(b0, min(b1, DEC_BATCH)) as b:
                        for j in range(PAGES):
                            at = b * PAGES + j
                            page = sp.value_load(table[0:1, bass.ds(at, 1)], min_val=0, max_val=n_pool - 1)
                            sp.dma_start(pages[:, bass.ds(at, 1)].rearrange("p o v r g n -> p (o v r g n)"),
                                         pages_dram[bass.ds(page, 1)].rearrange("o p c -> (o p) c")
                                         ).then_inc(pages_landed[part], 16)

            @block.scalar
            def _(act):
                def load_weights(kv):
                    for dst, src in ((w1s, w1), (w2s, w2), (ps_, pos)):
                        act.dma_start(dst[:, kv], src[kv]).then_inc(w_landed[kv], 16)

                load_weights(0)
                for kv in range(2):
                    for g in range(2):
                        act.wait_ge(shuffled, 2 * kv + g + 1)
                        act.activation(pages[:, DEC_BATCH * PAGES:, kv, :, g, :].rearrange("p j r n -> p j n r"),
                                       turn_bank(kv, g).rearrange("p (j n r) -> p j n r", j=PAGES, r=PAIR_STEPS),
                                       ACT.Copy).then_inc(own_ready, 1)
                load_weights(1)
                for j, (part, kv, g, hh) in enumerate(units):
                    b0, b1 = parts[part]
                    if j == first_of[kv]:
                        act.wait_ge(bias_ps, kv + 1)
                        act.activation(bias[:, 2 * kv:2 * kv + 2], bp[:, 0, 2 * kv:2 * kv + 2], ACT.Copy
                                       ).then_inc(bias_ready, 1)
                        act.wait_ge(bias_ready, kv + 1)
                    act.wait_ge(hid_ps, j + 1)
                    if j == 0:
                        act.wait_ge(own_ready, 4)
                    act.activation(hid[kv][:, hh, g, b0 * N_CHUNK:b1 * N_CHUNK],
                                   hp[:, j % 4, 1:1 + (b1 - b0) * N_CHUNK], ACT.Silu,
                                   bias=bias[:, 2 * kv + hh:2 * kv + hh + 1]).then_inc(hid_ready, 1)

            @block.tensor
            def _(pe):
                pe.wait_ge(rows_landed, 32)
                for kv in range(2):
                    for g in range(2):
                        gs = slice(g * HEAD_DIM, (g + 1) * HEAD_DIM)
                        for odd in range(2):
                            mm = pe.matmul(turn_bank(kv, g)[odd * HEAD_DIM:(odd + 1) * HEAD_DIM, :],
                                           core.ident[gs, gs], rows_t[gs, kv, odd::2], start=True, stop=True)
                        mm.then_inc(shuffled, 1)

                def position_bias(kv):
                    pe.wait_ge(w_landed[kv], 48)
                    for half in range(2):
                        for k in range(2 * PAIR_STEPS):
                            mm = pe.matmul(bp[:, 0, 2 * kv + half:2 * kv + half + 1],
                                           w1s[:, kv, k, half * P:(half + 1) * P], ps_[:, kv, k:k + 1],
                                           start=k == 0, stop=k == 2 * PAIR_STEPS - 1)
                    mm.then_inc(bias_ps, 1)

                pe.wait_ge(own_ready, 4)
                pe.wait_ge(zeroed, 1)
                for j, (part, kv, g, hh) in enumerate(units):
                    b0, b1 = parts[part]
                    if j >= 4:
                        pe.wait_ge(hid_ready, j - 3)
                    if j == first_of[kv]:
                        position_bias(kv)
                    if (kv, g, hh) == (0, 0, 0):
                        pe.wait_ge(pages_landed[part], (min(b1, DEC_BATCH) - b0) * PAGES * 16)
                    pe.matmul(hp[:, j % 4, 0:1 + (b1 - b0) * N_CHUNK], zeros[:, 0:P],
                              zeros[:, 0:1 + (b1 - b0) * N_CHUNK], start=True, stop=False)
                    for k in range(2 * PAIR_STEPS):
                        later, r = divmod(k, PAIR_STEPS)
                        at = hp[:, j % 4, 1 - later:1 - later + (b1 - b0) * N_CHUNK]
                        mm = pe.matmul(at.rearrange("p (b n) -> p b n", n=PAGES),
                                       w1s[:, kv, k, hh * P:(hh + 1) * P],
                                       pages[:, b0 * PAGES:b1 * PAGES, kv, r, g, :],
                                       start=False, stop=k == 2 * PAIR_STEPS - 1)
                    mm.then_inc(hid_ps, 1)
                pe.wait_ge(hid_ready, done_of[0])
                for n, c in ((0, slice(0, DEC_BATCH * N_CHUNK)), (1, slice(DEC_BATCH * N_CHUNK, SEQS * N_CHUNK))):
                    for g in range(2):
                        for hh in range(2):
                            mm = pe.matmul(op[g * HEAD_DIM:(g + 1) * HEAD_DIM, n, 0:c.stop - c.start],
                                           w2s[:, 0, hh, :], hid[0][:, hh, g, c], start=hh == 0, stop=hh == 1)
                mm.then_inc(out_ps, 1)
                pe.wait_ge(hid_ready, done_of[1])
                pe.wait_ge(out_ready, 2)
                for b in range(SEQS):
                    for g in range(2):
                        at = ((b % 4) * 2 + g) * HEAD_DIM
                        for hh in range(2):
                            mm = pe.matmul(op[:N_CMP, b // 4, at:at + HEAD_DIM],
                                           hid[1][:, hh, g, b * N_CHUNK:b * N_CHUNK + N_CMP], w2s[:, 1, hh, :],
                                           start=hh == 0, stop=hh == 1)
                    if b % 4 == 3 or b == SEQS - 1:
                        mm.then_inc(out_ps, 1)

            @block.vector
            def _(dve):
                dve.memset(zeros[:], 0.0).then_inc(zeroed, 1)
                dve.wait_ge(out_ps, 1)
                for n, (b0, b1) in enumerate(((0, DEC_BATCH), (DEC_BATCH, SEQS))):
                    dve.tensor_copy(kc[:, b0 * N_CMP:b1 * N_CMP].rearrange("p (b n) -> p b n", n=N_CMP),
                                    op[:, n, 0:(b1 - b0) * N_CHUNK].rearrange("p (b n) -> p b n", n=N_CHUNK)
                                    [:, :, 0:N_CMP]).then_inc(out_ready, 1)
                for n in range(vc_banks):
                    cols = min(4, SEQS - 4 * n) * 2 * HEAD_DIM
                    dve.wait_ge(out_ps, n + 2)
                    dve.tensor_copy(vc[:N_CMP, n * 512:n * 512 + cols], op[:N_CMP, n, 0:cols]
                                    ).then_inc(out_ready, 1)


def lay_cmp_pages(a):
    n = a.shape[1]
    return np.ascontiguousarray(a[0].reshape(n, PAGES, PAIR_STEPS, 2, 2, 2, HEAD_DIM)
                                .transpose(0, 3, 6, 4, 2, 5, 1)).reshape(n, P, 4 * PAIR_STEPS * PAGES)


def lay_cmp_w1(a):
    return np.ascontiguousarray(a[0].reshape(2, PAIR_STEPS, 2, HEAD_DIM, CMP_HIDDEN).transpose(2, 3, 0, 1, 4)
                                ).reshape(P, 2 * PAIR_STEPS, CMP_HIDDEN)


def lay_cmp_w2(a):
    return np.ascontiguousarray(a[0].reshape(2, P, HEAD_DIM).transpose(1, 0, 2))


def lay_cmp_pos(a):
    return np.ascontiguousarray(a[0].reshape(2 * PAIR_STEPS, 2, HEAD_DIM).transpose(1, 2, 0)).reshape(P, -1)


NSA_HEADS, KV_GROUPS, GROUP_HEADS = 8, 2, 4
WINDOW = 512
BUCKETS, MAX_DIST = 32, 128
ROW_LEN = 400
ZERO_DIST = 255
SKEW, COPIES = ROW_LEN - 1, P * ROW_LEN
CMP_NEAR = 17
SCALE = HEAD_DIM ** -0.5


def make_bucket_rows():
    dist = ZERO_DIST - np.arange(ROW_LEN)
    n = np.maximum(dist, 0)
    exact = BUCKETS // 2
    large = exact + (np.log(np.maximum(n, exact).astype(np.float32) / exact) / np.log(MAX_DIST / exact)
                     * (BUCKETS - exact)).astype(np.int32)
    bucket = np.where(n < exact, n, np.minimum(large, BUCKETS - 1))
    rows = (bucket[None, :] == np.arange(BUCKETS)[:, None]).astype(np.float32)
    rows[BUCKETS - 1] -= 1.0
    return rows


def bias_rows_stage(core, rel_bias, bucket_rows, rows_dram):
    nc = core.nc
    with ExitStack() as ctx:
        sb = lambda name, shape: ctx.enter_context(nc.sbuf_tensor(f"rows_{name}", shape, F32))
        rel, hot = sb("rel", [BUCKETS, NSA_HEADS]), sb("hot", [BUCKETS, ROW_LEN])
        bias, win = sb("bias", [NSA_HEADS, ROW_LEN]), sb("win", [1, ROW_LEN])
        ps = ctx.enter_context(nc.psum_tensor("rows_ps", [P, 512], F32))
        landed, product, filled, stored = map(core.sem, ("rel_landed", "rows_product", "rows_filled", "rows_stored"))
        with nc.Block() as block:

            @block.sync
            def _(sp):
                sp.dma_start(rel[:], rel_bias).then_inc(landed, 16)
                sp.dma_start(hot[:], bucket_rows).then_inc(landed, 16)
                sp.wait_ge(filled, 4)
                for dst, src in ((rows_dram[0:NSA_HEADS], bias), (rows_dram[NSA_HEADS:NSA_HEADS + 1], win)):
                    n = src.shape[0]
                    sp.dma_start(dst, src[:].rearrange("h (o u) -> h o u", o=1).to_broadcast([n, P, ROW_LEN])
                                 ).then_inc(stored, 16)
                sp.wait_ge(stored, 32)

            @block.tensor
            def _(pe):
                pe.wait_ge(landed, 32)
                pe.matmul(ps[:NSA_HEADS, 0:ROW_LEN], rel[:], hot[:], start=True, stop=True).then_inc(product, 1)

            @block.vector
            def _(dve):
                dve.memset(win[:, 0:P], NEG).then_inc(filled, 1)
                dve.memset(win[:, P:], 0.0).then_inc(filled, 1)
                dve.memset(bias[:, ZERO_DIST + 1:], NEG).then_inc(filled, 1)
                dve.wait_ge(product, 1)
                dve.tensor_copy(bias[:, 0:ZERO_DIST + 1], ps[:NSA_HEADS, 0:ZERO_DIST + 1]).then_inc(filled, 1)


def from_rows(rows_dram, offset, dims):
    return bass.AP(rows_dram.tensor, offset, dims)


def prompt_nsa_stage(core, nat, kc, vc, proj, rows_dram, o_t):
    nc = core.nc
    H = NSA_HEADS
    tiles = SEQ // P
    with ExitStack() as ctx:
        sb = lambda name, shape, dt=F32: ctx.enter_context(nc.sbuf_tensor(f"pn_{name}", shape, dt))
        ps = lambda name, n: ctx.enter_context(nc.psum_tensor(f"pn_{name}_ps", [P, n, 512], F32))
        q_raw, q = sb("q_raw", [P, 2, H, P]), sb("q", [P, 2, H, P], F32R)
        raw = sb("raw", [P, 3, KV_GROUPS * SEQ])
        k_hi, k_lo = (sb(f"k_{part}", [P, 2, KV_GROUPS * SEQ], F32R) for part in ("hi", "lo"))
        near_hi, near_lo = (sb(f"near_bias_{part}", [P, H, 2 * P], F32R) for part in ("hi", "lo"))
        win, eye = sb("window_mask", [P, P], F32R), sb("eye", [P, P], F32R)
        cmp_width = N_CHUNK + 8 * (tiles - 1)
        cmpb_hi, cmpb_lo = (sb(f"cmp_bias_{part}", [P, H, cmp_width], F32R) for part in ("hi", "lo"))
        kc_hi, kc_lo = (sb(f"kc_{part}", [P, KV_GROUPS, N_CHUNK], F32R) for part in ("hi", "lo"))
        near0 = 8 * (tiles - 1) - 9
        gates = sb("gates", [P, tiles, H, 3])
        prob = sb("prob", [P, 2, 1024])
        probt = sb("prob_t", [P, 2, 1024])
        neg_max = sb("neg_max", [P, 2, 2])
        sums, rec, mix = sb("sums", [P, 2, 3]), sb("rec", [P, 2, 3]), sb("mix", [P, 2, 3])
        o = sb("o", [P, 2, INNER])
        half_heads, stage_len = H // 2, CMP_STRIDE * (CMP_NEAR - 1) + 1
        flat_prob, flat_probt, flat_o = (a[:].rearrange("p s c -> p (s c)") for a in (prob, probt, o))
        staged = [a[:, 0:half_heads * stage_len].rearrange("p (h c) -> p h c", c=stage_len)
                  for a in (flat_prob, flat_probt)]
        after = half_heads * stage_len
        kc_raw = flat_prob[:, after:after + KV_GROUPS * N_CHUNK].rearrange("p (g n) -> p g n", n=N_CHUNK)
        win_raw = flat_probt[:, after:after + P]
        cmpb = flat_o[:, 0:H * cmp_width].rearrange("p (h c) -> p h c", c=cmp_width)
        s_ps, t_ps, o_ps = ps("s", 4), ps("t", 2), ps("o", 2)
        gates_ready, filled, near_landed, win_landed, cmpb_landed, kc_landed = map(
            core.sem, ("gates_ready", "pn_filled", "near_landed", "window_landed", "cmp_bias_landed",
                       "kc_landed"))
        k_landed = [core.sem(f"k_landed_{n}") for n in range(2)]
        q_landed = [core.sem(f"q_landed_{n}") for n in range(2)]
        hi_done, split_done, q_hi, q_ready = map(core.sem, ("pn_hi_done", "pn_split_done", "q_hi", "q_ready"))
        s_ready, max_ready, p_ready, t_ready, pt_act, pt_dve = map(
            core.sem, ("s_ready", "max_ready", "p_ready", "t_ready", "pt_act", "pt_dve"))
        pv_ready, rec_ready, mix_ready, part_ready, o_ready, ot_ps, ot_ready = map(
            core.sem, ("pv_ready", "rec_ready", "mix_ready", "o_part_ready", "o_ready", "o_t_ps", "o_t_ready"))

        units = [(i, g, r, b) for i in range(tiles) for r in range(GROUP_HEADS) for g in range(KV_GROUPS)
                 for b in range(2)]
        U = len(units)

        def key_tiles(u):
            i, _, _, b = units[u]
            return range(max(0, i - WINDOW // P) if b else 0, i + 1)

        to_split = [
            (raw[:, 0, :], k_hi[:, 0, :], k_lo[:, 0, :], k_landed[0], 64),
            (raw[:, 2, :], near_hi[:].rearrange("p h c -> p (h c)"), near_lo[:].rearrange("p h c -> p (h c)"),
             near_landed, 16),
            (raw[:, 1, :], k_hi[:, 1, :], k_lo[:, 1, :], k_landed[1], 64),
            (kc_raw, kc_hi[:], kc_lo[:], kc_landed, 64),
            (cmpb, cmpb_hi[:], cmpb_lo[:], filled, 5),
            (win_raw, win[:], None, win_landed, 16),
            (core.ident, eye[:], None, None, 0)]
        splits = sum(lo is not None for _, _, lo, _, _ in to_split)
        per_tile = 2 * H
        turn_at = 3
        pack_at = 6

        def load_q(sp, i):
            if i >= 2:
                sp.wait_ge(q_ready, i - 1)
            for part in (0, 1):
                for g in range(KV_GROUPS):
                    sp.dma_start(q_raw[part * HEAD_DIM:(part + 1) * HEAD_DIM, i % 2,
                                       g * GROUP_HEADS:(g + 1) * GROUP_HEADS, :],
                                 proj[12:16, g * HEAD_DIM:(g + 1) * HEAD_DIM, i * P:(i + 1) * P]
                                 .rearrange("r d t -> d r t")).then_inc(q_landed[i % 2], 16)

        act_copies, dve_copies = [0], [0]
        for u in range(U):
            n, b = len(key_tiles(u)), units[u][3]
            act_copies.append(act_copies[-1] + (1 if not b else 1 + (n > 4)))
            dve_copies.append(dve_copies[-1] + (n > 4 if not b else 1))

        with nc.Block() as block:

            @block.sync
            def _(sp):
                def load_keys(n):
                    for part in (0, 1):
                        for g in range(KV_GROUPS):
                            sp.dma_start(raw[part * HEAD_DIM:(part + 1) * HEAD_DIM, n, g * SEQ:(g + 1) * SEQ],
                                         proj[KV_TILE0 + 2 + n, g * HEAD_DIM:(g + 1) * HEAD_DIM, 0:SEQ]
                                         ).then_inc(k_landed[n], 16)

                load_keys(0)
                sp.dma_start(raw[:, 2, :].rearrange("p (h c) -> p h c", h=H),
                             from_rows(rows_dram, P - 1, [[SKEW, P], [COPIES, H], [1, 2 * P]])
                             ).then_inc(near_landed, 16)
                load_q(sp, 0)
                for n in range(2):
                    sp.dma_start(staged[n], from_rows(
                        rows_dram, n * half_heads * COPIES + ZERO_DIST + CMP_BLOCK - 1 - 9 * CMP_STRIDE,
                        [[SKEW, P], [COPIES, half_heads], [1, stage_len]])).then_inc(cmpb_landed, 16)
                load_keys(1)
                sp.wait_ge(filled, 3)
                for part in (0, 1):
                    for g in range(KV_GROUPS):
                        sp.dma_start(kc_raw[part * HEAD_DIM:(part + 1) * HEAD_DIM, g, 0:N_CMP],
                                     kc[g * HEAD_DIM:(g + 1) * HEAD_DIM, DEC_BATCH * N_CMP:]
                                     ).then_inc(kc_landed, 16)
                sp.dma_start(win_raw, from_rows(rows_dram, H * COPIES + P - 1, [[SKEW, P], [1, P]])
                             ).then_inc(win_landed, 16)
                for i in range(1, tiles):
                    load_q(sp, i)

            @block.gpsimd
            def _(pool):
                pool.memset(cmpb[:, :, 0:near0], 0.0).then_inc(filled, 1)
                pool.memset(cmpb[:, :, near0 + CMP_NEAR:], NEG).then_inc(filled, 1)
                pool.memset(kc_raw, 0.0).then_inc(filled, 1)
                pool.wait_ge(cmpb_landed, 32)
                for n in range(2):
                    pool.tensor_copy(cmpb[:, n * half_heads:(n + 1) * half_heads, near0:near0 + CMP_NEAR],
                                     staged[n][:, :, ::CMP_STRIDE]).then_inc(filled, 1)

            @block.tensor
            def _(pe):
                def scores(u):
                    i, g, r, b = units[u]
                    h = g * GROUP_HEADS + r
                    qs = q[:, i % 2, h, :]
                    kt = key_tiles(u)
                    s = 2 * (u % 2)
                    if u % per_tile == 0:
                        pe.wait_ge(q_ready, i + 1)
                    if u >= 2:
                        pe.wait_ge(p_ready, u - 1)
                    for c in range(0, len(kt), 4):
                        part = kt[c:c + 4]
                        bank = s_ps[:, s + c // 4, :]
                        keys = slice(g * SEQ + part[0] * P, g * SEQ + (part[-1] + 1) * P)
                        pe.matmul(bank[:, 0:len(part) * P], qs, k_hi[:, b, keys], start=True, stop=False)
                        mm = pe.matmul(bank[:, 0:len(part) * P], qs, k_lo[:, b, keys], start=False, stop=True)
                        close = [j for j in part if i - j < 2]
                        if close:
                            at = bank[:, (close[0] - part[0]) * P:(close[-1] - part[0] + 1) * P]
                            cols = slice((1 - i + close[0]) * P, (2 - i + close[-1]) * P)
                            for table in (near_hi, near_lo):
                                mm = pe.matmul(at, eye[:], table[:, h, cols], start=False, stop=True,
                                               skip_group_check=True)
                        if b and i - part[0] == WINDOW // P:
                            mm = pe.matmul(bank[:, 0:P], eye[:], win[:], start=False, stop=True,
                                           skip_group_check=True)
                    if b:
                        at = s_ps[:, s + 1, P:P + N_CHUNK]
                        pe.matmul(at, qs, kc_hi[:, g, :], start=True, stop=False)
                        pe.matmul(at, qs, kc_lo[:, g, :], start=False, stop=False)
                        c0 = 8 * (tiles - 1 - i)
                        pe.matmul(at, eye[:], cmpb_hi[:, h, c0:c0 + N_CHUNK], start=False, stop=False)
                        mm = pe.matmul(at, eye[:], cmpb_lo[:, h, c0:c0 + N_CHUNK], start=False, stop=True)
                    mm.then_inc(s_ready, 1)

                def turn(u):
                    pe.wait_ge(p_ready, u + 1)
                    pe.wait_ge(pt_act, act_copies[u])
                    pe.wait_ge(pt_dve, dve_copies[u])
                    if u % per_tile == turn_at + 1 and units[u][0]:
                        pe.wait_ge(ot_ready, units[u][0])
                    for n in range(len(key_tiles(u))):
                        mm = pe.transpose(t_ps[:, n // 4, (n % 4) * P:(n % 4 + 1) * P],
                                          prob[:, u % 2, n * P:(n + 1) * P], core.ident[:])
                    if units[u][3]:
                        mm = pe.transpose(t_ps[:N_CMP, 1, P:2 * P], prob[:, u % 2, 5 * P:5 * P + N_CMP],
                                          core.ident[:])
                    mm.then_inc(t_ready, 1)

                def values(u):
                    i, g, r, b = units[u]
                    n = u // 2
                    pe.wait_ge(pt_act, act_copies[u + 1])
                    pe.wait_ge(pt_dve, dve_copies[u + 1])
                    if not b and n >= 2:
                        pe.wait_ge(o_ready, n - 1)
                    kt = key_tiles(u)
                    at = o_ps[:, n % 2, (1 + b) * HEAD_DIM:(2 + b) * HEAD_DIM]
                    vcol = b * P + g * HEAD_DIM
                    for m, j in enumerate(kt):
                        mm = pe.matmul(at, probt[:, u % 2, m * P:(m + 1) * P], nat[:, j, vcol:vcol + HEAD_DIM],
                                       start=m == 0, stop=m == len(kt) - 1)
                    if b:
                        vg = (DEC_BATCH * 2 + g) * HEAD_DIM
                        mm = pe.matmul(o_ps[:, n % 2, 0:HEAD_DIM], probt[:N_CMP, u % 2, 5 * P:6 * P],
                                       vc[:N_CMP, vg:vg + HEAD_DIM], start=True, stop=True)
                    mm.then_inc(pv_ready, 1)

                def turn_output(i, u):
                    pe.wait_ge(o_ready, (i + 1) * H)
                    pe.wait_ge(pt_act, act_copies[u + 1])
                    pe.wait_ge(pt_dve, dve_copies[u + 1])
                    for r in range(GROUP_HEADS):
                        mm = pe.transpose(t_ps[:, 0, r * P:(r + 1) * P], o[:, i % 2, r * P:(r + 1) * P],
                                          core.ident[:])
                    mm.then_inc(ot_ps, 1)

                pe.wait_ge(hi_done, len(to_split))
                pe.wait_ge(split_done, splits)
                scores(0)
                scores(1)
                for u in range(U):
                    turn(u)
                    if u + 2 < U:
                        scores(u + 2)
                    if u:
                        values(u - 1)
                    if u % per_tile == turn_at and units[u][0]:
                        turn_output(units[u][0] - 1, u)
                values(U - 1)
                turn_output(tiles - 1, U - 1)

            @block.scalar
            def _(act):
                def pack(i):
                    act.wait_ge(q_landed[i % 2], 64 * (i // 2 + 1))
                    if i >= 2:
                        act.wait_ge(s_ready, per_tile * (i - 1))
                    act.activation(q[:, i % 2], q_raw[:, i % 2], ACT.Copy, scale=SCALE).then_inc(q_hi, 1)

                for n, (source, hi, _, arrival, count) in enumerate(to_split):
                    if n == 2:
                        pack(0)
                    if arrival is not None:
                        act.wait_ge(arrival, count)
                    act.activation(hi, source, ACT.Copy).then_inc(hi_done, 1)
                act.activation(gates[:].rearrange("p t h c -> p t (h c)"), nat[:, 0:tiles, 264:288], ACT.Sigmoid
                               ).then_inc(gates_ready, 1)

                def exp(u):
                    i, g, r, b = units[u]
                    n = u // 2
                    w = len(key_tiles(u)) * P
                    s = s_ps[:, 2 * (u % 2):2 * (u % 2) + 2, :].rearrange("p a c -> p (a c)")
                    act.wait_ge(max_ready, u + 1)
                    if u >= 2:
                        act.wait_ge(t_ready, u - 1)
                    if n >= 2:
                        act.wait_ge(rec_ready, n - 1)
                    e = act.activation(prob[:, u % 2, 0:w], s[:, 0:w], ACT.Exp, bias=neg_max[:, u % 2, 0:1],
                                       accum_out=sums[:, n % 2, 1 + b:2 + b])
                    if b:
                        e = act.activation(prob[:, u % 2, 5 * P:5 * P + N_CMP], s[:, 5 * P:5 * P + N_CMP],
                                           ACT.Exp, bias=neg_max[:, u % 2, 1:2], accum_out=sums[:, n % 2, 0:1])
                    e.then_inc(p_ready, 1)

                def copy(u):
                    n, b = len(key_tiles(u)), units[u][3]
                    act.wait_ge(t_ready, u + 1)
                    if u >= 2:
                        act.wait_ge(pv_ready, u - 1)
                    if not b:
                        w = min(n, 4) * P
                        act.activation(probt[:, u % 2, 0:w], t_ps[:, 0, 0:w], ACT.Copy).then_inc(pt_act, 1)
                    else:
                        if n > 4:
                            act.activation(probt[:, u % 2, 4 * P:5 * P], t_ps[:, 1, 0:P], ACT.Copy
                                           ).then_inc(pt_act, 1)
                        act.activation(probt[:N_CMP, u % 2, 5 * P:6 * P], t_ps[:N_CMP, 1, P:2 * P], ACT.Copy
                                       ).then_inc(pt_act, 1)

                def take_output(i):
                    act.wait_ge(ot_ps, i + 1)
                    act.activation(o_t[:, :, i * P:(i + 1) * P],
                                   t_ps[:, 0, :].rearrange("p (r t) -> p r t", t=P), ACT.Copy
                                   ).then_inc(ot_ready, 1)

                exp(0)
                for u in range(U):
                    if u % per_tile == pack_at and u + per_tile < U:
                        pack(units[u][0] + 1)
                    if u + 1 < U:
                        exp(u + 1)
                    copy(u)
                    if u % per_tile == turn_at and units[u][0]:
                        take_output(units[u][0] - 1)
                take_output(tiles - 1)

            @block.vector
            def _(dve):
                def maxima(u):
                    b = units[u][3]
                    w = len(key_tiles(u)) * P
                    s = s_ps[:, 2 * (u % 2):2 * (u % 2) + 2, :].rearrange("p a c -> p (a c)")
                    dve.wait_ge(s_ready, u + 1)
                    m = dve.tensor_reduce(neg_max[:, u % 2, 0:1], s[:, 0:w], AX_X, ALU.max, negate=True)
                    if b:
                        m = dve.tensor_reduce(neg_max[:, u % 2, 1:2], s[:, 5 * P:5 * P + N_CMP], AX_X, ALU.max,
                                              negate=True)
                    m.then_inc(max_ready, 1)

                def copy(u):
                    n, b = len(key_tiles(u)), units[u][3]
                    dve.wait_ge(t_ready, u + 1)
                    if u >= 2:
                        dve.wait_ge(pv_ready, u - 1)
                    if b:
                        w = min(n, 4) * P
                        dve.tensor_copy(probt[:, u % 2, 0:w], t_ps[:, 0, 0:w]).then_inc(pt_dve, 1)
                    elif n > 4:
                        dve.tensor_copy(probt[:, u % 2, 4 * P:n * P], t_ps[:, 1, 0:(n - 4) * P]
                                        ).then_inc(pt_dve, 1)

                def weights(n):
                    i, g, r, _ = units[2 * n]
                    h = g * GROUP_HEADS + r
                    dve.wait_ge(p_ready, 2 * n + 2)
                    dve.reciprocal(rec[:, n % 2, :], sums[:, n % 2, :]).then_inc(rec_ready, 1)
                    dve.wait_ge(rec_ready, n + 1)
                    mixed = dve.tensor_tensor(mix[:, n % 2, :], rec[:, n % 2, :], gates[:, i, h, :], ALU.mult)
                    if i == 0:
                        mixed.then_inc(mix_ready, 1)
                        dve.wait_ge(mix_ready, 2 * n + 1)
                        mixed = dve.tensor_tensor(mix[:, n % 2, 0:1], mix[:, n % 2, 0:1], core.sees_cmp[:],
                                                  ALU.mult)
                    mixed.then_inc(mix_ready, 1)

                def mix_count(n):
                    return 2 * (n + 1) if n < H else n + 1 + H

                def combine(n):
                    i, g, r, _ = units[2 * n]
                    at = o[:, i % 2, (2 * r + g) * HEAD_DIM:(2 * r + g + 1) * HEAD_DIM]
                    dve.wait_ge(mix_ready, mix_count(n))
                    dve.wait_ge(pv_ready, 2 * n + 2)
                    if i >= 2:
                        dve.wait_ge(ot_ps, i - 1)
                    for k in range(3):
                        part = o_ps[:, n % 2, k * HEAD_DIM:(k + 1) * HEAD_DIM]
                        if k == 0:
                            dve.tensor_scalar(at, part, mix[:, n % 2, 0:1], None, ALU.mult
                                              ).then_inc(part_ready, 1)
                        else:
                            dve.wait_ge(part_ready, 2 * n + k)
                            dve.scalar_tensor_tensor(at, part, mix[:, n % 2, k:k + 1], at, ALU.mult, ALU.add
                                                     ).then_inc(part_ready if k == 1 else o_ready, 1)

                def pack(i):
                    up = slice(HEAD_DIM, P)
                    dve.wait_ge(q_hi, i + 1)
                    dve.scalar_tensor_tensor(q[up, i % 2], q_raw[up, i % 2], SCALE, q[up, i % 2].bitcast(F32),
                                             ALU.mult, ALU.subtract).then_inc(q_ready, 1)

                for n, (source, hi, lo, _, _) in enumerate(to_split):
                    if n == 2:
                        pack(0)
                    if lo is not None:
                        dve.wait_ge(hi_done, n + 1)
                        dve.tensor_tensor(lo, source, hi.bitcast(F32), ALU.subtract).then_inc(split_done, 1)
                dve.wait_ge(gates_ready, 1)
                maxima(0)
                for u in range(U):
                    if u % per_tile == pack_at and u + per_tile < U:
                        pack(units[u][0] + 1)
                    if u + 1 < U:
                        maxima(u + 1)
                    copy(u)
                    if units[u][3]:
                        weights(u // 2)
                        if u > 1:
                            combine(u // 2 - 1)
                combine(U // 2 - 1)


SLC_BLOCK = 64
PAST = SEQ
N_SLC = -(-(PAST + DEC_SEQ) // SLC_BLOCK)
FREE_BLOCKS = N_SLC - 3
NEW = SAMPLE
PAIRS = DEC_BATCH // 2
RULES = P + N_SLC + FREE_BLOCKS


def make_rules():
    c = np.zeros((P, RULES), np.float32)
    i = np.arange(P)
    key = (i // 32) * DEC_SEQ + i % DEC_SEQ
    c[:, :P] = key[:, None] == key[None, :]
    start = np.arange(N_CMP) * CMP_STRIDE
    block = np.arange(N_SLC) * SLC_BLOCK
    c[:N_CMP, P:P + N_SLC] = (start[:, None] < block[None, :] + SLC_BLOCK) & \
        (start[:, None] + CMP_BLOCK - 1 >= block[None, :])
    c[:, P + N_SLC:] = 1.0 + np.arange(FREE_BLOCKS)
    return c


def sample_nsa_stage(core, nat, kc, vc, proj, rows_dram, rules, page_table, slc_pages, win_kv, gates_dram,
                     o_t, n_pool):
    nc = core.nc
    H = NSA_HEADS
    G = GROUP_HEADS * DEC_SEQ
    with ExitStack() as ctx:
        sb = lambda name, shape, dt=F32: ctx.enter_context(nc.sbuf_tensor(f"sn_{name}", shape, dt))
        ps = lambda name, n: ctx.enter_context(nc.psum_tensor(f"sn_{name}_ps", [P, n, 512], F32))
        q_in, q = sb("q_in", [P, GROUP_HEADS, NEW]), sb("q", [P, DEC_BATCH, G])
        ks, kw = sb("ks_new", [P, NEW]), sb("kw_new", [P, NEW])
        rule = sb("rules", [P, RULES])
        table = sb("page_table", [1, DEC_BATCH * PAGES], I32)
        SLOTS = 3
        past = sb("slc_pages", [P, SLOTS, 2, PAGES, 2 * P])
        win = sb("win_kv", [P, SLOTS, 2, 2 * WINDOW])
        near, edge, cmpb = sb("near", [P, P]), sb("window_edge", [P, DEC_SEQ]), sb("cmp_bias", [P, N_CMP])
        newb = sb("new_bias", [P, PAIRS, NEW])
        gate_nat, gates = sb("gate_nat", [NEW, 3 * H]), sb("gates", [P, PAIRS, 3])
        pc, pcn = sb("p_cmp", [P, PAIRS, N_CMP]), sb("p_cmp_normed", [P, PAIRS, N_CMP])
        pct = sb("p_cmp_t", [P, PAIRS, P])
        imp, least, ranked, last, drop = (sb("imp", [P, PAIRS, N_SLC]), sb("least", [P, PAIRS]),
                                          sb("ranked", [P, PAIRS, FREE_BLOCKS]), sb("last", [P, PAIRS]),
                                          sb("drop", [P, PAIRS, FREE_BLOCKS]))
        ncm, csum, crec = sb("cmp_neg_max", [P, PAIRS]), sb("cmp_sum", [P, PAIRS]), sb("cmp_rec", [P, PAIRS])
        all_parts, maxes, all_sums, totals = (sb("max_parts", [P, 2, 2, 2]), sb("neg_max", [P, 2, 2]),
                                              sb("sums", [P, 2, 2, 2]), sb("sum_total", [P, 2, 2]))
        mixes = sb("mix", [P, 2, 2])
        PW = PAST + NEW + WINDOW + NEW + N_CMP
        W0, C0 = PAST + NEW, PAST + NEW + WINDOW + NEW
        probs, probt = sb("prob", [P, 2, PW]), sb("prob_t", [P, 16, P])
        s_ps, t_ps, o_ps, m_ps = ps("s", 4), ps("t", 2), ps("o", 1), ps("m", 1)

        landed, filled, gate_done, gate_stored, q_ready, table_landed = map(
            core.sem, ("sn_landed", "sn_filled", "gate_sigmoid", "gate_stored", "sn_q_ready", "sn_table"))
        new_landed = core.sem("new_bias_landed")
        past_landed = [core.sem(f"past_landed_{s}") for s in range(SLOTS)]
        c_ready, cmax, pc_ready, crec_ready, pcn_ready, pct_ps, pct_ready, imp_ps, imp_ready, impg_ps = map(
            core.sem, ("c_scores", "c_max", "pc_ready", "c_rec", "pcn_ready", "pct_ps", "pct_ready", "imp_ps",
                       "imp_ready", "imp_group_ps"))
        rank, drop_ready = map(core.sem, ("rank_steps", "drop_ready"))
        s_ready, dropped, parts_ready, max_ready, p_ready, total_ready, rec_ready, mix_ready, scaled = map(
            core.sem, ("sn_s_ready", "dropped", "max_parts_ready", "sn_max_ready", "sn_p_ready",
                       "sn_total", "sn_rec", "sn_mix", "sn_scaled"))
        t_ready, pt_act, pt_dve, pv_ready, o_ready = map(
            core.sem, ("sn_t_ready", "sn_pt_act", "sn_pt_dve", "sn_pv_ready", "sn_o_ready"))

        with nc.Block() as block:

            @block.sync
            def _(sp):
                sp.dma_start(table[:], page_table).then_inc(table_landed, 16)
                sp.dma_start(q_in[:], proj[12:16, :, SEQ:TOKENS].rearrange("i p t -> p i t")).then_inc(landed, 16)
                sp.dma_start(ks[:], proj[KV_TILE0 + 2, :, SEQ:TOKENS]).then_inc(landed, 16)
                sp.dma_start(kw[:], proj[KV_TILE0 + 3, :, SEQ:TOKENS]).then_inc(landed, 16)
                sp.dma_start(rule[:], rules).then_inc(landed, 16)
                sp.wait_ge(table_landed, 16)

                def load(bt):
                    s = bt % SLOTS
                    if bt >= SLOTS:
                        sp.wait_ge(pv_ready, bt - SLOTS + 1)
                    for b2 in range(2):
                        b = 2 * bt + b2
                        for j in range(PAGES):
                            page = sp.value_load(table[0:1, b * PAGES + j:b * PAGES + j + 1],
                                                 min_val=0, max_val=n_pool - 1)
                            sp.dma_start(past[:, s, b2, j, :],
                                         slc_pages[bass.ds(page, 1)].rearrange("o p c -> (o p) c")
                                         ).then_inc(past_landed[s], 16)
                        sp.dma_start(win[:, s, b2, :], win_kv[b]).then_inc(past_landed[s], 16)

                for bt in range(PAIRS):
                    load(bt)

            @block.gpsimd
            def _(pool):
                pool.memset(newb[:], NEG).then_inc(filled, 1)
                pool.memset(cmpb[:, 0:N_CMP - 8], 0.0).then_inc(filled, 1)
                pool.wait_ge(landed, 16 * 8)
                pool.tensor_copy(cmpb[:, N_CMP - 8:], near[:, CMP_STRIDE - 1::CMP_STRIDE]).then_inc(filled, 1)
                pool.wait_ge(q_ready, 1)
                for r in range(GROUP_HEADS):
                    pool.tensor_copy(q[:, :, r * DEC_SEQ:(r + 1) * DEC_SEQ],
                                     q_in[:, r, :].rearrange("p (b t) -> p b t", t=DEC_SEQ)).then_inc(q_ready, 1)

            @block.scalar
            def _(act):
                act.activation(gate_nat[:], nat[:NEW, TOK_TILES - 1, 264:288], ACT.Sigmoid).then_inc(gate_done, 1)
                act.wait_ge(gate_done, 1)
                act.dma_start(gates_dram, gate_nat[:]).then_inc(gate_stored, 16)
                half = H * DEC_SEQ
                for b2 in range(2):
                    rows = slice(b2 * half, (b2 + 1) * half)
                    act.dma_start(near[rows, :], from_rows(rows_dram, P - 1, [[COPIES, H], [SKEW, DEC_SEQ], [1, P]])
                                  ).then_inc(landed, 16)
                    act.dma_start(edge[rows, :], from_rows(rows_dram, H * COPIES + P - 1,
                                                           [[0, H], [SKEW, DEC_SEQ], [1, DEC_SEQ]])
                                  ).then_inc(landed, 16)
                act.wait_ge(filled, 2)
                for bt in range(PAIRS):
                    for b2 in range(2):
                        b = 2 * bt + b2
                        rows = slice(b2 * half, (b2 + 1) * half)
                        act.dma_start(newb[rows, bt, b * DEC_SEQ:(b + 1) * DEC_SEQ], from_rows(
                            rows_dram, 2 * P - 1, [[COPIES, H], [SKEW, DEC_SEQ], [1, DEC_SEQ]])
                                      ).then_inc(new_landed, 16)
                act.wait_ge(gate_stored, 16)
                for bt in range(PAIRS):
                    for b2 in range(2):
                        b = 2 * bt + b2
                        rows = slice(b2 * half, (b2 + 1) * half)
                        act.dma_start(gates[rows, bt, :], bass.AP(
                            gates_dram.tensor, b * DEC_SEQ * 3 * H, [[3, H], [3 * H, DEC_SEQ], [1, 3]])
                                      ).then_inc(new_landed, 16)
                act.wait_ge(landed, 16 * 8)
                act.activation(q_in[:], q_in[:], ACT.Copy, scale=SCALE).then_inc(q_ready, 1)
                act.wait_ge(cmax, 1)
                for bt in range(PAIRS):
                    act.activation(pc[:, bt, :], m_ps[:, 0, bt * N_CMP:(bt + 1) * N_CMP], ACT.Exp,
                                   bias=ncm[:, bt:bt + 1], accum_out=csum[:, bt:bt + 1]).then_inc(pc_ready, 1)
                act.wait_ge(pct_ps, 1)
                act.activation(pct[:N_CMP].rearrange("p b c -> p (b c)"), t_ps[:N_CMP, 0, :], ACT.Copy
                               ).then_inc(pct_ready, 1)

                def exp(bt):
                    prob, neg_max, sums = (a[:, bt % 2] for a in (probs, maxes, all_sums))
                    act.wait_ge(max_ready, bt + 1)
                    if bt >= 2:
                        act.wait_ge(t_ready, 4 * (bt - 1))
                        act.wait_ge(total_ready, bt - 1)
                    for br, (c0, bank, n) in enumerate(((0, 0, PAST), (W0, 2, WINDOW))):
                        act.activation(prob[:, c0:c0 + n], s_ps[:, bank:bank + n // 512, :].rearrange(
                            "p a c -> p (a c)"), ACT.Exp, bias=neg_max[:, br:br + 1],
                            accum_out=sums[:, br, 0:1])
                        e = act.activation(prob[:, c0 + n:c0 + n + NEW], s_ps[:, 3, br * NEW:(br + 1) * NEW],
                                           ACT.Exp, bias=neg_max[:, br:br + 1], accum_out=sums[:, br, 1:2])
                    e.then_inc(p_ready, 1)

                exp(0)
                for bt in range(PAIRS):
                    for n in range(0, 4, 2):
                        act.wait_ge(t_ready, 4 * bt + n + 1)
                        if bt:
                            act.wait_ge(pv_ready, bt)
                        act.activation(probt[:, 4 * n:4 * n + 4, :].rearrange("p a c -> p (a c)"), t_ps[:, 0, :],
                                       ACT.Copy).then_inc(pt_act, 1)
                    if bt + 1 < PAIRS:
                        exp(bt + 1)

            @block.tensor
            def _(pe):
                def row(b2, g):
                    return slice((2 * b2 + g) * G, (2 * b2 + g + 1) * G)

                def group(g):
                    return slice(g * HEAD_DIM, (g + 1) * HEAD_DIM)

                every = [(b2, g) for b2 in range(2) for g in range(KV_GROUPS)]
                pe.wait_ge(q_ready, 1 + GROUP_HEADS)
                pe.wait_ge(landed, 16 * 8)
                pe.wait_ge(filled, 3)
                for bt in range(PAIRS):
                    at = m_ps[:, 0, bt * N_CMP:(bt + 1) * N_CMP]
                    for b2, g in every:
                        b = 2 * bt + b2
                        pe.matmul(at[row(b2, g)], q[group(g), b, :], kc[group(g), b * N_CMP:(b + 1) * N_CMP],
                                  start=True, stop=True)
                    mm = pe.matmul(at, core.ident[:], cmpb[:], start=False, stop=True, skip_group_check=True)
                mm.then_inc(c_ready, 1)
                pe.wait_ge(pcn_ready, PAIRS)
                for bt in range(PAIRS):
                    mm = pe.transpose(t_ps[:N_CMP, 0, bt * P:(bt + 1) * P], pcn[:, bt, :], core.ident[:])
                mm.then_inc(pct_ps, 1)
                pe.wait_ge(pct_ready, 1)
                for bt in range(PAIRS):
                    mm = pe.matmul(m_ps[:, 0, bt * N_SLC:(bt + 1) * N_SLC], pct[:N_CMP, bt, :],
                                   rule[:N_CMP, P:P + N_SLC], start=True, stop=True)
                mm.then_inc(imp_ps, 1)
                pe.wait_ge(imp_ready, 1)
                pe.matmul(m_ps[:, 0, 256:256 + PAIRS * N_SLC], rule[:, 0:P],
                          imp[:].rearrange("p b s -> p (b s)"), start=True, stop=True).then_inc(impg_ps, 1)
                pe.wait_ge(new_landed, 16 * 16)

                def scores(bt):
                    s = bt % SLOTS
                    pe.wait_ge(past_landed[s], 16 * 2 * (PAGES + 1) * (bt // SLOTS + 1))
                    if bt:
                        pe.wait_ge(p_ready, bt)
                    for half in range(2):
                        for b2, g in every:
                            pe.matmul(s_ps[row(b2, g), half, :].rearrange("p (j t) -> p j t", t=P),
                                      q[group(g), 2 * bt + b2, :], past[group(g), s, b2, 4 * half:4 * half + 4, 0:P],
                                      start=True, stop=True)
                    pe.matmul(s_ps[:, 1, 3 * P:], core.ident[:], near[:], start=False, stop=True,
                              skip_group_check=True)
                    for b2, g in every:
                        pe.matmul(s_ps[row(b2, g), 2, :], q[group(g), 2 * bt + b2, :], win[group(g), s, b2, 0:WINDOW],
                                  start=True, stop=True)
                    pe.matmul(s_ps[:, 2, 3 * P:], core.ident[:], near[:], start=False, stop=True,
                              skip_group_check=True)
                    pe.matmul(s_ps[:, 2, 0:DEC_SEQ], core.ident[:], edge[:], start=False, stop=True,
                              skip_group_check=True)
                    for br, keys in enumerate((ks, kw)):
                        at = s_ps[:, 3, br * NEW:(br + 1) * NEW]
                        for b2, g in every:
                            pe.matmul(at[row(b2, g)], q[group(g), 2 * bt + b2, :], keys[group(g), :],
                                      start=True, stop=True)
                        mm = pe.matmul(at, core.ident[:], newb[:, bt, :], start=False, stop=True,
                                       skip_group_check=True)
                    mm.then_inc(s_ready, 1)

                scores(0)
                for bt in range(PAIRS):
                    s = bt % SLOTS
                    prob = probs[:, bt % 2]
                    if bt + 1 < PAIRS:
                        scores(bt + 1)
                    pe.wait_ge(scaled, 3 * (bt + 1))
                    for n in range(4):
                        if n >= 2 or bt:
                            if n % 2 == 0:
                                pe.wait_ge(pt_act, 2 * bt + n // 2)
                            else:
                                pe.wait_ge(pt_dve, 2 * bt + n // 2)
                        if n < 3:
                            c0 = (0, 4 * P, W0)[n]
                            for m in range(4):
                                mm = pe.transpose(t_ps[:, n % 2, m * P:(m + 1) * P],
                                                  prob[:, c0 + m * P:c0 + (m + 1) * P], core.ident[:])
                        else:
                            for m, (c0, w) in enumerate(((PAST, NEW), (W0 + WINDOW, NEW), (C0, N_CMP))):
                                mm = pe.transpose(t_ps[:w, 1, m * P:(m + 1) * P], prob[:, c0:c0 + w], core.ident[:])
                        mm.then_inc(t_ready, 1)
                    pe.wait_ge(pt_act, 2 * bt + 2)
                    pe.wait_ge(pt_dve, 2 * bt + 2)
                    for b2 in range(2):
                        b = 2 * bt + b2

                        def values(g):
                            tiles = [(past[:, s, b2, j, P + g * HEAD_DIM:P + (g + 1) * HEAD_DIM], P, j)
                                     for j in range(PAGES)]
                            tiles += [(win[:, s, b2, WINDOW + j * P + g * HEAD_DIM:
                                           WINDOW + j * P + (g + 1) * HEAD_DIM], P, 8 + j)
                                      for j in range(WINDOW // P)]
                            tiles += [(nat[:NEW, TOK_TILES - 1, br * P + g * HEAD_DIM:br * P + (g + 1) * HEAD_DIM],
                                       NEW, 12 + br) for br in range(2)]
                            return tiles + [(vc[:N_CMP, (2 * b + g) * HEAD_DIM:(2 * b + g + 1) * HEAD_DIM], N_CMP, 14)]

                        both = list(zip(*(values(g) for g in range(KV_GROUPS))))
                        for n, tile in enumerate(both):
                            for g, (v, k, slot) in enumerate(tile):
                                at = o_ps[group(g), 0, 0:GROUP_HEADS * NEW].rearrange(
                                    "p (r t) -> p r t", t=NEW)[:, :, b * DEC_SEQ:(b + 1) * DEC_SEQ]
                                mm = pe.matmul(at, v, probt[:k, slot, row(b2, g)].rearrange(
                                    "p (r t) -> p r t", t=DEC_SEQ), start=n == 0, stop=n == len(both) - 1)
                    mm.then_inc(pv_ready, 1)

            @block.vector
            def _(dve):
                dve.wait_ge(c_ready, 1)
                dve.tensor_reduce(ncm[:], m_ps[:, 0, 0:PAIRS * N_CMP].rearrange("p (b n) -> p b n", n=N_CMP), AX_X,
                                  ALU.max, negate=True).then_inc(cmax, 1)
                dve.wait_ge(pc_ready, PAIRS)
                dve.reciprocal(crec[:], csum[:]).then_inc(crec_ready, 1)
                dve.wait_ge(crec_ready, 1)
                for bt in range(PAIRS):
                    dve.tensor_scalar(pcn[:, bt, :], pc[:, bt, :], crec[:, bt:bt + 1], None, ALU.mult
                                      ).then_inc(pcn_ready, 1)
                dve.wait_ge(imp_ps, 1)
                dve.tensor_copy(imp[:].rearrange("p b s -> p (b s)"), m_ps[:, 0, 0:PAIRS * N_SLC]
                                ).then_inc(imp_ready, 1)
                dve.wait_ge(impg_ps, 1)
                ranks = m_ps[:, 0, 256:256 + PAIRS * N_SLC].rearrange("p (b s) -> p b s", s=N_SLC)[
                    :, :, 1:1 + FREE_BLOCKS]
                number = rule[:, P + N_SLC:]
                dve.tensor_reduce(least[:], ranks, AX_X, ALU.min).then_inc(rank, 1)
                dve.wait_ge(rank, 1)
                for bt in range(PAIRS):
                    dve.scalar_tensor_tensor(ranked[:, bt, :], ranks[:, bt, :], least[:, bt:bt + 1], number,
                                             ALU.is_le, ALU.mult).then_inc(rank, 1)
                dve.wait_ge(rank, 1 + PAIRS)
                dve.tensor_reduce(last[:], ranked[:], AX_X, ALU.max).then_inc(rank, 1)
                dve.wait_ge(rank, 2 + PAIRS)
                for bt in range(PAIRS):
                    dve.tensor_scalar(drop[:, bt, :], number, last[:, bt:bt + 1], NEG, ALU.is_equal, ALU.mult
                                      ).then_inc(drop_ready, 1)
                dve.wait_ge(drop_ready, PAIRS)
                dve.wait_ge(new_landed, 16 * 16)

                def maxima(bt):
                    parts, neg_max = all_parts[:, bt % 2], maxes[:, bt % 2]
                    dve.wait_ge(s_ready, bt + 1)
                    flat = s_ps[:, 0:2, :].rearrange("p a c -> p (a c)")
                    ranked_keys = flat[:, SLC_BLOCK:SLC_BLOCK * (1 + FREE_BLOCKS)].rearrange(
                        "p (s t) -> p s t", t=SLC_BLOCK)
                    dve.tensor_tensor(ranked_keys, ranked_keys,
                                      drop[:, bt, :].rearrange("p (s o) -> p s o", o=1).to_broadcast(
                                          [P, FREE_BLOCKS, SLC_BLOCK]), ALU.add).then_inc(dropped, 1)
                    dve.wait_ge(dropped, bt + 1)
                    dve.tensor_reduce(parts[:, 0, 0:1], flat, AX_X, ALU.max, negate=True)
                    dve.tensor_reduce(parts[:, 0, 1:2], s_ps[:, 2, :], AX_X, ALU.max, negate=True)
                    dve.tensor_reduce(parts[:, 1, :], s_ps[:, 3, 0:2 * NEW].rearrange("p (b t) -> p b t", t=NEW),
                                      AX_X, ALU.max, negate=True).then_inc(parts_ready, 1)
                    dve.wait_ge(parts_ready, bt + 1)
                    dve.tensor_tensor(neg_max, parts[:, 0, :], parts[:, 1, :], ALU.min).then_inc(max_ready, 1)

                maxima(0)
                for bt in range(PAIRS):
                    prob, sums, total, mix = (a[:, bt % 2] for a in (probs, all_sums, totals, mixes))
                    dve.wait_ge(p_ready, bt + 1)
                    dve.tensor_tensor(total, sums[:, :, 0], sums[:, :, 1], ALU.add).then_inc(total_ready, 1)
                    dve.wait_ge(total_ready, bt + 1)
                    dve.reciprocal(total, total).then_inc(rec_ready, 1)
                    dve.wait_ge(rec_ready, bt + 1)
                    dve.tensor_tensor(mix, total, gates[:, bt, 1:3], ALU.mult).then_inc(mix_ready, 1)
                    dve.wait_ge(mix_ready, bt + 1)
                    dve.tensor_scalar(prob[:, 0:W0], prob[:, 0:W0], mix[:, 0:1], None, ALU.mult).then_inc(scaled, 1)
                    dve.tensor_scalar(prob[:, W0:C0], prob[:, W0:C0], mix[:, 1:2], None, ALU.mult
                                      ).then_inc(scaled, 1)
                    dve.tensor_scalar(prob[:, C0:], pcn[:, bt, :], gates[:, bt, 0:1], None, ALU.mult
                                      ).then_inc(scaled, 1)
                    for n in range(1, 4, 2):
                        dve.wait_ge(t_ready, 4 * bt + n + 1)
                        if bt:
                            dve.wait_ge(pv_ready, bt)
                        if n == 1:
                            dve.tensor_copy(probt[:, 4:8, :].rearrange("p a c -> p (a c)"), t_ps[:, 1, :]
                                            ).then_inc(pt_dve, 1)
                        else:
                            dve.tensor_copy(probt[:NEW, 12:14, :].rearrange("p a c -> p (a c)"),
                                            t_ps[:NEW, 1, 0:2 * P])
                            dve.tensor_copy(probt[:N_CMP, 14, :], t_ps[:N_CMP, 1, 2 * P:3 * P]).then_inc(pt_dve, 1)
                    if bt + 1 < PAIRS:
                        maxima(bt + 1)
                dve.wait_ge(pv_ready, PAIRS)
                dve.tensor_copy(o_t[:, :, SEQ:TOKENS],
                                o_ps[:, 0, 0:GROUP_HEADS * NEW].rearrange("p (r t) -> p r t", t=NEW)
                                ).then_inc(o_ready, 1)
                dve.memset(o_t[:, :, TOKENS:], 0.0).then_inc(o_ready, 1)


def lay_slc_pages(a):
    k = a[0, :, :, 0].reshape(-1, P, P).transpose(0, 2, 1)
    return np.ascontiguousarray(np.concatenate([k, a[0, :, :, 1].reshape(-1, P, P)], axis=2))


def lay_win(a):
    k = a[0, :, :, 0].reshape(DEC_BATCH, WINDOW, P).transpose(0, 2, 1)
    v = a[0, :, :, 1].reshape(DEC_BATCH, WINDOW // P, P, P).transpose(0, 2, 1, 3).reshape(DEC_BATCH, P, WINDOW)
    return np.ascontiguousarray(np.concatenate([k, v], axis=2))


MEM_TOKENS, MEM_HEADS = 256, 4
MT = MEM_TOKENS // P
MI = MEM_HEADS * HEAD_DIM


def mem_kv_stage(core, m_hi, m_lo, w, kt_out, v_out, later=()):
    nc = core.nc
    with ExitStack() as ctx:
        sb = lambda name, shape, dt=F32: ctx.enter_context(nc.sbuf_tensor(f"mkv_{name}", shape, dt))
        raw = sb("w_raw", [P, KT, 2 * MI])
        w_hi, w_lo = sb("w_hi", [P, KT, 2 * MI], F32R), sb("w_lo", [P, KT, 2 * MI], F32R)
        out = sb("out", [P, 2 * MT, MI])
        ps = ctx.enter_context(nc.psum_tensor("mkv_ps", [P, 2 * MT, 512], F32))
        landed, hi_ready, lo_ready, ps_ready, out_ready, stored = map(
            core.sem, ("mkv_landed", "mkv_hi", "mkv_lo", "mkv_ps_ready", "mkv_out", "mkv_stored"))
        with nc.Block() as block:

            @block.sync
            def _(sp):
                sp.dma_start(raw[:], w).then_inc(landed, 16)
                for dst, src, sem in later:
                    sp.dma_start(dst, src).then_inc(sem, 16)
                for n in range(2 * MT):
                    sp.wait_ge(out_ready, n + 1)
                    sp.dma_start((kt_out if n < MT else v_out)[:, n % MT, :], out[:, n, :]).then_inc(stored, 16)
                sp.wait_ge(stored, 16 * 2 * MT)

            @block.scalar
            def _(act):
                act.wait_ge(landed, 16)
                act.activation(w_hi[:], raw[:], ACT.Copy).then_inc(hi_ready, 1)

            @block.vector
            def _(dve):
                dve.wait_ge(hi_ready, 1)
                dve.tensor_tensor(w_lo[:], raw[:], w_hi[:].bitcast(F32), ALU.subtract).then_inc(lo_ready, 1)
                for n in range(2 * MT):
                    dve.wait_ge(ps_ready, n + 1)
                    dve.tensor_copy(out[:, n, :], ps[:, n, 0:MI]).then_inc(out_ready, 1)

            @block.tensor
            def _(pe):
                pe.wait_ge(lo_ready, 1)
                for n in range(MT):
                    c = slice(n * P, (n + 1) * P)
                    for k in range(KT):
                        mm = passes(pe, ps[:, n, 0:MEM_TOKENS], w_hi[:, k, c], w_lo[:, k, c],
                                    m_hi[:, k, 0:MEM_TOKENS], m_lo[:, k, 0:MEM_TOKENS], k == 0, k == KT - 1)
                    mm.then_inc(ps_ready, 1)
                for n in range(MT):
                    c = slice(n * P, (n + 1) * P)
                    for k in range(KT):
                        mm = passes(pe, ps[:, MT + n, 0:MI], m_hi[:, k, c], m_lo[:, k, c],
                                    w_hi[:, k, MI:], w_lo[:, k, MI:], k == 0, k == KT - 1)
                    mm.then_inc(ps_ready, 1)


def mem_attend_stage(core, q_dram, kt_p, v_p, kv_s, o_hi, o_lo):
    nc = core.nc
    units = SEQ // P + 2
    prompt_units = SEQ // P
    PADQ = 32
    with ExitStack() as ctx:
        sb = lambda name, shape, dt=F32: ctx.enter_context(nc.sbuf_tensor(f"ma_{name}", shape, dt))
        ps = lambda name, n: ctx.enter_context(nc.psum_tensor(f"ma_{name}_ps", [P, n, 512], F32))
        q_raw, qh = sb("q_raw", [P, MEM_HEADS, SEQ]), sb("q_prompt", [P, MEM_HEADS, SEQ], F32R)
        k_raw = sb("k_raw", [P, MEM_HEADS, MEM_TOKENS])
        k_hi, k_lo = (sb(f"k_{part}", [P, MEM_HEADS, MEM_TOKENS], F32R) for part in ("hi", "lo"))
        q = sb("q", [P, MT, SAMPLE])
        qp = sb("q_padded", [P, MT, DEC_BATCH, PADQ])
        v = sb("v", [P, MT, MI])
        kvs = sb("kv_sample", [P, DEC_BATCH, 4, MEM_TOKENS])
        prob, probt = sb("prob", [P, 2, 4, MEM_TOKENS]), sb("prob_t", [P, 2, 8, P])
        neg_max, sums, rec = sb("neg_max", [P, 2, 4]), sb("sums", [P, 2, 4]), sb("rec", [P, 2, 4])
        s_ps, t_ps, o_ps = ps("s", 4), ps("t", 2), ps("o", 2)
        landed, q_ready, pad_ready = map(core.sem, ("ma_landed", "ma_q_ready", "ma_pad_ready"))
        pack_landed, pack_hi, pack_lo = map(core.sem, ("ma_pack_landed", "ma_pack_hi", "ma_pack_lo"))
        s_ready, max_ready, p_ready, rec_ready, scaled, t_ready, pt_act, pt_dve, pv_ready, hi_ready, lo_ready = map(
            core.sem, ("ma_s", "ma_max", "ma_p", "ma_rec", "ma_scaled", "ma_t", "ma_pt_act", "ma_pt_dve", "ma_pv",
                       "ma_hi", "ma_lo"))

        def out_cols(u):
            if u < prompt_units:
                return slice(u * P, (u + 1) * P)
            half = SAMPLE // 2
            return slice(SEQ + (u - prompt_units) * half, SEQ + (u - prompt_units + 1) * half)

        def out_tile(u):
            n = out_cols(u)
            return o_ps[:, u % 2, 0:MT * P].rearrange("p (m t) -> p m t", t=P)[:, :, 0:n.stop - n.start]

        with nc.Block() as block:

            @block.sync
            def _(sp):
                for part in range(2):
                    for h in range(MEM_HEADS):
                        rows = slice((h % 2) * HEAD_DIM, (h % 2 + 1) * HEAD_DIM)
                        half = slice(part * HEAD_DIM, (part + 1) * HEAD_DIM)
                        sp.dma_start(k_raw[half, h, :], kt_p[rows, h // 2, :]).then_inc(pack_landed, 16)
                        sp.dma_start(q_raw[half, h, :], q_dram[h // 2, rows, 0:SEQ]).then_inc(pack_landed, 16)
                sp.dma_start(q[:], q_dram[:, :, SEQ:TOKENS].rearrange("i p t -> p i t")).then_inc(landed, 16)
                sp.dma_start(v[:], v_p).then_inc(landed, 16)
                sp.dma_start(kvs[:], kv_s).then_inc(landed, 16)

            @block.gpsimd
            def _(pool):
                pool.memset(qp[:], 0.0).then_inc(pad_ready, 1)
                pool.wait_ge(pad_ready, 1)
                pool.wait_ge(q_ready, 1)
                for m in range(MT):
                    pool.tensor_copy(qp[:, m, :, 0:DEC_SEQ],
                                     q[:, m, :].rearrange("p (b t) -> p b t", t=DEC_SEQ)).then_inc(pad_ready, 1)

            @block.scalar
            def _(act):
                act.wait_ge(pack_landed, 16 * 4 * MEM_HEADS)
                act.activation(k_hi[:], k_raw[:], ACT.Copy).then_inc(pack_hi, 1)
                for part in range(2):
                    c = slice(part * (SEQ // 2), (part + 1) * (SEQ // 2))
                    act.activation(qh[:, :, c], q_raw[:, :, c], ACT.Copy, scale=SCALE).then_inc(pack_hi, 1)
                act.wait_ge(landed, 48)
                act.activation(q[:], q[:], ACT.Copy, scale=SCALE).then_inc(q_ready, 1)

                def exp(u):
                    act.wait_ge(max_ready, u + 1)
                    if u >= 2:
                        act.wait_ge(t_ready, 2 * (u - 1))
                    for n in range(4):
                        at = s_ps[:, 2 * (u % 2) + n // 2, (n % 2) * MEM_TOKENS:(n % 2 + 1) * MEM_TOKENS]
                        e = act.activation(prob[:, u % 2, n, :], at, ACT.Exp, bias=neg_max[:, u % 2, n:n + 1],
                                           accum_out=sums[:, u % 2, n:n + 1])
                    e.then_inc(p_ready, 1)

                def round_hi(u):
                    act.wait_ge(pv_ready, u + 1)
                    act.activation(o_hi[:, 0:MT, out_cols(u)], out_tile(u), ACT.Copy).then_inc(hi_ready, 1)

                exp(0)
                for u in range(units):
                    if u + 1 < units:
                        exp(u + 1)
                    act.wait_ge(t_ready, 2 * u + 1)
                    if u >= 2:
                        act.wait_ge(pv_ready, u - 1)
                    act.activation(probt[:, u % 2, 0:4, :].rearrange("p a c -> p (a c)"), t_ps[:, 0, :], ACT.Copy
                                   ).then_inc(pt_act, 1)
                    if u:
                        round_hi(u - 1)
                round_hi(units - 1)

            @block.vector
            def _(dve):
                def maxima(u):
                    dve.wait_ge(s_ready, u + 1)
                    s = s_ps[:, 2 * (u % 2):2 * (u % 2) + 2, :].rearrange("p a (h m) -> p (a h) m", m=MEM_TOKENS)
                    dve.tensor_reduce(neg_max[:, u % 2, :], s, AX_X, ALU.max, negate=True).then_inc(max_ready, 1)

                dve.wait_ge(pack_hi, 1)
                dve.tensor_tensor(k_lo[:], k_raw[:], k_hi[:].bitcast(F32), ALU.subtract).then_inc(pack_lo, 1)
                for part in range(2):
                    c, up = slice(part * (SEQ // 2), (part + 1) * (SEQ // 2)), slice(HEAD_DIM, P)
                    dve.wait_ge(pack_hi, part + 2)
                    dve.scalar_tensor_tensor(qh[up, :, c], q_raw[up, :, c], SCALE, qh[up, :, c].bitcast(F32),
                                             ALU.mult, ALU.subtract).then_inc(pack_lo, 1)
                def rest(u):
                    dve.wait_ge(hi_ready, u + 1)
                    dve.tensor_tensor(o_lo[:, 0:MT, out_cols(u)], out_tile(u),
                                      o_hi[:, 0:MT, out_cols(u)].bitcast(F32), ALU.subtract).then_inc(lo_ready, 1)

                maxima(0)
                for u in range(units):
                    if u + 1 < units:
                        maxima(u + 1)
                    dve.wait_ge(p_ready, u + 1)
                    dve.reciprocal(rec[:, u % 2, :], sums[:, u % 2, :]).then_inc(rec_ready, 1)
                    dve.wait_ge(rec_ready, u + 1)
                    dve.tensor_tensor(prob[:, u % 2], prob[:, u % 2],
                                      rec[:, u % 2, :].rearrange("p (n o) -> p n o", o=1).to_broadcast(
                                          [P, 4, MEM_TOKENS]), ALU.mult).then_inc(scaled, 1)
                    dve.wait_ge(t_ready, 2 * u + 2)
                    if u >= 2:
                        dve.wait_ge(pv_ready, u - 1)
                    dve.tensor_copy(probt[:, u % 2, 4:8, :].rearrange("p a c -> p (a c)"), t_ps[:, 1, :]
                                    ).then_inc(pt_dve, 1)
                    if u:
                        rest(u - 1)
                rest(units - 1)

            @block.tensor
            def _(pe):
                def head_rows(h):
                    return slice((h % 2) * HEAD_DIM, (h % 2 + 1) * HEAD_DIM)

                def scores(u):
                    if u >= 2:
                        pe.wait_ge(p_ready, u - 1)
                    if u == prompt_units // 2:
                        pe.wait_ge(pack_lo, 3)
                    for n in range(4):
                        at = s_ps[:, 2 * (u % 2) + n // 2, (n % 2) * MEM_TOKENS:(n % 2 + 1) * MEM_TOKENS]
                        if u < prompt_units:
                            turn = qh[:, n, u * P:(u + 1) * P]
                            pe.matmul(at, turn, k_hi[:, n, :], start=True, stop=False)
                            mm = pe.matmul(at, turn, k_lo[:, n, :], start=False, stop=True)
                            continue
                        b = (u - prompt_units) * 4 + n
                        for h in range(MEM_HEADS):
                            mm = pe.matmul(at[h * PADQ:(h + 1) * PADQ], qp[head_rows(h), h // 2, b, :],
                                           kvs[head_rows(h), b, h // 2, :], start=True, stop=True)
                    mm.then_inc(s_ready, 1)

                def values(u):
                    pe.wait_ge(pt_act, u + 1)
                    pe.wait_ge(pt_dve, u + 1)
                    if u >= 2:
                        pe.wait_ge(lo_ready, u - 1)
                    for pair in range(MEM_HEADS // 2):
                        heads = (2 * pair, 2 * pair + 1)
                        if u < prompt_units:
                            for m in range(MT):
                                for h in heads:
                                    hc = slice(h * HEAD_DIM, (h + 1) * HEAD_DIM)
                                    mm = pe.matmul(o_ps[head_rows(h), u % 2, pair * P:(pair + 1) * P], v[:, m, hc],
                                                   probt[:, u % 2, 2 * h + m, :], start=m == 0, stop=m == MT - 1)
                            continue
                        for n in range(4):
                            b = (u - prompt_units) * 4 + n
                            c = pair * P + n * DEC_SEQ
                            for m in range(MT):
                                for h in heads:
                                    hc = slice(h * HEAD_DIM, (h + 1) * HEAD_DIM)
                                    mm = pe.matmul(o_ps[head_rows(h), u % 2, c:c + DEC_SEQ], kvs[:, b, 2 + m, hc],
                                                   probt[:, u % 2, 2 * n + m, h * PADQ:h * PADQ + DEC_SEQ],
                                                   start=m == 0, stop=m == MT - 1)
                    mm.then_inc(pv_ready, 1)

                pe.wait_ge(pack_lo, 2)
                scores(0)
                scores(1)
                pe.wait_ge(landed, 48)
                pe.wait_ge(pad_ready, 1 + MT)
                for u in range(units):
                    pe.wait_ge(scaled, u + 1)
                    if u:
                        pe.wait_ge(pt_act, u)
                        pe.wait_ge(pt_dve, u)
                    for n in range(4):
                        for m in range(MT):
                            mm = pe.transpose(t_ps[:, n // 2, ((n % 2) * MT + m) * P:((n % 2) * MT + m + 1) * P],
                                              prob[:, u % 2, n, m * P:(m + 1) * P], core.ident[:])
                        if n % 2:
                            mm.then_inc(t_ready, 1)
                    if u + 2 < units:
                        scores(u + 2)
                    if u:
                        values(u - 1)
                values(units - 1)


GAINS = ("norm_ffn1", "norm_mix", "norm_mem_q", "norm_mem_kv", "norm_ffn2", "norm_final")


def wait_stage(core, sem):
    with core.nc.Block() as block:

        @block.sync
        def _(sp):
            sp.wait_ge(sem, 16)


def load_stage(core, pairs, dram_pairs=()):
    landed, copied = core.sem("inputs_landed"), core.sem("dram_copied")
    with core.nc.Block() as block:

        @block.sync
        def _(sp):
            for dst, src in pairs:
                sp.dma_start(dst, src).then_inc(landed, 16)
            for dst, src in dram_pairs:
                sp.dma_start(dst, src).then_inc(copied, 16)
            sp.wait_ge(landed, 16 * len(pairs))
            if dram_pairs:
                sp.wait_ge(copied, 16 * len(dram_pairs))


def trunk(nc, i, o):
    with ExitStack() as ctx:
        core = Core(nc, ctx)
        sb = lambda stack, name, shape, dt=F32: stack.enter_context(nc.sbuf_tensor(name, shape, dt))
        n_pool = i["slc_pages"].shape[0]
        rows = nc.dram_tensor("scratch_bias_rows", (NSA_HEADS + 1, P, ROW_LEN), F32, kind="Internal").ap()
        gates_dram = nc.dram_tensor("scratch_gates", (NEW, 3 * NSA_HEADS), F32, kind="Internal").ap()
        q_mem = nc.dram_tensor("scratch_mem_q", (MT, P, TP), F32, kind="Internal").ap()
        consts_stage(core, i["consts"])
        gains = sb(ctx, "gains", [P, len(GAINS), KT])
        inner_gains = sb(ctx, "inner_gains", [P, 2 * 4])
        gain = {name: gains[:, n, :] for n, name in enumerate(GAINS)}
        x = sb(ctx, "x", [P, KT, TP])
        def split(stack, name, tiles=KT):
            return [sb(stack, f"{name}_{part}", [P, tiles, TP], F32R) for part in ("hi", "lo")]

        model = ((0, KT, core.mean_model),)

        x_landed, win_copied = (nc.alloc_semaphore(name=name) for name in ("x_landed", "window_rows_copied"))
        with ExitStack() as c:
            h_hi, h_lo = split(c, "h_ffn1")
            with ExitStack() as c2:
                mem = sb(c2, "mem", [P, KT, MEM_TOKENS])
                load_stage(core, [(gains[:], i["gains"]), (inner_gains[:], i["inner_gains"]), (mem[:], i["mem"])])
                norm_stage(core, mem, gain["norm_mem_kv"], core.mean_model, h_hi, h_lo, "norm_mem_kv",
                           width=MEM_TOKENS, parts=1)
                mem_kv_stage(core, h_hi, h_lo, i["w_mem_kv"], o["mem_kt"], o["mem_v"],
                             later=[(x[:], i["x"], x_landed), (o["win_old"], i["win_rows"], win_copied)])
            bias_rows_stage(core, i["rel_bias"], i["bucket_rows"], rows)
            core.clear_sems()
            wait_stage(core, x_landed)
            ffn_stage(core, x, gain["norm_ffn1"], h_hi, h_lo, i["w_ffn1_in"], i["w_ffn1_out"], "ffn1")
        core.clear_sems()
        with ExitStack() as c:
            mixed = sb(c, "mixed", [P, 2 * 4, TP])
            with ExitStack() as c1:
                nat = sb(c1, "nat", [P, TOK_TILES, NAT])
                with ExitStack() as c2:
                    h_hi, h_lo = split(c2, "h_mix")
                    gemm_stage(core, h_hi, h_lo, i["w_mix"], KT, 20, "mix", store=o["proj"],
                               norm_of=(x, gain["norm_mix"], model))
                    natural_stage(core, h_hi, h_lo, i["w_nat"], nat, "nat")
                with ExitStack() as c2:
                    xc = sb(c2, "xc", [P, XBC, TOKENS])
                    y = mixed[:, 0:4, :]
                    conv_stage(core, o["proj"], i["conv_state"], i["conv_w"], i["conv_b"], xc, y)
                    ssd_stage(core, nat, xc, i["dt_bias"], i["a_log"], i["d_skip"], i["ssd_state"], y,
                              o["ssd_p"], o["ssd_s"])
                core.clear_sems()
                kc, vc = sb(c1, "kc", [P, SEQS * N_CMP]), sb(c1, "vc", [P, SEQS * 2 * HEAD_DIM])
                compress_stage(core, o["proj"], i["cmp_pages"], i["page_table"],
                               *([i[f"{name}_{kv}"] for kv in range(2)] for name in ("cmp_w1", "cmp_w2", "cmp_pos")),
                               kc, vc, mixed[:, 4:8, :].rearrange("p i t -> p (i t)"), n_pool)
                core.clear_sems()
                o_t = mixed[:, 4:8, :]
                prompt_nsa_stage(core, nat, kc, vc, o["proj"], rows, o_t)
                sample_nsa_stage(core, nat, kc, vc, o["proj"], rows, i["rules"], i["page_table"],
                                 i["slc_pages"], i["win_kv"], gates_dram, o_t, n_pool)
                core.clear_sems()
                load_stage(core, [], [(o["v_rows"], nat[:, :, 0:2 * P])])
            h_hi, h_lo = split(c, "h_out")
            gemm_stage(core, h_hi, h_lo, i["w_out"], KT, KT, "wout", add_to=x,
                       norm_of=(mixed, inner_gains, ((0, 4, core.mean_inner), (4, 4, core.mean_inner))))
        with ExitStack() as c:
            h_hi, h_lo = split(c, "h")
            gemm_stage(core, h_hi, h_lo, i["w_mem_q"], KT, MT, "memq", store=q_mem,
                       norm_of=(x, gain["norm_mem_q"], model))
            mem_attend_stage(core, q_mem, o["mem_kt"], o["mem_v"], i["mem_kv_sample"], h_hi, h_lo)
            gemm_stage(core, h_hi, h_lo, i["w_mem_out"], MT, KT, "memout", add_to=x)
            core.clear_sems()
            ffn_stage(core, x, gain["norm_ffn2"], h_hi, h_lo, i["w_ffn2_in"], i["w_ffn2_out"], "ffn2")
        final_norm_stage(core, x, gain["norm_final"], sb(ctx, "y", [P, KT, TP]), o["y"])
        wait_stage(core, win_copied)



def lay_tokens(*parts):
    t = np.concatenate([a.reshape(-1, a.shape[-1]) for a in parts])
    return np.ascontiguousarray(t.T.reshape(-1, P, t.shape[0]).transpose(1, 0, 2))


def lay_tiles(w):
    k = w.shape[0] // P
    return np.ascontiguousarray(w.reshape(k, P, -1, P).transpose(2, 1, 0, 3)).reshape(-1, P, k * P)


def lay_ffn_in(w):
    return np.ascontiguousarray(w.reshape(KT, P, 2, FT, P).transpose(3, 1, 2, 0, 4)).reshape(FT, P, 2 * KT * P)


def lay_ffn_out(w):
    return np.ascontiguousarray(w.reshape(FT // 2, 2, P, D_MODEL).transpose(0, 2, 1, 3))


def group_major():
    f = np.arange(INNER).reshape(KV_GROUPS, GROUP_HEADS, HEAD_DIM)
    return f.transpose(1, 0, 2).reshape(-1)


Z0, XBC0, DT0 = 0, INNER, INNER + XBC * P
Q0 = DT0 + SSD_HEADS
KV0 = Q0 + INNER
GL0 = KV0 + 6 * P


def kernel(x_prompt, x_sample, cache_kv_cmp, cache_kv_slc, state_win_kv, state_ssd, state_conv, cache_mem_kv,
           page_table, mem_prompt, norm_ffn1, w_ffn1_in, w_ffn1_out, norm_mix, w_in, conv_w, conv_b, dt_bias,
           a_log, d_skip, norm_ssd_out, cmp_pos_k, cmp_w1_k, cmp_w2_k, cmp_pos_v, cmp_w1_v, cmp_w2_v,
           norm_nsa_out, w_out, norm_mem_q, norm_mem_kv, w_mem_q, w_mem_kv, w_mem_out, norm_ffn2, w_ffn2_in,
           w_ffn2_out, rel_bias, norm_final):
    import concourse.bacc as bacc
    from concourse.bass_utils import run_bass_kernel_spmd

    a = np.asarray
    per_tile = lambda g: np.ascontiguousarray(a(g).reshape(-1, P).T)
    spread = lambda v: np.ascontiguousarray(np.broadcast_to(a(v), (P, SSD_HEADS)))
    order = group_major()
    w = a(w_in)[0]
    kv_cols = [np.arange(KV0 + n * P, KV0 + (n + 1) * P) for n in range(6)]
    mix = np.concatenate([np.arange(Z0, DT0), Q0 + order, kv_cols[0], kv_cols[1], kv_cols[2], kv_cols[4]])
    natural = np.concatenate([kv_cols[3], kv_cols[5], np.arange(DT0, Q0), np.arange(GL0, w.shape[1])])
    pad = np.zeros((TP - TOKENS, D_MODEL), np.float32)
    mem_kv = a(cache_mem_kv)[0]
    mem_k = mem_kv[:, :, 0].reshape(DEC_BATCH, MEM_TOKENS, MT, P).transpose(3, 0, 2, 1)
    mem_v = mem_kv[:, :, 1].reshape(DEC_BATCH, MT, P, MI).transpose(2, 0, 1, 3)
    ins = {
        "x": lay_tokens(a(x_prompt), a(x_sample), pad),
        "mem": lay_tokens(a(mem_prompt)),
        "gains": np.ascontiguousarray(np.stack([per_tile(g) for g in (
            norm_ffn1, norm_mix, norm_mem_q, norm_mem_kv, norm_ffn2, norm_final)], axis=1)),
        "inner_gains": np.ascontiguousarray(np.concatenate([per_tile(norm_ssd_out),
                                                      per_tile(a(norm_nsa_out)[0][order])], axis=1)),
        "consts": make_consts(), "rules": make_rules(), "bucket_rows": make_bucket_rows(),
        "rel_bias": np.ascontiguousarray(a(rel_bias)),
        "w_ffn1_in": lay_ffn_in(a(w_ffn1_in)[0]), "w_ffn1_out": lay_ffn_out(a(w_ffn1_out)[0]),
        "w_ffn2_in": lay_ffn_in(a(w_ffn2_in)[0]), "w_ffn2_out": lay_ffn_out(a(w_ffn2_out)[0]),
        "w_mix": lay_tiles(w[:, mix]),
        "w_nat": np.ascontiguousarray(w[:, natural].reshape(KT, P, NAT).transpose(1, 0, 2)),
        "w_out": lay_tiles(a(w_out)[0][np.concatenate([np.arange(INNER), INNER + order])]),
        "w_mem_q": lay_tiles(a(w_mem_q)[0]), "w_mem_out": lay_tiles(a(w_mem_out)[0]),
        "w_mem_kv": np.ascontiguousarray(a(w_mem_kv)[0].reshape(KT, P, 2 * MI).transpose(1, 0, 2)),
        "conv_state": lay_conv_state(a(state_conv)), "conv_w": lay_conv_w(a(conv_w)), "conv_b": per_tile(conv_b),
        "dt_bias": spread(dt_bias), "a_log": spread(a_log), "d_skip": lay_d_skip(a(d_skip)),
        "ssd_state": lay_state(a(state_ssd)),
        "page_table": np.ascontiguousarray(a(page_table).reshape(1, -1)),
        "cmp_pages": lay_cmp_pages(a(cache_kv_cmp)), "slc_pages": lay_slc_pages(a(cache_kv_slc)),
        "win_kv": lay_win(a(state_win_kv)),
        "win_rows": np.ascontiguousarray(a(state_win_kv)[0, :, DEC_SEQ:].reshape(DEC_BATCH, -1)),
        "mem_kv_sample": np.ascontiguousarray(np.concatenate([mem_k, mem_v], axis=2)),
    }
    for kv, (pos, w1, w2) in enumerate(((cmp_pos_k, cmp_w1_k, cmp_w2_k), (cmp_pos_v, cmp_w1_v, cmp_w2_v))):
        ins[f"cmp_pos_{kv}"], ins[f"cmp_w1_{kv}"] = lay_cmp_pos(a(pos)), lay_cmp_w1(a(w1))
        ins[f"cmp_w2_{kv}"] = lay_cmp_w2(a(w2))
    outs = {
        "y": (P, KT, TP), "proj": (20, P, TP), "v_rows": (P, TOK_TILES, 2 * P),
        "ssd_p": (P, INNER), "ssd_s": (P, DEC_BATCH, INNER),
        "mem_kt": (P, MT, MEM_TOKENS), "mem_v": (P, MT, MI),
        "win_old": (DEC_BATCH, (WINDOW - DEC_SEQ) * 4 * HEAD_DIM),
    }
    nc = bacc.Bacc("TRN2", target_bir_lowering=False, num_devices=1)
    i = {k: nc.dram_tensor(f"in_{k}", v.shape, mybir.dt.from_np(v.dtype), kind="ExternalInput").ap()
         for k, v in ins.items()}
    o = {k: nc.dram_tensor(f"out_{k}", s, F32, kind="ExternalOutput").ap() for k, s in outs.items()}
    trunk(nc, i, o)
    r = run_bass_kernel_spmd(nc, [{f"in_{k}": v for k, v in ins.items()}], core_ids=[0]).results[0]
    r = {k: a(r[f"out_{k}"]) for k in outs}

    y = r["y"].transpose(1, 0, 2).reshape(D_MODEL, TP).T
    proj = r["proj"].transpose(0, 2, 1)
    v = r["v_rows"].transpose(1, 0, 2).reshape(-1, 2 * P)
    kc, vc, ks, kw = (proj[KV_TILE0 + n] for n in range(4))
    vs, vw = v[:TP, :P], v[:TP, P:]
    heads = (KV_GROUPS, HEAD_DIM)

    def rows_p(k, v_, first=0):
        return np.stack([k[first:SEQ].reshape(1, -1, *heads), v_[first:SEQ].reshape(1, -1, *heads)], axis=2)[None]

    def rows_s(k, v_):
        return np.stack([k[SEQ:TOKENS].reshape(DEC_BATCH, DEC_SEQ, *heads),
                         v_[SEQ:TOKENS].reshape(DEC_BATCH, DEC_SEQ, *heads)], axis=2)[None]

    xbc = proj[XBC_TILE0:XBC_TILE0 + XBC].transpose(1, 0, 2).reshape(TP, -1)
    pad = TAPS - 1
    mem_k = r["mem_kt"].transpose(1, 0, 2).reshape(MI, MEM_TOKENS).T.reshape(MEM_TOKENS, MEM_HEADS, HEAD_DIM)
    mem_v = r["mem_v"].transpose(1, 0, 2).reshape(MEM_TOKENS, MEM_HEADS, HEAD_DIM)
    win_old = r["win_old"].reshape(1, DEC_BATCH, WINDOW - DEC_SEQ, 2, *heads)
    c = np.ascontiguousarray
    return (
        c(y[:SEQ]).reshape(1, SEQ, D_MODEL), c(y[SEQ:TOKENS]).reshape(DEC_BATCH, DEC_SEQ, D_MODEL),
        c(rows_p(kc, vc)), c(rows_p(ks, vs)), c(rows_p(kw, vw, SEQ - WINDOW)),
        c(r["ssd_p"].reshape(P, SSD_HEADS, HEAD_DIM).transpose(1, 2, 0))[None, None],
        c(xbc[SEQ - pad:SEQ])[None, None],
        c(np.stack([mem_k, mem_v], axis=1))[None, None],
        c(rows_s(kc, vc)), c(rows_s(ks, vs)),
        c(np.concatenate([win_old, rows_s(kw, vw)], axis=2)),
        c(r["ssd_s"].reshape(P, DEC_BATCH, SSD_HEADS, HEAD_DIM).transpose(1, 2, 3, 0))[None],
        c(xbc[SEQ:TOKENS].reshape(DEC_BATCH, DEC_SEQ, -1)[:, DEC_SEQ - pad:])[None],
    )
```
